# Optimizing a Trainium2 kernel written in Bass

```python
import jax, jax.numpy as jnp
from jax import lax
import numpy as np
import math

D_MODEL = 1024
BATCH = 1
SEQ = 256
DEPTH = 2

CHUNK = 64
EPS = 1e-6
GMLP_BLOCK = 128
A_HEADS = 4
A_WIDTH = D_MODEL // 2
A_HEAD_DIM = A_WIDTH // A_HEADS
POOL_WINDOWS = (2, 4, 8, 16)
B_GROUPS = len(POOL_WINDOWS)
B_WIDTH = D_MODEL // 2
B_GROUP_DIM = B_WIDTH // B_GROUPS
AB_IN_WIDTH = 2 * A_WIDTH + B_WIDTH
AB_OUT_WIDTH = A_WIDTH + B_WIDTH
RWKV_HEAD_DIM = 64
RWKV_HEADS = D_MODEL // RWKV_HEAD_DIM
DECAY_RANK = max(32, round(1.8 * D_MODEL ** 0.5 / 32) * 32)
AAA_RANK = max(32, round(1.8 * D_MODEL ** 0.5 / 32) * 32)
MV_RANK = max(32, round(1.3 * D_MODEL ** 0.5 / 32) * 32)
GATE_RANK = max(32, round(0.6 * D_MODEL ** 0.8 / 32) * 32)
GN_EPS = 64e-5
FFN_HIDDEN = ((8 * D_MODEL // 3 + 255) // 256) * 256
N_EVEN = (DEPTH + 1) // 2
N_ODD = DEPTH // 2


def rms_norm(x, g):
    xf = x.astype(jnp.float32)
    y = xf * lax.rsqrt(jnp.mean(xf * xf, axis=-1, keepdims=True) + EPS)
    return (y * g.astype(jnp.float32)).astype(x.dtype)

def gmlp_spatial_gate(u, v, sgu_gain, w_s, b_s):
    bsz, seq, _ = u.shape
    v = rms_norm(v, sgu_gain)
    v = v.reshape(bsz, seq // GMLP_BLOCK, GMLP_BLOCK, A_HEADS, A_HEAD_DIM)
    chunk_id = jnp.arange(GMLP_BLOCK) // CHUNK
    mask = chunk_id[:, None] >= chunk_id[None, :]
    w = jnp.where(mask[None], w_s, 0)
    mixed = jnp.einsum('hij,bnjhd->bnihd', w, v) + b_s.T[None, None, :, :, None]
    return u * mixed.reshape(bsz, seq, A_WIDTH)

def multiscale_pool(z, w_pool, pool_scale):
    bsz, seq, _ = z.shape
    zf = z.astype(jnp.float32).reshape(bsz, seq, B_GROUPS, B_GROUP_DIM)
    csum = jnp.cumsum(zf, axis=1)
    t = jnp.arange(seq)
    means = []
    for gi, win in enumerate(POOL_WINDOWS):
        cg = csum[:, :, gi]
        prev = jnp.pad(cg, ((0, 0), (win, 0), (0, 0)))[:, :seq]
        count = jnp.minimum(t + 1, win).astype(jnp.float32)[None, :, None]
        means.append((cg - prev) / count)
    pooled = (jnp.stack(means, axis=2) - zf).astype(z.dtype)
    y = jnp.einsum('bsgc,gcd->bsgd', pooled, w_pool).reshape(bsz, seq, B_WIDTH)
    return y * pool_scale

def hybrid_ab_mixer(hn, w_in, w_out, sgu_gain, sgu_w_s, sgu_bias, pool_w, pool_scale):
    z = hn @ w_in
    za = jax.nn.gelu(z[..., :2 * A_WIDTH], approximate=False)
    y_a = gmlp_spatial_gate(za[..., :A_WIDTH], za[..., A_WIDTH:], sgu_gain, sgu_w_s, sgu_bias)
    y_b = multiscale_pool(z[..., 2 * A_WIDTH:], pool_w, pool_scale)
    return jnp.concatenate([y_a, y_b], axis=-1) @ w_out

def wkv7_scan(r, w, k, v, a, b):
    bsz, _, nh, n = r.shape
    xs = tuple(jnp.moveaxis(t, 1, 0) for t in (r, w, k, v, a, b))

    def step(state, inp):
        r_t, w_t, k_t, v_t, a_t, b_t = inp
        sa = jnp.einsum('bhvk,bhk->bhv', state, a_t)
        state = (state * w_t[:, :, None, :] + sa[..., None] * b_t[:, :, None, :]
                 + v_t[..., None] * k_t[:, :, None, :])
        return state, jnp.einsum('bhvk,bhk->bhv', state, r_t)

    s0 = jnp.zeros((bsz, nh, n, n), jnp.float32)
    _, ys = lax.scan(step, s0, xs)
    return jnp.moveaxis(ys, 0, 1)

def rwkv7_time_mix(h, mu, w_r, w_k, w_v, w_o, w0, w1, w2, a0, a1, a2, g1, g2,
                   k_k, k_a, r_k, ln_w, ln_b, v_first, vres):
    bsz, seq, d = h.shape
    f32 = jnp.float32
    xx = jnp.pad(h, ((0, 0), (1, 0), (0, 0)))[:, :-1] - h
    xr, xw, xk, xv, xa, xg = [h + xx * mu[i] for i in range(6)]
    r = xr @ w_r
    wlog = -jax.nn.softplus(-(w0 + jnp.tanh(xw @ w1) @ w2).astype(f32)) - 0.5
    k = xk @ w_k
    v = xv @ w_v
    if vres is None:
        v_first = v
    else:
        v0, v1, v2 = vres
        v = v + (v_first - v) * jax.nn.sigmoid(v0 + (xv @ v1) @ v2)
    a = jax.nn.sigmoid(a0 + (xa @ a1) @ a2)
    g = jax.nn.sigmoid(xg @ g1) @ g2

    def heads(t):
        return t.reshape(bsz, seq, RWKV_HEADS, RWKV_HEAD_DIM).astype(f32)

    kk = heads(k * k_k)
    kk = kk / jnp.maximum(jnp.sqrt(jnp.sum(kk * kk, axis=-1, keepdims=True)), 1e-12)
    k = k * (1 + (a - 1) * k_a)
    rh, kh, vh, ah = heads(r), heads(k), heads(v), heads(a)
    decay = heads(jnp.exp(-jnp.exp(wlog)))
    y = wkv7_scan(rh, decay, kh, vh, -kk, kk * ah)
    mean = jnp.mean(y, axis=-1, keepdims=True)
    var = jnp.mean(jnp.square(y - mean), axis=-1, keepdims=True)
    y = ((y - mean) * lax.rsqrt(var + GN_EPS)).reshape(bsz, seq, d)
    y = y * ln_w.astype(f32) + ln_b.astype(f32)
    bonus = jnp.sum(rh * kh * r_k.astype(f32), axis=-1, keepdims=True) * vh
    y = (y + bonus.reshape(bsz, seq, d)).astype(h.dtype)
    return (y * g) @ w_o, v_first

def swiglu(hn, w_gate, w_up, w_down):
    return (jax.nn.silu(hn @ w_gate) * (hn @ w_up)) @ w_down

def first_inputs(seed: int = 0) -> dict:
    key = jax.random.key(seed)
    ks = iter(jax.random.split(key, 48))
    D = D_MODEL

    def nrm(shape, scale):
        return scale * jax.random.normal(next(ks), shape, jnp.float32)

    def uni(shape, lo, hi):
        return jax.random.uniform(next(ks), shape, jnp.float32, lo, hi)

    nv = max(N_ODD - 1, 0)
    return {
        "x": nrm((BATCH, SEQ, D), 1.0),
        "mix_norm": 1.0 + nrm((DEPTH, D), 0.02),
        "ffn_norm": 1.0 + nrm((DEPTH, D), 0.02),
        "final_norm": 1.0 + nrm((D,), 0.02),
        "ab_w_in": nrm((N_EVEN, D, AB_IN_WIDTH), D ** -0.5),
        "ab_w_out": nrm((N_EVEN, AB_OUT_WIDTH, D), AB_OUT_WIDTH ** -0.5),
        "sgu_gain": 1.0 + nrm((N_EVEN, A_WIDTH), 0.02),
        "sgu_w_s": nrm((N_EVEN, A_HEADS, GMLP_BLOCK, GMLP_BLOCK), GMLP_BLOCK ** -0.5),
        "sgu_bias": 1.0 + nrm((N_EVEN, A_HEADS, GMLP_BLOCK), 0.1),
        "pool_w": nrm((N_EVEN, B_GROUPS, B_GROUP_DIM, B_GROUP_DIM), B_GROUP_DIM ** -0.5),
        "pool_scale": 0.5 + nrm((N_EVEN, B_WIDTH), 0.1),
        "rwkv_mu": uni((N_ODD, 6, D), 0.0, 1.0),
        "rwkv_w_r": nrm((N_ODD, D, D), D ** -0.5),
        "rwkv_w_k": nrm((N_ODD, D, D), D ** -0.5),
        "rwkv_w_v": nrm((N_ODD, D, D), D ** -0.5),
        "rwkv_w_o": nrm((N_ODD, D, D), D ** -0.5),
        "rwkv_w0": uni((N_ODD, D), -6.0, 0.0),
        "rwkv_w1": nrm((N_ODD, D, DECAY_RANK), D ** -0.5),
        "rwkv_w2": nrm((N_ODD, DECAY_RANK, D), 0.1 * DECAY_RANK ** -0.5),
        "rwkv_a0": nrm((N_ODD, D), 0.1),
        "rwkv_a1": nrm((N_ODD, D, AAA_RANK), D ** -0.5),
        "rwkv_a2": nrm((N_ODD, AAA_RANK, D), 0.1 * AAA_RANK ** -0.5),
        "rwkv_g1": nrm((N_ODD, D, GATE_RANK), D ** -0.5),
        "rwkv_g2": nrm((N_ODD, GATE_RANK, D), GATE_RANK ** -0.5),
        "rwkv_k_k": 0.85 + nrm((N_ODD, D), 0.05),
        "rwkv_k_a": 1.0 + nrm((N_ODD, D), 0.05),
        "rwkv_r_k": nrm((N_ODD, RWKV_HEADS, RWKV_HEAD_DIM), 0.1),
        "rwkv_ln_w": 1.0 + nrm((N_ODD, D), 0.05),
        "rwkv_ln_b": nrm((N_ODD, D), 0.02),
        "rwkv_v0": nrm((nv, D), 0.5),
        "rwkv_v1": nrm((nv, D, MV_RANK), D ** -0.5),
        "rwkv_v2": nrm((nv, MV_RANK, D), 0.1 * MV_RANK ** -0.5),
        "ffn_w_gate": nrm((DEPTH, D, FFN_HIDDEN), D ** -0.5),
        "ffn_w_up": nrm((DEPTH, D, FFN_HIDDEN), D ** -0.5),
        "ffn_w_down": nrm((DEPTH, FFN_HIDDEN, D), FFN_HIDDEN ** -0.5),
    }

def first_block(x, mix_norm, ffn_norm, final_norm, ab_w_in, ab_w_out, sgu_gain, sgu_w_s,
              sgu_bias, pool_w, pool_scale, rwkv_mu, rwkv_w_r, rwkv_w_k, rwkv_w_v,
              rwkv_w_o, rwkv_w0, rwkv_w1, rwkv_w2, rwkv_a0, rwkv_a1, rwkv_a2, rwkv_g1,
              rwkv_g2, rwkv_k_k, rwkv_k_a, rwkv_r_k, rwkv_ln_w, rwkv_ln_b, rwkv_v0,
              rwkv_v1, rwkv_v2, ffn_w_gate, ffn_w_up, ffn_w_down):
    h = x
    v_first = None
    for layer in range(DEPTH):
        hn = rms_norm(h, mix_norm[layer])
        i = layer // 2
        if layer % 2 == 0:
            h = h + hybrid_ab_mixer(hn, ab_w_in[i], ab_w_out[i], sgu_gain[i], sgu_w_s[i],
                                    sgu_bias[i], pool_w[i], pool_scale[i])
        else:
            vres = None if i == 0 else (rwkv_v0[i - 1], rwkv_v1[i - 1], rwkv_v2[i - 1])
            y, v_first = rwkv7_time_mix(
                hn, rwkv_mu[i], rwkv_w_r[i], rwkv_w_k[i], rwkv_w_v[i], rwkv_w_o[i],
                rwkv_w0[i], rwkv_w1[i], rwkv_w2[i], rwkv_a0[i], rwkv_a1[i], rwkv_a2[i],
                rwkv_g1[i], rwkv_g2[i], rwkv_k_k[i], rwkv_k_a[i], rwkv_r_k[i],
                rwkv_ln_w[i], rwkv_ln_b[i], v_first, vres)
            h = h + y
        h = h + swiglu(rms_norm(h, ffn_norm[layer]), ffn_w_gate[layer], ffn_w_up[layer],
                       ffn_w_down[layer])
    return rms_norm(h, final_norm)


DEPTH_2 = 1

CONV_DIM = 1024
CONV_KERNEL = 31
N_HEADS = 8
QK_NOPE_DIM = 128
QK_ROPE_DIM = 64
V_HEAD_DIM = 128
Q_LORA_RANK = 384
KV_LORA_RANK = 256
ROPE_THETA = 10000.0
Q_BLOCK = 128
D_FF = 4 * D_MODEL
N_BRANCHES = 2

IN_WIDTHS = (2 * CONV_DIM, Q_LORA_RANK, KV_LORA_RANK, QK_ROPE_DIM, N_BRANCHES * D_MODEL)
IN_DIM = sum(IN_WIDTHS)
IN_SPLIT = tuple(int(v) for v in np.cumsum(IN_WIDTHS)[:-1])


def rms_norm_2(x, g):
    xf = x.astype(jnp.float32)
    y = xf * lax.rsqrt(jnp.mean(xf * xf, axis=-1, keepdims=True) + EPS)
    return (y * g.astype(jnp.float32)).astype(x.dtype)

def layer_norm(x, g, b):
    xf = x.astype(jnp.float32)
    mu = jnp.mean(xf, axis=-1, keepdims=True)
    var = jnp.mean(jnp.square(xf - mu), axis=-1, keepdims=True)
    y = (xf - mu) * lax.rsqrt(var + EPS)
    return (y * g.astype(jnp.float32) + b.astype(jnp.float32)).astype(x.dtype)

def rope_tables(positions):
    inv_freq = 1.0 / (ROPE_THETA ** (jnp.arange(0, QK_ROPE_DIM, 2, dtype=jnp.float32) / QK_ROPE_DIM))
    ang = positions.astype(jnp.float32)[..., None] * inv_freq
    return jnp.cos(ang), jnp.sin(ang)

def apply_rope(t, cos, sin):
    t1, t2 = jnp.split(t, 2, axis=-1)
    cos = cos.astype(t.dtype)
    sin = sin.astype(t.dtype)
    return jnp.concatenate([t1 * cos - t2 * sin, t2 * cos + t1 * sin], axis=-1)

def causal_depthwise_conv(u, w, b):
    return lax.conv_general_dilated(
        u, w[:, None, :].astype(u.dtype), window_strides=(1,),
        padding=[(CONV_KERNEL - 1, 0)],
        dimension_numbers=("NWC", "WIO", "NWC"),
        feature_group_count=CONV_DIM) + b

def mla_attention(q_nope, q_rope, k_nope, k_rope, v):
    b, s, h, _ = q_nope.shape
    nb = s // Q_BLOCK
    scale = 1.0 / math.sqrt(QK_NOPE_DIM + QK_ROPE_DIM)
    qn = jnp.moveaxis(q_nope.reshape(b, nb, Q_BLOCK, h, QK_NOPE_DIM), 1, 0)
    qr = jnp.moveaxis(q_rope.reshape(b, nb, Q_BLOCK, h, QK_ROPE_DIM), 1, 0)
    k_idx = jnp.arange(s)

    def one_block(args):
        qn_b, qr_b, blk = args
        sc = (jnp.einsum("bqhd,bkhd->bhqk", qn_b, k_nope)
              + jnp.einsum("bqhr,bkr->bhqk", qr_b, k_rope)).astype(jnp.float32) * scale
        q_idx = blk * Q_BLOCK + jnp.arange(Q_BLOCK)
        causal = q_idx[:, None] >= k_idx[None, :]
        sc = jnp.where(causal[None, None], sc, -1e30)
        p = jax.nn.softmax(sc, axis=-1).astype(v.dtype)
        return jnp.einsum("bhqk,bkhd->bqhd", p, v)

    out = lax.map(one_block, (qn, qr, jnp.arange(nb)))
    return jnp.moveaxis(out, 0, 1).reshape(b, s, h * V_HEAD_DIM)

def token_mixer(h, cos, sin, w_in, conv_w, conv_b, conv_norm_g, conv_norm_b, w_conv_out,
                q_norm_g, w_uq, kv_norm_g, w_ukv, w_attn_out, w_out):
    b, s, _ = h.shape
    z = h @ w_in
    u_glu, q_lat, kv_lat, k_r, gate_logits = jnp.split(z, IN_SPLIT, axis=-1)

    ua, ub = jnp.split(u_glu, 2, axis=-1)
    u = ua * jax.nn.sigmoid(ub)
    u = causal_depthwise_conv(u, conv_w, conv_b)
    u = jax.nn.silu(layer_norm(u, conv_norm_g, conv_norm_b))
    y_a = u @ w_conv_out

    q = (rms_norm_2(q_lat, q_norm_g) @ w_uq).reshape(b, s, N_HEADS, QK_NOPE_DIM + QK_ROPE_DIM)
    q_nope, q_rope = jnp.split(q, [QK_NOPE_DIM], axis=-1)
    q_rope = apply_rope(q_rope, cos[:, :, None, :], sin[:, :, None, :])
    kv = (rms_norm_2(kv_lat, kv_norm_g) @ w_ukv).reshape(b, s, N_HEADS, QK_NOPE_DIM + V_HEAD_DIM)
    k_nope, v = jnp.split(kv, [QK_NOPE_DIM], axis=-1)
    k_rope = apply_rope(k_r, cos, sin)
    o = mla_attention(q_nope, q_rope, k_nope, k_rope, v)
    y_b = o @ w_attn_out

    g_a, g_b = jnp.split(jax.nn.sigmoid(gate_logits), N_BRANCHES, axis=-1)
    return (g_a * y_a + g_b * y_b) @ w_out

def second_inputs(seed: int = 0) -> dict:
    key = jax.random.key(seed)
    ks = jax.random.split(key, 32)
    L = DEPTH_2

    def nrm(k, shape, fan_in, mult=1.0):
        return jax.random.normal(k, shape, jnp.float32) * (mult * fan_in ** -0.5)

    def gain(k, shape):
        return 1.0 + 0.05 * jax.random.normal(k, shape, jnp.float32)

    offsets = jax.random.randint(ks[2], (BATCH, 1), 0, 1024, dtype=jnp.int32)
    positions = offsets + jnp.arange(SEQ, dtype=jnp.int32)[None, :]
    return {
        "x": jax.random.normal(ks[0], (BATCH, SEQ, D_MODEL), jnp.float32),
        "c": jax.random.normal(ks[1], (BATCH, D_MODEL), jnp.float32),
        "positions": positions,
        "w_ada": nrm(ks[3], (L, D_MODEL, 6 * D_MODEL), D_MODEL, 0.2),
        "b_ada": 0.01 * jax.random.normal(ks[4], (L, 6 * D_MODEL), jnp.float32),
        "g_pre_mix": gain(ks[5], (L, D_MODEL)),
        "g_post_mix": gain(ks[6], (L, D_MODEL)),
        "g_pre_mlp": gain(ks[7], (L, D_MODEL)),
        "g_post_mlp": gain(ks[8], (L, D_MODEL)),
        "w_in": nrm(ks[9], (L, D_MODEL, IN_DIM), D_MODEL),
        "conv_w": nrm(ks[10], (L, CONV_KERNEL, CONV_DIM), CONV_KERNEL),
        "conv_b": 0.01 * jax.random.normal(ks[11], (L, CONV_DIM), jnp.float32),
        "conv_norm_g": gain(ks[12], (L, CONV_DIM)),
        "conv_norm_b": 0.01 * jax.random.normal(ks[13], (L, CONV_DIM), jnp.float32),
        "w_conv_out": nrm(ks[14], (L, CONV_DIM, D_MODEL), CONV_DIM),
        "q_norm_g": gain(ks[15], (L, Q_LORA_RANK)),
        "w_uq": nrm(ks[16], (L, Q_LORA_RANK, N_HEADS * (QK_NOPE_DIM + QK_ROPE_DIM)), Q_LORA_RANK),
        "kv_norm_g": gain(ks[17], (L, KV_LORA_RANK)),
        "w_ukv": nrm(ks[18], (L, KV_LORA_RANK, N_HEADS * (QK_NOPE_DIM + V_HEAD_DIM)), KV_LORA_RANK),
        "w_attn_out": nrm(ks[19], (L, N_HEADS * V_HEAD_DIM, D_MODEL), N_HEADS * V_HEAD_DIM),
        "w_out": nrm(ks[20], (L, D_MODEL, D_MODEL), D_MODEL),
        "w_mlp_in": nrm(ks[21], (L, D_MODEL, D_FF), D_MODEL),
        "w_mlp_out": nrm(ks[22], (L, D_FF, D_MODEL), D_FF),
    }

def second_block(x, c, positions, w_ada, b_ada, g_pre_mix, g_post_mix, g_pre_mlp, g_post_mlp,
              w_in, conv_w, conv_b, conv_norm_g, conv_norm_b, w_conv_out,
              q_norm_g, w_uq, kv_norm_g, w_ukv, w_attn_out, w_out, w_mlp_in, w_mlp_out):
    cos, sin = rope_tables(positions)
    c_act = jax.nn.silu(c)
    for l in range(DEPTH_2):
        mod = c_act @ w_ada[l] + b_ada[l]
        shift1, scale1, gate1, shift2, scale2, gate2 = [m[:, None, :] for m in jnp.split(mod, 6, axis=-1)]

        h = rms_norm_2(x, g_pre_mix[l]) * (1.0 + scale1) + shift1
        y = token_mixer(h, cos, sin, w_in[l], conv_w[l], conv_b[l], conv_norm_g[l], conv_norm_b[l],
                        w_conv_out[l], q_norm_g[l], w_uq[l], kv_norm_g[l], w_ukv[l],
                        w_attn_out[l], w_out[l])
        x = x + gate1 * rms_norm_2(y, g_post_mix[l])

        h = rms_norm_2(x, g_pre_mlp[l]) * (1.0 + scale2) + shift2
        y = jnp.square(jax.nn.relu(h @ w_mlp_in[l])) @ w_mlp_out[l]
        x = x + gate2 * rms_norm_2(y, g_post_mlp[l])
    return x


def setup_inputs(seed=0):
    out = dict(first_inputs(seed))
    for name, value in second_inputs(seed + 1).items():
        if name != "x":
            out[name + "_2"] = value
    return out


def reference(
    x, mix_norm, ffn_norm, final_norm, ab_w_in, ab_w_out, sgu_gain, sgu_w_s, sgu_bias, pool_w,
    pool_scale, rwkv_mu, rwkv_w_r, rwkv_w_k, rwkv_w_v, rwkv_w_o, rwkv_w0, rwkv_w1, rwkv_w2,
    rwkv_a0, rwkv_a1, rwkv_a2, rwkv_g1, rwkv_g2, rwkv_k_k, rwkv_k_a, rwkv_r_k, rwkv_ln_w,
    rwkv_ln_b, rwkv_v0, rwkv_v1, rwkv_v2, ffn_w_gate, ffn_w_up, ffn_w_down, c_2, positions_2,
    w_ada_2, b_ada_2, g_pre_mix_2, g_post_mix_2, g_pre_mlp_2, g_post_mlp_2, w_in_2, conv_w_2,
    conv_b_2, conv_norm_g_2, conv_norm_b_2, w_conv_out_2, q_norm_g_2, w_uq_2, kv_norm_g_2,
    w_ukv_2, w_attn_out_2, w_out_2, w_mlp_in_2, w_mlp_out_2,
):
    x = first_block(
        x, mix_norm, ffn_norm, final_norm, ab_w_in, ab_w_out, sgu_gain, sgu_w_s, sgu_bias,
        pool_w, pool_scale, rwkv_mu, rwkv_w_r, rwkv_w_k, rwkv_w_v, rwkv_w_o, rwkv_w0, rwkv_w1,
        rwkv_w2, rwkv_a0, rwkv_a1, rwkv_a2, rwkv_g1, rwkv_g2, rwkv_k_k, rwkv_k_a, rwkv_r_k,
        rwkv_ln_w, rwkv_ln_b, rwkv_v0, rwkv_v1, rwkv_v2, ffn_w_gate, ffn_w_up, ffn_w_down,
    )
    return second_block(
        x, c_2, positions_2, w_ada_2, b_ada_2, g_pre_mix_2, g_post_mix_2, g_pre_mlp_2,
        g_post_mlp_2, w_in_2, conv_w_2, conv_b_2, conv_norm_g_2, conv_norm_b_2, w_conv_out_2,
        q_norm_g_2, w_uq_2, kv_norm_g_2, w_ukv_2, w_attn_out_2, w_out_2, w_mlp_in_2,
        w_mlp_out_2,
    )


_drawn_inputs = setup_inputs


def setup_inputs(seed=0):
    import zlib

    import numpy as np

    out = dict(_drawn_inputs(seed))
    spreads = {}
    factors = {'ffn_norm': 2.889,
     'final_norm': 2.98,
     'sgu_gain': 6.13,
     'rwkv_w1': 8.0,
     'rwkv_w2': 8.0,
     'rwkv_a0': 3.2,
     'rwkv_a1': 3.386,
     'rwkv_a2': 3.439,
     'rwkv_k_k': 3.658,
     'rwkv_ln_w': 3.125,
     'rwkv_ln_b': 6.662,
     'b_ada_2': 3.875,
     'g_pre_mix_2': 7.677,
     'g_post_mix_2': 28.172,
     'g_pre_mlp_2': 24.687,
     'g_post_mlp_2': 30.048,
     'conv_b_2': 64.0,
     'conv_norm_g_2': 44.976,
     'conv_norm_b_2': 200.0,
     'q_norm_g_2': 8.0,
     'kv_norm_g_2': 8.0}
    for name, (base, spread) in spreads.items():
        noise = np.random.default_rng([zlib.crc32(name.encode()), seed]).standard_normal(out[name].shape)
        drawn = base * np.exp(spread * noise) if base else spread * noise
        out[name] = __import__('jax').numpy.asarray(drawn.astype(out[name].dtype))
    for name, factor in factors.items():
        out[name] = (out[name] * factor).astype(out[name].dtype)
    return out
```

```python
from contextlib import ExitStack

import numpy as np
import concourse.bass as bass
from concourse import mybir

F32 = mybir.dt.float32
F32R = mybir.dt.float32r
I32 = mybir.dt.int32
ACT = mybir.ActivationFunctionType
ALU = mybir.AluOpType
AX_X = mybir.AxisListType.X

P = 128
D = 1024
SEQ = 256
NT = SEQ // P
KT = D // P
EPS = 1e-6
GN_EPS = 64e-5
FFN = 2816
FC = 256
NFFN = FFN // FC
DFF = 4096
NMLP = DFF // FC
AW = 512
WINDOWS = (2, 4, 8, 16)
RH = 16
HD = 64
CH = 64
RANK = 64
GRANK = 160
NH = 8
NOPE, ROPE, VD = 128, 64, 128
QL, KL = 384, 256
CK = 31
SLOT = 2048
DECAY = float(np.exp(-0.5))
SCALE = float(1.0 / np.sqrt(NOPE + ROPE))

ROWS = {}
_at = 0
for _n, _k in (("mix_norm", 16), ("ffn_norm", 16), ("mu", 48), ("sgu_bias", 4), ("pool_scale", 4),
               ("g_pre_mix", 8), ("g_pre_mlp", 8), ("cn_g", 8), ("cn_b", 8), ("conv_b", 8),
               ("q_norm", 3), ("kv_norm", 2)):
    ROWS[_n] = _at
    _at += _k
CONVW = _at
NCOL = CONVW + KT * CK

MASKS = ("ident", "diag_ts", "off_ts", "diag_st", "strict_st", "incl_st", "causal")
MI = {n: i * P for i, n in enumerate(MASKS)}
MCH = len(MASKS) * P
MFREQ = MCH + 2
NMASK = MFREQ + 32


def constants():
    a = np.arange(P)
    r, c = a[:, None], a[None, :]
    same = (r // CH) == (c // CH)
    near = (r // 16) == (c // 16)
    m = {
        "ident": r == c,
        "diag_ts": (c < r) & near,
        "off_ts": (c < r) & same & ~near,
        "diag_st": (r < c) & near,
        "strict_st": (r < c) & same,
        "incl_st": (r <= c) & same,
    }
    out = np.zeros((P, NMASK), np.float32)
    for n, v in m.items():
        out[:, MI[n]:MI[n] + P] = v
    out[:, MI["causal"]:MI["causal"] + P] = np.where(c <= r, 0.0, -1e30)
    out[:, MCH:MCH + 2] = (r // CH) == np.arange(2)[None, :]
    freq = 1.0 / (np.float32(10000.0) ** (np.arange(0, ROPE, 2, dtype=np.float32) / np.float32(ROPE)))
    out[:, MFREQ:MFREQ + 32] = freq.astype(np.float32)[None, :]
    pool = np.zeros((P, 3, 4, P), np.float32)
    for g, w in enumerate(WINDOWS):
        inside = (r <= c) & (r > c - w)
        pool[:, 0, g] = np.where(inside, 1.0 / np.minimum(c + 1, w), 0.0) - (r == c)
        pool[:, 1, g] = np.where(inside, 1.0 / w, 0.0) - (r == c)
        pool[:, 2, g] = np.where(r - P > c - w, 1.0 / w, 0.0)
    return out, pool.reshape(P, 12 * P).astype(np.float32)


SHARED = {
    "ff_act": (("ffn0.act", 22), ("ffn1.act", 22), ("mlp.act", 32)),
    "ff_mT": (("ffn0.mT", 11), ("ffn1.mT", 11), ("mlp.mT", 16)),
    "ff_h": (("ffn0.h", 11), ("ffn1.h", 11), ("mlp.h", 16)),
    "ff_gh": (("ffn0.gh", 11), ("ffn1.gh", 11), ("mlp.gh", 16)),
    "ff_gl": (("ffn0.gl", 11), ("ffn1.gl", 11), ("mlp.gl", 16)),
    "pool_1": (("ones", 1), ("acc_zero", 1)),
    "pe_1": (("cols_T", 1), ("rw.T", 4)),
    "pe_2": (("wst_T", 1), ("ffn1.T", 4)),
    "pe_3": (("mix0.T", 4), ("mod_T", 1)),
    "pe_4": (("spatial", 2), ("gates_T", 1)),
    "pe_5": (("pooled_T", 2), ("pre.T", 4)),
    "pe_6": (("yb_T", 2), ("u_T", 4)),
    "pe_7": (("ya_T", 2), ("lq.T", 3)),
    "pe_8": (("ffn0.T", 4), ("ro_T", 3)),
    "pe_9": (("mix1.T", 4), ("at.s", 8)),
    "pe_10": (("rank_T", 3), ("at.T", 8)),
    "pe_11": (("logit", 8), ("at.o", 8)),
    "pe_12": (("cum", 1), ("cmean", 1)),
    "pe_13": (("pc_T", 1), ("cvar", 1)),
    "pe_14": (("wkv.T", 8), ("ym.T", 4)),
    "pe_15": (("wkv.gram", 16), ("pre2.T", 4)),
    "act_1": (("mix0.std", 1), ("pre.std", 1)),
    "act_2": (("mix0.xh", 8), ("pre.xh", 2)),
    "act_3": (("u_ready", 2), ("sincos", 1)),
    "act_4": (("v_ready", 2), ("glu_s", 8)),
    "act_5": (("v_std", 1), ("lat", 4)),
    "act_6": (("zb_ready", 2), ("u_put", 4)),
    "act_7": (("ab.yh", 4), ("lat_std", 1)),
    "act_8": (("ab.xh", 2), ("gatev", 8)),
    "act_9": (("ffn0.std", 1), ("lq.xh", 5)),
    "act_10": (("ffn0.xh", 8), ("qn", 4)),
    "act_11": (("mix1.std", 1), ("qraw", 2)),
    "act_12": (("mix1.hT", 8), ("kn", 4)),
    "act_13": (("rank", 3), ("vt", 4)),
    "act_14": (("sig", 4), ("ro_put", 3)),
    "act_15": (("rate", 4), ("at.e", 16)),
    "act_16": (("rkv.xh", 6), ("at.xh", 8)),
    "act_17": (("rkv", 12), ("cv.xh", 2)),
    "act_18": (("kk_norm", 1), ("at.pT", 8)),
    "act_19": (("cum_read", 4), ("cv_std", 1)),
    "act_20": (("exps", 4), ("cv_act", 8)),
    "act_21": (("pc", 2), ("ym.xh", 4)),
    "act_22": (("wkv.ar", 16), ("post1.std", 1)),
    "act_23": (("wkv.x2c", 16), ("pre2.std", 1)),
    "act_24": (("wkv.gkvc", 8), ("pre2.xh", 2)),
    "act_25": (("wkv.x4c", 16), ("post2.std", 1)),
    "dve_1": (("mix0.ss", 1), ("ffn1.hn", 2)),
    "dve_2": (("mix0.hn", 2), ("ffn1.xl", 8)),
    "dve_3": (("cols", 2), ("ffn1.add", 4)),
    "dve_4": (("wst", 1), ("fin.ss", 1)),
    "dve_5": (("mix0.xl", 8), ("fin.hn", 2)),
    "dve_6": (("v_ss", 1), ("modc", 1)),
    "dve_7": (("v_normed", 2), ("gates", 4)),
    "dve_8": (("ya", 8), ("pre.ss", 1)),
    "dve_9": (("pooled", 2), ("pre.hn", 2)),
    "dve_10": (("ab.xl", 8), ("pre.hT", 8)),
    "dve_11": (("mix0.add", 4), ("pre.xl", 8)),
    "dve_12": (("ffn0.ss", 1), ("angle", 1)),
    "dve_13": (("ffn0.hn", 2), ("glu", 8)),
    "dve_14": (("ffn0.xl", 8), ("lat_ss", 1)),
    "dve_15": (("ffn0.add", 4), ("lat_n", 4)),
    "dve_16": (("mix1.ss", 1), ("conv_step", 248)),
    "dve_17": (("mix1.hn", 2), ("lq.xl", 5)),
    "dve_18": (("mixed", 6), ("roped", 2)),
    "dve_19": (("rkv.xl", 24), ("at.max", 8)),
    "dve_20": (("kk_ss", 1), ("at.sc", 16)),
    "dve_21": (("bonus", 1), ("at.p", 16)),
    "dve_22": (("cum_prev", 4), ("at.xl", 8)),
    "dve_23": (("scaled", 16), ("csq", 1)),
    "dve_24": (("wkv.bk", 16), ("cv_ss", 1)),
    "dve_25": (("wkv.masked", 24), ("yb", 4)),
    "dve_26": (("wkv.t1", 8), ("cv_n", 1)),
    "dve_27": (("wkv.t2c", 8), ("cv.xl", 8)),
    "dve_28": (("wkv.t4c", 8), ("ymix", 4)),
    "dve_29": (("wkv.t8c", 8), ("ym.xl", 8)),
    "dve_30": (("wkv.r2c", 8), ("post1.ss", 1)),
    "dve_31": (("wkv.r3c", 8), ("post1.hn", 2)),
    "dve_32": (("wkv.r4c", 8), ("post1.add", 2)),
    "dve_33": (("wkv.done", 8), ("pre2.ss", 1)),
    "dve_34": (("state", 3), ("pre2.hn", 2)),
    "dve_35": (("ysum", 4), ("pre2.hT", 8)),
    "dve_36": (("gn_var", 1), ("pre2.xl", 8)),
    "dve_37": (("y_gated", 4), ("post2.ss", 1)),
    "dve_38": (("rw.xl", 8), ("post2.hn", 2)),
    "dve_39": (("mix1.add", 4), ("post2.add", 2)),
}
HOME, BASE = {}, {}
for _home, _names in SHARED.items():
    _at = 0
    for _n, _k in _names:
        HOME[_n], BASE[_n] = _home, _at
        _at += _k


def B(name):
    return BASE.get(name, 0)


class Plan:

    def __init__(self):
        self.uses, self.loads, self.next = [0, 0, 0], [0, 0, 0], 0
        self.order, self.at = [], {}

    def block(self, name, width=SLOT, dmas=1):
        s = self.next
        self.next = (s + 1) % 3
        self.loads[s] += 16 * dmas
        self.at[name] = (s, self.uses[s], self.loads[s], width)
        self.uses[s] += 1
        self.order.append(name)

    def loop(self, name, uses, dmas):
        self.at[name] = (list(self.uses), list(self.loads))
        for s in range(3):
            self.uses[s] += uses[s]
            self.loads[s] += 16 * uses[s] * dmas[s]
        self.next = 0
        self.order.append(name)


def make_plan():
    p = Plan()
    for n in range(3):
        for k in range(2):
            p.block(("ab_in", n, k))
    for n in range(2):
        for k in range(2):
            p.block(("ab_out", n, k))
    p.loop("ffn0", [NFFN] * 3, [2, 2, 1])
    for w in ("k", "r", "v", "o"):
        for n in range(2):
            for k in range(2):
                p.block((w, n, k))
    p.loop("ffn1", [NFFN] * 3, [2, 2, 1])
    for n in range(4):
        for k in range(2):
            p.block(("glu", n, k), dmas=2)
    for n, w in ((0, QL), (1, KL + ROPE)):
        for k in range(2):
            p.block(("lat", n, k), width=4 * w)
    for n in range(4):
        for k in range(2):
            p.block(("gate", n, k))
    for n in range(4):
        p.block(("uq", n), width=3 * 384)
    for n in range(2):
        p.block(("ukv", n))
    for w in ("attn_out", "conv_out", "out"):
        for n in range(2):
            for k in range(2):
                p.block((w, n, k))
    p.loop("mlp", [NMLP // 2, NMLP // 2, NMLP], [1, 1, 1])
    return p


def build(nc, A, masks_d, pool_d, out):
    plan = make_plan()
    ctx = ExitStack()
    with ctx:
        def sb(name, shape, dt=F32):
            return ctx.enter_context(nc.sbuf_tensor(name, shape, dt))

        sems = {}

        def S(name):
            name = HOME.get(name, name)
            if name not in sems:
                sems[name] = ctx.enter_context(nc.semaphore(name.replace(".", "_")))
            return sems[name]

        raw = sb("raw", [P, 3, SLOT])
        wh = sb("wh", [P, 3, SLOT], F32R)
        wl = sb("wl", [P, 3, SLOT], F32R)
        h = sb("h", [P, NT, D])
        xh = sb("xh", [P, KT, SEQ], F32R)
        xl = sb("xl", [P, KT, SEQ], F32R)
        gh = sb("gh", [P, 2, SEQ], F32R)
        gl = sb("gl", [P, 2, SEQ], F32R)
        wide = sb("wide", [P, 11 * 2048])
        side = sb("side", [P, D])
        lowr = sb("lowr", [P, 4 * SEQ])
        masks = sb("masks", [P, NMASK])
        cols = sb("cols", [P, NCOL])
        ones = sb("ones", [P, P])
        small = sb("small", [P, 512])
        posi = sb("posi", [P, NT], I32)
        ps = ctx.enter_context(nc.psum_tensor("ps", [P, 8, 512], F32))

        def W(i, off=0, n=2048):
            return wide[:, i * 2048 + off:i * 2048 + off + n]

        def W3(i, a, off=0, n=2048):
            return W(i, off, n).rearrange("p (a b) -> p a b", a=a)

        ident = masks[:, 0:P]

        def mask4(name):
            return masks[:, MI[name]:MI[name] + P].unsqueeze(1).to_broadcast([P, 4, P])

        def col(name, i=0):
            return cols[:, ROWS[name] + i:ROWS[name] + i + 1]

        sm_at = [0]

        def sm(n):
            sm_at[0] += n
            assert sm_at[0] <= 512
            return small[:, sm_at[0] - n:sm_at[0]]

        NORMS = ("mix0", "ffn0", "mix1", "ffn1", "fin", "pre", "post1", "pre2", "post2")
        nss = {n: sm(2) for n in NORMS}
        nsd = {n: sm(2) for n in NORMS}
        nrs = {n: sm(2) for n in NORMS}
        vss, vsd, vrs = sm(2), sm(2), sm(2)
        qss, qsd, qrs = sm(4), sm(4), sm(4)
        kss, bon, mean, gvar = sm(32), sm(32), sm(32), sm(32)
        pc = sm(64)
        ccol = sm(8)
        modc = sm(32)
        sc1, sc2 = sm(8), sm(8)
        posf = sm(2)
        amax, asum, arec = sm(4), sm(4), sm(4)

        hn = W3(5, NT)
        silu = W3(10, NT, 0, 512)
        hmid = W3(10, NT, 512, 512)

        raw_loaded = [S(f"raw_loaded{i}") for i in range(3)]
        hi_ready = [S(f"hi_ready{i}") for i in range(3)]
        lo_ready = [S(f"lo_ready{i}") for i in range(3)]
        w_used = [S(f"w_used{i}") for i in range(3)]

        def used(eng, name):
            s, use, _, _ = plan.at[name]
            eng.wait_ge(w_used[s], use + 1)

        def kblock(w, n0, n, k):
            return w[k * 512:(k + 1) * 512, n0:n0 + n].rearrange("(a p) n -> p a n", p=P)

        w_in = A["w_in_2"][0]
        LAT0 = 2 * D
        GATE0 = LAT0 + QL + KL + ROPE
        SRC = {"ab_in": A["ab_w_in"][0], "ab_out": A["ab_w_out"][0], "k": A["rwkv_w_k"][0], "r": A["rwkv_w_r"][0],
               "v": A["rwkv_w_v"][0], "o": A["rwkv_w_o"][0], "attn_out": A["w_attn_out_2"][0],
               "conv_out": A["w_conv_out_2"][0], "out": A["w_out_2"][0]}

        def sources(name):
            s, _, _, width = plan.at[name]
            flat = raw[:, s, 0:width]
            what = name[0]
            if what == "glu":
                v = flat.rearrange("p (a n) -> p a n", a=4)
                n0 = name[1] * 256
                return [(kblock(w_in, n0, 256, name[2]), v[:, :, 0:256]),
                        (kblock(w_in, D + n0, 256, name[2]), v[:, :, 256:512])]
            if what == "lat":
                n0, n = (LAT0, QL) if name[1] == 0 else (LAT0 + QL, KL + ROPE)
                return [(kblock(w_in, n0, n, name[2]), flat.rearrange("p (a n) -> p a n", a=4))]
            if what == "gate":
                return [(kblock(w_in, GATE0 + name[1] * 512, 512, name[2]), flat.rearrange("p (a n) -> p a n", a=4))]
            if what == "uq":
                return [(A["w_uq_2"][0][:, name[1] * 384:(name[1] + 1) * 384].rearrange("(a p) n -> p a n", p=P),
                         flat.rearrange("p (a n) -> p a n", a=3))]
            if what == "ukv":
                return [(A["w_ukv_2"][0][:, name[1] * 1024:(name[1] + 1) * 1024].rearrange("(a p) n -> p a n", p=P),
                         flat.rearrange("p (a n) -> p a n", a=2))]
            return [(kblock(SRC[what], name[1] * 512, 512, name[2]), flat.rearrange("p (a n) -> p a n", a=4))]

        block = ctx.enter_context(nc.Block())

        @block.sync
        def _(sp):
            def load_block(name):
                s, use, _, _ = plan.at[name]
                if use:
                    sp.wait_ge(lo_ready[s], use)
                for src, dst in sources(name):
                    sp.dma_start(dst, src).then_inc(raw_loaded[s], 16)

            def load_ffn(l):
                uses, _ = plan.at[f"ffn{l}"]
                gate, up, down = A["ffn_w_gate"][l], A["ffn_w_up"][l], A["ffn_w_down"][l]

                def load_gu(c):
                    n0 = c * FC if isinstance(c, int) else sp.snap(c * FC)
                    for k in range(2):
                        dst = raw[:, k, :].rearrange("p (a n) -> p a n", a=4)
                        sp.wait_ge(lo_ready[k], uses[k] + c)
                        for j, w in enumerate((gate, up)):
                            sp.dma_start(dst[:, :, j * FC:(j + 1) * FC],
                                         w[k * 512:(k + 1) * 512, bass.ds(n0, FC)].rearrange("(a p) n -> p a n", p=P))\
                              .then_inc(raw_loaded[k], 16)

                def load_down(c):
                    r0 = c * FC if isinstance(c, int) else sp.snap(c * FC)
                    sp.wait_ge(lo_ready[2], uses[2] + c)
                    sp.dma_start(raw[:, 2, :].rearrange("p (a n) -> p a n", a=2),
                                 down[bass.ds(r0, FC), :].rearrange("(a p) n -> p a n", p=P))\
                      .then_inc(raw_loaded[2], 16)

                load_gu(0)
                with sp.Fori(0, NFFN - 1) as i:
                    load_gu(i + 1)
                    load_down(i)
                load_down(NFFN - 1)

            def load_mlp():
                uses, _ = plan.at["mlp"]
                up, down = A["w_mlp_in_2"][0], A["w_mlp_out_2"][0]

                def load_up(s, c, use):
                    n0 = c * FC if isinstance(c, int) else sp.snap(c * FC)
                    sp.wait_ge(lo_ready[s], uses[s] + use)
                    sp.dma_start(raw[:, s, :].rearrange("p (a n) -> p a n", a=KT),
                                 up[:, bass.ds(n0, FC)].rearrange("(a p) n -> p a n", p=P)).then_inc(raw_loaded[s], 16)

                def load_down(c):
                    r0 = c * FC if isinstance(c, int) else sp.snap(c * FC)
                    sp.wait_ge(lo_ready[2], uses[2] + c)
                    sp.dma_start(raw[:, 2, :].rearrange("p (a n) -> p a n", a=2),
                                 down[bass.ds(r0, FC), :].rearrange("(a p) n -> p a n", p=P)).then_inc(raw_loaded[2], 16)

                load_up(0, 0, 0)
                with sp.Fori(0, NMLP // 2 - 1) as i:
                    load_up(1, i * 2 + 1, i)
                    load_down(i * 2)
                    load_up(0, i * 2 + 2, i + 1)
                    load_down(i * 2 + 1)
                load_up(1, NMLP - 1, NMLP // 2 - 1)
                load_down(NMLP - 2)
                load_down(NMLP - 1)

            for name in plan.order:
                if name in ("ffn0", "ffn1"):
                    load_ffn(int(name[3]))
                elif name == "mlp":
                    load_mlp()
                else:
                    load_block(name)
            sp.wait_ge(S("stored"), B("stored") + 32)

        ada_src = A["w_ada_2"][0].rearrange("(p k) n -> p k n", k=KT)
        NADA = 6 * D // 256
        ada_raw = [W3(3, KT), W3(4, KT)]
        ada_acc = wide[:, 0:6 * D]

        @block.gpsimd
        def _(pool):
            nc.gpsimd.memset(ones[:, :], 1.0).then_inc(S("ones"), 1)
            pool.wait_ge(S("ones"), B("ones") + 1)
            nc.gpsimd.memset(lowr[64:65, 0:2 * SEQ], 1.0).then_inc(S("lowr_one"), 1)
            pool.wait_ge(S("wst"), B("wst") + 1)
            pool.wait_ge(S("lowr_one"), B("lowr_one") + 1)
            nc.gpsimd.memset(W3(4, 4, 512, 512)[64:128, :, 0:64], 0.0).then_inc(S("wst_masked"), 1)
            pool.wait_ge(S("wkv.done"), B("wkv.done") + 8)
            pool.wait_ge(S("wst_masked"), B("wst_masked") + 1)
            nc.gpsimd.memset(W(4, 0, D)[0:64, :], 0.0).then_inc(S("s0_zero"), 1)
            pool.wait_ge(S("rw.xl"), B("rw.xl") + 8)
            pool.wait_ge(S("mix1.add"), B("mix1.add") + 4)
            pool.wait_ge(S("s0_zero"), B("s0_zero") + 1)
            nc.gpsimd.memset(ada_acc, 0.0).then_inc(S("acc_zero"), 1)
            pool.wait_ge(S("acc_zero"), B("acc_zero") + 1)
            pool.dma_start(ada_acc[0:1, :], A["b_ada_2"]).then_inc(S("acc_bias"), 16)
            pool.dma_start(ada_raw[0], ada_src[:, :, 0:256]).then_inc(S("ada0"), 16)
            pool.dma_start(ada_raw[1], ada_src[:, :, 256:512]).then_inc(S("ada1"), 16)
            for j in range(1, NADA // 2):
                pool.wait_ge(S("ada_step"), B("ada_step") + 16 * j)
                for b in range(2):
                    pool.dma_start(ada_raw[b], ada_src[:, :, (2 * j + b) * 256:(2 * j + b + 1) * 256])\
                        .then_inc(S(f"ada{b}"), 16)

        @block.tensor
        def _(pe):
            def mm3(o, lh, ll, rh, rl, start, stop):
                pe.matmul(o, lh, rh, start=start, stop=False)
                pe.matmul(o, ll, rh, start=False, stop=False)
                return pe.matmul(o, lh, rl, start=False, stop=stop)

            def tok(t):
                return slice(t * P, (t + 1) * P)

            def arrive(name):
                s, use, _, _ = plan.at[name]
                pe.wait_ge(lo_ready[s], use + 1)
                return s

            def half(s, kts, outs, n, start, stop):
                for t in range(NT):
                    for j, kt in enumerate(kts):
                        m = mm3(outs[t], xh[:, kt, tok(t)], xl[:, kt, tok(t)],
                                wh[:, s, j * n:(j + 1) * n], wl[:, s, j * n:(j + 1) * n],
                                start and j == 0, stop and j == len(kts) - 1)
                return m

            def linear(what, xname, n_chunks, xcount=0, n=512, free=None, banks=None):
                for c in range(n_chunks):
                    if free:
                        free(c)
                    o = [ps[:, 2 * (c % 2) + t, 0:n] for t in range(NT)]
                    for k in range(2):
                        s = arrive((what, c, k))
                        if c == 0:
                            pe.wait_ge(S(xname), B(xname) + xcount + 4 * (k + 1))
                        half(s, range(4 * k, 4 * k + 4), o, n, k == 0, k == 1).then_inc(w_used[s], 1)

            def norm_transposes(name):
                for t in range(NT):
                    pe.wait_ge(S(name + ".hn"), B(name + ".hn") + t + 1)
                    for kt in range(KT):
                        m = pe.transpose(ps[:, 4 + kt // 2, (kt % 2) * SEQ + t * P:(kt % 2) * SEQ + (t + 1) * P],
                                         hn[:, t, kt * P:(kt + 1) * P], ident)
                        if t == NT - 1 and kt % 2:
                            m.then_inc(S(name + ".T"), 1)

            def ffn_loop(l):
                f = f"ffn{l}"
                uses, _ = plan.at[f]

                def gu_half(k, c, last):
                    pe.wait_ge(lo_ready[k], uses[k] + c + 1)
                    pe.wait_ge(lo_ready[k], uses[k] + 1)
                    m = half(k, range(4 * k, 4 * k + 4), [ps[:, 4, :], ps[:, 5, :]], 512, k == 0, k == 1)
                    m.then_inc(w_used[k], 1)

                def body(i, first, last):
                    if not last:
                        pe.wait_ge(S(f + ".h"), B(f + ".h") + i + 1)
                        gu_half(0, i + 1, False)
                    pe.wait_ge(S(f + ".h"), B(f + ".h") + i + 1)
                    pe.wait_ge(S(f + ".h"), B(f + ".h") + 1)
                    for t in range(NT):
                        for j in range(2):
                            m = pe.transpose(ps[:, 6, j * SEQ + t * P:j * SEQ + (t + 1) * P],
                                             hmid[:, t, j * P:(j + 1) * P], ident)
                    m.then_inc(S(f + ".mT"), 1)
                    if not last:
                        gu_half(1, i + 1, True)
                    pe.wait_ge(S(f + ".gl"), B(f + ".gl") + i + 1)
                    pe.wait_ge(lo_ready[2], uses[2] + i + 1)
                    pe.wait_ge(lo_ready[2], uses[2] + 1)
                    for j in range(2):
                        for t in range(NT):
                            for n in range(2):
                                w = slice(j * D + n * 512, j * D + (n + 1) * 512)
                                m = mm3(ps[:, 2 * t + n, :], gh[:, j, tok(t)], gl[:, j, tok(t)], wh[:, 2, w], wl[:, 2, w],
                                        first and j == 0, last and j == 1)
                    m.then_inc(w_used[2], 1)

                for k in range(2):
                    pe.wait_ge(S(f + ".xl"), B(f + ".xl") + 4 * (k + 1))
                    if k == 0:
                        pe.wait_ge(S(f + ".xl"), B(f + ".xl") + 8)
                    gu_half(k, 0, True)
                body(0, True, False)
                with pe.Fori(1, NFFN - 1) as i:
                    body(i, False, False)
                body(NFFN - 1, False, True)

            def mlp_loop():
                uses, _ = plan.at["mlp"]

                def up(s, c, use, quarter):
                    if quarter == 0:
                        pe.wait_ge(lo_ready[s], uses[s] + use + 1)
                        pe.wait_ge(lo_ready[s], uses[s] + 1)
                    for t in range(NT):
                        for kt in range(4 * quarter, 4 * quarter + 4):
                            m = mm3(ps[:, 4 + t, 0:FC], xh[:, kt, tok(t)], xl[:, kt, tok(t)],
                                    wh[:, s, kt * FC:(kt + 1) * FC], wl[:, s, kt * FC:(kt + 1) * FC],
                                    kt == 0, kt == KT - 1)
                    if quarter == 1:
                        m.then_inc(w_used[s], 1)

                def body(c, s_next, use_next, first, last):
                    if not last:
                        pe.wait_ge(S("mlp.h"), B("mlp.h") + c + 1)
                        up(s_next, c + 1, use_next, 0)
                    pe.wait_ge(S("mlp.h"), B("mlp.h") + c + 1)
                    pe.wait_ge(S("mlp.h"), B("mlp.h") + 1)
                    for t in range(NT):
                        for j in range(2):
                            m = pe.transpose(ps[:, 6, j * SEQ + t * P:j * SEQ + (t + 1) * P],
                                             hmid[:, t, j * P:(j + 1) * P], ident)
                    m.then_inc(S("mlp.mT"), 1)
                    if not last:
                        up(s_next, c + 1, use_next, 1)
                    pe.wait_ge(S("mlp.gl"), B("mlp.gl") + c + 1)
                    pe.wait_ge(lo_ready[2], uses[2] + c + 1)
                    pe.wait_ge(lo_ready[2], uses[2] + 1)
                    for j in range(2):
                        for t in range(NT):
                            for n in range(2):
                                w = slice(j * D + n * 512, j * D + (n + 1) * 512)
                                m = mm3(ps[:, 2 * t + n, :], gh[:, j, tok(t)], gl[:, j, tok(t)], wh[:, 2, w], wl[:, 2, w],
                                        first and j == 0, last and j == 1)
                    m.then_inc(w_used[2], 1)

                pe.wait_ge(S("pre2.xl"), B("pre2.xl") + 8)
                up(0, 0, 0, 0)
                up(0, 0, 0, 1)
                body(0, 1, 0, True, False)
                with pe.Fori(0, NMLP // 2 - 1) as i:
                    body(i * 2 + 1, 0, i + 1, False, False)
                    body(i * 2 + 2, 1, i + 1, False, False)
                body(NMLP - 1, 0, 0, False, True)

            def turn(dst, src, nk=P):
                return pe.transpose(dst, src, masks[0:nk, 0:nk])

            pe.wait_ge(S("rows"), B("rows") + 16 * 14)
            turn(ps[:, 0, 0:P], W(6, 0, P))
            turn(ps[:, 0, P:P + 5], W(6, P, P)[0:5, :], 5)
            for kt in range(KT):
                m = turn(ps[:, 1, kt * CK:(kt + 1) * CK], W(6, 256 + kt * P, P)[0:CK, :], CK)
            m.then_inc(S("cols_T"), 1)
            pe.wait_ge(S("mixw"), B("mixw") + 16 * 4)
            for i in range(4):
                m = turn(ps[:, 2, i * P:(i + 1) * P], W(4, i * P, P))
            m.then_inc(S("wst_T"), 1)

            norm_transposes("mix0")

            def ab_free(c):
                if c == 0:
                    pe.wait_ge(S("wst"), B("wst") + 1)
                if c == 2:
                    pe.wait_ge(S("u_ready"), B("u_ready") + 2)
            linear("ab_in", "mix0.xl", 3, free=ab_free)
            pe.wait_ge(S("wst_masked"), B("wst_masked") + 1)
            pe.wait_ge(S("v_normed"), B("v_normed") + 2)
            wst = W3(4, 4, 512, 512)
            za = W3(0, NT)
            zb = W3(1, NT, 0, 1024)
            for t in range(NT):
                for i in range(4):
                    m = pe.matmul(ps[:, 4 + t, i * P:(i + 1) * P], wst[:, i, :], za[:, t, AW + i * P:AW + (i + 1) * P],
                                  start=True, stop=True)
                m.then_inc(S("spatial"), 1)
            pe.wait_ge(S("zb_ready"), B("zb_ready") + 2)
            pmat = W(3, 0, 12 * P).rearrange("p (a g n) -> p a g n", a=3, g=4)
            for g in range(4):
                o = ps[:, 6 + g // 2, (g % 2) * SEQ:(g % 2) * SEQ + SEQ]
                zg = [zb[:, t, g * P:(g + 1) * P] for t in range(NT)]
                pe.matmul(o[:, 0:P], zg[0], pmat[:, 0, g, :], start=True, stop=True)
                pe.matmul(o[:, P:SEQ], zg[1], pmat[:, 1, g, :], start=True, stop=False)
                m = pe.matmul(o[:, P:SEQ], zg[0], pmat[:, 2, g, :], start=False, stop=True)
                if g % 2:
                    m.then_inc(S("pooled_T"), 1)
            pe.wait_ge(S("ya"), B("ya") + 8)
            pe.wait_ge(S("pooled"), B("pooled") + 2)
            poolw = W3(4, 4, 1024, 512)
            pooled = W3(2, 4, 0, 1024)
            for g in range(4):
                m = pe.matmul(ps[:, 4 + g // 2, (g % 2) * SEQ:(g % 2) * SEQ + SEQ], poolw[:, g, :], pooled[:, g, :],
                              start=True, stop=True)
                if g % 2:
                    m.then_inc(S("yb_T"), 1)
            ya = W3(2, NT, 1024, 1024)
            for kt in range(4):
                for t in range(NT):
                    m = turn(ps[:, 6 + kt // 2, (kt % 2) * SEQ + t * P:(kt % 2) * SEQ + (t + 1) * P],
                             ya[:, t, kt * P:(kt + 1) * P])
                if kt % 2:
                    m.then_inc(S("ya_T"), 1)
            linear("ab_out", "ab.xl", 2, free=lambda c: pe.wait_ge(S("ab.xl"), B("ab.xl") + 8))
            norm_transposes("ffn0")
            ffn_loop(0)

            norm_transposes("mix1")
            w1 = W3(10, KT, 0, 512)
            a1 = W3(10, KT, 512, 512)
            g1 = W3(6, KT, 0, KT * GRANK)
            mix = {"w": W3(2, KT), "a": W3(3, KT), "g": W3(2, KT)}
            pe.wait_ge(S("rw_w1"), B("rw_w1") + 48)
            pe.wait_ge(S("mix1.hT"), B("mix1.hT") + 8)
            for n, (what, w) in enumerate((("w", w1), ("a", a1))):
                pe.wait_ge(S("mixed"), B("mixed") + n + 1)
                for kt in range(KT):
                    m = pe.matmul(ps[0:RANK, 4 + n, 0:SEQ], w[:, kt, :], mix[what][:, kt, :], start=kt == 0, stop=kt == KT - 1)
                m.then_inc(S("rank_T"), 1)
            pe.wait_ge(S("mixed"), B("mixed") + 3)
            for part, (r0, r1) in enumerate(((0, P), (P, GRANK))):
                for kt in range(KT):
                    m = pe.matmul(ps[0:r1 - r0, 6 + part, 0:SEQ], g1[:, kt, r0:r1], mix["g"][:, kt, :],
                                  start=kt == 0, stop=kt == KT - 1)
            m.then_inc(S("rank_T"), 1)
            pe.wait_ge(S("rw_w2"), B("rw_w2") + 64)
            for n in range(2):
                pe.wait_ge(S("rank"), B("rank") + n + 1)
                pe.wait_ge(S("lowr_one"), B("lowr_one") + 1)
                w2 = W(4, n * D, D)
                for t in range(NT):
                    for c in range(2):
                        if n == 1:
                            pe.wait_ge(S("sig"), B("sig") + 2 * t + c + 1)
                        m = pe.matmul(ps[:, 2 * t + c, :], lowr[0:RANK + 1, n * SEQ + t * P:n * SEQ + (t + 1) * P],
                                      w2[0:RANK + 1, c * 512:(c + 1) * 512], start=True, stop=True)
                        m.then_inc(S("logit"), 1)
            pe.wait_ge(S("rank"), B("rank") + 3)
            sig = W3(7, NT)
            incl = masks[:, MI["incl_st"]:MI["incl_st"] + P]
            for t in range(NT):
                for c in range(2):
                    m = pe.matmul(ps[:, 4 + 2 * t + c, :], incl, sig[:, t, c * 512:(c + 1) * 512], start=True, stop=True)
            m.then_inc(S("cum"), 1)
            for n, what in enumerate("krv"):
                def rkv_free(c, n=n):
                    if n == 0:
                        if c == 0:
                            pe.wait_ge(S("rate"), B("rate") + 4)
                    else:
                        pe.wait_ge(S("rkv"), B("rkv") + 4 * (n - 1) + 2 * c + 2)
                linear(what, "rkv.xl", 2, xcount=8 * n, free=rkv_free)
            pe.wait_ge(S("exps"), B("exps") + 4)
            for t in range(NT):
                for hp in range(RH // 2):
                    o = hp * 4 + 2 * t
                    m = pe.matmul(ps[:, 4, o:o + 2], sig[:, t, hp * P:(hp + 1) * P], masks[:, MCH:MCH + 2], start=True, stop=True)
            m.then_inc(S("pc_T"), 1)

            bk = wide[:, 2048:3 * 2048].rearrange("p (t h x c) -> p t h x c", t=NT, h=RH, x=2)
            rr = W(0).rearrange("p (t h c) -> p t h c", t=NT, h=RH)
            aa = W(10).rearrange("p (t h c) -> p t h c", t=NT, h=RH)
            vv = W(6).rearrange("p (t h c) -> p t h c", t=NT, h=RH)
            tmp = WKV_TMP(W)
            pe.wait_ge(S("scaled"), B("scaled") + 16)
            for g in range(8):
                t, h0 = g // 4, 4 * (g % 4)

                def each(fn, sem):
                    for u in range(4):
                        m = fn(u)
                    m.then_inc(S("wkv." + sem), 1)

                def q(b, u, n=P):
                    return ps[:, b, u * n:(u + 1) * n]

                if g == 0:
                    pe.wait_ge(S("pc"), B("pc") + 2)
                    pe.wait_ge(S("rkv"), B("rkv") + 12)
                else:
                    pe.wait_ge(S("wkv.done"), B("wkv.done") + g)
                for u in range(4):
                    turn(ps[0:64, u // 2, (u % 2) * SEQ:(u % 2) * SEQ + P], aa[:, t, h0 + u, :])
                    turn(ps[0:64, u // 2, (u % 2) * SEQ + P:(u % 2 + 1) * SEQ], rr[:, t, h0 + u, :])
                    turn(ps[0:64, 2, u * P:(u + 1) * P], bk[:, t, h0 + u, 0, :])
                    m = turn(ps[0:64, 3, u * P:(u + 1) * P], bk[:, t, h0 + u, 1, :])
                m.then_inc(S("wkv.T"), 1)
                pe.wait_ge(S("wkv.ar"), B("wkv.ar") + 2 * (g + 1))
                pe.wait_ge(S("wkv.bk"), B("wkv.bk") + 2 * (g + 1))
                for u in range(4):
                    ar = tmp["ar"][0:64, u * SEQ:(u + 1) * SEQ]
                    pe.matmul(ps[:, 4 + u // 2, (u % 2) * SEQ:(u % 2 + 1) * SEQ], tmp["bT"][0:64, u * P:(u + 1) * P], ar,
                              start=True, stop=True)
                for u in range(4):
                    m = pe.matmul(q(0, u), tmp["ar"][0:64, u * SEQ:u * SEQ + P], tmp["bT"][0:64, u * P:(u + 1) * P], start=True, stop=True)
                m.then_inc(S("wkv.gram"), 1)
                for u in range(4):
                    ar = tmp["ar"][0:64, u * SEQ:(u + 1) * SEQ]
                    m = pe.matmul(ps[:, 6 + u // 2, (u % 2) * SEQ:(u % 2 + 1) * SEQ], tmp["kT"][0:64, u * P:(u + 1) * P], ar,
                                  start=True, stop=True)
                m.then_inc(S("wkv.gram"), 1)

                def T(n, u):
                    return tmp[n][:, u * P:(u + 1) * P]

                def mul(b, l, r, sem):
                    each(lambda u: pe.matmul(q(b, u), T(l, u), T(r, u), start=True, stop=True), sem)

                pe.wait_ge(S("wkv.masked"), B("wkv.masked") + 3 * g + 1)
                mul(1, "xt", "x", "x2")
                mul(2, "x", "xt", "x2t")
                pe.wait_ge(S("wkv.masked"), B("wkv.masked") + 3 * g + 2)
                for u in range(4):
                    m = pe.matmul(ps[:, 3, u * 64:(u + 1) * 64], T("gk", u), vv[:, t, h0 + u, :], start=True, stop=True)
                m.then_inc(S("wkv.gkv"), 1)
                pe.wait_ge(S("wkv.x2c"), B("wkv.x2c") + 2 * (g + 1))
                pe.wait_ge(S("wkv.t1"), B("wkv.t1") + g + 1)
                mul(0, "x2", "tt", "t2")
                pe.wait_ge(S("wkv.masked"), B("wkv.masked") + 3 * g + 3)
                mul(4, "x2t", "x2", "x4")
                mul(5, "x2", "x2t", "x4t")
                pe.wait_ge(S("wkv.x4c"), B("wkv.x4c") + 2 * (g + 1))
                pe.wait_ge(S("wkv.t2c"), B("wkv.t2c") + g + 1)
                mul(1, "x4", "tt", "t4")
                mul(2, "x4t", "x4", "x8")
                pe.wait_ge(S("wkv.x8c"), B("wkv.x8c") + g + 1)
                pe.wait_ge(S("wkv.t4c"), B("wkv.t4c") + g + 1)
                mul(0, "x8", "tt", "t8")
                pe.wait_ge(S("wkv.t8c"), B("wkv.t8c") + g + 1)
                pe.wait_ge(S("wkv.gkvc"), B("wkv.gkvc") + g + 1)
                for u in range(4):
                    pe.matmul(ps[:, 4, u * P:u * P + 64], T("tt", u), tmp["gkv"][:, u * 64:(u + 1) * 64], start=True, stop=True)
                    m = pe.matmul(ps[:, 4, u * P + 64:(u + 1) * P], T("tt", u), aa[:, t, h0 + u, :], start=True, stop=True)
                m.then_inc(S("wkv.r1"), 1)
                mul(5, "off", "tt", "mt")
                pe.wait_ge(S("wkv.mtc"), B("wkv.mtc") + g + 1)
                pe.wait_ge(S("wkv.r1c"), B("wkv.r1c") + g + 1)
                mul(1, "mt", "r1", "r2")
                pe.wait_ge(S("wkv.r2c"), B("wkv.r2c") + g + 1)
                mul(2, "mt", "r2", "r3")
                pe.wait_ge(S("wkv.r3c"), B("wkv.r3c") + g + 1)
                mul(0, "mt", "r2", "r4")
                pe.wait_ge(S("wkv.r4c"), B("wkv.r4c") + g + 1)
                for u in range(4):
                    for p in range(2):
                        rows = slice(64 * p, 64 * p + 64)
                        u_, w_ = tmp["r2"][rows, u * P:u * P + 64], tmp["r2"][rows, u * P + 64:(u + 1) * P]
                        if 0 < 2 * t + p < 3:
                            pe.matmul(ps[0:64, F_BANK[p], u * 64:(u + 1) * 64], w_, bk[rows, t, h0 + u, 0, :], start=True, stop=True)
                        if 2 * t + p == 3:
                            continue
                        o = ps[0:64, G_BANK[p], u * 64:(u + 1) * 64]
                        pe.matmul(o, bk[rows, t, h0 + u, 0, :], u_, start=True, stop=False)
                        m = pe.matmul(o, bk[rows, t, h0 + u, 1, :], vv[rows, t, h0 + u, :], start=False, stop=True)
                m.then_inc(S("wkv.fg"), 1)
                for u in range(4):
                    w_ = tmp["r2"][:, u * P + 64:(u + 1) * P]
                    pe.matmul(ps[0:64, 5, u * P:(u + 1) * P], w_, T("mrb", u), start=True, stop=False)
                    pe.matmul(ps[0:64, 5, u * P:(u + 1) * P], rr[:, t, h0 + u, :], ident, start=False, stop=True)
                    o = ps[:, 6, u * 64:(u + 1) * 64]
                    pe.matmul(o, T("mrb", u), tmp["r2"][:, u * P:u * P + 64], start=True, stop=False)
                    m = pe.matmul(o, T("mrk", u), vv[:, t, h0 + u, :], start=False, stop=True)
                m.then_inc(S("wkv.eh"), 1)

            st = W(4, 0, D).rearrange("p (t h c) -> p t h c", t=1, h=RH)
            states = wide[:, 4 * 2048:5 * 2048].rearrange("p (t h c) -> p t h c", t=NT, h=RH)
            ft = W3(8, 2).rearrange("p a (h c) -> p a h c", h=RH)
            chain = W(5, 0, D).rearrange("p (h c) -> p h c", h=RH)
            for c in (1, 2):
                pe.wait_ge(S("state"), B("state") + c)
                for i in range(RH):
                    m = pe.matmul(ps[0:64, i // 8, (i % 8) * 64:(i % 8 + 1) * 64], ft[0:64, c - 1, i, :], chain[0:64, i, :],
                                  start=True, stop=True)
                m.then_inc(S("state_F"), 1)
            pe.wait_ge(S("s0_zero"), B("s0_zero") + 1)
            pe.wait_ge(S("state_put"), B("state_put") + 3)
            for t in range(NT):
                for i in range(RH):
                    e2 = wide[:, 2048 + (t * RH + i) * P:2048 + (t * RH + i + 1) * P]
                    m = pe.matmul(ps[:, 2 + 2 * t + i // 8, (i % 8) * 64:(i % 8 + 1) * 64], e2, states[:, t, i, :],
                                  start=True, stop=True)
                m.then_inc(S("y_T"), 1)
            pe.wait_ge(S("g2"), B("g2") + 32)
            pe.wait_ge(S("ysum"), B("ysum") + 4)
            g2a, g2b = W(9, 0, D), W(9, D, D)
            for t in range(NT):
                for c in range(2):
                    o = ps[:, 2 + 2 * t + c, :]
                    pe.matmul(o, lowr[:, 2 * SEQ + t * P:2 * SEQ + (t + 1) * P], g2a[:, c * 512:(c + 1) * 512], start=True, stop=False)
                    m = pe.matmul(o, lowr[0:GRANK - P, 3 * SEQ + t * P:3 * SEQ + (t + 1) * P], g2b[0:GRANK - P, c * 512:(c + 1) * 512],
                                  start=False, stop=True)
            m.then_inc(S("gate_T"), 1)
            y = W3(0, NT)
            pe.wait_ge(S("y_gated"), B("y_gated") + 4)
            for kp in range(4):
                for j in range(2):
                    for t in range(NT):
                        kt = 2 * kp + j
                        m = turn(ps[:, (6 + kp) % 8, j * SEQ + t * P:j * SEQ + (t + 1) * P], y[:, t, kt * P:(kt + 1) * P])
                m.then_inc(S("rw.T"), 1)

            def o_free(c):
                if c == 0:
                    pe.wait_ge(S("rw.xl"), B("rw.xl") + 8)
            linear("o", "rw.xl", 2, free=o_free)
            norm_transposes("ffn1")
            ffn_loop(1)

            pe.wait_ge(S("ada_step"), B("ada_step") + 8 * NADA)
            pe.wait_ge(S("ffn1.add"), B("ffn1.add") + 4)
            for n, m_ in enumerate((0, 1, 3, 4)):
                for kt in range(KT):
                    m = pe.matmul(ps[:, 0, n * KT + kt:n * KT + kt + 1], ada_acc[:, m_ * D + kt * P:m_ * D + (kt + 1) * P],
                                  ones[:, 0:1], start=True, stop=True)
            m.then_inc(S("mod_T"), 1)
            for n, m_ in enumerate((2, 5)):
                for c in range(2):
                    if n == 0 and c == 0:
                        pe.wait_ge(S("ones"), B("ones") + 1)
                    m = pe.matmul(ps[:, 4 + 2 * n + c, :], ones[:, :],
                                  ada_acc[:, m_ * D + c * 512:m_ * D + (c + 1) * 512], start=True, stop=True)
            m.then_inc(S("gates_T"), 1)
            pe.wait_ge(S("gates"), B("gates") + 4)
            norm_transposes("pre")

            def glu_free(c):
                if c == 0:
                    pe.wait_ge(S("modc"), B("modc") + 1)
                if c >= 2:
                    pe.wait_ge(S("glu"), B("glu") + 2 * (c - 1))
            linear("glu", "pre.xl", 4, free=glu_free)
            uu = W3(10, 4, 0, 1024)
            for n, nw in ((0, QL), (1, KL + ROPE)):
                pe.wait_ge(S("glu"), B("glu") + 2 * (n + 3))
                o = [ps[:, 2 * (n % 2) + t, 0:nw] for t in range(NT)]
                for k in range(2):
                    s = arrive(("lat", n, k))
                    half(s, range(4 * k, 4 * k + 4), o, nw, k == 0, k == 1).then_inc(w_used[s], 1)
            for c in range(4):
                pe.wait_ge(S("glu"), B("glu") + 2 * (c + 1))
                for j in range(2):
                    for t in range(NT):
                        m = turn(ps[:, 4 + c, j * SEQ + t * P:j * SEQ + (t + 1) * P],
                                 W(U_AT[c][0], U_AT[c][1] + t * 256 + j * P, P))
                m.then_inc(S("u_T"), 1)

            def gate_free(c):
                if c < 2:
                    pe.wait_ge(S("lat"), B("lat") + 2 * (c + 1))
                else:
                    pe.wait_ge(S("gatev"), B("gatev") + 2 * (c - 1))
            linear("gate", "pre.xl", 4, free=gate_free)
            lat = W(3, 0, 2 * 704).rearrange("p (t n) -> p t n", t=NT)
            pe.wait_ge(S("lat_n"), B("lat_n") + 4)
            pe.wait_ge(S("u_put"), B("u_put") + 4)
            for kt in range(5):
                for t in range(NT):
                    m = turn(ps[:, 4 + kt // 2, (kt % 2) * SEQ + t * P:(kt % 2) * SEQ + (t + 1) * P],
                             lat[:, t, kt * P:(kt + 1) * P])
                if kt % 2 or kt == 4:
                    m.then_inc(S("lq.T"), 1)
            pe.wait_ge(S("gatev"), B("gatev") + 8)
            pe.wait_ge(S("lq.xl"), B("lq.xl") + 5)
            for j in range(4):
                s = arrive(("uq", j))
                w4 = [x[:, s, 0:3 * 384].rearrange("p (k i c) -> p k i c", k=3, i=2) for x in (wh, wl)]
                if j >= 2:
                    pe.wait_ge(S("qn"), B("qn") + j - 1)
                for i in range(2):
                    for kt in range(3):
                        mm3(ps[:, j % 2, i * SEQ:(i + 1) * SEQ], w4[0][:, kt, i, 0:NOPE], w4[1][:, kt, i, 0:NOPE],
                            xh[:, kt, :], xl[:, kt, :], kt == 0, kt == 2)
                for t in range(NT):
                    for kt in range(3):
                        m = mm3(ps[:, 2 + t, j * P:(j + 1) * P], xh[:, kt, tok(t)], xl[:, kt, tok(t)],
                                w4[0][:, kt, :, NOPE:NOPE + ROPE], w4[1][:, kt, :, NOPE:NOPE + ROPE], kt == 0, kt == 2)
                m.then_inc(w_used[s], 1)
            for j in range(2):
                s = arrive(("ukv", j))
                w4 = [x[:, s, :].rearrange("p (k i c) -> p k i c", k=2, i=4) for x in (wh, wl)]
                if j:
                    pe.wait_ge(S("kn"), B("kn") + 2)
                    pe.wait_ge(S("vt"), B("vt") + 2)
                for i in range(4):
                    for kt in range(2):
                        mm3(ps[:, 4 + i // 2, (i % 2) * SEQ:(i % 2 + 1) * SEQ], w4[0][:, kt, i, 0:NOPE], w4[1][:, kt, i, 0:NOPE],
                            xh[:, 3 + kt, :], xl[:, 3 + kt, :], kt == 0, kt == 1)
                for t in range(NT):
                    for kt in range(2):
                        m = mm3(ps[:, 6 + t, :], xh[:, 3 + kt, tok(t)], xl[:, 3 + kt, tok(t)],
                                w4[0][:, kt, :, NOPE:NOPE + VD], w4[1][:, kt, :, NOPE:NOPE + VD], kt == 0, kt == 1)
                m.then_inc(w_used[s], 1)
            ro = W(3, 0, 1280).rearrange("p (t n) -> p t n", t=NT)
            pe.wait_ge(S("roped"), B("roped") + 2)
            pe.wait_ge(S("qn"), B("qn") + 4)
            for kt in range(5):
                b = (0, 0, 1, 1, 2)[kt]
                for t in range(NT):
                    m = turn(ps[:, b, (kt % 2) * SEQ + t * P:(kt % 2) * SEQ + (t + 1) * P], ro[:, t, kt * P:(kt + 1) * P])
                if kt in (1, 3, 4):
                    m.then_inc(S("ro_T"), 1)
            qn = W3(4, NH)
            kn = W3(9, NH)
            qr = W(1, 256, 5 * SEQ).rearrange("p (a n) -> p a n", a=5)
            vt = W3(5, NT)
            pT = [W(8, 1152 + b * 384, 384) for b in range(2)]
            pp = [W3(10, NT, 512 * b, 512) for b in range(2)]
            pe.wait_ge(S("ro_put"), B("ro_put") + 3)
            pe.wait_ge(S("kn"), B("kn") + 4)
            pe.wait_ge(S("vt"), B("vt") + 4)

            def scores(i):
                if i >= 2:
                    pe.wait_ge(S("at.sc"), B("at.sc") + 2 * (i - 1))
                rows = slice(64 * (i % 2), 64 * (i % 2) + 64)
                for t in range(NT):
                    nk = P * (t + 1)
                    o = ps[:, i % 2, t * SEQ:t * SEQ + nk]
                    pe.matmul(o, qn[:, i, tok(t)], kn[:, i, 0:nk], start=True, stop=False)
                    m = pe.matmul(o, qr[rows, i // 2, tok(t)], qr[rows, 4, 0:nk], start=False, stop=True)
                m.then_inc(S("at.s"), 1)

            def weigh(i):
                pe.wait_ge(S("at.p"), B("at.p") + 2 * (i + 1))
                if i >= 2:
                    pe.wait_ge(S("at.pT"), B("at.pT") + i - 1)
                b = i % 2
                turn(ps[:, 2 + b, 0:P], pp[b][:, 0, 0:P])
                turn(ps[:, 2 + b, P:2 * P], pp[b][:, 1, 0:P])
                turn(ps[:, 2 + b, 2 * P:3 * P], pp[b][:, 1, P:SEQ]).then_inc(S("at.T"), 1)
                pe.wait_ge(S("at.pT"), B("at.pT") + i + 1)
                if i >= 2:
                    pe.wait_ge(S("at.xl"), B("at.xl") + i - 1)
                hc = slice(i * VD, (i + 1) * VD)
                pe.matmul(ps[:, 4 + b, 0:P], vt[:, 0, hc], pT[b][:, 0:P], start=True, stop=True)
                pe.matmul(ps[:, 4 + b, P:SEQ], vt[:, 0, hc], pT[b][:, P:2 * P], start=True, stop=False)
                pe.matmul(ps[:, 4 + b, P:SEQ], vt[:, 1, hc], pT[b][:, 2 * P:3 * P], start=False, stop=True).then_inc(S("at.o"), 1)

            scores(0)
            for i in range(NH):
                if i + 1 < NH:
                    scores(i + 1)
                weigh(i)

            def ao_free(c):
                if c == 0:
                    pe.wait_ge(S("at.pT"), B("at.pT") + NH)
                    pe.wait_ge(S("at.sc"), B("at.sc") + 2 * NH)
            linear("attn_out", "at.xl", 2, free=ao_free)
            cv = W3(2, KT)
            pe.wait_ge(S("conv_step"), B("conv_step") + CK * KT)
            for kt in range(KT):
                m = pe.matmul(ps[:, 4, 0:SEQ], ones[:, :], cv[:, kt, :], start=kt == 0, stop=kt == KT - 1)
            m.then_inc(S("cmean"), 1)
            pe.wait_ge(S("csq"), B("csq") + 1)
            sq = W3(5, KT)
            for kt in range(KT):
                m = pe.matmul(ps[:, 5, 0:SEQ], ones[:, :], sq[:, kt, :], start=kt == 0, stop=kt == KT - 1)
            m.then_inc(S("cvar"), 1)
            linear("conv_out", "cv.xl", 2, free=lambda c: pe.wait_ge(S("yb"), B("yb") + 2 * (c + 1)))
            pe.wait_ge(S("ymix"), B("ymix") + 4)
            ym = W3(9, NT)
            for kp in range(4):
                for j in range(2):
                    for t in range(NT):
                        kt = 2 * kp + j
                        m = turn(ps[:, 4 + kp, j * SEQ + t * P:j * SEQ + (t + 1) * P], ym[:, t, kt * P:(kt + 1) * P])
                m.then_inc(S("ym.T"), 1)
            linear("out", "ym.xl", 2)
            norm_transposes("pre2")
            mlp_loop()

        @block.scalar
        def _(act):
            n_chain = [0]

            def link(ins):
                ins.then_inc(S("act_chain"), 1)
                n_chain[0] += 1
                act.wait_ge(S("act_chain"), B("act_chain") + n_chain[0])

            def split_hi(s, use, loaded, width=SLOT):
                act.wait_ge(raw_loaded[s], loaded)
                if not isinstance(use, int) or use > 0:
                    act.wait_ge(w_used[s], use)
                if not isinstance(use, int):
                    act.wait_ge(raw_loaded[s], 16)
                act.activation(wh[:, s, 0:width], raw[:, s, 0:width], ACT.Copy).then_inc(hi_ready[s], 1)

            def split(*names):
                for name in names:
                    s, use, loaded, width = plan.at[name]
                    split_hi(s, use, loaded, width)

            def split_all(what, n, k=2):
                split(*[(what, c, j) for c in range(n) for j in range(k)])

            def norm_std(name):
                act.wait_ge(S(name + ".ss"), B(name + ".ss") + 1)
                act.activation(nsd[name], nss[name], ACT.Sqrt).then_inc(S(name + ".std"), 1)

            def norm_hi(name, gain, base, dst=None, sem=".xh"):
                for kp in range(4):
                    act.wait_ge(S(name + ".T"), B(name + ".T") + kp + 1)
                    for j in range(2):
                        kt = 2 * kp + j
                        d = xh if dst is None else dst
                        act.activation(d[:, kt, :], ps[:, 4 + kp, j * SEQ:(j + 1) * SEQ], ACT.Identity,
                                       scale=col(gain, base + kt)).then_inc(S(name + sem), 1)

            def norm_modulated_hi(name):
                hT = W3(7, KT) if name == "pre" else W3(2, KT)
                act.wait_ge(S(name + ".hT"), B(name + ".hT") + KT)
                for k in range(2):
                    o = slice(4 * k, 4 * k + 4)
                    act.activation(xh[:, o, :], hT[:, o, :], ACT.Copy).then_inc(S(name + ".xh"), 1)

            def copy_hi(name, banks):
                for kp, b in enumerate(banks):
                    act.wait_ge(S(name + ".T"), B(name + ".T") + kp + 1)
                    act.activation(xh[:, 2 * kp:2 * kp + 2, :], ps[:, b, :].rearrange("p (a n) -> p a n", a=2), ACT.Copy)\
                       .then_inc(S(name + ".xh"), 1)

            def ffn_loop(f, uses, loads, per, fn):
                def gu(k, c):
                    split_hi(k, uses[k] + c, loads[k] + per[k] * c + per[k])

                def body(i, last):
                    if not last:
                        gu(0, i + 1)
                    act.wait_ge(w_used[1], uses[1] + i + 1)
                    if not isinstance(i, int):
                        act.wait_ge(S(f + ".h"), B(f + ".h") + i)
                        act.wait_ge(S(f + ".h"), B(f + ".h") + 1)
                    elif i > 0:
                        act.wait_ge(S(f + ".h"), B(f + ".h") + i)
                    for t in range(NT):
                        act.activation(silu[:, t, :], ps[:, 4 + t, 0:FC], fn).then_inc(S(f + ".act"), 1)
                    if not last:
                        gu(1, i + 1)
                    act.wait_ge(S(f + ".mT"), B(f + ".mT") + i + 1)
                    act.wait_ge(w_used[2], uses[2] + i)
                    act.wait_ge(S(f + ".mT"), B(f + ".mT") + 1)
                    act.activation(gh[:, :, :], ps[:, 6, :].rearrange("p (a n) -> p a n", a=2), ACT.Copy).then_inc(S(f + ".gh"), 1)
                    split_hi(2, uses[2] + i, loads[2] + per[2] * i + per[2])

                gu(0, 0)
                gu(1, 0)
                body(0, False)
                with act.Fori(1, NFFN - 1) as i:
                    body(i, False)
                body(NFFN - 1, True)

            def mlp_loop():
                uses, loads = plan.at["mlp"]

                def up(s, use):
                    split_hi(s, uses[s] + use, loads[s] + 16 * use + 16)

                def body(c, s, use, s_next, use_next, last):
                    if not last:
                        up(s_next, use_next)
                    act.wait_ge(w_used[s], uses[s] + use + 1)
                    if not (isinstance(c, int) and c == 0):
                        act.wait_ge(S("mlp.h"), B("mlp.h") + c)
                        act.wait_ge(S("mlp.h"), B("mlp.h") + 1)
                    for t in range(NT):
                        act.activation(silu[:, t, :], ps[:, 4 + t, 0:FC], ACT.Relu).then_inc(S("mlp.act"), 1)
                    act.wait_ge(S("mlp.mT"), B("mlp.mT") + c + 1)
                    act.wait_ge(w_used[2], uses[2] + c)
                    act.wait_ge(S("mlp.mT"), B("mlp.mT") + 1)
                    act.activation(gh[:, :, :], ps[:, 6, :].rearrange("p (a n) -> p a n", a=2), ACT.Copy).then_inc(S("mlp.gh"), 1)
                    split_hi(2, uses[2] + c, loads[2] + 16 * c + 16)

                up(0, 0)
                body(0, 0, 0, 1, 0, False)
                with act.Fori(0, NMLP // 2 - 1) as i:
                    body(i * 2 + 1, 1, i, 0, i + 1, False)
                    body(i * 2 + 2, 0, i + 1, 1, i + 1, False)
                body(NMLP - 1, 1, NMLP // 2 - 1, 0, 0, True)

            def rows(ap):
                return ap.rearrange("l (k p) -> (l k) p", p=P)

            act.dma_start(h[:, :, :], A["x"][0].rearrange("(t p) n -> p t n", p=P)).then_inc(S("x_loaded"), 16)
            act.dma_start(masks[:, :], masks_d).then_inc(S("masks"), 16)
            vr = W(6, 0, P)

            def row_load(name, src, k):
                r = ROWS[name]
                d = vr[r:r + k, :] if r < P else W(6, P, P)[r - P:r - P + k, :]
                act.dma_start(d, src).then_inc(S("rows"), 16)
            row_load("mix_norm", rows(A["mix_norm"]), 16)
            row_load("ffn_norm", rows(A["ffn_norm"]), 16)
            row_load("mu", rows(A["rwkv_mu"][0]), 48)
            row_load("sgu_bias", A["sgu_bias"][0], 4)
            row_load("pool_scale", rows(A["pool_scale"]), 4)
            row_load("g_pre_mix", rows(A["g_pre_mix_2"]), 8)
            row_load("g_pre_mlp", rows(A["g_pre_mlp_2"]), 8)
            row_load("cn_g", rows(A["conv_norm_g_2"]), 8)
            row_load("cn_b", rows(A["conv_norm_b_2"]), 8)
            row_load("conv_b", rows(A["conv_b_2"]), 8)
            row_load("q_norm", rows(A["q_norm_g_2"]), 3)
            row_load("kv_norm", rows(A["kv_norm_g_2"]), 2)
            act.dma_start(W(6, 256, D)[0:CK, :], A["conv_w_2"][0]).then_inc(S("rows"), 16)
            act.dma_start(ccol, A["c_2"][0].rearrange("(p k) -> p k", k=KT)).then_inc(S("rows"), 16)
            act.dma_start(W3(4, 4, 0, 512), A["sgu_w_s"][0].rearrange("h i j -> i h j")).then_inc(S("mixw"), 16)
            act.dma_start(W3(4, 4, 1024, 512), A["pool_w"][0].rearrange("g c d -> c g d")).then_inc(S("mixw"), 16)
            act.dma_start(W(4, 1536, 512), A["sgu_gain"][0].partition_broadcast(P)).then_inc(S("mixw"), 16)
            act.dma_start(W(3, 0, 12 * P), pool_d).then_inc(S("mixw"), 16)
            act.dma_start(posi[:, :], A["positions_2"][0].rearrange("(t p) -> p t", p=P), allow_slow_non_contiguous=True).then_inc(S("pos"), 16)

            norm_std("mix0")
            act.wait_ge(S("cols"), B("cols") + 2)
            norm_hi("mix0", "mix_norm", 0)
            split(("ab_in", 0, 0), ("ab_in", 0, 1), ("ab_in", 1, 0))
            za = W3(0, NT)
            zb = W3(1, NT, 0, 1024)
            used(act, ("ab_in", 0, 1))
            for t in range(NT):
                act.activation(za[:, t, 0:AW], ps[:, t, :], ACT.Gelu).then_inc(S("u_ready"), 1)
            split(("ab_in", 1, 1), ("ab_in", 2, 0), ("ab_in", 2, 1))
            used(act, ("ab_in", 1, 1))
            for t in range(NT):
                act.activation(za[:, t, AW:D], ps[:, 2 + t, :], ACT.Gelu).then_inc(S("v_ready"), 1)
            act.wait_ge(S("v_ss"), B("v_ss") + 1)
            act.activation(vsd, vss, ACT.Sqrt).then_inc(S("v_std"), 1)
            used(act, ("ab_in", 2, 1))
            for t in range(NT):
                act.activation(zb[:, t, :], ps[:, t, :], ACT.Copy).then_inc(S("zb_ready"), 1)
            split(("ab_out", 0, 0), ("ab_out", 0, 1))
            used(act, ("ab_in", 2, 1))
            for b in range(2):
                act.wait_ge(S("yb_T"), B("yb_T") + b + 1)
                for j in range(2):
                    kt = 2 * b + j
                    act.activation(xh[:, 4 + kt, :], ps[:, 4 + b, j * SEQ:(j + 1) * SEQ], ACT.Identity,
                                   scale=col("pool_scale", kt)).then_inc(S("ab.yh"), 1)
            for b in range(2):
                act.wait_ge(S("ya_T"), B("ya_T") + b + 1)
                act.activation(xh[:, 2 * b:2 * b + 2, :], ps[:, 6 + b, :].rearrange("p (a n) -> p a n", a=2), ACT.Copy)\
                   .then_inc(S("ab.xh"), 1)
            split(("ab_out", 1, 0), ("ab_out", 1, 1))

            norm_std("ffn0")
            norm_hi("ffn0", "ffn_norm", 0)
            u_, l_ = plan.at["ffn0"]
            ffn_loop("ffn0", u_, l_, (32, 32, 16), ACT.Silu)

            act.wait_ge(S("ffn0.h"), B("ffn0.h") + NFFN)
            act.wait_ge(S("ffn0.mT"), B("ffn0.mT") + NFFN)
            act.dma_start(W3(10, KT, 0, 512), A["rwkv_w1"][0].rearrange("(a p) n -> p a n", p=P)).then_inc(S("rw_w1"), 16)
            act.dma_start(W3(10, KT, 512, 512), A["rwkv_a1"][0].rearrange("(a p) n -> p a n", p=P)).then_inc(S("rw_w1"), 16)
            act.dma_start(W3(6, KT, 0, KT * GRANK), A["rwkv_g1"][0].rearrange("(a p) n -> p a n", p=P)).then_inc(S("rw_w1"), 16)
            act.dma_start(W(4, 0, D)[0:RANK, :], A["rwkv_w2"][0]).then_inc(S("rw_w2"), 16)
            act.dma_start(W(4, 0, D)[RANK:RANK + 1, :], A["rwkv_w0"]).then_inc(S("rw_w2"), 16)
            act.dma_start(W(4, D, D)[0:RANK, :], A["rwkv_a2"][0]).then_inc(S("rw_w2"), 16)
            act.dma_start(W(4, D, D)[RANK:RANK + 1, :], A["rwkv_a0"]).then_inc(S("rw_w2"), 16)
            act.dma_start(W(9, 0, D), A["rwkv_k_k"][0].partition_broadcast(P)).then_inc(S("rw_vec"), 16)
            act.dma_start(W(9, D, D), A["rwkv_k_a"][0].partition_broadcast(P)).then_inc(S("rw_vec"), 16)
            act.dma_start(side[:, :], A["rwkv_r_k"][0].rearrange("h c -> (h c)").partition_broadcast(P)).then_inc(S("rw_vec"), 16)
            norm_std("mix1")
            norm_hi("mix1", "mix_norm", KT, dst=W3(0, KT), sem=".hT")
            split(("k", 0, 0), ("k", 0, 1), ("k", 1, 0))
            act.wait_ge(S("rank_T"), B("rank_T") + 1)
            act.activation(lowr[0:RANK, 0:SEQ], ps[0:RANK, 4, 0:SEQ], ACT.Tanh).then_inc(S("rank"), 1)
            act.wait_ge(S("rank_T"), B("rank_T") + 2)
            act.activation(lowr[0:RANK, SEQ:2 * SEQ], ps[0:RANK, 5, 0:SEQ], ACT.Copy).then_inc(S("rank"), 1)
            act.wait_ge(S("rank_T"), B("rank_T") + 3)
            act.activation(lowr[:, 2 * SEQ:3 * SEQ], ps[:, 6, 0:SEQ], ACT.Sigmoid)
            act.activation(lowr[0:GRANK - P, 3 * SEQ:4 * SEQ], ps[0:GRANK - P, 7, 0:SEQ], ACT.Sigmoid).then_inc(S("rank"), 1)
            sig = W3(7, NT)
            rate = W3(8, NT)
            for n, (dst, name) in enumerate(((sig, "sig"), (rate, "rate"))):
                for t in range(NT):
                    for c in range(2):
                        act.wait_ge(S("logit"), B("logit") + 4 * n + 2 * t + c + 1)
                        act.activation(dst[:, t, c * 512:(c + 1) * 512], ps[:, 2 * t + c, :], ACT.Sigmoid).then_inc(S(name), 1)
            rkv = {"k": W3(5, NT), "r": W3(4, NT), "v": W3(6, NT)}
            mixes = {"k": W3(3, KT), "r": W3(2, KT), "v": W3(3, KT)}

            def mix_hi(n, what, k):
                act.wait_ge(S("mixed"), B("mixed") + 4 + n)
                if n:
                    used(act, ("krv"[n - 1], 1, k))
                act.activation(xh[:, 4 * k:4 * k + 4, :], mixes[what][:, 4 * k:4 * k + 4, :], ACT.Copy).then_inc(S("rkv.xh"), 1)

            def take(n, what, c):
                used(act, (what, c, 1))
                for t in range(NT):
                    act.activation(rkv[what][:, t, c * 512:(c + 1) * 512], ps[:, 2 * c + t, :], ACT.Copy).then_inc(S("rkv"), 1)

            mix_hi(0, "k", 0)
            mix_hi(0, "k", 1)
            split(("k", 1, 1), ("r", 0, 0))
            take(0, "k", 0)
            split(("r", 0, 1),)
            mix_hi(1, "r", 0)
            mix_hi(1, "r", 1)
            split(("r", 1, 0))
            take(0, "k", 1)
            act.wait_ge(S("kk_ss"), B("kk_ss") + 1)
            act.activation(kss, kss, ACT.Sqrt).then_inc(S("kk_norm"), 1)
            split(("r", 1, 1), ("v", 0, 0))
            take(1, "r", 0)
            split(("v", 0, 1))
            mix_hi(2, "v", 0)
            mix_hi(2, "v", 1)
            split(("v", 1, 0))
            take(1, "r", 1)
            split(("v", 1, 1))
            act.wait_ge(S("cum"), B("cum") + 1)
            act.wait_ge(S("rkv.xl"), B("rkv.xl") + 24)
            for t in range(NT):
                for c in range(2):
                    n = 2 * t + c
                    if n:
                        act.wait_ge(S("scaled"), B("scaled") + 4 * n)
                    cum = ps[:, 4 + n, :]
                    act.activation(W(3, 0, 512), cum, ACT.Exp, scale=-DECAY)
                    act.activation(W(3, 512, 512), cum, ACT.Exp, scale=DECAY).then_inc(S("cum_read"), 1)
                    act.wait_ge(S("cum_prev"), B("cum_prev") + n + 1)
                    act.activation(W(3, 1536, 512), W(3, 1024, 512), ACT.Exp, scale=-DECAY).then_inc(S("exps"), 1)
            take(2, "v", 0)
            take(2, "v", 1)
            split(("o", 0, 0), ("o", 0, 1), ("o", 1, 0))
            act.wait_ge(S("pc_T"), B("pc_T") + 1)
            pcv = pc.rearrange("p (h x c) -> p h x c", h=RH // 2, x=2)
            for x in range(2):
                act.activation(pcv[0:64, :, x, :], ps[64 * x:64 * x + 64, 4, 0:32].rearrange("p (h c) -> p h c", c=4), ACT.Exp,
                               scale=-DECAY).then_inc(S("pc"), 1)

            tmp = WKV_TMP(W)
            gs = wide[:, 3 * 2048:4 * 2048]
            fts = W3(8, 2).rearrange("p a (h c) -> p a h c", h=RH)
            yv = W(0).rearrange("p (t h c) -> p t h c", t=NT, h=RH)
            gall = WKV_G(W, side)

            def evac(sem, k, b, dst, done, n=512):
                act.wait_ge(S("wkv." + sem), B("wkv." + sem) + k)
                act.activation(tmp[dst][:, 0:n], ps[:, b, 0:n], ACT.Copy).then_inc(S("wkv." + done), 1)

            for g in range(8):
                t, h0 = g // 4, 4 * (g % 4)
                act.wait_ge(S("wkv.T"), B("wkv.T") + g + 1)
                for b in range(2):
                    act.activation(tmp["ar"][0:64, b * 512:(b + 1) * 512], ps[0:64, b, :], ACT.Copy).then_inc(S("wkv.ar"), 1)
                evac("x2", g + 1, 1, "x2", "x2c")
                evac("x2t", g + 1, 2, "x2t", "x2c")
                evac("gkv", g + 1, 3, "gkv", "gkvc", 256)
                evac("x4", g + 1, 4, "x4", "x4c")
                evac("x4t", g + 1, 5, "x4t", "x4c")
                evac("x8", g + 1, 2, "x8", "x8c")
                evac("r1", g + 1, 4, "r1", "r1c")
                evac("mt", g + 1, 5, "mt", "mtc")
                act.wait_ge(S("wkv.fg"), B("wkv.fg") + g + 1)
                for x in range(2):
                    c = 2 * t + x
                    if c < 3:
                        act.activation(gall[c][0:64, h0:h0 + 4, :],
                                       ps[0:64, G_BANK[x], 0:256].rearrange("p (u c) -> p u c", u=4), ACT.Copy)
                act.wait_ge(S("wkv.eh"), B("wkv.eh") + g + 1)
                act.activation(yv[:, t, h0:h0 + 4, :], ps[:, 6, 0:256].rearrange("p (u c) -> p u c", u=4), ACT.Copy)\
                   .then_inc(S("wkv.hc"), 1)

            states = wide[:, 4 * 2048:5 * 2048].rearrange("p (t n) -> p t n", t=NT)
            chain = W(5, 0, D)
            act.wait_ge(S("wkv.done"), B("wkv.done") + 8)
            act.dma_start(W(7, 0, D), A["rwkv_ln_w"][0].partition_broadcast(P)).then_inc(S("ln_vec"), 16)
            act.dma_start(W(7, D, D), A["rwkv_ln_b"][0].partition_broadcast(P)).then_inc(S("ln_vec"), 16)
            act.dma_start(W(9, 0, D), A["rwkv_g2"][0][0:P, :]).then_inc(S("g2"), 16)
            act.dma_start(W(9, D, D)[0:GRANK - P, :], A["rwkv_g2"][0][P:GRANK, :]).then_inc(S("g2"), 16)
            for c in (1, 2, 3):
                act.wait_ge(S("state"), B("state") + c)
                p = c % 2
                act.activation(states[64 * p:64 * p + 64, c // 2, :], chain[0:64, :], ACT.Copy).then_inc(S("state_put"), 1)
            act.wait_ge(S("gn_var"), B("gn_var") + 1)
            act.activation(gvar, gvar, ACT.Sqrt).then_inc(S("gn_std"), 1)
            copy_hi("rw", (6, 7, 0, 1))
            split(("o", 1, 1))

            norm_std("ffn1")
            norm_hi("ffn1", "ffn_norm", KT)
            act.wait_ge(S("rows"), B("rows") + 16 * 14)
            act.activation(ccol, ccol, ACT.Silu).then_inc(S("c_act"), 1)
            u_, l_ = plan.at["ffn1"]
            ffn_loop("ffn1", u_, l_, (32, 32, 16), ACT.Silu)

            act.dma_start(W(8, 0, D), A["final_norm"].partition_broadcast(P)).then_inc(S("fin_vec"), 16)
            act.dma_start(W(6, 0, D), A["g_post_mix_2"][0].partition_broadcast(P)).then_inc(S("post_vec"), 16)
            act.dma_start(W(6, D, D), A["g_post_mlp_2"][0].partition_broadcast(P)).then_inc(S("post_vec"), 16)
            norm_std("fin")
            norm_std("pre")
            norm_modulated_hi("pre")
            split(("glu", 0, 0), ("glu", 0, 1), ("glu", 1, 0))
            act.wait_ge(S("angle"), B("angle") + 1)
            act.activation(lowr[:, 0:64], lowr[:, 0:64], ACT.Sin)
            act.activation(lowr[:, 64:128], lowr[:, 64:128], ACT.Sin).then_inc(S("sincos"), 1)
            ub = lowr[:, 512:1024].rearrange("p (t n) -> p t n", t=NT)
            nxt = [("glu", 1, 1), ("glu", 2, 0), ("glu", 2, 1), ("glu", 3, 0), ("glu", 3, 1), ("lat", 0, 0), ("lat", 0, 1), ("lat", 1, 0)]
            for c in range(4):
                used(act, ("glu", c, 1))
                if c:
                    act.wait_ge(S("glu"), B("glu") + 2 * c)
                for t in range(NT):
                    act.activation(ub[:, t, :], ps[:, 2 * (c % 2) + t, 256:512], ACT.Sigmoid).then_inc(S("glu_s"), 1)
                split(*nxt[2 * c:2 * c + 2])
            lat = W(3, 0, 2 * 704).rearrange("p (t n) -> p t n", t=NT)
            used(act, ("lat", 0, 1))
            for t in range(NT):
                act.activation(lat[:, t, 0:QL], ps[:, t, 0:QL], ACT.Copy).then_inc(S("lat"), 1)
            split(("lat", 1, 1), ("gate", 0, 0))
            used(act, ("lat", 1, 1))
            for t in range(NT):
                act.activation(lat[:, t, QL:704], ps[:, 2 + t, 0:KL + ROPE], ACT.Copy).then_inc(S("lat"), 1)
            split(("gate", 0, 1))
            up_ = U_PAD(wide)
            for c in range(4):
                act.wait_ge(S("u_T"), B("u_T") + c + 1)
                act.activation(up_[:, 2 * c:2 * c + 2, CK - 1:CK - 1 + SEQ], ps[:, 4 + c, :].rearrange("p (a n) -> p a n", a=2),
                               ACT.Copy).then_inc(S("u_put"), 1)
            split(("gate", 1, 0))
            act.wait_ge(S("lat_ss"), B("lat_ss") + 1)
            act.activation(qsd, qss, ACT.Sqrt).then_inc(S("lat_std"), 1)
            gates = wide[:, 6 * 2048:8 * 2048].rearrange("p (t n) -> p t n", t=NT)
            nxt = [[("gate", 1, 1), ("gate", 2, 0)], [("gate", 2, 1), ("gate", 3, 0)], [("gate", 3, 1), ("uq", 0)], [("uq", 1), ("uq", 2)]]
            for c in range(4):
                used(act, ("gate", c, 1))
                if c == 0:
                    act.wait_ge(S("gates"), B("gates") + 4)
                for t in range(NT):
                    act.activation(gates[:, t, c * 512:(c + 1) * 512], ps[:, 2 * (c % 2) + t, :], ACT.Sigmoid).then_inc(S("gatev"), 1)
                split(*nxt[c])
            for kt in range(5):
                act.wait_ge(S("lq.T"), B("lq.T") + kt // 2 + 1)
                act.activation(xh[:, kt, :], ps[:, 4 + kt // 2, (kt % 2) * SEQ:(kt % 2 + 1) * SEQ], ACT.Identity,
                               scale=col("q_norm", kt) if kt < 3 else col("kv_norm", kt - 3)).then_inc(S("lq.xh"), 1)
            qn = W3(4, NH)
            kn = W3(9, NH)
            nxt = [[("uq", 3)], [("ukv", 0)], [("ukv", 1)], []]
            for j in range(4):
                used(act, ("uq", j))
                act.activation(qn[:, 2 * j:2 * j + 2, :], ps[:, j % 2, :].rearrange("p (a n) -> p a n", a=2), ACT.Copy).then_inc(S("qn"), 1)
                split(*nxt[j])
            qraw = W(8, 0, 2 * 9 * 64).rearrange("p (t n) -> p t n", t=NT)
            for t in range(NT):
                act.activation(qraw[:, t, 0:512], ps[:, 2 + t, :], ACT.Copy).then_inc(S("qraw"), 1)
            for j in range(2):
                used(act, ("ukv", j))
                for b in range(2):
                    act.activation(kn[:, 4 * j + 2 * b:4 * j + 2 * b + 2, :], ps[:, 4 + b, :].rearrange("p (a n) -> p a n", a=2), ACT.Copy)\
                       .then_inc(S("kn"), 1)
                vt = W3(5, NT)
                for t in range(NT):
                    act.activation(vt[:, t, j * 512:(j + 1) * 512], ps[:, 6 + t, :], ACT.Copy).then_inc(S("vt"), 1)
            qr = W(1, 256, 5 * SEQ).rearrange("p (a n) -> p a n", a=5)
            for b in range(3):
                n = 2 if b < 2 else 1
                act.wait_ge(S("ro_T"), B("ro_T") + b + 1)
                act.activation(qr[:, 2 * b:2 * b + n, :], ps[:, b, 0:n * SEQ].rearrange("p (a n) -> p a n", a=n), ACT.Copy)\
                   .then_inc(S("ro_put"), 1)
            split(("attn_out", 0, 0), ("attn_out", 0, 1), ("attn_out", 1, 0))
            pp = [W3(10, NT, 512 * b, 512) for b in range(2)]
            pT = [W(8, 1152 + b * 384, 384) for b in range(2)]

            def weigh(i):
                b = i % 2
                act.wait_ge(S("at.T"), B("at.T") + i + 1)
                if i >= 2:
                    act.wait_ge(S("at.o"), B("at.o") + i - 1)
                act.activation(pT[b], ps[:, 2 + b, 0:384], ACT.Copy).then_inc(S("at.pT"), 1)
                act.wait_ge(S("at.o"), B("at.o") + i + 1)
                act.activation(xh[:, i, :], ps[:, 4 + b, 0:SEQ], ACT.Copy).then_inc(S("at.xh"), 1)
            for i in range(NH):
                b = i % 2
                act.wait_ge(S("at.max"), B("at.max") + i + 1)
                for t in range(NT):
                    nk = P * (t + 1)
                    act.activation(pp[b][:, t, 0:nk], pp[b][:, t, 0:nk], ACT.Exp, bias=amax[:, 2 * b + t:2 * b + t + 1],
                                   accum_out=asum[:, 2 * b + t:2 * b + t + 1]).then_inc(S("at.e"), 1)
                if i:
                    weigh(i - 1)
            weigh(NH - 1)
            split(("attn_out", 1, 1), ("conv_out", 0, 0), ("conv_out", 0, 1))
            act.wait_ge(S("cv_ss"), B("cv_ss") + 1)
            act.activation(lowr[:, 256:512], lowr[:, 256:512], ACT.Sqrt).then_inc(S("cv_std"), 1)
            cv = W3(2, KT)
            act.wait_ge(S("cv_n"), B("cv_n") + 1)
            for kt in range(KT):
                act.activation(cv[:, kt, :], cv[:, kt, :], ACT.Silu, bias=col("cn_b", kt), scale=col("cn_g", kt))\
                   .then_inc(S("cv_act"), 1)
            used(act, ("attn_out", 1, 1))
            act.wait_ge(S("cv_act"), B("cv_act") + KT)
            for k in range(2):
                act.activation(xh[:, 4 * k:4 * k + 4, :], cv[:, 4 * k:4 * k + 4, :], ACT.Copy).then_inc(S("cv.xh"), 1)
            split(("conv_out", 1, 0), ("conv_out", 1, 1), ("out", 0, 0), ("out", 0, 1))
            used(act, ("conv_out", 1, 1))
            copy_hi("ym", (4, 5, 6, 7))
            split(("out", 1, 0), ("out", 1, 1))
            norm_std("post1")
            norm_std("pre2")
            norm_modulated_hi("pre2")
            mlp_loop()
            norm_std("post2")
            for t in range(NT):
                act.wait_ge(S("post2.add"), B("post2.add") + t + 1)
                act.dma_start(out[0, t * P:(t + 1) * P, :], h[:, t, :]).then_inc(S("stored"), 16)

        @block.vector
        def _(v):
            n_chain = [0]

            def link(ins):
                ins.then_inc(S("dve_chain"), 1)
                n_chain[0] += 1
                v.wait_ge(S("dve_chain"), B("dve_chain") + n_chain[0])

            def f32(ap):
                return ap.bitcast(F32)

            def split_lo(s, use, width=SLOT):
                v.wait_ge(hi_ready[s], use + 1)
                if not isinstance(use, int):
                    v.wait_ge(hi_ready[s], 1)
                v.tensor_tensor(wl[:, s, 0:width], raw[:, s, 0:width], f32(wh[:, s, 0:width]), ALU.subtract).then_inc(lo_ready[s], 1)

            def split(*names):
                for name in names:
                    s, use, _, width = plan.at[name]
                    split_lo(s, use, width)

            def mean_square(src, n, dst, junk):
                return v.tensor_tensor_reduce(out=junk, in0=src, in1=src, scale=1.0 / n, scalar=EPS, op0=ALU.mult, op1=ALU.add,
                                              accum_out=dst)

            def norm(name, src=None, dst=None):
                src = h if src is None else src
                dst = hn if dst is None else dst
                for t in range(NT):
                    m = mean_square(src[:, t, :], D, nss[name][:, t:t + 1], dst[:, t, :])
                m.then_inc(S(name + ".ss"), 1)
                v.wait_ge(S(name + ".std"), B(name + ".std") + 1)
                link(v.reciprocal(nrs[name], nsd[name]))
                for t in range(NT):
                    v.tensor_scalar(dst[:, t, :], src[:, t, :], nrs[name][:, t:t + 1], None, ALU.mult).then_inc(S(name + ".hn"), 1)

            def norm_lo(name, gain, base):
                for kp in range(4):
                    v.wait_ge(S(name + ".xh"), B(name + ".xh") + 2 * kp + 2)
                    for j in range(2):
                        kt = 2 * kp + j
                        v.scalar_tensor_tensor(out=xl[:, kt, :], in0=ps[:, 4 + kp, j * SEQ:(j + 1) * SEQ], scalar=col(gain, base + kt),
                                               in1=f32(xh[:, kt, :]), op0=ALU.mult, op1=ALU.subtract).then_inc(S(name + ".xl"), 1)

            def norm_modulated(name, scale, shift):
                hT = W3(7, KT) if name == "pre" else W3(2, KT)
                for kp in range(4):
                    v.wait_ge(S(name + ".T"), B(name + ".T") + kp + 1)
                    for j in range(2):
                        kt = 2 * kp + j
                        v.tensor_scalar(hT[:, kt, :], ps[:, 4 + kp, j * SEQ:(j + 1) * SEQ], scale[:, kt:kt + 1], shift[:, kt:kt + 1],
                                        ALU.mult, ALU.add).then_inc(S(name + ".hT"), 1)
                for k in range(2):
                    v.wait_ge(S(name + ".xh"), B(name + ".xh") + k + 1)
                    o = slice(4 * k, 4 * k + 4)
                    v.wait_ge(S(name + ".hT"), B(name + ".hT") + KT)
                    v.tensor_tensor(xl[:, o, :], hT[:, o, :], f32(xh[:, o, :]), ALU.subtract).then_inc(S(name + ".xl"), 4)

            def copy_lo(name, banks):
                for kp, b in enumerate(banks):
                    v.wait_ge(S(name + ".xh"), B(name + ".xh") + kp + 1)
                    o = slice(2 * kp, 2 * kp + 2)
                    v.tensor_tensor(xl[:, o, :], ps[:, b, :].rearrange("p (a n) -> p a n", a=2), f32(xh[:, o, :]), ALU.subtract)\
                     .then_inc(S(name + ".xl"), 2)

            def add_residual(name):
                for t in range(NT):
                    for c in range(2):
                        o = slice(c * 512, (c + 1) * 512)
                        v.tensor_tensor(h[:, t, o], h[:, t, o], ps[:, 2 * t + c, :], ALU.add).then_inc(S(name), 1)
                v.wait_ge(S(name), B(name) + 4)

            def add_linear(lin, name):
                for c in range(2):
                    used(v, (lin, c, 1))
                    for t in range(NT):
                        o = slice(c * 512, (c + 1) * 512)
                        v.tensor_tensor(h[:, t, o], h[:, t, o], ps[:, 2 * c + t, :], ALU.add).then_inc(S(name), 1)
                v.wait_ge(S(name), B(name) + 4)

            def ada(j):
                for k in range(KT):
                    for b in range(2):
                        n = 16 * j + 2 * k + b
                        if k == 0:
                            v.wait_ge(S(f"ada{b}"), B(f"ada{b}") + 16 * (j + 1))
                            v.wait_ge(S("ada_step"), B("ada_step") + 16 * j) if not (isinstance(j, int) and j == 0) else None
                        else:
                            v.wait_ge(S("ada_step"), B("ada_step") + n - 1)
                        c0 = (2 * j + b) * 256
                        o = ada_acc[:, c0:c0 + 256]
                        v.scalar_tensor_tensor(out=o, in0=ada_raw[b][:, k, :], scalar=ccol[:, k:k + 1], in1=o,
                                               op0=ALU.mult, op1=ALU.add).then_inc(S("ada_step"), 1)

            def ffn_loop(f, uses, with_ada):
                def body(i, last, n=None):
                    if not last:
                        split_lo(0, uses[0] + i + 1)
                    if not (isinstance(i, int) and i == 0):
                        v.wait_ge(S(f + ".mT"), B(f + ".mT") + i)
                    for t in range(NT):
                        v.wait_ge(S(f + ".act"), B(f + ".act") + i * 2 + t + 1)
                        if not isinstance(i, int):
                            v.wait_ge(S(f + ".act"), B(f + ".act") + 1)
                        m = v.tensor_tensor(hmid[:, t, :], silu[:, t, :], ps[:, 4 + t, FC:2 * FC], ALU.mult)
                    m.then_inc(S(f + ".h"), 1)
                    if not last:
                        split_lo(1, uses[1] + i + 1)
                    v.wait_ge(S(f + ".gh"), B(f + ".gh") + i + 1)
                    if not isinstance(i, int):
                        v.wait_ge(S(f + ".gh"), B(f + ".gh") + 1)
                    v.tensor_tensor(gl[:, :, :], ps[:, 6, :].rearrange("p (a n) -> p a n", a=2), f32(gh[:, :, :]), ALU.subtract)\
                     .then_inc(S(f + ".gl"), 1)
                    split_lo(2, uses[2] + i)

                split_lo(0, uses[0])
                split_lo(1, uses[1])
                if with_ada:
                    for i in range(NFFN):
                        body(i, i == NFFN - 1)
                        ada(i)
                else:
                    body(0, False)
                    with v.Fori(1, NFFN - 1) as i:
                        body(i, False)
                    body(NFFN - 1, True)

            def mlp_loop():
                uses, _ = plan.at["mlp"]

                def body(c, s_next, use_next, last):
                    if not last:
                        split_lo(s_next, uses[s_next] + use_next)
                    if not (isinstance(c, int) and c == 0):
                        v.wait_ge(S("mlp.mT"), B("mlp.mT") + c)
                    for t in range(NT):
                        v.wait_ge(S("mlp.act"), B("mlp.act") + c * 2 + t + 1)
                        if not isinstance(c, int):
                            v.wait_ge(S("mlp.act"), B("mlp.act") + 1)
                        m = v.tensor_tensor(hmid[:, t, :], silu[:, t, :], silu[:, t, :], ALU.mult)
                    m.then_inc(S("mlp.h"), 1)
                    v.wait_ge(S("mlp.gh"), B("mlp.gh") + c + 1)
                    if not isinstance(c, int):
                        v.wait_ge(S("mlp.gh"), B("mlp.gh") + 1)
                    v.tensor_tensor(gl[:, :, :], ps[:, 6, :].rearrange("p (a n) -> p a n", a=2), f32(gh[:, :, :]), ALU.subtract)\
                     .then_inc(S("mlp.gl"), 1)
                    split_lo(2, uses[2] + c)

                split_lo(0, uses[0])
                body(0, 1, 0, False)
                with v.Fori(0, NMLP // 2 - 1) as i:
                    body(i * 2 + 1, 0, i + 1, False)
                    body(i * 2 + 2, 1, i + 1, False)
                body(NMLP - 1, 0, 0, True)

            v.wait_ge(S("x_loaded"), B("x_loaded") + 16)
            norm("mix0")
            v.wait_ge(S("cols_T"), B("cols_T") + 1)
            v.tensor_copy(cols[:, 0:CONVW], ps[:, 0, 0:CONVW]).then_inc(S("cols"), 1)
            v.tensor_copy(cols[:, CONVW:NCOL], ps[:, 1, 0:KT * CK]).then_inc(S("cols"), 1)
            v.wait_ge(S("wst_T"), B("wst_T") + 1)
            v.tensor_copy(W(4, 512, 512), ps[:, 2, :]).then_inc(S("wst"), 1)
            v.wait_ge(S("cols"), B("cols") + 2)
            norm_lo("mix0", "mix_norm", 0)
            split(*[("ab_in", n, k) for n in range(3) for k in range(2)])
            za = W3(0, NT)
            v.wait_ge(S("v_ready"), B("v_ready") + 2)
            for t in range(NT):
                m = mean_square(za[:, t, AW:D], AW, vss[:, t:t + 1], W(2, t * 512, 512))
            m.then_inc(S("v_ss"), 1)
            v.wait_ge(S("v_std"), B("v_std") + 1)
            link(v.reciprocal(vrs, vsd))
            v.wait_ge(S("mixw"), B("mixw") + 64)
            for t in range(NT):
                v.scalar_tensor_tensor(out=za[:, t, AW:D], in0=za[:, t, AW:D], scalar=vrs[:, t:t + 1], in1=W(4, 1536, 512),
                                       op0=ALU.mult, op1=ALU.mult).then_inc(S("v_normed"), 1)
            ya = W3(2, NT, 1024, 1024)
            v.wait_ge(S("u_ready"), B("u_ready") + 2)
            for t in range(NT):
                v.wait_ge(S("spatial"), B("spatial") + t + 1)
                for i in range(4):
                    o = slice(i * P, (i + 1) * P)
                    v.scalar_tensor_tensor(out=ya[:, t, o], in0=ps[:, 4 + t, o], scalar=col("sgu_bias", i), in1=za[:, t, o],
                                           op0=ALU.add, op1=ALU.mult).then_inc(S("ya"), 1)
            for b in range(2):
                v.wait_ge(S("pooled_T"), B("pooled_T") + b + 1)
                v.tensor_copy(W(2, b * 512, 512), ps[:, 6 + b, :]).then_inc(S("pooled"), 1)
            split(("ab_out", 0, 0), ("ab_out", 0, 1))
            for b in range(2):
                v.wait_ge(S("ab.yh"), B("ab.yh") + 2 * (b + 1))
                for j in range(2):
                    kt = 2 * b + j
                    v.scalar_tensor_tensor(out=xl[:, 4 + kt, :], in0=ps[:, 4 + b, j * SEQ:(j + 1) * SEQ], scalar=col("pool_scale", kt),
                                           in1=f32(xh[:, 4 + kt, :]), op0=ALU.mult, op1=ALU.subtract).then_inc(S("ab.xl"), 1)
            for b in range(2):
                v.wait_ge(S("ab.xh"), B("ab.xh") + b + 1)
                o = slice(2 * b, 2 * b + 2)
                v.tensor_tensor(xl[:, o, :], ps[:, 6 + b, :].rearrange("p (a n) -> p a n", a=2), f32(xh[:, o, :]), ALU.subtract)\
                 .then_inc(S("ab.xl"), 2)
            split(("ab_out", 1, 0), ("ab_out", 1, 1))
            add_linear("ab_out", "mix0.add")

            norm("ffn0")
            norm_lo("ffn0", "ffn_norm", 0)
            ffn_loop("ffn0", plan.at["ffn0"][0], False)
            v.wait_ge(w_used[2], plan.at["ffn0"][0][2] + NFFN)
            add_residual("ffn0.add")

            norm("mix1")
            hT, xx = W3(0, KT), W3(1, KT)
            v.wait_ge(S("mix1.hT"), B("mix1.hT") + KT)
            v.tensor_tensor(xx[:, :, 1:SEQ], hT[:, :, 0:SEQ - 1], hT[:, :, 1:SEQ], ALU.subtract)
            link(v.tensor_scalar(xx[:, :, 0:1], hT[:, :, 0:1], -1.0, None, ALU.mult))

            def mix(i, dst):
                for kt in range(KT):
                    m = v.scalar_tensor_tensor(out=dst[:, kt, :], in0=xx[:, kt, :], scalar=col("mu", i * KT + kt), in1=hT[:, kt, :],
                                               op0=ALU.mult, op1=ALU.add)
                m.then_inc(S("mixed"), 1)

            def mix_lo(n, src, k):
                v.wait_ge(S("rkv.xh"), B("rkv.xh") + 2 * n + k + 1)
                o = slice(4 * k, 4 * k + 4)
                v.tensor_tensor(xl[:, o, :], src[:, o, :], f32(xh[:, o, :]), ALU.subtract).then_inc(S("rkv.xl"), 4)

            mix(1, W3(2, KT))
            mix(4, W3(3, KT))
            v.wait_ge(S("rank_T"), B("rank_T") + 1)
            mix(5, W3(2, KT))
            v.wait_ge(S("rank_T"), B("rank_T") + 2)
            mix(2, W3(3, KT))
            mix_lo(0, W3(3, KT), 0)
            mix_lo(0, W3(3, KT), 1)
            split(("k", 0, 0), ("k", 0, 1), ("k", 1, 0))
            v.wait_ge(S("rank_T"), B("rank_T") + 3)
            mix(0, W3(2, KT))
            v.wait_ge(S("rkv.xl"), B("rkv.xl") + 8)
            mix(3, W3(3, KT))
            split(("k", 1, 1), ("r", 0, 0), ("r", 0, 1))
            mix_lo(1, W3(2, KT), 0)
            mix_lo(1, W3(2, KT), 1)
            split(("r", 1, 0))
            r, k, vv, sig, rate, kk = W3(4, NT), W3(5, NT), W3(6, NT), W3(7, NT), W3(8, NT), W3(10, NT)

            def vec(w, off):
                return W(w, off, D).unsqueeze(1).to_broadcast([P, NT, D])

            def heads(ap):
                return ap.rearrange("p t (h c) -> p (t h) c", c=HD)

            def per_head(ap):
                return ap.unsqueeze(2).to_broadcast([P, NT * RH, HD])

            t0 = W3(0, NT)
            v.wait_ge(S("rw_vec"), B("rw_vec") + 48)
            v.wait_ge(S("rkv"), B("rkv") + 4)
            v.wait_ge(S("mixed"), B("mixed") + 6)
            link(v.tensor_tensor(kk, k, vec(9, 0), ALU.mult))
            link(v.tensor_tensor(t0, kk, kk, ALU.mult))
            v.tensor_reduce(kss, heads(t0), AX_X, ALU.add).then_inc(S("kk_ss"), 1)
            split(("r", 1, 1), ("v", 0, 0))
            v.wait_ge(S("rate"), B("rate") + 4)
            link(v.scalar_tensor_tensor(out=t0, in0=rate, scalar=-1.0, in1=vec(9, D), op0=ALU.add, op1=ALU.mult))
            link(v.scalar_tensor_tensor(out=k, in0=t0, scalar=1.0, in1=k, op0=ALU.add, op1=ALU.mult))
            v.wait_ge(S("kk_norm"), B("kk_norm") + 1)
            link(v.tensor_scalar(kss, kss, 1e-12, None, ALU.max))
            link(v.reciprocal(kss, kss))
            link(v.tensor_tensor(heads(kk), heads(kk), per_head(kss), ALU.mult))
            link(v.scalar_tensor_tensor(out=rate, in0=kk, scalar=-1.0, in1=rate, op0=ALU.mult, op1=ALU.mult))
            split(("v", 0, 1))
            mix_lo(2, W3(3, KT), 0)
            mix_lo(2, W3(3, KT), 1)
            split(("v", 1, 0))
            v.wait_ge(S("rkv"), B("rkv") + 8)
            link(v.tensor_tensor(t0, r, k, ALU.mult))
            link(v.tensor_tensor(t0, t0, side[:, :].unsqueeze(1).to_broadcast([P, NT, D]), ALU.mult))
            v.tensor_reduce(bon, heads(t0), AX_X, ALU.add).then_inc(S("bonus"), 1)
            split(("v", 1, 1))
            bk = wide[:, 2048:3 * 2048].rearrange("p (t h x c) -> p t h x c", t=NT, h=RH, x=2)
            v.wait_ge(S("bonus"), B("bonus") + 1)
            for t in range(NT):
                for c in range(2):
                    n = 2 * t + c
                    o = slice(c * 512, (c + 1) * 512)
                    v.wait_ge(S("cum_read"), B("cum_read") + n + 1)
                    v.tensor_tensor(W(3, 1024, 512), ps[:, 4 + n, :], sig[:, t, o], ALU.subtract).then_inc(S("cum_prev"), 1)
                    pin = W(3, 512, 512).rearrange("p (h c) -> p h c", c=HD)
                    v.tensor_tensor(t0[:, t, o], r[:, t, o], W(3, 0, 512), ALU.mult).then_inc(S("scaled"), 1)
                    v.tensor_tensor(bk[:, t, 8 * c:8 * c + 8, 0, :], rate[:, t, o].rearrange("p (h c) -> p h c", c=HD), pin, ALU.mult)\
                     .then_inc(S("scaled"), 1)
                    v.tensor_tensor(bk[:, t, 8 * c:8 * c + 8, 1, :], k[:, t, o].rearrange("p (h c) -> p h c", c=HD), pin, ALU.mult)\
                     .then_inc(S("scaled"), 1)
                    v.wait_ge(S("exps"), B("exps") + n + 1)
                    v.tensor_tensor(kk[:, t, o], kk[:, t, o], W(3, 1536, 512), ALU.mult).then_inc(S("scaled"), 1)
            split(("o", 0, 0), ("o", 0, 1), ("o", 1, 0))

            tmp = WKV_TMP(W)

            def four(ap):
                return ap.rearrange("p (u c) -> p u c", u=4)

            for g in range(8):
                t, h0 = g // 4, 4 * (g % 4)
                v.wait_ge(S("wkv.T"), B("wkv.T") + g + 1)
                v.tensor_copy(tmp["bT"][0:64, :], ps[0:64, 2, :]).then_inc(S("wkv.bk"), 1)
                v.tensor_copy(tmp["kT"][0:64, :], ps[0:64, 3, :]).then_inc(S("wkv.bk"), 1)
                gb = ps[:, 4:6, :].rearrange("p b (u x c) -> p (b u) x c", u=2, x=2)
                gk = ps[:, 6:8, :].rearrange("p b (u x c) -> p (b u) x c", u=2, x=2)
                v.wait_ge(S("wkv.gram"), B("wkv.gram") + 2 * g + 1)
                v.tensor_tensor(four(tmp["xt"]), gb[:, :, 0, :], mask4("diag_st"), ALU.mult)
                v.tensor_tensor(four(tmp["x"]), four(ps[:, 0, :]), mask4("diag_ts"), ALU.mult).then_inc(S("wkv.masked"), 1)
                v.wait_ge(S("wkv.gram"), B("wkv.gram") + 2 * g + 2)
                v.tensor_tensor(four(tmp["gk"]), gk[:, :, 0, :], mask4("strict_st"), ALU.mult).then_inc(S("wkv.masked"), 1)
                v.tensor_tensor(four(tmp["off"]), four(ps[:, 0, :]), mask4("off_ts"), ALU.mult)
                v.wait_ge(S("wkv.masked"), B("wkv.masked") + 3 * g + 1)
                v.tensor_tensor(four(tmp["tt"]), four(tmp["xt"]), mask4("ident"), ALU.add).then_inc(S("wkv.t1"), 1)
                v.tensor_tensor(four(tmp["mrb"]), gb[:, :, 1, :], mask4("incl_st"), ALU.mult)
                v.tensor_tensor(four(tmp["mrk"]), gk[:, :, 1, :], mask4("incl_st"), ALU.mult).then_inc(S("wkv.masked"), 1)

                def accumulate(sem, b, dst, base, done):
                    v.wait_ge(S("wkv." + sem), B("wkv." + sem) + g + 1)
                    v.tensor_tensor(tmp[dst], tmp[base], ps[:, b, :], ALU.add).then_inc(S("wkv." + done), 1)
                v.wait_ge(S("wkv.t1"), B("wkv.t1") + g + 1)
                accumulate("t2", 0, "tt", "tt", "t2c")
                v.wait_ge(S("wkv.t2c"), B("wkv.t2c") + g + 1)
                accumulate("t4", 1, "tt", "tt", "t4c")
                v.wait_ge(S("wkv.t4c"), B("wkv.t4c") + g + 1)
                accumulate("t8", 0, "tt", "tt", "t8c")
                v.wait_ge(S("wkv.r1c"), B("wkv.r1c") + g + 1)
                accumulate("r2", 1, "r2", "r1", "r2c")
                accumulate("r3", 2, "r2", "r1", "r3c")
                accumulate("r4", 0, "r2", "r1", "r4c")
                v.wait_ge(S("wkv.fg"), B("wkv.fg") + g + 1)
                ft = W3(8, 2).rearrange("p a (h c) -> p a h c", h=RH)
                fp = ps[0:64, F_BANK[1 - t], 0:256].rearrange("p (u c) -> p u c", u=4)
                v.tensor_tensor(ft[0:64, t, h0:h0 + 4, :], fp,
                                masks[0:64, 0:64].unsqueeze(1).to_broadcast([64, 4, 64]), ALU.add)
                v.wait_ge(S("wkv.eh"), B("wkv.eh") + g + 1)
                ep = ps[0:64, 5, :].rearrange("p (u x c) -> p u x c", u=4, x=2)
                e2 = bk[:, t, h0:h0 + 4, :, :]
                v.memset(e2[0:64, :, 1, :], 0.0)
                v.memset(e2[64:128, :, 0, :], 0.0)
                v.tensor_copy(e2[0:64, :, 0, :], ep[:, :, 0, :])
                v.wait_ge(S("wkv.hc"), B("wkv.hc") + g + 1)
                v.tensor_copy(e2[64:128, :, 1, :], ep[:, :, 1, :]).then_inc(S("wkv.done"), 1)

            gall = WKV_G(W, side)
            chain = W(5, 0, D).rearrange("p (h c) -> p h c", h=RH)
            ctmp = W(5, D, D).rearrange("p (h c) -> p h c", h=RH)
            pch = pc.rearrange("p (h c) -> p h c", c=4)

            def decay(c):
                return pch[0:64, :, c:c + 1].to_broadcast([64, RH, HD])

            v.wait_ge(S("pc"), B("pc") + 2)
            v.tensor_tensor(chain[0:64], gall[0][0:64], decay(0), ALU.mult).then_inc(S("state"), 1)
            for c in (1, 2):
                v.wait_ge(S("state_F"), B("state_F") + c)
                for b in range(2):
                    m = v.tensor_tensor(ctmp[0:64, 8 * b:8 * b + 8, :], ps[0:64, b, :].rearrange("p (h c) -> p h c", c=HD),
                                        gall[c][0:64, 8 * b:8 * b + 8, :], ALU.add)
                link(m)
                v.wait_ge(S("state_put"), B("state_put") + c)
                v.tensor_tensor(chain[0:64], ctmp[0:64], decay(c), ALU.mult).then_inc(S("state"), 1)
            y = W3(0, NT)
            for t in range(NT):
                v.wait_ge(S("y_T"), B("y_T") + t + 1)
                for c in range(2):
                    o = slice(c * 512, (c + 1) * 512)
                    v.tensor_tensor(y[:, t, o], y[:, t, o], ps[:, 2 + 2 * t + c, :], ALU.add).then_inc(S("ysum"), 1)
            v.wait_ge(S("ysum"), B("ysum") + 4)
            yh = heads(y)
            t1 = W3(5, NT)
            link(v.tensor_reduce(mean, yh, AX_X, ALU.add))
            link(v.tensor_scalar(mean, mean, 1.0 / HD, None, ALU.mult))
            link(v.tensor_tensor(yh, yh, per_head(mean), ALU.subtract))
            link(v.tensor_tensor(t1, y, y, ALU.mult))
            link(v.tensor_reduce(gvar, heads(t1), AX_X, ALU.add))
            v.tensor_scalar(gvar, gvar, 1.0 / HD, GN_EPS, ALU.mult, ALU.add).then_inc(S("gn_var"), 1)
            v.wait_ge(S("ln_vec"), B("ln_vec") + 32)
            link(v.tensor_tensor(heads(t1), heads(vv), per_head(bon), ALU.mult))
            link(v.tensor_tensor(t1, t1, vec(7, D), ALU.add))
            v.wait_ge(S("gn_std"), B("gn_std") + 1)
            link(v.reciprocal(gvar, gvar))
            link(v.tensor_tensor(yh, yh, per_head(gvar), ALU.mult))
            link(v.tensor_tensor(y, y, vec(7, 0), ALU.mult))
            link(v.tensor_tensor(y, y, t1, ALU.add))
            v.wait_ge(S("gate_T"), B("gate_T") + 1)
            for t in range(NT):
                for c in range(2):
                    o = slice(c * 512, (c + 1) * 512)
                    v.tensor_tensor(y[:, t, o], y[:, t, o], ps[:, 2 + 2 * t + c, :], ALU.mult).then_inc(S("y_gated"), 1)
            copy_lo("rw", (6, 7, 0, 1))
            split(("o", 1, 1))
            add_linear("o", "mix1.add")

            norm("ffn1")
            norm_lo("ffn1", "ffn_norm", KT)
            v.wait_ge(S("c_act"), B("c_act") + 1)
            v.wait_ge(S("acc_bias"), B("acc_bias") + 16)
            ffn_loop("ffn1", plan.at["ffn1"][0], True)
            v.wait_ge(w_used[2], plan.at["ffn1"][0][2] + NFFN)
            add_residual("ffn1.add")

            ada(NFFN)
            norm("fin")
            v.wait_ge(S("fin_vec"), B("fin_vec") + 16)
            v.wait_ge(S("fin.hn"), B("fin.hn") + 2)
            for t in range(NT):
                link(v.tensor_tensor(h[:, t, :], hn[:, t, :], W(8, 0, D), ALU.mult))
            v.wait_ge(S("mod_T"), B("mod_T") + 1)
            v.tensor_copy(modc, ps[:, 0, 0:32]).then_inc(S("modc"), 1)
            v.wait_ge(S("modc"), B("modc") + 1)
            link(v.scalar_tensor_tensor(out=sc1, in0=modc[:, 8:16], scalar=1.0, in1=cols[:, ROWS["g_pre_mix"]:ROWS["g_pre_mix"] + 8],
                                        op0=ALU.add, op1=ALU.mult))
            link(v.scalar_tensor_tensor(out=sc2, in0=modc[:, 24:32], scalar=1.0, in1=cols[:, ROWS["g_pre_mlp"]:ROWS["g_pre_mlp"] + 8],
                                        op0=ALU.add, op1=ALU.mult))
            v.wait_ge(S("gates_T"), B("gates_T") + 1)
            v.wait_ge(S("post_vec"), B("post_vec") + 32)
            gb1, gb2 = GB1(W), side
            for n, dst in enumerate((gb1, gb2)):
                for c in range(2):
                    o = slice(c * 512, (c + 1) * 512)
                    v.tensor_tensor(dst[:, o], ps[:, 4 + 2 * n + c, :], W(6, n * D + c * 512, 512), ALU.mult).then_inc(S("gates"), 1)
            norm("pre")
            norm_modulated("pre", sc1, modc[:, 0:8])
            split(("glu", 0, 0), ("glu", 0, 1), ("glu", 1, 0))
            v.wait_ge(S("pos"), B("pos") + 16)
            link(v.tensor_copy(posf, posi[:, :]))
            freq = masks[:, MFREQ:MFREQ + 32]
            ang = lowr[:, 128:192]
            turns = lowr[:, 192:256]
            for t in range(NT):
                m = v.tensor_scalar(ang[:, t * 32:(t + 1) * 32], freq, posf[:, t:t + 1], None, ALU.mult)
            link(m)
            link(v.tensor_scalar(turns, ang, float(1 / (2 * np.pi)), 12582912.0, ALU.mult, ALU.add))
            link(v.tensor_scalar(turns, turns, 12582912.0, None, ALU.subtract))
            for part in (6.28125, 0.0019340515136718750, float(2 * np.pi - 6.28125 - 0.0019340515136718750)):
                link(v.scalar_tensor_tensor(out=ang, in0=turns, scalar=-part, in1=ang, op0=ALU.mult, op1=ALU.add))
            link(v.tensor_scalar(lowr[:, 0:64], ang, -3.1415925, 3.1415925, ALU.max, ALU.min))
            link(v.scalar_tensor_tensor(out=ang, in0=lowr[:, 0:64], scalar=-1.0, in1=lowr[:, 0:64], op0=ALU.mult, op1=ALU.max))
            v.tensor_scalar(lowr[:, 64:128], ang, -1.0, float(np.pi / 2), ALU.mult, ALU.add).then_inc(S("angle"), 1)
            ub = lowr[:, 512:1024].rearrange("p (t n) -> p t n", t=NT)
            upad = U_PAD(wide)
            nxt = [("glu", 1, 1), ("glu", 2, 0), ("glu", 2, 1), ("glu", 3, 0), ("glu", 3, 1), ("lat", 0, 0), ("lat", 0, 1), ("lat", 1, 0)]
            for c in range(4):
                for t in range(NT):
                    v.wait_ge(S("glu_s"), B("glu_s") + 2 * c + t + 1)
                    v.tensor_tensor(W(U_AT[c][0], U_AT[c][1] + t * 256, 256), ps[:, 2 * (c % 2) + t, 0:256], ub[:, t, :], ALU.mult)\
                     .then_inc(S("glu"), 1)
                split(*nxt[2 * c:2 * c + 2])
            split(("lat", 1, 1), ("gate", 0, 0), ("gate", 0, 1))
            lat = W(3, 0, 2 * 704).rearrange("p (t n) -> p t n", t=NT)
            v.wait_ge(S("lat"), B("lat") + 4)
            for t in range(NT):
                mean_square(lat[:, t, 0:QL], QL, qss[:, t:t + 1], W(2, t * D, QL))
                m = mean_square(lat[:, t, QL:QL + KL], KL, qss[:, 2 + t:3 + t], W(2, t * D + 512, KL))
            m.then_inc(S("lat_ss"), 1)
            v.memset(upad[:, :, 0:CK - 1], 0.0)
            split(("gate", 1, 0))
            v.wait_ge(S("lat_std"), B("lat_std") + 1)
            link(v.reciprocal(qrs, qsd))
            for t in range(NT):
                v.tensor_scalar(lat[:, t, 0:QL], lat[:, t, 0:QL], qrs[:, t:t + 1], None, ALU.mult).then_inc(S("lat_n"), 1)
                v.tensor_scalar(lat[:, t, QL:QL + KL], lat[:, t, QL:QL + KL], qrs[:, 2 + t:3 + t], None, ALU.mult).then_inc(S("lat_n"), 1)
            cv = W3(2, KT)
            taps = [(kt, k) for k in range(CK) for kt in range(KT)]

            def conv(n):
                for _ in range(min(n, len(taps))):
                    kt, k = taps.pop(0)
                    w = cols[:, CONVW + kt * CK + k:CONVW + kt * CK + k + 1]
                    src = upad[:, kt, k:k + SEQ]
                    if k == 0:
                        m = v.tensor_scalar(cv[:, kt, :], src, w, col("conv_b", kt), ALU.mult, ALU.add)
                    else:
                        v.wait_ge(S("conv_step"), B("conv_step") + (k - 1) * KT + kt + 1)
                        m = v.scalar_tensor_tensor(out=cv[:, kt, :], in0=src, scalar=w, in1=cv[:, kt, :], op0=ALU.mult, op1=ALU.add)
                    m.then_inc(S("conv_step"), 1)
            v.wait_ge(S("u_put"), B("u_put") + 4)
            for name in [("gate", 1, 1), ("gate", 2, 0), ("gate", 2, 1), ("gate", 3, 0), ("gate", 3, 1), ("uq", 0), ("uq", 1), ("uq", 2)]:
                split(name)
                conv(9)
            for b in range(3):
                v.wait_ge(S("lq.xh"), B("lq.xh") + min(2 * b + 2, 5))
                for kt in range(2 * b, min(2 * b + 2, 5)):
                    v.scalar_tensor_tensor(out=xl[:, kt, :], in0=ps[:, 4 + b, (kt % 2) * SEQ:(kt % 2 + 1) * SEQ],
                                           scalar=col("q_norm", kt) if kt < 3 else col("kv_norm", kt - 3), in1=f32(xh[:, kt, :]),
                                           op0=ALU.mult, op1=ALU.subtract).then_inc(S("lq.xl"), 1)
            for name in [("uq", 3), ("ukv", 0), ("ukv", 1)]:
                conv(9)
                split(name)
            qraw = W(8, 0, 2 * 9 * 64).rearrange("p (t n) -> p t n", t=NT)
            ro = W(3, 0, 1280).rearrange("p (t n) -> p t n", t=NT)
            v.wait_ge(S("qraw"), B("qraw") + 2)
            v.wait_ge(S("lq.T"), B("lq.T") + 3)
            for t in range(NT):
                m = v.tensor_copy(qraw[:, t, 512:576], lat[:, t, QL + KL:704])
            link(m)
            v.wait_ge(S("sincos"), B("sincos") + 1)
            ropet = W(10, 0, 2 * 288)
            for t in range(NT):
                src = qraw[:, t, :].rearrange("p (h x c) -> p h x c", x=2, c=32)
                dst = ro[:, t, 0:576].rearrange("p (h x c) -> p h x c", x=2, c=32)
                sn = lowr[:, t * 32:(t + 1) * 32].unsqueeze(1).to_broadcast([P, 9, 32])
                cs = lowr[:, 64 + t * 32:64 + (t + 1) * 32].unsqueeze(1).to_broadcast([P, 9, 32])
                ta = ropet[:, 0:288].rearrange("p (h c) -> p h c", c=32)
                tb = ropet[:, 288:576].rearrange("p (h c) -> p h c", c=32)
                v.tensor_tensor(dst[:, :, 0, :], src[:, :, 0, :], cs, ALU.mult)
                v.tensor_tensor(dst[:, :, 1, :], src[:, :, 1, :], cs, ALU.mult)
                v.tensor_tensor(ta, src[:, :, 1, :], sn, ALU.mult)
                link(v.tensor_tensor(tb, src[:, :, 0, :], sn, ALU.mult))
                v.tensor_tensor(dst[:, :, 0, :], dst[:, :, 0, :], ta, ALU.subtract)
                link(v.tensor_tensor(dst[:, :, 1, :], dst[:, :, 1, :], tb, ALU.add))
                v.tensor_copy(ro[:, t, 576:640], ro[:, t, 512:576]).then_inc(S("roped"), 1)
            split(("attn_out", 0, 0), ("attn_out", 0, 1), ("attn_out", 1, 0))
            pp = [W3(10, NT, 512 * b, 512) for b in range(2)]
            causal = masks[:, MI["causal"]:MI["causal"] + P]

            def finish(i):
                b = i % 2
                v.wait_ge(S("at.e"), B("at.e") + 2 * (i + 1))
                link(v.reciprocal(arec[:, 2 * b:2 * b + 2], asum[:, 2 * b:2 * b + 2]))
                for t in range(NT):
                    nk = P * (t + 1)
                    v.tensor_scalar(pp[b][:, t, 0:nk], pp[b][:, t, 0:nk], arec[:, 2 * b + t:2 * b + t + 1], None, ALU.mult)\
                     .then_inc(S("at.p"), 1)

            def out_lo(i):
                v.wait_ge(S("at.xh"), B("at.xh") + i + 1)
                v.tensor_tensor(xl[:, i, :], ps[:, 4 + i % 2, 0:SEQ], f32(xh[:, i, :]), ALU.subtract).then_inc(S("at.xl"), 1)

            for i in range(NH):
                b = i % 2
                v.wait_ge(S("at.s"), B("at.s") + i + 1)
                if i >= 2:
                    v.wait_ge(S("at.T"), B("at.T") + i - 1)
                v.scalar_tensor_tensor(out=pp[b][:, 0, 0:P], in0=ps[:, b, 0:P], scalar=SCALE, in1=causal, op0=ALU.mult, op1=ALU.add)
                v.tensor_scalar(pp[b][:, 1, 0:P], ps[:, b, SEQ:SEQ + P], SCALE, None, ALU.mult).then_inc(S("at.sc"), 1)
                v.scalar_tensor_tensor(out=pp[b][:, 1, P:SEQ], in0=ps[:, b, SEQ + P:2 * SEQ], scalar=SCALE, in1=causal, op0=ALU.mult,
                                       op1=ALU.add).then_inc(S("at.sc"), 1)
                v.wait_ge(S("at.sc"), B("at.sc") + 2 * (i + 1))
                for t in range(NT):
                    m = v.tensor_reduce(amax[:, 2 * b + t:2 * b + t + 1], pp[b][:, t, 0:P * (t + 1)], AX_X, ALU.max)
                link(m)
                v.tensor_scalar(amax[:, 2 * b:2 * b + 2], amax[:, 2 * b:2 * b + 2], -1.0, None, ALU.mult).then_inc(S("at.max"), 1)
                conv(9)
                finish(i)
                if i:
                    out_lo(i - 1)
            out_lo(NH - 1)
            split(("attn_out", 1, 1), ("conv_out", 0, 0), ("conv_out", 0, 1))
            conv(len(taps))
            v.wait_ge(S("conv_step"), B("conv_step") + CK * KT)
            v.wait_ge(S("cmean"), B("cmean") + 1)
            cmean = lowr[:, 512:768]
            link(v.tensor_scalar(cmean, ps[:, 4, 0:SEQ], 1.0 / D, None, ALU.mult))
            link(v.tensor_tensor(cv, cv, cmean.unsqueeze(1).to_broadcast([P, KT, SEQ]), ALU.subtract))
            v.wait_ge(S("at.o"), B("at.o") + NH)
            v.tensor_tensor(W3(5, KT), cv, cv, ALU.mult).then_inc(S("csq"), 1)
            v.wait_ge(S("cvar"), B("cvar") + 1)
            v.tensor_scalar(lowr[:, 256:512], ps[:, 5, 0:SEQ], 1.0 / D, EPS, ALU.mult, ALU.add).then_inc(S("cv_ss"), 1)
            v.wait_ge(S("cv_std"), B("cv_std") + 1)
            link(v.reciprocal(lowr[:, 768:1024], lowr[:, 256:512]))
            v.tensor_tensor(cv, cv, lowr[:, 768:1024].unsqueeze(1).to_broadcast([P, KT, SEQ]), ALU.mult).then_inc(S("cv_n"), 1)
            gates = wide[:, 6 * 2048:8 * 2048].rearrange("p (t n) -> p t n", t=NT)
            ym = W3(9, NT)
            for c in range(2):
                used(v, ("attn_out", c, 1))
                for t in range(NT):
                    o = slice(c * 512, (c + 1) * 512)
                    v.tensor_tensor(ym[:, t, o], ps[:, 2 * c + t, :], gates[:, t, D + c * 512:D + (c + 1) * 512], ALU.mult)\
                     .then_inc(S("yb"), 1)
            for k in range(2):
                v.wait_ge(S("cv.xh"), B("cv.xh") + k + 1)
                o = slice(4 * k, 4 * k + 4)
                v.tensor_tensor(xl[:, o, :], cv[:, o, :], f32(xh[:, o, :]), ALU.subtract).then_inc(S("cv.xl"), 4)
            split(("conv_out", 1, 0), ("conv_out", 1, 1), ("out", 0, 0), ("out", 0, 1))
            for c in range(2):
                used(v, ("conv_out", c, 1))
                for t in range(NT):
                    o = slice(c * 512, (c + 1) * 512)
                    g_ = gates[:, t, c * 512:(c + 1) * 512]
                    link(v.tensor_tensor(g_, ps[:, 2 * c + t, :], g_, ALU.mult))
                    v.tensor_tensor(ym[:, t, o], ym[:, t, o], g_, ALU.add).then_inc(S("ymix"), 1)
            copy_lo("ym", (4, 5, 6, 7))
            split(("out", 1, 0), ("out", 1, 1))
            y2 = W3(9, NT)

            def post(name, banks, gb, ready):
                for t in range(NT):
                    for c in range(2):
                        ready(c)
                        m = v.tensor_copy(y2[:, t, c * 512:(c + 1) * 512], ps[:, banks[t][c], :])
                link(m)
                norm(name, src=y2, dst=hn)
                v.wait_ge(S(name + ".hn"), B(name + ".hn") + 2)
                for t in range(NT):
                    link(v.tensor_tensor(hn[:, t, :], hn[:, t, :], gb, ALU.mult))
                    v.tensor_tensor(h[:, t, :], h[:, t, :], hn[:, t, :], ALU.add).then_inc(S(name + ".add"), 1)
                v.wait_ge(S(name + ".add"), B(name + ".add") + 2)
            post("post1", ((0, 2), (1, 3)), gb1, lambda c: used(v, ("out", c, 1)))
            norm("pre2")
            norm_modulated("pre2", sc2, modc[:, 16:24])
            mlp_loop()
            v.wait_ge(w_used[2], plan.at["mlp"][0][2] + NMLP)
            post("post2", ((0, 1), (2, 3)), gb2[:, :], lambda c: None)


U_AT = ((8, 0), (8, 512), (8, 1024), (8, 1536))


def GB1(W):
    return W(10, 1024, D)


def U_PAD(wide):
    n = SEQ + CK - 1
    return wide[:, 0:KT * n].rearrange("p (a n) -> p a n", a=KT)


F_BANK, G_BANK = (3, 1), (4, 2)


def WKV_TMP(W):
    t = {}
    spots = [(w, o) for w in (4, 5, 7, 9) for o in range(0, 2048, 512)]
    t["ar"] = W(4, 0, 1024)
    names = ("bT", "kT", "x", "xt", "off", "mrb", "gk", "mrk", "tt", "x2", "x2t", "gkv", "r1", "r2")
    for n, (w, o) in zip(names, spots[2:]):
        t[n] = W(w, o, 512)
    t["x4"], t["x4t"], t["x8"], t["mt"] = t["x"], t["xt"], t["x2"], t["x2t"]
    return t


def WKV_G(W, side):
    aps = (W(3, 0, D), W(3, D, D), side[:, :])
    return [a.rearrange("p (h c) -> p h c", h=RH) for a in aps]


INS = ["x", "mix_norm", "ffn_norm", "final_norm", "ab_w_in", "ab_w_out", "sgu_gain", "sgu_w_s", "sgu_bias", "pool_w",
       "pool_scale", "rwkv_mu", "rwkv_w_r", "rwkv_w_k", "rwkv_w_v", "rwkv_w_o", "rwkv_w0", "rwkv_w1", "rwkv_w2", "rwkv_a0",
       "rwkv_a1", "rwkv_a2", "rwkv_g1", "rwkv_g2", "rwkv_k_k", "rwkv_k_a", "rwkv_r_k", "rwkv_ln_w", "rwkv_ln_b",
       "ffn_w_gate", "ffn_w_up", "ffn_w_down", "c_2", "positions_2", "w_ada_2", "b_ada_2", "g_pre_mix_2", "g_post_mix_2",
       "g_pre_mlp_2", "g_post_mlp_2", "w_in_2", "conv_w_2", "conv_b_2", "conv_norm_g_2", "conv_norm_b_2", "w_conv_out_2",
       "q_norm_g_2", "w_uq_2", "kv_norm_g_2", "w_ukv_2", "w_attn_out_2", "w_out_2", "w_mlp_in_2", "w_mlp_out_2"]


def kernel(**inputs):
    import concourse.bacc as bacc
    from concourse.bass_utils import run_bass_kernel_spmd

    nc = bacc.Bacc("TRN2", target_bir_lowering=False, num_devices=1)
    arrays, aps = {}, {}
    for name in INS:
        a = np.ascontiguousarray(inputs[name])
        arrays[f"in_{name}"] = a
        aps[name] = nc.dram_tensor(f"in_{name}", a.shape, mybir.dt.from_np(a.dtype), kind="ExternalInput").ap()
    consts = []
    for name, a in zip(("const_masks", "const_pool"), constants()):
        arrays[name] = a
        consts.append(nc.dram_tensor(name, a.shape, F32, kind="ExternalInput").ap())
    out = nc.dram_tensor("out", (1, SEQ, D), F32, kind="ExternalOutput").ap()
    build(nc, aps, *consts, out)
    r = run_bass_kernel_spmd(nc, [arrays], core_ids=[0])
    return r.results[0]["out"]
```

```python
from contextlib import ExitStack

import numpy as np
import concourse.bass as bass
from concourse import mybir

F32 = mybir.dt.float32
F32R = mybir.dt.float32r
I32 = mybir.dt.int32
ACT = mybir.ActivationFunctionType
ALU = mybir.AluOpType
AX_X = mybir.AxisListType.X

P = 128
D = 1024
SEQ = 256
NT = SEQ // P
KT = D // P
EPS = 1e-6
GN_EPS = 64e-5
FFN = 2816
FC = 256
NFFN = FFN // FC
DFF = 4096
NMLP = DFF // FC
AW = 512
WINDOWS = (2, 4, 8, 16)
RH = 16
HD = 64
CH = 64
RANK = 64
GRANK = 160
NH = 8
NOPE, ROPE, VD = 128, 64, 128
QL, KL = 384, 256
CK = 31
SLOT = 2048
DECAY = float(np.exp(-0.5))
SCALE = float(1.0 / np.sqrt(NOPE + ROPE))

ROWS = {}
_at = 0
for _n, _k in (("mix_norm", 16), ("ffn_norm", 16), ("mu", 48), ("sgu_bias", 4), ("pool_scale", 4),
               ("g_pre_mix", 8), ("g_pre_mlp", 8), ("cn_g", 8), ("cn_b", 8), ("conv_b", 8),
               ("q_norm", 3), ("kv_norm", 2)):
    ROWS[_n] = _at
    _at += _k
CONVW = _at
NCOL = CONVW + KT * CK

MASKS = ("ident", "diag_ts", "off_ts", "diag_st", "strict_st", "incl_st", "causal")
MI = {n: i * P for i, n in enumerate(MASKS)}
MCH = len(MASKS) * P
MFREQ = MCH + 2
MEPS = MFREQ + 32
NMASK = MEPS + 1


def constants():
    a = np.arange(P)
    r, c = a[:, None], a[None, :]
    same = (r // CH) == (c // CH)
    near = (r // 16) == (c // 16)
    m = {
        "ident": r == c,
        "diag_ts": (c < r) & near,
        "off_ts": (c < r) & same & ~near,
        "diag_st": (r < c) & near,
        "strict_st": (r < c) & same,
        "incl_st": (r <= c) & same,
    }
    out = np.zeros((P, NMASK), np.float32)
    for n, v in m.items():
        out[:, MI[n]:MI[n] + P] = v
    out[:, MI["causal"]:MI["causal"] + P] = np.where(c <= r, 0.0, -1e30)
    out[:, MCH:MCH + 2] = (r // CH) == np.arange(2)[None, :]
    freq = 1.0 / (np.float32(10000.0) ** (np.arange(0, ROPE, 2, dtype=np.float32) / np.float32(ROPE)))
    out[:, MFREQ:MFREQ + 32] = freq.astype(np.float32)[None, :]
    out[:, MEPS] = EPS
    pool = np.zeros((P, 3, 4, P), np.float32)
    for g, w in enumerate(WINDOWS):
        inside = (r <= c) & (r > c - w)
        pool[:, 0, g] = np.where(inside, 1.0 / np.minimum(c + 1, w), 0.0) - (r == c)
        pool[:, 1, g] = np.where(inside, 1.0 / w, 0.0) - (r == c)
        pool[:, 2, g] = np.where(r - P > c - w, 1.0 / w, 0.0)
    return out, pool.reshape(P, 12 * P).astype(np.float32)


SHARED = {
    "ff_act": (("ffn0.act", 22), ("ffn1.act", 22), ("mlp.act", 16)),
    "ff_mT": (("ffn0.mT", 11), ("ffn1.mT", 11), ("mlp.mT", 16)),
    "ff_h": (("ffn0.h", 11), ("ffn1.h", 11), ("mlp.h", 16)),
    "ff_gh": (("ffn0.gh", 11), ("ffn1.gh", 11), ("mlp.gh", 16)),
    "ff_gl": (("ffn0.gl", 11), ("ffn1.gl", 11), ("mlp.gl", 16)),
    "pool_1": (("ones", 1), ("acc_zero", 1)),
    "pe_1": (("cols_T", 1), ("gate_T", 1)),
    "pe_2": (("wst_T", 1), ("rw.T", 4)),
    "pe_3": (("mix0.T", 4), ("ffn1.T", 4)),
    "pe_4": (("spatial", 2), ("mod_T", 1)),
    "pe_5": (("pooled_T", 2), ("gates_T", 1)),
    "pe_6": (("yb_T", 2), ("pre.T", 4)),
    "pe_7": (("ya_T", 2), ("u_T", 4)),
    "pe_8": (("ffn0.T", 4), ("lq.T", 3)),
    "pe_9": (("mix1.T", 4), ("ro_T", 3)),
    "pe_10": (("rank_T", 3), ("at.s", 8)),
    "pe_11": (("logit", 8), ("at.T", 8)),
    "pe_12": (("cum", 1), ("conv_mm", 8)),
    "pe_13": (("pc_T", 1), ("at.o", 8)),
    "pe_14": (("wkv.T", 8), ("cmean", 1)),
    "pe_15": (("wkv.gram", 16), ("cvar", 1)),
    "pe_16": (("wkv.gram_ts", 8), ("ym.T", 4)),
    "pe_17": (("wkv.x2", 8), ("pre2.T", 4)),
    "act_1": (("mix0.sq", 1), ("ffn1.std", 1), ("post2.std", 1)),
    "act_2": (("mix0.std", 1), ("ffn1.xh", 8)),
    "act_3": (("mix0.xh", 8), ("c_act", 1)),
    "act_4": (("u_ready", 2), ("fin.sq", 1)),
    "act_5": (("v_ready", 2), ("fin.std", 1)),
    "act_6": (("v_std", 1), ("pre.sq", 1)),
    "act_7": (("zb_ready", 2), ("pre.std", 1)),
    "act_8": (("ab.yh", 4), ("pre.xh", 2)),
    "act_9": (("ab.xh", 2), ("sincos", 1)),
    "act_10": (("ffn0.sq", 1), ("glu_s", 8)),
    "act_11": (("ffn0.std", 1), ("lat", 4)),
    "act_12": (("ffn0.xh", 8), ("u_put", 4)),
    "act_13": (("mix1.sq", 1), ("lat_std", 1)),
    "act_14": (("mix1.std", 1), ("gatev", 8)),
    "act_15": (("mix1.hT", 8), ("lq.xh", 5)),
    "act_16": (("rank", 3), ("qn", 4)),
    "act_17": (("sig", 4), ("qraw", 2)),
    "act_18": (("rate", 4), ("kn", 4)),
    "act_19": (("rkv.xh", 6), ("ro_put", 3)),
    "act_20": (("rkv", 12), ("at.pT", 8)),
    "act_21": (("kk_norm", 1), ("vt", 4)),
    "act_22": (("cum_read", 4), ("diag", 93)),
    "act_23": (("exps", 4), ("at.e", 16)),
    "act_24": (("pc", 2), ("at.xh", 8)),
    "act_25": (("wkv.ar", 8), ("conv_pe", 3)),
    "act_26": (("wkv.x2c", 16), ("csq", 2)),
    "act_27": (("wkv.gkvc", 8), ("cv_std", 1)),
    "act_28": (("wkv.x4c", 16), ("cv_act", 8)),
    "act_29": (("wkv.x8c", 8), ("cv.xh", 2)),
    "act_30": (("wkv.r1c", 8), ("ym.xh", 4)),
    "act_31": (("wkv.mtc", 8), ("post1.sq", 2)),
    "act_32": (("wkv.hc", 8), ("post1.std", 1)),
    "act_33": (("state_put", 3), ("pre2.sq", 1)),
    "act_34": (("gn_std", 1), ("pre2.std", 1)),
    "act_35": (("rw.xh", 4), ("pre2.xh", 2)),
    "act_36": (("ffn1.sq", 1), ("post2.sq", 2)),
    "dve_1": (("mix0.ss", 1), ("mix1.add", 4)),
    "dve_2": (("mix0.hn", 2), ("ffn1.ss", 1)),
    "dve_3": (("cols", 2), ("ffn1.hn", 2)),
    "dve_4": (("wst", 1), ("ffn1.xl", 8)),
    "dve_5": (("mix0.xl", 8), ("ffn1.add", 4)),
    "dve_6": (("v_ss", 1), ("fin.ss", 1)),
    "dve_7": (("v_normed", 2), ("fin.hn", 2)),
    "dve_8": (("ya", 8), ("fin.h", 2)),
    "dve_9": (("pooled", 2), ("modc", 1)),
    "dve_10": (("ab.xl", 8), ("pre.ss", 1)),
    "dve_11": (("mix0.add", 4), ("pre.hn", 2)),
    "dve_12": (("ffn0.ss", 1), ("pre.hT", 8)),
    "dve_13": (("ffn0.hn", 2), ("pre.xl", 8)),
    "dve_14": (("ffn0.xl", 8), ("gates", 4)),
    "dve_15": (("ffn0.add", 4), ("angle", 1)),
    "dve_16": (("mix1.ss", 1), ("glu", 8)),
    "dve_17": (("mix1.hn", 2), ("lat_ss", 1)),
    "dve_18": (("mixed", 6), ("lat_n", 4)),
    "dve_19": (("rkv.xl", 24), ("lq.xl", 5)),
    "dve_20": (("kk_ss", 1), ("conv_step", 155)),
    "dve_21": (("bonus", 1), ("roped", 2)),
    "dve_22": (("cum_prev", 4), ("at.sc", 16)),
    "dve_23": (("scaled", 16), ("at.max", 8)),
    "dve_24": (("wkv.bk", 8), ("at.p", 16)),
    "dve_25": (("wkv.gb", 8), ("at.xl", 8)),
    "dve_26": (("wkv.gk", 8), ("cv_c", 2)),
    "dve_27": (("wkv.x", 8), ("cv_ss", 1)),
    "dve_28": (("wkv.t1", 8), ("cv_n", 2)),
    "dve_29": (("wkv.t2c", 8), ("yb", 4)),
    "dve_30": (("wkv.t4c", 8), ("cv.xl", 8)),
    "dve_31": (("wkv.t8c", 8), ("ymix", 4)),
    "dve_32": (("wkv.r2c", 8), ("ym.xl", 8)),
    "dve_33": (("wkv.r3c", 8), ("post1.hn", 2)),
    "dve_34": (("wkv.r4c", 8), ("post1.add", 2)),
    "dve_35": (("wkv.done", 8), ("pre2.ss", 1)),
    "dve_36": (("state", 3), ("pre2.hn", 2)),
    "dve_37": (("ysum", 4), ("pre2.hT", 8)),
    "dve_38": (("gn_var", 1), ("pre2.xl", 8)),
    "dve_39": (("y_gated", 4), ("post2.hn", 2)),
    "dve_40": (("rw.xl", 8), ("post2.add", 2)),
}
HOME, BASE = {}, {}
for _home, _names in SHARED.items():
    _at = 0
    for _n, _k in _names:
        HOME[_n], BASE[_n] = _home, _at
        _at += _k


def B(name):
    return BASE.get(name, 0)


class Plan:

    def __init__(self):
        self.uses, self.loads, self.next = [0, 0, 0], [0, 0, 0], 0
        self.order, self.at = [], {}

    def block(self, name, width=SLOT, dmas=1):
        s = self.next
        self.next = (s + 1) % 3
        self.loads[s] += 16 * dmas
        self.at[name] = (s, self.uses[s], self.loads[s], width)
        self.uses[s] += 1
        self.order.append(name)

    def loop(self, name, uses, dmas):
        self.at[name] = (list(self.uses), list(self.loads))
        for s in range(3):
            self.uses[s] += uses[s]
            self.loads[s] += 16 * uses[s] * dmas[s]
        self.next = 0
        self.order.append(name)


def make_plan():
    p = Plan()
    for n in range(3):
        for k in range(2):
            p.block(("ab_in", n, k))
    for n in range(2):
        for k in range(2):
            p.block(("ab_out", n, k))
    p.loop("ffn0", [NFFN] * 3, [2, 2, 1])
    for w in ("k", "r", "v", "o"):
        for n in range(2):
            for k in range(2):
                p.block((w, n, k))
    p.loop("ffn1", [NFFN] * 3, [2, 2, 1])
    for n in range(4):
        for k in range(2):
            p.block(("glu", n, k), dmas=2)
    for n, w in ((0, QL), (1, KL + ROPE)):
        for k in range(2):
            p.block(("lat", n, k), width=4 * w)
    for n in range(4):
        for k in range(2):
            p.block(("gate", n, k))
    for n in range(4):
        p.block(("uq", n), width=3 * 384)
    for n in range(2):
        p.block(("ukv", n))
    for w in ("attn_out", "conv_out", "out"):
        for n in range(2):
            for k in range(2):
                p.block((w, n, k))
    p.loop("mlp", [NMLP // 2, NMLP // 2, NMLP], [1, 1, 1])
    return p


def build(nc, A, masks_d, pool_d, out):
    plan = make_plan()
    ctx = ExitStack()
    with ctx:
        def sb(name, shape, dt=F32):
            return ctx.enter_context(nc.sbuf_tensor(name, shape, dt))

        sems = {}

        def S(name):
            name = HOME.get(name, name)
            if name not in sems:
                sems[name] = ctx.enter_context(nc.semaphore(name.replace(".", "_")))
            return sems[name]

        raw = sb("raw", [P, 3, SLOT])
        wh = sb("wh", [P, 3, SLOT], F32R)
        wl = sb("wl", [P, 3, SLOT], F32R)
        h = sb("h", [P, NT, D])
        xh = sb("xh", [P, KT, SEQ], F32R)
        xl = sb("xl", [P, KT, SEQ], F32R)
        gh = sb("gh", [P, 2, SEQ], F32R)
        gl = sb("gl", [P, 2, SEQ], F32R)
        wide = sb("wide", [P, 11 * 2048])
        side = sb("side", [P, D])
        lowr = sb("lowr", [P, 4 * SEQ])
        masks = sb("masks", [P, NMASK])
        cols = sb("cols", [P, NCOL])
        ones = sb("ones", [P, P])
        small = sb("small", [P, 512])
        posi = sb("posi", [P, NT], I32)
        ps = ctx.enter_context(nc.psum_tensor("ps", [P, 8, 512], F32))

        def W(i, off=0, n=2048):
            return wide[:, i * 2048 + off:i * 2048 + off + n]

        def W3(i, a, off=0, n=2048):
            return W(i, off, n).rearrange("p (a b) -> p a b", a=a)

        ident = masks[:, 0:P]

        eps = masks[:, MEPS:MEPS + 1]

        def mask4(name):
            return masks[:, MI[name]:MI[name] + P].unsqueeze(1).to_broadcast([P, 4, P])

        def mask22(name):
            return masks[:, MI[name]:MI[name] + P].unsqueeze(1).unsqueeze(1).to_broadcast([P, 2, 2, P])

        def col(name, i=0):
            return cols[:, ROWS[name] + i:ROWS[name] + i + 1]

        sm_at = [0]

        def sm(n):
            sm_at[0] += n
            assert sm_at[0] <= 512
            return small[:, sm_at[0] - n:sm_at[0]]

        NORMS = ("mix0", "ffn0", "mix1", "ffn1", "fin", "pre", "post1", "pre2", "post2")
        nss = {n: sm(2) for n in NORMS}
        nsd = {n: sm(2) for n in NORMS}
        nrs = {n: sm(2) for n in NORMS}
        vss, vsd, vrs = sm(2), sm(2), sm(2)
        qss, qsd, qrs = sm(4), sm(4), sm(4)
        kss, bon, mean, gvar = sm(32), sm(32), sm(32), sm(32)
        pc = sm(64)
        ccol = sm(8)
        modc = sm(32)
        sc1, sc2 = sm(8), sm(8)
        posf = sm(2)
        amax, asum, arec = sm(4), sm(4), sm(4)

        hn = W3(5, NT)
        silu = W3(10, NT, 0, 512)
        hmid = W3(10, NT, 512, 512)

        raw_loaded = [S(f"raw_loaded{i}") for i in range(3)]
        hi_ready = [S(f"hi_ready{i}") for i in range(3)]
        lo_ready = [S(f"lo_ready{i}") for i in range(3)]
        w_used = [S(f"w_used{i}") for i in range(3)]

        def used(eng, name):
            s, use, _, _ = plan.at[name]
            eng.wait_ge(w_used[s], use + 1)

        def kblock(w, n0, n, k):
            return w[k * 512:(k + 1) * 512, n0:n0 + n].rearrange("(a p) n -> p a n", p=P)

        w_in = A["w_in_2"][0]
        LAT0 = 2 * D
        GATE0 = LAT0 + QL + KL + ROPE
        SRC = {"ab_in": A["ab_w_in"][0], "ab_out": A["ab_w_out"][0], "k": A["rwkv_w_k"][0], "r": A["rwkv_w_r"][0],
               "v": A["rwkv_w_v"][0], "o": A["rwkv_w_o"][0], "attn_out": A["w_attn_out_2"][0],
               "conv_out": A["w_conv_out_2"][0], "out": A["w_out_2"][0]}

        def sources(name):
            s, _, _, width = plan.at[name]
            flat = raw[:, s, 0:width]
            what = name[0]
            if what == "glu":
                v = flat.rearrange("p (a n) -> p a n", a=4)
                n0 = name[1] * 256
                return [(kblock(w_in, n0, 256, name[2]), v[:, :, 0:256]),
                        (kblock(w_in, D + n0, 256, name[2]), v[:, :, 256:512])]
            if what == "lat":
                n0, n = (LAT0, QL) if name[1] == 0 else (LAT0 + QL, KL + ROPE)
                return [(kblock(w_in, n0, n, name[2]), flat.rearrange("p (a n) -> p a n", a=4))]
            if what == "gate":
                return [(kblock(w_in, GATE0 + name[1] * 512, 512, name[2]), flat.rearrange("p (a n) -> p a n", a=4))]
            if what == "uq":
                return [(A["w_uq_2"][0][:, name[1] * 384:(name[1] + 1) * 384].rearrange("(a p) n -> p a n", p=P),
                         flat.rearrange("p (a n) -> p a n", a=3))]
            if what == "ukv":
                return [(A["w_ukv_2"][0][:, name[1] * 1024:(name[1] + 1) * 1024].rearrange("(a p) n -> p a n", p=P),
                         flat.rearrange("p (a n) -> p a n", a=2))]
            return [(kblock(SRC[what], name[1] * 512, 512, name[2]), flat.rearrange("p (a n) -> p a n", a=4))]

        block = ctx.enter_context(nc.Block())

        @block.sync
        def _(sp):
            def load_block(name):
                s, use, _, _ = plan.at[name]
                if name == ("o", 0, 0):
                    sp.wait_ge(S("wkv.done"), B("wkv.done") + 8)
                if use:
                    sp.wait_ge(lo_ready[s], use)
                for src, dst in sources(name):
                    sp.dma_start(dst, src).then_inc(raw_loaded[s], 16)

            def load_ffn(l):
                uses, _ = plan.at[f"ffn{l}"]
                gate, up, down = A["ffn_w_gate"][l], A["ffn_w_up"][l], A["ffn_w_down"][l]

                def load_gu(c):
                    n0 = c * FC if isinstance(c, int) else sp.snap(c * FC)
                    for k in range(2):
                        dst = raw[:, k, :].rearrange("p (a n) -> p a n", a=4)
                        sp.wait_ge(lo_ready[k], uses[k] + c)
                        for j, w in enumerate((gate, up)):
                            sp.dma_start(dst[:, :, j * FC:(j + 1) * FC],
                                         w[k * 512:(k + 1) * 512, bass.ds(n0, FC)].rearrange("(a p) n -> p a n", p=P))\
                              .then_inc(raw_loaded[k], 16)

                def load_down(c):
                    r0 = c * FC if isinstance(c, int) else sp.snap(c * FC)
                    sp.wait_ge(lo_ready[2], uses[2] + c)
                    sp.dma_start(raw[:, 2, :].rearrange("p (a n) -> p a n", a=2),
                                 down[bass.ds(r0, FC), :].rearrange("(a p) n -> p a n", p=P))\
                      .then_inc(raw_loaded[2], 16)

                load_gu(0)
                with sp.Fori(0, NFFN - 1) as i:
                    load_gu(i + 1)
                    load_down(i)
                load_down(NFFN - 1)

            def load_mlp():
                uses, _ = plan.at["mlp"]
                up, down = A["w_mlp_in_2"][0], A["w_mlp_out_2"][0]

                def load_up(s, c, use):
                    n0 = c * FC if isinstance(c, int) else sp.snap(c * FC)
                    sp.wait_ge(lo_ready[s], uses[s] + use)
                    sp.dma_start(raw[:, s, :].rearrange("p (a n) -> p a n", a=KT),
                                 up[:, bass.ds(n0, FC)].rearrange("(a p) n -> p a n", p=P)).then_inc(raw_loaded[s], 16)

                def load_down(c):
                    r0 = c * FC if isinstance(c, int) else sp.snap(c * FC)
                    sp.wait_ge(lo_ready[2], uses[2] + c)
                    sp.dma_start(raw[:, 2, :].rearrange("p (a n) -> p a n", a=2),
                                 down[bass.ds(r0, FC), :].rearrange("(a p) n -> p a n", p=P)).then_inc(raw_loaded[2], 16)

                load_up(0, 0, 0)
                load_up(1, 1, 0)
                with sp.Fori(0, NMLP // 2 - 1) as i:
                    load_up(0, i * 2 + 2, i + 1)
                    load_down(i * 2)
                    load_up(1, i * 2 + 3, i + 1)
                    load_down(i * 2 + 1)
                load_down(NMLP - 2)
                load_down(NMLP - 1)

            for name in plan.order:
                if name in ("ffn0", "ffn1"):
                    load_ffn(int(name[3]))
                elif name == "mlp":
                    load_mlp()
                else:
                    load_block(name)
            sp.wait_ge(S("stored"), B("stored") + 32)

        ada_src = A["w_ada_2"][0].rearrange("(p k) n -> p k n", k=KT)
        NADA = 6 * D // 256
        ada_raw = [W3(w, KT) for w in (3, 4, 7, 9)]
        ada_acc = wide[:, 0:6 * D]

        @block.gpsimd
        def _(pool):
            nc.gpsimd.memset(ones[:, :], 1.0).then_inc(S("ones"), 1)
            pool.wait_ge(S("ones"), B("ones") + 1)
            nc.gpsimd.memset(lowr[64:65, 0:2 * SEQ], 1.0).then_inc(S("lowr_one"), 1)
            pool.wait_ge(S("wst"), B("wst") + 1)
            pool.wait_ge(S("lowr_one"), B("lowr_one") + 1)
            nc.gpsimd.memset(W3(4, 4, 512, 512)[64:128, :, 0:64], 0.0).then_inc(S("wst_masked"), 1)
            pool.wait_ge(S("wkv.done"), B("wkv.done") + 8)
            pool.wait_ge(S("wst_masked"), B("wst_masked") + 1)
            nc.gpsimd.memset(W(4, 0, D)[0:64, :], 0.0).then_inc(S("s0_zero"), 1)
            pool.wait_ge(S("rw.xl"), B("rw.xl") + 8)
            pool.wait_ge(S("mix1.add"), B("mix1.add") + 4)
            pool.wait_ge(S("s0_zero"), B("s0_zero") + 1)
            nc.gpsimd.memset(ada_acc, 0.0).then_inc(S("acc_zero"), 1)
            pool.wait_ge(S("acc_zero"), B("acc_zero") + 1)
            pool.dma_start(ada_acc[0:1, :], A["b_ada_2"]).then_inc(S("acc_bias"), 16)
            for j in range(NADA // 2):
                if j >= 2:
                    pool.wait_ge(S("ada_step"), B("ada_step") + 16 * (j - 1))
                for b in range(2):
                    pool.dma_start(ada_raw[2 * (j % 2) + b], ada_src[:, :, (2 * j + b) * 256:(2 * j + b + 1) * 256])\
                        .then_inc(S(f"ada{2 * (j % 2) + b}"), 16)

        @block.tensor
        def _(pe):
            def mm3(o, lh, ll, rh, rl, start, stop):
                pe.matmul(o, lh, rh, start=start, stop=False)
                pe.matmul(o, ll, rh, start=False, stop=False)
                return pe.matmul(o, lh, rl, start=False, stop=stop)

            def tok(t):
                return slice(t * P, (t + 1) * P)

            def arrive(name):
                s, use, _, _ = plan.at[name]
                pe.wait_ge(lo_ready[s], use + 1)
                return s

            def half(s, kts, outs, n, start, stop):
                for t in range(NT):
                    for j, kt in enumerate(kts):
                        m = mm3(outs[t], xh[:, kt, tok(t)], xl[:, kt, tok(t)],
                                wh[:, s, j * n:(j + 1) * n], wl[:, s, j * n:(j + 1) * n],
                                start and j == 0, stop and j == len(kts) - 1)
                return m

            def linear(what, xname, n_chunks, xcount=0, n=512, free=None, banks=None):
                for c in range(n_chunks):
                    if free:
                        free(c)
                    o = [ps[:, 2 * (c % 2) + t, 0:n] for t in range(NT)]
                    for k in range(2):
                        s = arrive((what, c, k))
                        if c == 0:
                            pe.wait_ge(S(xname), B(xname) + xcount + 4 * (k + 1))
                        half(s, range(4 * k, 4 * k + 4), o, n, k == 0, k == 1).then_inc(w_used[s], 1)

            def norm_transposes(name):
                for t in range(NT):
                    pe.wait_ge(S(name + ".hn"), B(name + ".hn") + t + 1)
                    for kt in range(KT):
                        m = pe.transpose(ps[:, 4 + kt // 2, (kt % 2) * SEQ + t * P:(kt % 2) * SEQ + (t + 1) * P],
                                         hn[:, t, kt * P:(kt + 1) * P], ident)
                        if t == NT - 1 and kt % 2:
                            m.then_inc(S(name + ".T"), 1)

            def ffn_loop(l):
                f = f"ffn{l}"
                uses, _ = plan.at[f]

                def gu_half(k, c, last):
                    pe.wait_ge(lo_ready[k], uses[k] + c + 1)
                    pe.wait_ge(lo_ready[k], uses[k] + 1)
                    m = half(k, range(4 * k, 4 * k + 4), [ps[:, 4, :], ps[:, 5, :]], 512, k == 0, k == 1)
                    m.then_inc(w_used[k], 1)

                def body(i, first, last):
                    if not last:
                        pe.wait_ge(S(f + ".h"), B(f + ".h") + i + 1)
                        gu_half(0, i + 1, False)
                    pe.wait_ge(S(f + ".h"), B(f + ".h") + i + 1)
                    pe.wait_ge(S(f + ".h"), B(f + ".h") + 1)
                    for t in range(NT):
                        for j in range(2):
                            m = pe.transpose(ps[:, 6, j * SEQ + t * P:j * SEQ + (t + 1) * P],
                                             hmid[:, t, j * P:(j + 1) * P], ident)
                    m.then_inc(S(f + ".mT"), 1)
                    if not last:
                        gu_half(1, i + 1, True)
                    pe.wait_ge(S(f + ".gl"), B(f + ".gl") + i + 1)
                    pe.wait_ge(lo_ready[2], uses[2] + i + 1)
                    pe.wait_ge(lo_ready[2], uses[2] + 1)
                    for j in range(2):
                        for t in range(NT):
                            for n in range(2):
                                w = slice(j * D + n * 512, j * D + (n + 1) * 512)
                                m = mm3(ps[:, 2 * t + n, :], gh[:, j, tok(t)], gl[:, j, tok(t)], wh[:, 2, w], wl[:, 2, w],
                                        first and j == 0, last and j == 1)
                    m.then_inc(w_used[2], 1)

                for k in range(2):
                    pe.wait_ge(S(f + ".xl"), B(f + ".xl") + 4 * (k + 1))
                    gu_half(k, 0, True)
                body(0, True, False)
                with pe.Fori(1, NFFN - 1) as i:
                    body(i, False, False)
                body(NFFN - 1, False, True)

            def mlp_loop():
                uses, _ = plan.at["mlp"]

                def up(s, use, t):
                    if t == 0:
                        pe.wait_ge(lo_ready[s], uses[s] + use + 1)
                        pe.wait_ge(lo_ready[s], uses[s] + 1)
                    for kt in range(KT):
                        m = mm3(ps[:, 4 + s, t * FC:(t + 1) * FC], xh[:, kt, tok(t)], xl[:, kt, tok(t)],
                                wh[:, s, kt * FC:(kt + 1) * FC], wl[:, s, kt * FC:(kt + 1) * FC],
                                kt == 0, kt == KT - 1)
                    if t == NT - 1:
                        m.then_inc(w_used[s], 1)

                def body(c, s_next, use_next, first, last):
                    if not last:
                        if not first:
                            pe.wait_ge(S("mlp.act"), B("mlp.act") + c)
                        up(s_next, use_next, 0)
                    pe.wait_ge(S("mlp.h"), B("mlp.h") + c + 1)
                    pe.wait_ge(S("mlp.h"), B("mlp.h") + 1)
                    for t in range(NT):
                        for j in range(2):
                            m = pe.transpose(ps[:, 6, j * SEQ + t * P:j * SEQ + (t + 1) * P],
                                             hmid[:, t, j * P:(j + 1) * P], ident)
                    m.then_inc(S("mlp.mT"), 1)
                    if not last:
                        up(s_next, use_next, 1)
                    pe.wait_ge(S("mlp.gl"), B("mlp.gl") + c + 1)
                    pe.wait_ge(lo_ready[2], uses[2] + c + 1)
                    pe.wait_ge(lo_ready[2], uses[2] + 1)
                    for j in range(2):
                        for t in range(NT):
                            for n in range(2):
                                w = slice(j * D + n * 512, j * D + (n + 1) * 512)
                                m = mm3(ps[:, 2 * t + n, :], gh[:, j, tok(t)], gl[:, j, tok(t)], wh[:, 2, w], wl[:, 2, w],
                                        first and j == 0, last and j == 1)
                    m.then_inc(w_used[2], 1)

                pe.wait_ge(S("pre2.xl"), B("pre2.xl") + 8)
                up(0, 0, 0)
                up(0, 0, 1)
                body(0, 1, 0, True, False)
                with pe.Fori(0, NMLP // 2 - 1) as i:
                    body(i * 2 + 1, 0, i + 1, False, False)
                    body(i * 2 + 2, 1, i + 1, False, False)
                body(NMLP - 1, 0, 0, False, True)

            def turn(dst, src, nk=P):
                return pe.transpose(dst, src, masks[0:nk, 0:nk])

            pe.wait_ge(S("rows"), B("rows") + 16 * 14)
            turn(ps[:, 0, 0:P], W(6, 0, P))
            turn(ps[:, 0, P:P + 5], W(6, P, P)[0:5, :], 5)
            for kt in range(KT):
                m = turn(ps[:, 1, kt * CK:(kt + 1) * CK], W(6, 256 + kt * P, P)[0:CK, :], CK)
            m.then_inc(S("cols_T"), 1)
            pe.wait_ge(S("mixw"), B("mixw") + 16 * 4)
            for i in range(4):
                m = turn(ps[:, 2, i * P:(i + 1) * P], W(4, i * P, P))
            m.then_inc(S("wst_T"), 1)

            norm_transposes("mix0")

            def ab_free(c):
                if c == 0:
                    pe.wait_ge(S("wst"), B("wst") + 1)
                if c == 2:
                    pe.wait_ge(S("u_ready"), B("u_ready") + 2)
            linear("ab_in", "mix0.xl", 3, free=ab_free)
            pe.wait_ge(S("wst_masked"), B("wst_masked") + 1)
            pe.wait_ge(S("v_normed"), B("v_normed") + 2)
            wst = W3(4, 4, 512, 512)
            za = W3(0, NT)
            zb = W3(1, NT, 0, 1024)
            for t in range(NT):
                for i in range(4):
                    m = pe.matmul(ps[:, 4 + t, i * P:(i + 1) * P], wst[:, i, :], za[:, t, AW + i * P:AW + (i + 1) * P],
                                  start=True, stop=True)
                m.then_inc(S("spatial"), 1)
            pe.wait_ge(S("zb_ready"), B("zb_ready") + 2)
            pmat = W(3, 0, 12 * P).rearrange("p (a g n) -> p a g n", a=3, g=4)
            for g in range(4):
                o = ps[:, 6 + g // 2, (g % 2) * SEQ:(g % 2) * SEQ + SEQ]
                zg = [zb[:, t, g * P:(g + 1) * P] for t in range(NT)]
                pe.matmul(o[:, 0:P], zg[0], pmat[:, 0, g, :], start=True, stop=True)
                pe.matmul(o[:, P:SEQ], zg[1], pmat[:, 1, g, :], start=True, stop=False)
                m = pe.matmul(o[:, P:SEQ], zg[0], pmat[:, 2, g, :], start=False, stop=True)
                if g % 2:
                    m.then_inc(S("pooled_T"), 1)
            pe.wait_ge(S("ya"), B("ya") + 8)
            pe.wait_ge(S("pooled"), B("pooled") + 2)
            poolw = W3(4, 4, 1024, 512)
            pooled = W3(2, 4, 0, 1024)
            for g in range(4):
                m = pe.matmul(ps[:, 4 + g // 2, (g % 2) * SEQ:(g % 2) * SEQ + SEQ], poolw[:, g, :], pooled[:, g, :],
                              start=True, stop=True)
                if g % 2:
                    m.then_inc(S("yb_T"), 1)
            ya = W3(2, NT, 1024, 1024)
            for kt in range(4):
                for t in range(NT):
                    m = turn(ps[:, 6 + kt // 2, (kt % 2) * SEQ + t * P:(kt % 2) * SEQ + (t + 1) * P],
                             ya[:, t, kt * P:(kt + 1) * P])
                if kt % 2:
                    m.then_inc(S("ya_T"), 1)
            linear("ab_out", "ab.xl", 2, free=lambda c: pe.wait_ge(S("ab.xl"), B("ab.xl") + 8))
            norm_transposes("ffn0")
            ffn_loop(0)

            norm_transposes("mix1")
            w1 = W3(10, KT, 0, 512)
            a1 = W3(10, KT, 512, 512)
            g1 = W3(6, KT, 0, KT * GRANK)
            mix = {"w": W3(2, KT), "a": W3(3, KT), "g": W3(2, KT)}
            pe.wait_ge(S("rw_w1"), B("rw_w1") + 48)
            pe.wait_ge(S("mix1.hT"), B("mix1.hT") + 8)
            for n, (what, w) in enumerate((("w", w1), ("a", a1))):
                pe.wait_ge(S("mixed"), B("mixed") + n + 1)
                for kt in range(KT):
                    m = pe.matmul(ps[0:RANK, 4 + n, 0:SEQ], w[:, kt, :], mix[what][:, kt, :], start=kt == 0, stop=kt == KT - 1)
                m.then_inc(S("rank_T"), 1)
            pe.wait_ge(S("mixed"), B("mixed") + 3)
            for part, (r0, r1) in enumerate(((0, P), (P, GRANK))):
                for kt in range(KT):
                    m = pe.matmul(ps[0:r1 - r0, 6 + part, 0:SEQ], g1[:, kt, r0:r1], mix["g"][:, kt, :],
                                  start=kt == 0, stop=kt == KT - 1)
            m.then_inc(S("rank_T"), 1)
            pe.wait_ge(S("rw_w2"), B("rw_w2") + 64)
            for n in range(2):
                pe.wait_ge(S("rank"), B("rank") + n + 1)
                pe.wait_ge(S("lowr_one"), B("lowr_one") + 1)
                w2 = W(4, n * D, D)
                for t in range(NT):
                    for c in range(2):
                        if n == 1:
                            pe.wait_ge(S("sig"), B("sig") + 2 * t + c + 1)
                        m = pe.matmul(ps[:, 2 * t + c, :], lowr[0:RANK + 1, n * SEQ + t * P:n * SEQ + (t + 1) * P],
                                      w2[0:RANK + 1, c * 512:(c + 1) * 512], start=True, stop=True)
                        m.then_inc(S("logit"), 1)
            pe.wait_ge(S("rank"), B("rank") + 3)
            sig = W3(7, NT)
            incl = masks[:, MI["incl_st"]:MI["incl_st"] + P]
            for t in range(NT):
                for c in range(2):
                    m = pe.matmul(ps[:, 4 + 2 * t + c, :], incl, sig[:, t, c * 512:(c + 1) * 512], start=True, stop=True)
            m.then_inc(S("cum"), 1)
            for n, what in enumerate("krv"):
                def rkv_free(c, n=n):
                    if n == 0:
                        if c == 0:
                            pe.wait_ge(S("rate"), B("rate") + 4)
                    else:
                        pe.wait_ge(S("rkv"), B("rkv") + 4 * (n - 1) + 2 * c + 2)
                linear(what, "rkv.xl", 2, xcount=8 * n, free=rkv_free)
            pe.wait_ge(S("exps"), B("exps") + 4)
            for t in range(NT):
                for hp in range(RH // 2):
                    o = hp * 4 + 2 * t
                    m = pe.matmul(ps[:, 4, o:o + 2], sig[:, t, hp * P:(hp + 1) * P], masks[:, MCH:MCH + 2], start=True, stop=True)
            m.then_inc(S("pc_T"), 1)

            rr, aa, vv = [W(w) for w in (0, 10, 6)]
            tmps = WKV_TMP(W, raw)
            pe.wait_ge(S("scaled"), B("scaled") + 16)
            pe.wait_ge(S("pc"), B("pc") + 2)
            pe.wait_ge(S("rkv"), B("rkv") + 12)

            def bank(g, i):
                return ps[:, 4 * (g % 2) + i, :]

            def T(g, name, n, w=P):
                return tmps[g % 2][name][:, n * w:(n + 1) * w]

            def mul(g, b, l, r, sem):
                for n in range(4):
                    m = pe.matmul(bank(g, b)[:, n * P:(n + 1) * P], T(g, l, n), T(g, r, n), start=True, stop=True)
                m.then_inc(S("wkv." + sem), 1)

            def flip(g):
                if g >= 2:
                    pe.wait_ge(S("wkv.done"), B("wkv.done") + g - 1)
                    pe.wait_ge(S("wkv.hc"), B("wkv.hc") + g - 1)
                for q in range(2):
                    h = HEAD0(g) + 2 * q
                    turn(bank(g, 0)[:, q * SEQ:q * SEQ + P], aa[:, HEAD(g, h)[0]:HEAD(g, h)[0] + P])
                    turn(bank(g, 0)[:, q * SEQ + P:(q + 1) * SEQ], rr[:, HEAD(g, h)[0]:HEAD(g, h)[0] + P])
                    for x in range(2):
                        m = turn(bank(g, 1)[:, x * SEQ + q * P:x * SEQ + (q + 1) * P], BK(wide, g, h, x, P))
                m.then_inc(S("wkv.T"), 1)

            def gram(g):
                pe.wait_ge(S("wkv.ar"), B("wkv.ar") + g + 1)
                pe.wait_ge(S("wkv.bk"), B("wkv.bk") + g + 1)
                for x in range(2):
                    for n in range(4):
                        e, q = n // 2, n % 2
                        rows = slice(64 * e, 64 * e + 64)
                        m = pe.matmul(bank(g, 2 * x + e)[:, q * SEQ:(q + 1) * SEQ],
                                      tmps[g % 2]["bk"][rows, x * SEQ + q * P:x * SEQ + (q + 1) * P],
                                      tmps[g % 2]["ar"][rows, q * SEQ:(q + 1) * SEQ], start=True, stop=True)
                    m.then_inc(S("wkv.gram"), 1)

            def gram_ts(g):
                pe.wait_ge(S("wkv.gb"), B("wkv.gb") + g + 1)
                for n in range(4):
                    e, q = n // 2, n % 2
                    rows = slice(64 * e, 64 * e + 64)
                    m = pe.matmul(bank(g, e)[:, q * P:(q + 1) * P], tmps[g % 2]["ar"][rows, q * SEQ:q * SEQ + P],
                                  tmps[g % 2]["bk"][rows, q * P:(q + 1) * P], start=True, stop=True)
                m.then_inc(S("wkv.gram_ts"), 1)

            def power2(g):
                pe.wait_ge(S("wkv.gk"), B("wkv.gk") + g + 1)
                pe.wait_ge(S("wkv.x"), B("wkv.x") + g + 1)
                mul(g, 2, "xt", "x", "x2")
                mul(g, 3, "x", "xt", "x2t")

            def gram_v(g):
                pe.wait_ge(S("wkv.t1"), B("wkv.t1") + g + 1)
                for n in range(4):
                    v0 = HEAD(g, HEAD0(g) + HN(n))[0]
                    m = pe.matmul(bank(g, 0)[:, n * 64:(n + 1) * 64], T(g, "gk", n), vv[:, v0:v0 + 64], start=True, stop=True)
                m.then_inc(S("wkv.gkv"), 1)

            def power4(g):
                pe.wait_ge(S("wkv.x2c"), B("wkv.x2c") + 2 * (g + 1))
                mul(g, 1, "x2", "tt", "t2")
                mul(g, 2, "x2t", "x2", "x4")
                mul(g, 3, "x2", "x2t", "x4t")

            def power8(g):
                pe.wait_ge(S("wkv.x4c"), B("wkv.x4c") + 2 * (g + 1))
                pe.wait_ge(S("wkv.t2c"), B("wkv.t2c") + g + 1)
                pe.wait_ge(S("wkv.gkvc"), B("wkv.gkvc") + g + 1)
                mul(g, 0, "x4t", "x4", "x8")
                mul(g, 1, "x4", "tt", "t4")

            def inverse(g):
                pe.wait_ge(S("wkv.x8c"), B("wkv.x8c") + g + 1)
                pe.wait_ge(S("wkv.t4c"), B("wkv.t4c") + g + 1)
                mul(g, 1, "x8", "tt", "t8")

            def applied(g):
                pe.wait_ge(S("wkv.t8c"), B("wkv.t8c") + g + 1)
                for n in range(4):
                    a0 = HEAD(g, HEAD0(g) + HN(n))[0]
                    pe.matmul(bank(g, 2)[:, n * P:n * P + 64], T(g, "tt", n), T(g, "gkv", n, 64), start=True, stop=True)
                    m = pe.matmul(bank(g, 2)[:, n * P + 64:(n + 1) * P], T(g, "tt", n), aa[:, a0:a0 + 64], start=True, stop=True)
                m.then_inc(S("wkv.r1"), 1)
                mul(g, 3, "off", "tt", "mt")

            def off_1(g):
                pe.wait_ge(S("wkv.r1c"), B("wkv.r1c") + g + 1)
                pe.wait_ge(S("wkv.mtc"), B("wkv.mtc") + g + 1)
                mul(g, 1, "mt", "r1", "r2")

            def off_2(g):
                pe.wait_ge(S("wkv.r2c"), B("wkv.r2c") + g + 1)
                mul(g, 0, "mt", "r2", "r3")

            def off_3(g):
                pe.wait_ge(S("wkv.r3c"), B("wkv.r3c") + g + 1)
                mul(g, 1, "mt", "r2", "r4")

            def state_parts(g):
                pe.wait_ge(S("wkv.r4c"), B("wkv.r4c") + g + 1)
                for p in range(2):
                    c = 2 * (g // 4) + p
                    rows = slice(64 * p, 64 * p + 64)
                    for n in range(4):
                        h, o = HEAD0(g) + HN(n), HN(n) * 64
                        v0 = HEAD(g, h)[0]
                        u_, w_ = T(g, "r2", n)[rows, 0:64], T(g, "r2", n)[rows, 64:P]
                        b_, k_ = [BK(wide, g, h, x, 64)[rows, :] for x in range(2)]
                        if 0 < c < 3:
                            pe.matmul(bank(g, 2 + p)[0:64, SEQ + o:SEQ + o + 64], w_, b_, start=True, stop=True)
                        if c < 3:
                            pe.matmul(bank(g, 2 + p)[0:64, o:o + 64], b_, u_, start=True, stop=False)
                            m = pe.matmul(bank(g, 2 + p)[0:64, o:o + 64], k_, vv[rows, v0:v0 + 64], start=False, stop=True)
                m.then_inc(S("wkv.fg"), 1)

            def out_parts(g):
                for n in range(4):
                    v0, o = HEAD(g, HEAD0(g) + HN(n))[0], HN(n)
                    pe.matmul(bank(g, 0)[0:64, o * P:(o + 1) * P], T(g, "r2", n)[:, 64:P], T(g, "mrb", n), start=True, stop=False)
                    pe.matmul(bank(g, 0)[0:64, o * P:(o + 1) * P], rr[:, v0:v0 + 64], ident, start=False, stop=True)
                    pe.matmul(bank(g, 1)[:, o * 64:(o + 1) * 64], T(g, "mrb", n), T(g, "r2", n)[:, 0:64], start=True, stop=False)
                    m = pe.matmul(bank(g, 1)[:, o * 64:(o + 1) * 64], T(g, "mrk", n), vv[:, v0:v0 + 64], start=False, stop=True)
                m.then_inc(S("wkv.eh"), 1)

            for pair in range(4):
                for step in (flip, gram, gram_ts, power2, gram_v, power4, power8, inverse, applied, off_1, off_2, off_3,
                             state_parts, out_parts):
                    step(2 * pair)
                    step(2 * pair + 1)

            st = W(4, 0, D).rearrange("p (t h c) -> p t h c", t=1, h=RH)
            states = wide[:, 4 * 2048:5 * 2048].rearrange("p (t h c) -> p t h c", t=NT, h=RH)
            ft = W3(8, 2).rearrange("p a (h c) -> p a h c", h=RH)
            chain = W(5, 0, D).rearrange("p (h c) -> p h c", h=RH)
            pe.wait_ge(S("wkv.hc"), B("wkv.hc") + 8)
            for c in (1, 2):
                pe.wait_ge(S("state"), B("state") + c)
                for i in range(RH):
                    m = pe.matmul(ps[0:64, i // 8, (i % 8) * 64:(i % 8 + 1) * 64], ft[0:64, c - 1, i, :], chain[0:64, i, :],
                                  start=True, stop=True)
                m.then_inc(S("state_F"), 1)
            pe.wait_ge(S("s0_zero"), B("s0_zero") + 1)
            pe.wait_ge(S("state_put"), B("state_put") + 3)
            for t in range(NT):
                for i in range(RH):
                    e2 = wide[:, 2048 + (t * RH + i) * P:2048 + (t * RH + i + 1) * P]
                    m = pe.matmul(ps[:, 2 + 2 * t + i // 8, (i % 8) * 64:(i % 8 + 1) * 64], e2, states[:, t, i, :],
                                  start=True, stop=True)
                m.then_inc(S("y_T"), 1)
            pe.wait_ge(S("g2"), B("g2") + 32)
            pe.wait_ge(S("ysum"), B("ysum") + 4)
            g2a, g2b = W(9, 0, D), W(9, D, D)
            for t in range(NT):
                for c in range(2):
                    o = ps[:, 2 + 2 * t + c, :]
                    pe.matmul(o, lowr[:, 2 * SEQ + t * P:2 * SEQ + (t + 1) * P], g2a[:, c * 512:(c + 1) * 512], start=True, stop=False)
                    m = pe.matmul(o, lowr[0:GRANK - P, 3 * SEQ + t * P:3 * SEQ + (t + 1) * P], g2b[0:GRANK - P, c * 512:(c + 1) * 512],
                                  start=False, stop=True)
            m.then_inc(S("gate_T"), 1)
            y = W3(0, NT)
            pe.wait_ge(S("y_gated"), B("y_gated") + 4)
            for kp in range(4):
                for j in range(2):
                    for t in range(NT):
                        kt = 2 * kp + j
                        m = turn(ps[:, (6 + kp) % 8, j * SEQ + t * P:j * SEQ + (t + 1) * P], y[:, t, kt * P:(kt + 1) * P])
                m.then_inc(S("rw.T"), 1)

            def o_free(c):
                if c == 0:
                    pe.wait_ge(S("rw.xl"), B("rw.xl") + 8)
            linear("o", "rw.xl", 2, free=o_free)
            norm_transposes("ffn1")
            ffn_loop(1)

            pe.wait_ge(S("ada_step"), B("ada_step") + 8 * NADA)
            pe.wait_ge(S("ffn1.add"), B("ffn1.add") + 4)
            for n, m_ in enumerate((0, 1, 3, 4)):
                for kt in range(KT):
                    m = pe.matmul(ps[:, 4, n * KT + kt:n * KT + kt + 1], ada_acc[:, m_ * D + kt * P:m_ * D + (kt + 1) * P],
                                  ones[:, 0:1], start=True, stop=True)
            m.then_inc(S("mod_T"), 1)
            for n, m_ in enumerate((2, 5)):
                for c in range(2):
                    if n == 0 and c == 0:
                        pe.wait_ge(S("ones"), B("ones") + 1)
                    m = pe.matmul(ps[:, 2 * n + c, :], ones[:, :],
                                  ada_acc[:, m_ * D + c * 512:m_ * D + (c + 1) * 512], start=True, stop=True)
            m.then_inc(S("gates_T"), 1)
            pe.wait_ge(S("modc"), B("modc") + 1)
            norm_transposes("pre")

            def glu_free(c):
                if c == 0:
                    pe.wait_ge(S("gates"), B("gates") + 4)
                if c >= 2:
                    pe.wait_ge(S("glu"), B("glu") + 2 * (c - 1))
            linear("glu", "pre.xl", 4, free=glu_free)
            uu = W3(10, 4, 0, 1024)
            for n, nw in ((0, QL), (1, KL + ROPE)):
                pe.wait_ge(S("glu"), B("glu") + 2 * (n + 3))
                o = [ps[:, 2 * (n % 2) + t, 0:nw] for t in range(NT)]
                for k in range(2):
                    s = arrive(("lat", n, k))
                    half(s, range(4 * k, 4 * k + 4), o, nw, k == 0, k == 1).then_inc(w_used[s], 1)
            for c in range(4):
                pe.wait_ge(S("glu"), B("glu") + 2 * (c + 1))
                for j in range(2):
                    for t in range(NT):
                        m = turn(ps[:, 4 + c, j * SEQ + t * P:j * SEQ + (t + 1) * P],
                                 W(U_AT[c][0], U_AT[c][1] + t * 256 + j * P, P))
                m.then_inc(S("u_T"), 1)

            lat = W(3, 0, 2 * 704).rearrange("p (t n) -> p t n", t=NT)

            def turn_latents():
                pe.wait_ge(S("lat_n"), B("lat_n") + 4)
                pe.wait_ge(S("u_put"), B("u_put") + 4)
                for kt in range(5):
                    for t in range(NT):
                        m = turn(ps[:, 4 + kt // 2, (kt % 2) * SEQ + t * P:(kt % 2) * SEQ + (t + 1) * P],
                                 lat[:, t, kt * P:(kt + 1) * P])
                    if kt % 2 or kt == 4:
                        m.then_inc(S("lq.T"), 1)

            def gate_free(c):
                if c == 3:
                    turn_latents()
                if c < 2:
                    pe.wait_ge(S("lat"), B("lat") + 2 * (c + 1))
                else:
                    pe.wait_ge(S("gatev"), B("gatev") + 2 * (c - 1))
            linear("gate", "pre.xl", 4, free=gate_free)
            pe.wait_ge(S("gatev"), B("gatev") + 8)
            pe.wait_ge(S("lq.xl"), B("lq.xl") + 5)
            for j in range(4):
                s = arrive(("uq", j))
                w4 = [x[:, s, 0:3 * 384].rearrange("p (k i c) -> p k i c", k=3, i=2) for x in (wh, wl)]
                if j >= 2:
                    pe.wait_ge(S("qn"), B("qn") + j - 1)
                for i in range(2):
                    for kt in range(3):
                        mm3(ps[:, j % 2, i * SEQ:(i + 1) * SEQ], w4[0][:, kt, i, 0:NOPE], w4[1][:, kt, i, 0:NOPE],
                            xh[:, kt, :], xl[:, kt, :], kt == 0, kt == 2)
                for t in range(NT):
                    for kt in range(3):
                        m = mm3(ps[:, 2 + t, j * P:(j + 1) * P], xh[:, kt, tok(t)], xl[:, kt, tok(t)],
                                w4[0][:, kt, :, NOPE:NOPE + ROPE], w4[1][:, kt, :, NOPE:NOPE + ROPE], kt == 0, kt == 2)
                m.then_inc(w_used[s], 1)
            for j in range(2):
                s = arrive(("ukv", j))
                w4 = [x[:, s, :].rearrange("p (k i c) -> p k i c", k=2, i=4) for x in (wh, wl)]
                if j:
                    pe.wait_ge(S("kn"), B("kn") + 2)
                    pe.wait_ge(S("vt"), B("vt") + 2)
                for i in range(4):
                    for kt in range(2):
                        mm3(ps[:, 4 + i // 2, (i % 2) * SEQ:(i % 2 + 1) * SEQ], w4[0][:, kt, i, 0:NOPE], w4[1][:, kt, i, 0:NOPE],
                            xh[:, 3 + kt, :], xl[:, 3 + kt, :], kt == 0, kt == 1)
                for t in range(NT):
                    for kt in range(2):
                        m = mm3(ps[:, 6 + t, :], xh[:, 3 + kt, tok(t)], xl[:, 3 + kt, tok(t)],
                                w4[0][:, kt, :, NOPE:NOPE + VD], w4[1][:, kt, :, NOPE:NOPE + VD], kt == 0, kt == 1)
                m.then_inc(w_used[s], 1)
            ro = W(3, 0, 1280).rearrange("p (t n) -> p t n", t=NT)
            pe.wait_ge(S("roped"), B("roped") + 2)
            pe.wait_ge(S("qn"), B("qn") + 4)
            for kt in range(5):
                b = (0, 0, 1, 1, 2)[kt]
                for t in range(NT):
                    m = turn(ps[:, b, (kt % 2) * SEQ + t * P:(kt % 2) * SEQ + (t + 1) * P], ro[:, t, kt * P:(kt + 1) * P])
                if kt in (1, 3, 4):
                    m.then_inc(S("ro_T"), 1)
            qn = W3(4, NH)
            kn = W3(9, NH)
            qr = W(1, 256, 5 * SEQ).rearrange("p (a n) -> p a n", a=5)
            vt = W3(5, NT)
            pT = [W(8, 1152 + b * 384, 384) for b in range(2)]
            pp = [W3(10, NT, 512 * b, 512) for b in range(2)]
            pe.wait_ge(S("ro_put"), B("ro_put") + 3)
            pe.wait_ge(S("kn"), B("kn") + 4)
            pe.wait_ge(S("vt"), B("vt") + 4)

            def scores(i):
                if i >= 2:
                    pe.wait_ge(S("at.sc"), B("at.sc") + 2 * (i - 1))
                rows = slice(64 * (i % 2), 64 * (i % 2) + 64)
                for t in range(NT):
                    nk = P * (t + 1)
                    o = ps[:, i % 2, t * SEQ:t * SEQ + nk]
                    pe.matmul(o, qn[:, i, tok(t)], kn[:, i, 0:nk], start=True, stop=False)
                    m = pe.matmul(o, qr[rows, i // 2, tok(t)], qr[rows, 4, 0:nk], start=False, stop=True)
                m.then_inc(S("at.s"), 1)

            diags = DIAGS(W, lowr)
            upad = U_PAD(wide)

            def conv_taps(i):
                batch = PE_TAPS[i * TAP_BATCH:(i + 1) * TAP_BATCH]
                pe.wait_ge(S("diag"), B("diag") + i * TAP_BATCH + len(batch))
                for d, (kt, k) in zip(diags[i % 2], batch):
                    m = pe.matmul(CONV_OUT(ps, kt), d, upad[:, kt, k:k + SEQ], start=k == 0, stop=k == CK - 1)
                m.then_inc(S("conv_mm"), 1)

            def weigh(i):
                pe.wait_ge(S("at.p"), B("at.p") + 2 * (i + 1))
                if i >= 2:
                    pe.wait_ge(S("at.pT"), B("at.pT") + i - 1)
                b = i % 2
                turn(ps[:, 2 + b, 0:P], pp[b][:, 0, 0:P])
                turn(ps[:, 2 + b, P:2 * P], pp[b][:, 1, 0:P])
                turn(ps[:, 2 + b, 2 * P:3 * P], pp[b][:, 1, P:SEQ]).then_inc(S("at.T"), 1)
                conv_taps(i)
                pe.wait_ge(S("at.pT"), B("at.pT") + i + 1)
                if i >= 2:
                    pe.wait_ge(S("at.xl"), B("at.xl") + i - 1)
                hc = slice(i * VD, (i + 1) * VD)
                pe.matmul(ps[:, 4 + b, 0:P], vt[:, 0, hc], pT[b][:, 0:P], start=True, stop=True)
                pe.matmul(ps[:, 4 + b, P:SEQ], vt[:, 0, hc], pT[b][:, P:2 * P], start=True, stop=False)
                pe.matmul(ps[:, 4 + b, P:SEQ], vt[:, 1, hc], pT[b][:, 2 * P:3 * P], start=False, stop=True).then_inc(S("at.o"), 1)

            scores(0)
            for i in range(NH):
                if i + 1 < NH:
                    scores(i + 1)
                weigh(i)

            def ao_free(c):
                if c == 0:
                    pe.wait_ge(S("at.pT"), B("at.pT") + NH)
                    pe.wait_ge(S("at.sc"), B("at.sc") + 2 * NH)
            linear("attn_out", "at.xl", 2, free=ao_free)
            cv = W3(2, KT)
            n_dve = KT - CONV_PE
            order = [(0, 2 * CK), (1, 2 * CK)] + [(kt, 0) for kt in range(n_dve, KT)] + [(kt, n_dve * CK) for kt in range(2, n_dve)]
            pe.wait_ge(S("conv_pe"), B("conv_pe") + CONV_PE)
            for n, (kt, steps) in enumerate(order):
                if steps:
                    pe.wait_ge(S("conv_step"), B("conv_step") + steps)
                m = pe.matmul(ps[:, 4, 0:SEQ], ones[:, :], cv[:, kt, :], start=n == 0, stop=n == KT - 1)
            m.then_inc(S("cmean"), 1)
            sq = W3(5, KT)
            for kt in range(KT):
                if kt % 4 == 0:
                    pe.wait_ge(S("csq"), B("csq") + kt // 4 + 1)
                m = pe.matmul(ps[:, 5, 0:SEQ], ones[:, :], sq[:, kt, :], start=kt == 0, stop=kt == KT - 1)
            m.then_inc(S("cvar"), 1)
            linear("conv_out", "cv.xl", 2, free=lambda c: pe.wait_ge(S("yb"), B("yb") + 2 * (c + 1)))
            pe.wait_ge(S("ymix"), B("ymix") + 4)
            ym = W3(9, NT)
            for kp in range(4):
                for j in range(2):
                    for t in range(NT):
                        kt = 2 * kp + j
                        m = turn(ps[:, 4 + kp, j * SEQ + t * P:j * SEQ + (t + 1) * P], ym[:, t, kt * P:(kt + 1) * P])
                m.then_inc(S("ym.T"), 1)
            linear("out", "ym.xl", 2)
            norm_transposes("pre2")
            mlp_loop()

        @block.scalar
        def _(act):
            n_chain = [0]

            def link(ins):
                ins.then_inc(S("act_chain"), 1)
                n_chain[0] += 1
                act.wait_ge(S("act_chain"), B("act_chain") + n_chain[0])

            def split_hi(s, use, loaded, width=SLOT):
                act.wait_ge(raw_loaded[s], loaded)
                if not isinstance(use, int) or use > 0:
                    act.wait_ge(w_used[s], use)
                if not isinstance(use, int):
                    act.wait_ge(raw_loaded[s], 16)
                act.activation(wh[:, s, 0:width], raw[:, s, 0:width], ACT.Copy).then_inc(hi_ready[s], 1)

            def split(*names):
                for name in names:
                    s, use, loaded, width = plan.at[name]
                    split_hi(s, use, loaded, width)

            def split_all(what, n, k=2):
                split(*[(what, c, j) for c in range(n) for j in range(k)])

            def norm_std(name, ready, count):
                act.wait_ge(S(ready), B(ready) + count)
                act.activation(hn[:, 1, :], h[:, 1, :], ACT.Square, scale=D ** -0.5, accum_out=nss[name][:, 1:2]).then_inc(S(name + ".sq"), 1)
                act.wait_ge(S(name + ".ss"), B(name + ".ss") + 1)
                act.wait_ge(S(name + ".sq"), B(name + ".sq") + 1)
                act.activation(nsd[name], nss[name], ACT.Sqrt, bias=eps).then_inc(S(name + ".std"), 1)

            def post_std(name, src):
                for t in range(NT):
                    act.activation(W3(9, NT)[:, t, :].rearrange("p (b n) -> p b n", b=2), src(t), ACT.Square, scale=D ** -0.5,
                                   accum_out=nss[name][:, t:t + 1]).then_inc(S(name + ".sq"), 1)
                act.wait_ge(S(name + ".sq"), B(name + ".sq") + 2)
                act.activation(nsd[name], nss[name], ACT.Sqrt, bias=eps).then_inc(S(name + ".std"), 1)

            def norm_hi(name, gain, base, dst=None, sem=".xh"):
                for kp in range(4):
                    act.wait_ge(S(name + ".T"), B(name + ".T") + kp + 1)
                    for j in range(2):
                        kt = 2 * kp + j
                        d = xh if dst is None else dst
                        act.activation(d[:, kt, :], ps[:, 4 + kp, j * SEQ:(j + 1) * SEQ], ACT.Identity,
                                       scale=col(gain, base + kt)).then_inc(S(name + sem), 1)

            def norm_modulated_hi(name):
                hT = W3(7, KT) if name == "pre" else W3(2, KT)
                act.wait_ge(S(name + ".hT"), B(name + ".hT") + KT)
                for k in range(2):
                    o = slice(4 * k, 4 * k + 4)
                    act.activation(xh[:, o, :], hT[:, o, :], ACT.Copy).then_inc(S(name + ".xh"), 1)

            def copy_hi(name, banks):
                for kp, b in enumerate(banks):
                    act.wait_ge(S(name + ".T"), B(name + ".T") + kp + 1)
                    act.activation(xh[:, 2 * kp:2 * kp + 2, :], ps[:, b, :].rearrange("p (a n) -> p a n", a=2), ACT.Copy)\
                       .then_inc(S(name + ".xh"), 1)

            def ffn_loop(f, uses, loads, per, fn):
                def gu(k, c):
                    split_hi(k, uses[k] + c, loads[k] + per[k] * c + per[k])

                def body(i, last):
                    if not last:
                        gu(0, i + 1)
                    act.wait_ge(w_used[1], uses[1] + i + 1)
                    if not isinstance(i, int):
                        act.wait_ge(S(f + ".h"), B(f + ".h") + i)
                        act.wait_ge(S(f + ".h"), B(f + ".h") + 1)
                    elif i > 0:
                        act.wait_ge(S(f + ".h"), B(f + ".h") + i)
                    for t in range(NT):
                        act.activation(silu[:, t, :], ps[:, 4 + t, 0:FC], fn).then_inc(S(f + ".act"), 1)
                    if not last:
                        gu(1, i + 1)
                    act.wait_ge(S(f + ".mT"), B(f + ".mT") + i + 1)
                    act.wait_ge(w_used[2], uses[2] + i)
                    act.wait_ge(S(f + ".mT"), B(f + ".mT") + 1)
                    act.activation(gh[:, :, :], ps[:, 6, :].rearrange("p (a n) -> p a n", a=2), ACT.Copy).then_inc(S(f + ".gh"), 1)
                    split_hi(2, uses[2] + i, loads[2] + per[2] * i + per[2])

                gu(0, 0)
                gu(1, 0)
                body(0, False)
                with act.Fori(1, NFFN - 1) as i:
                    body(i, False)
                body(NFFN - 1, True)

            def mlp_loop():
                uses, loads = plan.at["mlp"]

                def up(s, use):
                    split_hi(s, uses[s] + use, loads[s] + 16 * use + 16)

                def body(c, s, use, more):
                    act.wait_ge(w_used[s], uses[s] + use + 1)
                    if not (isinstance(c, int) and c == 0):
                        act.wait_ge(S("mlp.h"), B("mlp.h") + c)
                        act.wait_ge(S("mlp.h"), B("mlp.h") + 1)
                    act.activation(silu[:, :, :], ps[:, 4 + s, :].rearrange("p (t n) -> p t n", t=NT), ACT.Relu)\
                       .then_inc(S("mlp.act"), 1)
                    if more:
                        up(s, use + 1)
                    split_hi(2, uses[2] + c, loads[2] + 16 * c + 16)
                    act.wait_ge(S("mlp.mT"), B("mlp.mT") + c + 1)
                    act.wait_ge(w_used[2], uses[2] + c)
                    act.wait_ge(S("mlp.mT"), B("mlp.mT") + 1)
                    act.activation(gh[:, :, :], ps[:, 6, :].rearrange("p (a n) -> p a n", a=2), ACT.Copy).then_inc(S("mlp.gh"), 1)

                up(0, 0)
                up(1, 0)
                body(0, 0, 0, True)
                with act.Fori(0, NMLP // 2 - 2) as i:
                    body(i * 2 + 1, 1, i, True)
                    body(i * 2 + 2, 0, i + 1, True)
                body(NMLP - 3, 1, NMLP // 2 - 2, True)
                body(NMLP - 2, 0, NMLP // 2 - 1, False)
                body(NMLP - 1, 1, NMLP // 2 - 1, False)

            def rows(ap):
                return ap.rearrange("l (k p) -> (l k) p", p=P)

            act.dma_start(h[:, :, :], A["x"][0].rearrange("(t p) n -> p t n", p=P)).then_inc(S("x_loaded"), 16)
            act.dma_start(masks[:, :], masks_d).then_inc(S("masks"), 16)
            vr = W(6, 0, P)

            def row_load(name, src, k):
                r = ROWS[name]
                d = vr[r:r + k, :] if r < P else W(6, P, P)[r - P:r - P + k, :]
                act.dma_start(d, src).then_inc(S("rows"), 16)
            row_load("mix_norm", rows(A["mix_norm"]), 16)
            row_load("ffn_norm", rows(A["ffn_norm"]), 16)
            row_load("mu", rows(A["rwkv_mu"][0]), 48)
            row_load("sgu_bias", A["sgu_bias"][0], 4)
            row_load("pool_scale", rows(A["pool_scale"]), 4)
            row_load("g_pre_mix", rows(A["g_pre_mix_2"]), 8)
            row_load("g_pre_mlp", rows(A["g_pre_mlp_2"]), 8)
            row_load("cn_g", rows(A["conv_norm_g_2"]), 8)
            row_load("cn_b", rows(A["conv_norm_b_2"]), 8)
            row_load("conv_b", rows(A["conv_b_2"]), 8)
            row_load("q_norm", rows(A["q_norm_g_2"]), 3)
            row_load("kv_norm", rows(A["kv_norm_g_2"]), 2)
            act.dma_start(W(6, 256, D)[0:CK, :], A["conv_w_2"][0]).then_inc(S("rows"), 16)
            act.dma_start(ccol, A["c_2"][0].rearrange("(p k) -> p k", k=KT)).then_inc(S("rows"), 16)
            act.dma_start(W3(4, 4, 0, 512), A["sgu_w_s"][0].rearrange("h i j -> i h j")).then_inc(S("mixw"), 16)
            act.dma_start(W3(4, 4, 1024, 512), A["pool_w"][0].rearrange("g c d -> c g d")).then_inc(S("mixw"), 16)
            act.dma_start(W(4, 1536, 512), A["sgu_gain"][0].partition_broadcast(P)).then_inc(S("mixw"), 16)
            act.dma_start(W(3, 0, 12 * P), pool_d).then_inc(S("mixw"), 16)
            act.dma_start(posi[:, :], A["positions_2"][0].rearrange("(t p) -> p t", p=P), allow_slow_non_contiguous=True).then_inc(S("pos"), 16)

            act.wait_ge(S("masks"), B("masks") + 16)
            norm_std("mix0", "x_loaded", 16)
            act.wait_ge(S("cols"), B("cols") + 2)
            norm_hi("mix0", "mix_norm", 0)
            split(("ab_in", 0, 0), ("ab_in", 0, 1), ("ab_in", 1, 0))
            za = W3(0, NT)
            zb = W3(1, NT, 0, 1024)
            used(act, ("ab_in", 0, 1))
            for t in range(NT):
                act.activation(za[:, t, 0:AW], ps[:, t, :], ACT.Gelu).then_inc(S("u_ready"), 1)
            split(("ab_in", 1, 1), ("ab_in", 2, 0), ("ab_in", 2, 1))
            used(act, ("ab_in", 1, 1))
            for t in range(NT):
                act.activation(za[:, t, AW:D], ps[:, 2 + t, :], ACT.Gelu).then_inc(S("v_ready"), 1)
            act.wait_ge(S("v_ss"), B("v_ss") + 1)
            act.activation(vsd, vss, ACT.Sqrt).then_inc(S("v_std"), 1)
            used(act, ("ab_in", 2, 1))
            for t in range(NT):
                act.activation(zb[:, t, :], ps[:, t, :], ACT.Copy).then_inc(S("zb_ready"), 1)
            split(("ab_out", 0, 0), ("ab_out", 0, 1))
            used(act, ("ab_in", 2, 1))
            for b in range(2):
                act.wait_ge(S("yb_T"), B("yb_T") + b + 1)
                for j in range(2):
                    kt = 2 * b + j
                    act.activation(xh[:, 4 + kt, :], ps[:, 4 + b, j * SEQ:(j + 1) * SEQ], ACT.Identity,
                                   scale=col("pool_scale", kt)).then_inc(S("ab.yh"), 1)
            for b in range(2):
                act.wait_ge(S("ya_T"), B("ya_T") + b + 1)
                act.activation(xh[:, 2 * b:2 * b + 2, :], ps[:, 6 + b, :].rearrange("p (a n) -> p a n", a=2), ACT.Copy)\
                   .then_inc(S("ab.xh"), 1)
            split(("ab_out", 1, 0), ("ab_out", 1, 1))

            norm_std("ffn0", "mix0.add", 4)
            norm_hi("ffn0", "ffn_norm", 0)
            u_, l_ = plan.at["ffn0"]
            ffn_loop("ffn0", u_, l_, (32, 32, 16), ACT.Silu)

            act.wait_ge(S("ffn0.h"), B("ffn0.h") + NFFN)
            act.wait_ge(S("ffn0.mT"), B("ffn0.mT") + NFFN)
            act.dma_start(W3(10, KT, 0, 512), A["rwkv_w1"][0].rearrange("(a p) n -> p a n", p=P)).then_inc(S("rw_w1"), 16)
            act.dma_start(W3(10, KT, 512, 512), A["rwkv_a1"][0].rearrange("(a p) n -> p a n", p=P)).then_inc(S("rw_w1"), 16)
            act.dma_start(W3(6, KT, 0, KT * GRANK), A["rwkv_g1"][0].rearrange("(a p) n -> p a n", p=P)).then_inc(S("rw_w1"), 16)
            act.dma_start(W(4, 0, D)[0:RANK, :], A["rwkv_w2"][0]).then_inc(S("rw_w2"), 16)
            act.dma_start(W(4, 0, D)[RANK:RANK + 1, :], A["rwkv_w0"]).then_inc(S("rw_w2"), 16)
            act.dma_start(W(4, D, D)[0:RANK, :], A["rwkv_a2"][0]).then_inc(S("rw_w2"), 16)
            act.dma_start(W(4, D, D)[RANK:RANK + 1, :], A["rwkv_a0"]).then_inc(S("rw_w2"), 16)
            act.dma_start(W(9, 0, D), A["rwkv_k_k"][0].partition_broadcast(P)).then_inc(S("rw_vec"), 16)
            act.dma_start(W(9, D, D), A["rwkv_k_a"][0].partition_broadcast(P)).then_inc(S("rw_vec"), 16)
            act.dma_start(side[:, :], A["rwkv_r_k"][0].rearrange("h c -> (h c)").partition_broadcast(P)).then_inc(S("rw_vec"), 16)
            norm_std("mix1", "ffn0.add", 4)
            norm_hi("mix1", "mix_norm", KT, dst=W3(0, KT), sem=".hT")
            split(("k", 0, 0), ("k", 0, 1), ("k", 1, 0))
            act.wait_ge(S("rank_T"), B("rank_T") + 1)
            act.activation(lowr[0:RANK, 0:SEQ], ps[0:RANK, 4, 0:SEQ], ACT.Tanh).then_inc(S("rank"), 1)
            act.wait_ge(S("rank_T"), B("rank_T") + 2)
            act.activation(lowr[0:RANK, SEQ:2 * SEQ], ps[0:RANK, 5, 0:SEQ], ACT.Copy).then_inc(S("rank"), 1)
            act.wait_ge(S("rank_T"), B("rank_T") + 3)
            act.activation(lowr[:, 2 * SEQ:3 * SEQ], ps[:, 6, 0:SEQ], ACT.Sigmoid)
            act.activation(lowr[0:GRANK - P, 3 * SEQ:4 * SEQ], ps[0:GRANK - P, 7, 0:SEQ], ACT.Sigmoid).then_inc(S("rank"), 1)
            sig = W3(7, NT)
            rate = W3(8, NT)
            for n, (dst, name) in enumerate(((sig, "sig"), (rate, "rate"))):
                for t in range(NT):
                    for c in range(2):
                        act.wait_ge(S("logit"), B("logit") + 4 * n + 2 * t + c + 1)
                        act.activation(dst[:, t, c * 512:(c + 1) * 512], ps[:, 2 * t + c, :], ACT.Sigmoid).then_inc(S(name), 1)
            rkv = {"k": W3(5, NT), "r": W3(4, NT), "v": W3(6, NT)}
            mixes = {"k": W3(3, KT), "r": W3(2, KT), "v": W3(3, KT)}

            def mix_hi(n, what, k):
                act.wait_ge(S("mixed"), B("mixed") + 4 + n)
                if n:
                    used(act, ("krv"[n - 1], 1, k))
                act.activation(xh[:, 4 * k:4 * k + 4, :], mixes[what][:, 4 * k:4 * k + 4, :], ACT.Copy).then_inc(S("rkv.xh"), 1)

            def take(n, what, c):
                used(act, (what, c, 1))
                for t in range(NT):
                    act.activation(rkv[what][:, t, c * 512:(c + 1) * 512], ps[:, 2 * c + t, :], ACT.Copy).then_inc(S("rkv"), 1)

            mix_hi(0, "k", 0)
            mix_hi(0, "k", 1)
            split(("k", 1, 1), ("r", 0, 0))
            take(0, "k", 0)
            split(("r", 0, 1),)
            mix_hi(1, "r", 0)
            mix_hi(1, "r", 1)
            split(("r", 1, 0))
            take(0, "k", 1)
            act.wait_ge(S("kk_ss"), B("kk_ss") + 1)
            act.activation(kss, kss, ACT.Sqrt).then_inc(S("kk_norm"), 1)
            split(("r", 1, 1), ("v", 0, 0))
            take(1, "r", 0)
            split(("v", 0, 1))
            mix_hi(2, "v", 0)
            mix_hi(2, "v", 1)
            split(("v", 1, 0))
            take(1, "r", 1)
            split(("v", 1, 1))
            act.wait_ge(S("cum"), B("cum") + 1)
            act.wait_ge(S("rkv.xl"), B("rkv.xl") + 24)
            for t in range(NT):
                for c in range(2):
                    n = 2 * t + c
                    if n:
                        act.wait_ge(S("scaled"), B("scaled") + 4 * n)
                    cum = ps[:, 4 + n, :]
                    act.activation(W(3, 0, 512), cum, ACT.Exp, scale=-DECAY)
                    act.activation(W(3, 512, 512), cum, ACT.Exp, scale=DECAY).then_inc(S("cum_read"), 1)
                    act.wait_ge(S("cum_prev"), B("cum_prev") + n + 1)
                    act.activation(W(3, 1536, 512), W(3, 1024, 512), ACT.Exp, scale=-DECAY).then_inc(S("exps"), 1)
            take(2, "v", 0)
            take(2, "v", 1)
            act.wait_ge(S("pc_T"), B("pc_T") + 1)
            pcv = pc.rearrange("p (h x c) -> p h x c", h=RH // 2, x=2)
            for x in range(2):
                act.activation(pcv[0:64, :, x, :], ps[64 * x:64 * x + 64, 4, 0:32].rearrange("p (h c) -> p h c", c=4), ACT.Exp,
                               scale=-DECAY).then_inc(S("pc"), 1)

            tmps = WKV_TMP(W, raw)
            yv = W(0).rearrange("p (t h c) -> p t h c", t=NT, h=RH)
            gall = WKV_G(W, side)

            def bank(g, i):
                return ps[:, 4 * (g % 2) + i, :]

            def out_of(sem, b, dst, done, n=512):
                def step(g):
                    act.wait_ge(S("wkv." + sem), B("wkv." + sem) + g + 1)
                    act.activation(tmps[g % 2][dst][:, 0:n], bank(g, b)[:, 0:n], ACT.Copy).then_inc(S("wkv." + done), 1)
                return step

            def state_out(g):
                if g < 4:
                    act.wait_ge(S("wkv.fg"), B("wkv.fg") + g + 1)
                    act.activation(gall[0][0:64, HEAD0(g):HEAD0(g) + 4, :], bank(g, 2)[0:64, 0:256].rearrange("p (u c) -> p u c", u=4),
                                   ACT.Copy)

            def h_out(g):
                act.wait_ge(S("wkv.eh"), B("wkv.eh") + g + 1)
                act.activation(yv[:, g // 4, HEAD0(g):HEAD0(g) + 4, :], bank(g, 1)[:, 0:256].rearrange("p (u c) -> p u c", u=4), ACT.Copy)\
                   .then_inc(S("wkv.hc"), 1)

            for pair in range(4):
                for steps in ((out_of("T", 0, "ar", "ar"),),
                              (out_of("x2", 2, "x2", "x2c"), out_of("x2t", 3, "x2t", "x2c")),
                              (out_of("gkv", 0, "gkv", "gkvc", 256),),
                              (out_of("x4", 2, "x4", "x4c"), out_of("x4t", 3, "x4t", "x4c")),
                              (out_of("x8", 0, "x8", "x8c"),),
                              (out_of("r1", 2, "r1", "r1c"), out_of("mt", 3, "mt", "mtc")),
                              (state_out,), (h_out,)):
                    for g in (2 * pair, 2 * pair + 1):
                        for step in steps:
                            step(g)

            states = wide[:, 4 * 2048:5 * 2048].rearrange("p (t n) -> p t n", t=NT)
            chain = W(5, 0, D)
            act.wait_ge(S("wkv.done"), B("wkv.done") + 8)
            act.dma_start(W(7, 0, D), A["rwkv_ln_w"][0].partition_broadcast(P)).then_inc(S("ln_vec"), 16)
            act.dma_start(W(7, D, D), A["rwkv_ln_b"][0].partition_broadcast(P)).then_inc(S("ln_vec"), 16)
            act.dma_start(W(9, 0, D), A["rwkv_g2"][0][0:P, :]).then_inc(S("g2"), 16)
            act.dma_start(W(9, D, D)[0:GRANK - P, :], A["rwkv_g2"][0][P:GRANK, :]).then_inc(S("g2"), 16)
            for c in (1, 2, 3):
                act.wait_ge(S("state"), B("state") + c)
                p = c % 2
                act.activation(states[64 * p:64 * p + 64, c // 2, :], chain[0:64, :], ACT.Copy).then_inc(S("state_put"), 1)
            split(("o", 0, 0), ("o", 0, 1), ("o", 1, 0))
            act.wait_ge(S("gn_var"), B("gn_var") + 1)
            act.activation(gvar, gvar, ACT.Sqrt).then_inc(S("gn_std"), 1)
            copy_hi("rw", (6, 7, 0, 1))
            split(("o", 1, 1))

            norm_std("ffn1", "mix1.add", 4)
            norm_hi("ffn1", "ffn_norm", KT)
            act.wait_ge(S("rows"), B("rows") + 16 * 14)
            act.activation(ccol, ccol, ACT.Silu).then_inc(S("c_act"), 1)
            u_, l_ = plan.at["ffn1"]
            ffn_loop("ffn1", u_, l_, (32, 32, 16), ACT.Silu)

            act.dma_start(W(8, 0, D), A["final_norm"].partition_broadcast(P)).then_inc(S("fin_vec"), 16)
            act.dma_start(W(6, 0, D), A["g_post_mix_2"][0].partition_broadcast(P)).then_inc(S("post_vec"), 16)
            act.dma_start(W(6, D, D), A["g_post_mlp_2"][0].partition_broadcast(P)).then_inc(S("post_vec"), 16)
            norm_std("fin", "ffn1.add", 4)
            norm_std("pre", "fin.h", 2)
            split(("glu", 0, 0), ("glu", 0, 1))
            norm_modulated_hi("pre")
            split(("glu", 1, 0))
            act.wait_ge(S("angle"), B("angle") + 1)
            act.activation(lowr[:, 0:64], lowr[:, 0:64], ACT.Sin)
            act.activation(lowr[:, 64:128], lowr[:, 64:128], ACT.Sin).then_inc(S("sincos"), 1)
            ub = lowr[:, 512:1024].rearrange("p (t n) -> p t n", t=NT)
            nxt = [("glu", 1, 1), ("glu", 2, 0), ("glu", 2, 1), ("glu", 3, 0), ("glu", 3, 1), ("lat", 0, 0), ("lat", 0, 1), ("lat", 1, 0)]
            for c in range(4):
                used(act, ("glu", c, 1))
                if c:
                    act.wait_ge(S("glu"), B("glu") + 2 * c)
                for t in range(NT):
                    act.activation(ub[:, t, :], ps[:, 2 * (c % 2) + t, 256:512], ACT.Sigmoid).then_inc(S("glu_s"), 1)
                split(*nxt[2 * c:2 * c + 2])
            lat = W(3, 0, 2 * 704).rearrange("p (t n) -> p t n", t=NT)
            used(act, ("lat", 0, 1))
            for t in range(NT):
                act.activation(lat[:, t, 0:QL], ps[:, t, 0:QL], ACT.Copy).then_inc(S("lat"), 1)
            split(("lat", 1, 1), ("gate", 0, 0))
            used(act, ("lat", 1, 1))
            for t in range(NT):
                act.activation(lat[:, t, QL:704], ps[:, 2 + t, 0:KL + ROPE], ACT.Copy).then_inc(S("lat"), 1)
            split(("gate", 0, 1))
            up_ = U_PAD(wide)
            for c in range(4):
                act.wait_ge(S("u_T"), B("u_T") + c + 1)
                act.activation(up_[:, 2 * c:2 * c + 2, CK - 1:CK - 1 + SEQ], ps[:, 4 + c, :].rearrange("p (a n) -> p a n", a=2),
                               ACT.Copy).then_inc(S("u_put"), 1)
            split(("gate", 1, 0))
            act.wait_ge(S("lat_ss"), B("lat_ss") + 1)
            act.activation(qsd, qss, ACT.Sqrt).then_inc(S("lat_std"), 1)
            gates = wide[:, 6 * 2048:8 * 2048].rearrange("p (t n) -> p t n", t=NT)
            nxt = [[("gate", 1, 1), ("gate", 2, 0)], [("gate", 2, 1), ("gate", 3, 0)], [("gate", 3, 1), ("uq", 0)], [("uq", 1), ("uq", 2)]]
            for c in range(4):
                used(act, ("gate", c, 1))
                if c == 0:
                    act.wait_ge(S("gates"), B("gates") + 4)
                for t in range(NT):
                    act.activation(gates[:, t, c * 512:(c + 1) * 512], ps[:, 2 * (c % 2) + t, :], ACT.Sigmoid).then_inc(S("gatev"), 1)
                if c < 3:
                    split(*nxt[c])
                else:
                    for kt in range(5):
                        act.wait_ge(S("lq.T"), B("lq.T") + kt // 2 + 1)
                        act.activation(xh[:, kt, :], ps[:, 4 + kt // 2, (kt % 2) * SEQ:(kt % 2 + 1) * SEQ], ACT.Identity,
                                       scale=col("q_norm", kt) if kt < 3 else col("kv_norm", kt - 3)).then_inc(S("lq.xh"), 1)
            split(("uq", 1), ("uq", 2))
            qn = W3(4, NH)
            kn = W3(9, NH)
            nxt = [[("uq", 3)], [("ukv", 0)], [("ukv", 1)], []]
            for j in range(4):
                used(act, ("uq", j))
                act.activation(qn[:, 2 * j:2 * j + 2, :], ps[:, j % 2, :].rearrange("p (a n) -> p a n", a=2), ACT.Copy).then_inc(S("qn"), 1)
                split(*nxt[j])
            qraw = W(8, 0, 2 * 9 * 64).rearrange("p (t n) -> p t n", t=NT)
            for t in range(NT):
                act.activation(qraw[:, t, 0:512], ps[:, 2 + t, :], ACT.Copy).then_inc(S("qraw"), 1)
            for j in range(2):
                used(act, ("ukv", j))
                for b in range(2):
                    act.activation(kn[:, 4 * j + 2 * b:4 * j + 2 * b + 2, :], ps[:, 4 + b, :].rearrange("p (a n) -> p a n", a=2), ACT.Copy)\
                       .then_inc(S("kn"), 1)
                vt = W3(5, NT)
                for t in range(NT):
                    act.activation(vt[:, t, j * 512:(j + 1) * 512], ps[:, 6 + t, :], ACT.Copy).then_inc(S("vt"), 1)
            qr = W(1, 256, 5 * SEQ).rearrange("p (a n) -> p a n", a=5)
            for b in range(3):
                n = 2 if b < 2 else 1
                act.wait_ge(S("ro_T"), B("ro_T") + b + 1)
                act.activation(qr[:, 2 * b:2 * b + n, :], ps[:, b, 0:n * SEQ].rearrange("p (a n) -> p a n", a=n), ACT.Copy)\
                   .then_inc(S("ro_put"), 1)
            diags = DIAGS(W, lowr)
            act.wait_ge(S("glu"), B("glu") + 8)
            act.wait_ge(S("roped"), B("roped") + 2)

            def diag_taps(i):
                batch = PE_TAPS[i * TAP_BATCH:(i + 1) * TAP_BATCH]
                if i >= 2:
                    act.wait_ge(S("conv_mm"), B("conv_mm") + i - 1)
                for d, (kt, k) in zip(diags[i % 2], batch):
                    c = CONVW + kt * CK + k
                    act.activation(d, ident, ACT.Copy, scale=cols[:, c:c + 1]).then_inc(S("diag"), 1)
            diag_taps(0)
            pp = [W3(10, NT, 512 * b, 512) for b in range(2)]
            pT = [W(8, 1152 + b * 384, 384) for b in range(2)]

            def weights_T(i):
                act.wait_ge(S("at.T"), B("at.T") + i + 1)
                if i >= 2:
                    act.wait_ge(S("at.o"), B("at.o") + i - 1)
                act.activation(pT[i % 2], ps[:, 2 + i % 2, 0:384], ACT.Copy).then_inc(S("at.pT"), 1)

            def out_hi(i):
                act.wait_ge(S("at.o"), B("at.o") + i + 1)
                act.activation(xh[:, i, :], ps[:, 4 + i % 2, 0:SEQ], ACT.Copy).then_inc(S("at.xh"), 1)
            for i in range(NH):
                b = i % 2
                if i:
                    weights_T(i - 1)
                act.wait_ge(S("at.max"), B("at.max") + i + 1)
                for t in range(NT):
                    nk = P * (t + 1)
                    act.activation(pp[b][:, t, 0:nk], pp[b][:, t, 0:nk], ACT.Exp, bias=amax[:, 2 * b + t:2 * b + t + 1],
                                   accum_out=asum[:, 2 * b + t:2 * b + t + 1]).then_inc(S("at.e"), 1)
                if i + 1 < NH:
                    diag_taps(i + 1)
                if i:
                    out_hi(i - 1)
                if i < 3:
                    split((("attn_out", 0, 0), ("attn_out", 0, 1), ("attn_out", 1, 0))[i])
            weights_T(NH - 1)
            out_hi(NH - 1)
            act.wait_ge(S("conv_mm"), B("conv_mm") + NH)
            for kt in range(KT - CONV_PE, KT):
                act.activation(W3(2, KT)[:, kt, :], CONV_OUT(ps, kt), ACT.Identity, bias=col("conv_b", kt)).then_inc(S("conv_pe"), 1)
            split(("attn_out", 1, 1), ("conv_out", 0, 0), ("conv_out", 0, 1))
            cv = W3(2, KT)
            for k in range(2):
                o = slice(4 * k, 4 * k + 4)
                act.wait_ge(S("cv_c"), B("cv_c") + k + 1)
                if k == 0:
                    act.wait_ge(S("at.o"), B("at.o") + NH)
                act.activation(W3(5, KT)[:, o, :], cv[:, o, :], ACT.Square).then_inc(S("csq"), 1)
            act.wait_ge(S("cv_ss"), B("cv_ss") + 1)
            act.activation(lowr[:, 256:512], lowr[:, 256:512], ACT.Sqrt).then_inc(S("cv_std"), 1)
            used(act, ("attn_out", 1, 1))
            for k in range(2):
                o = slice(4 * k, 4 * k + 4)
                act.wait_ge(S("cv_n"), B("cv_n") + k + 1)
                for kt in range(4 * k, 4 * k + 4):
                    act.activation(cv[:, kt, :], cv[:, kt, :], ACT.Silu, bias=col("cn_b", kt), scale=col("cn_g", kt))\
                       .then_inc(S("cv_act"), 1)
                act.wait_ge(S("cv_act"), B("cv_act") + 4 * (k + 1))
                act.activation(xh[:, o, :], cv[:, o, :], ACT.Copy).then_inc(S("cv.xh"), 1)
            split(("conv_out", 1, 0), ("conv_out", 1, 1), ("out", 0, 0), ("out", 0, 1))
            used(act, ("conv_out", 1, 1))
            copy_hi("ym", (4, 5, 6, 7))
            split(("out", 1, 0), ("out", 1, 1))
            used(act, ("out", 0, 1))
            used(act, ("out", 1, 1))
            post_std("post1", POST1(ps))
            norm_std("pre2", "post1.add", 2)
            norm_modulated_hi("pre2")
            mlp_loop()
            act.wait_ge(w_used[2], plan.at["mlp"][0][2] + NMLP)
            post_std("post2", POST2(ps))
            for t in range(NT):
                act.wait_ge(S("post2.add"), B("post2.add") + t + 1)
                act.dma_start(out[0, t * P:(t + 1) * P, :], h[:, t, :]).then_inc(S("stored"), 16)

        @block.vector
        def _(v):
            n_chain = [0]

            def link(ins):
                ins.then_inc(S("dve_chain"), 1)
                n_chain[0] += 1
                v.wait_ge(S("dve_chain"), B("dve_chain") + n_chain[0])

            def f32(ap):
                return ap.bitcast(F32)

            def split_lo(s, use, width=SLOT):
                v.wait_ge(hi_ready[s], use + 1)
                if not isinstance(use, int):
                    v.wait_ge(hi_ready[s], 1)
                v.tensor_tensor(wl[:, s, 0:width], raw[:, s, 0:width], f32(wh[:, s, 0:width]), ALU.subtract).then_inc(lo_ready[s], 1)

            def split(*names):
                for name in names:
                    s, use, _, width = plan.at[name]
                    split_lo(s, use, width)

            def mean_square(src, n, dst, junk):
                return v.tensor_tensor_reduce(out=junk, in0=src, in1=src, scale=1.0 / n, scalar=EPS, op0=ALU.mult, op1=ALU.add,
                                              accum_out=dst)

            def norm(name):
                v.tensor_tensor_reduce(out=hn[:, 0, :], in0=h[:, 0, :], in1=h[:, 0, :], scale=1.0 / D, scalar=0.0, op0=ALU.mult,
                                       op1=ALU.add, accum_out=nss[name][:, 0:1]).then_inc(S(name + ".ss"), 1)
                v.wait_ge(S(name + ".std"), B(name + ".std") + 1)
                link(v.reciprocal(nrs[name], nsd[name]))
                for t in range(NT):
                    v.tensor_scalar(hn[:, t, :], h[:, t, :], nrs[name][:, t:t + 1], None, ALU.mult).then_inc(S(name + ".hn"), 1)

            def norm_lo(name, gain, base):
                for kp in range(4):
                    v.wait_ge(S(name + ".xh"), B(name + ".xh") + 2 * kp + 2)
                    for j in range(2):
                        kt = 2 * kp + j
                        v.scalar_tensor_tensor(out=xl[:, kt, :], in0=ps[:, 4 + kp, j * SEQ:(j + 1) * SEQ], scalar=col(gain, base + kt),
                                               in1=f32(xh[:, kt, :]), op0=ALU.mult, op1=ALU.subtract).then_inc(S(name + ".xl"), 1)

            def norm_modulated(name, scale, shift):
                hT = W3(7, KT) if name == "pre" else W3(2, KT)
                for kp in range(4):
                    v.wait_ge(S(name + ".T"), B(name + ".T") + kp + 1)
                    for j in range(2):
                        kt = 2 * kp + j
                        v.tensor_scalar(hT[:, kt, :], ps[:, 4 + kp, j * SEQ:(j + 1) * SEQ], scale[:, kt:kt + 1], shift[:, kt:kt + 1],
                                        ALU.mult, ALU.add).then_inc(S(name + ".hT"), 1)
                for k in range(2):
                    v.wait_ge(S(name + ".xh"), B(name + ".xh") + k + 1)
                    o = slice(4 * k, 4 * k + 4)
                    v.wait_ge(S(name + ".hT"), B(name + ".hT") + KT)
                    v.tensor_tensor(xl[:, o, :], hT[:, o, :], f32(xh[:, o, :]), ALU.subtract).then_inc(S(name + ".xl"), 4)

            def copy_lo(name, banks):
                for kp, b in enumerate(banks):
                    v.wait_ge(S(name + ".xh"), B(name + ".xh") + kp + 1)
                    o = slice(2 * kp, 2 * kp + 2)
                    v.tensor_tensor(xl[:, o, :], ps[:, b, :].rearrange("p (a n) -> p a n", a=2), f32(xh[:, o, :]), ALU.subtract)\
                     .then_inc(S(name + ".xl"), 2)

            def add_residual(name):
                for t in range(NT):
                    for c in range(2):
                        o = slice(c * 512, (c + 1) * 512)
                        v.tensor_tensor(h[:, t, o], h[:, t, o], ps[:, 2 * t + c, :], ALU.add).then_inc(S(name), 1)
                v.wait_ge(S(name), B(name) + 4)

            def add_linear(lin, name):
                for c in range(2):
                    used(v, (lin, c, 1))
                    for t in range(NT):
                        o = slice(c * 512, (c + 1) * 512)
                        v.tensor_tensor(h[:, t, o], h[:, t, o], ps[:, 2 * c + t, :], ALU.add).then_inc(S(name), 1)
                v.wait_ge(S(name), B(name) + 4)

            ada_left = [(j, k, b) for j in range(NADA // 2) for k in range(KT) for b in range(2)]

            def ada(count):
                for _ in range(min(count, len(ada_left))):
                    j, k, b = ada_left.pop(0)
                    buf, n = 2 * (j % 2) + b, 16 * j + 2 * k + b
                    if k == 0:
                        v.wait_ge(S(f"ada{buf}"), B(f"ada{buf}") + 16 * (j // 2 + 1))
                    else:
                        v.wait_ge(S("ada_step"), B("ada_step") + n - 1)
                    o = ada_acc[:, (2 * j + b) * 256:(2 * j + b + 1) * 256]
                    v.scalar_tensor_tensor(out=o, in0=ada_raw[buf][:, k, :], scalar=ccol[:, k:k + 1], in1=o,
                                           op0=ALU.mult, op1=ALU.add).then_inc(S("ada_step"), 1)

            def ffn_loop(f, uses, ride=(0, 0, 0)):
                def body(i, last):
                    if not last:
                        split_lo(0, uses[0] + i + 1)
                    if not (isinstance(i, int) and i == 0):
                        v.wait_ge(S(f + ".mT"), B(f + ".mT") + i)
                    for t in range(NT):
                        v.wait_ge(S(f + ".act"), B(f + ".act") + i * 2 + t + 1)
                        if not isinstance(i, int):
                            v.wait_ge(S(f + ".act"), B(f + ".act") + 1)
                        m = v.tensor_tensor(hmid[:, t, :], silu[:, t, :], ps[:, 4 + t, FC:2 * FC], ALU.mult)
                    m.then_inc(S(f + ".h"), 1)
                    ada(ride[0])
                    if not last:
                        split_lo(1, uses[1] + i + 1)
                    ada(ride[1])
                    v.wait_ge(S(f + ".gh"), B(f + ".gh") + i + 1)
                    if not isinstance(i, int):
                        v.wait_ge(S(f + ".gh"), B(f + ".gh") + 1)
                    v.tensor_tensor(gl[:, :, :], ps[:, 6, :].rearrange("p (a n) -> p a n", a=2), f32(gh[:, :, :]), ALU.subtract)\
                     .then_inc(S(f + ".gl"), 1)
                    split_lo(2, uses[2] + i)
                    ada(ride[2])

                split_lo(0, uses[0])
                split_lo(1, uses[1])
                body(0, False)
                if any(ride):
                    for i in range(1, NFFN - 1):
                        body(i, False)
                else:
                    with v.Fori(1, NFFN - 1) as i:
                        body(i, False)
                body(NFFN - 1, True)

            def mlp_loop():
                uses, _ = plan.at["mlp"]

                def body(c, s, use, more):
                    if not (isinstance(c, int) and c == 0):
                        v.wait_ge(S("mlp.mT"), B("mlp.mT") + c)
                    v.wait_ge(S("mlp.act"), B("mlp.act") + c + 1)
                    if not isinstance(c, int):
                        v.wait_ge(S("mlp.act"), B("mlp.act") + 1)
                    v.tensor_tensor(hmid[:, :, :], silu[:, :, :], silu[:, :, :], ALU.mult).then_inc(S("mlp.h"), 1)
                    if more:
                        split_lo(s, uses[s] + use + 1)
                    split_lo(2, uses[2] + c)
                    v.wait_ge(S("mlp.gh"), B("mlp.gh") + c + 1)
                    if not isinstance(c, int):
                        v.wait_ge(S("mlp.gh"), B("mlp.gh") + 1)
                    v.tensor_tensor(gl[:, :, :], ps[:, 6, :].rearrange("p (a n) -> p a n", a=2), f32(gh[:, :, :]), ALU.subtract)\
                     .then_inc(S("mlp.gl"), 1)

                split_lo(0, uses[0])
                split_lo(1, uses[1])
                body(0, 0, 0, True)
                with v.Fori(0, NMLP // 2 - 2) as i:
                    body(i * 2 + 1, 1, i, True)
                    body(i * 2 + 2, 0, i + 1, True)
                body(NMLP - 3, 1, NMLP // 2 - 2, True)
                body(NMLP - 2, 0, NMLP // 2 - 1, False)
                body(NMLP - 1, 1, NMLP // 2 - 1, False)

            v.wait_ge(S("x_loaded"), B("x_loaded") + 16)
            norm("mix0")
            v.wait_ge(S("cols_T"), B("cols_T") + 1)
            v.tensor_copy(cols[:, 0:CONVW], ps[:, 0, 0:CONVW]).then_inc(S("cols"), 1)
            v.tensor_copy(cols[:, CONVW:NCOL], ps[:, 1, 0:KT * CK]).then_inc(S("cols"), 1)
            v.wait_ge(S("wst_T"), B("wst_T") + 1)
            v.tensor_copy(W(4, 512, 512), ps[:, 2, :]).then_inc(S("wst"), 1)
            v.wait_ge(S("cols"), B("cols") + 2)
            norm_lo("mix0", "mix_norm", 0)
            split(*[("ab_in", n, k) for n in range(3) for k in range(2)])
            za = W3(0, NT)
            v.wait_ge(S("v_ready"), B("v_ready") + 2)
            for t in range(NT):
                m = mean_square(za[:, t, AW:D], AW, vss[:, t:t + 1], W(2, t * 512, 512))
            m.then_inc(S("v_ss"), 1)
            v.wait_ge(S("v_std"), B("v_std") + 1)
            link(v.reciprocal(vrs, vsd))
            v.wait_ge(S("mixw"), B("mixw") + 64)
            for t in range(NT):
                v.scalar_tensor_tensor(out=za[:, t, AW:D], in0=za[:, t, AW:D], scalar=vrs[:, t:t + 1], in1=W(4, 1536, 512),
                                       op0=ALU.mult, op1=ALU.mult).then_inc(S("v_normed"), 1)
            ya = W3(2, NT, 1024, 1024)
            v.wait_ge(S("u_ready"), B("u_ready") + 2)
            for t in range(NT):
                v.wait_ge(S("spatial"), B("spatial") + t + 1)
                for i in range(4):
                    o = slice(i * P, (i + 1) * P)
                    v.scalar_tensor_tensor(out=ya[:, t, o], in0=ps[:, 4 + t, o], scalar=col("sgu_bias", i), in1=za[:, t, o],
                                           op0=ALU.add, op1=ALU.mult).then_inc(S("ya"), 1)
            for b in range(2):
                v.wait_ge(S("pooled_T"), B("pooled_T") + b + 1)
                v.tensor_copy(W(2, b * 512, 512), ps[:, 6 + b, :]).then_inc(S("pooled"), 1)
            split(("ab_out", 0, 0), ("ab_out", 0, 1))
            for b in range(2):
                v.wait_ge(S("ab.yh"), B("ab.yh") + 2 * (b + 1))
                for j in range(2):
                    kt = 2 * b + j
                    v.scalar_tensor_tensor(out=xl[:, 4 + kt, :], in0=ps[:, 4 + b, j * SEQ:(j + 1) * SEQ], scalar=col("pool_scale", kt),
                                           in1=f32(xh[:, 4 + kt, :]), op0=ALU.mult, op1=ALU.subtract).then_inc(S("ab.xl"), 1)
            for b in range(2):
                v.wait_ge(S("ab.xh"), B("ab.xh") + b + 1)
                o = slice(2 * b, 2 * b + 2)
                v.tensor_tensor(xl[:, o, :], ps[:, 6 + b, :].rearrange("p (a n) -> p a n", a=2), f32(xh[:, o, :]), ALU.subtract)\
                 .then_inc(S("ab.xl"), 2)
            split(("ab_out", 1, 0), ("ab_out", 1, 1))
            add_linear("ab_out", "mix0.add")

            norm("ffn0")
            norm_lo("ffn0", "ffn_norm", 0)
            ffn_loop("ffn0", plan.at["ffn0"][0])
            v.wait_ge(w_used[2], plan.at["ffn0"][0][2] + NFFN)
            add_residual("ffn0.add")

            norm("mix1")
            hT, xx = W3(0, KT), W3(1, KT)
            v.wait_ge(S("mix1.hT"), B("mix1.hT") + KT)
            v.tensor_tensor(xx[:, :, 1:SEQ], hT[:, :, 0:SEQ - 1], hT[:, :, 1:SEQ], ALU.subtract)
            link(v.tensor_scalar(xx[:, :, 0:1], hT[:, :, 0:1], -1.0, None, ALU.mult))

            def mix(i, dst):
                for kt in range(KT):
                    m = v.scalar_tensor_tensor(out=dst[:, kt, :], in0=xx[:, kt, :], scalar=col("mu", i * KT + kt), in1=hT[:, kt, :],
                                               op0=ALU.mult, op1=ALU.add)
                m.then_inc(S("mixed"), 1)

            def mix_lo(n, src, k):
                v.wait_ge(S("rkv.xh"), B("rkv.xh") + 2 * n + k + 1)
                o = slice(4 * k, 4 * k + 4)
                v.tensor_tensor(xl[:, o, :], src[:, o, :], f32(xh[:, o, :]), ALU.subtract).then_inc(S("rkv.xl"), 4)

            mix(1, W3(2, KT))
            mix(4, W3(3, KT))
            v.wait_ge(S("rank_T"), B("rank_T") + 1)
            mix(5, W3(2, KT))
            v.wait_ge(S("rank_T"), B("rank_T") + 2)
            mix(2, W3(3, KT))
            mix_lo(0, W3(3, KT), 0)
            mix_lo(0, W3(3, KT), 1)
            split(("k", 0, 0), ("k", 0, 1), ("k", 1, 0))
            v.wait_ge(S("rank_T"), B("rank_T") + 3)
            mix(0, W3(2, KT))
            v.wait_ge(S("rkv.xl"), B("rkv.xl") + 8)
            mix(3, W3(3, KT))
            split(("k", 1, 1), ("r", 0, 0), ("r", 0, 1))
            mix_lo(1, W3(2, KT), 0)
            mix_lo(1, W3(2, KT), 1)
            split(("r", 1, 0))
            r, k, vv, sig, rate, kk = W3(4, NT), W3(5, NT), W3(6, NT), W3(7, NT), W3(8, NT), W3(10, NT)

            def vec(w, off):
                return W(w, off, D).unsqueeze(1).to_broadcast([P, NT, D])

            def heads(ap):
                return ap.rearrange("p t (h c) -> p (t h) c", c=HD)

            def per_head(ap):
                return ap.unsqueeze(2).to_broadcast([P, NT * RH, HD])

            t0 = W3(0, NT)
            v.wait_ge(S("rw_vec"), B("rw_vec") + 48)
            v.wait_ge(S("rkv"), B("rkv") + 4)
            v.wait_ge(S("mixed"), B("mixed") + 6)
            link(v.tensor_tensor(kk, k, vec(9, 0), ALU.mult))
            link(v.tensor_tensor(t0, kk, kk, ALU.mult))
            v.tensor_reduce(kss, heads(t0), AX_X, ALU.add).then_inc(S("kk_ss"), 1)
            split(("r", 1, 1), ("v", 0, 0))
            v.wait_ge(S("rate"), B("rate") + 4)
            link(v.scalar_tensor_tensor(out=t0, in0=rate, scalar=-1.0, in1=vec(9, D), op0=ALU.add, op1=ALU.mult))
            link(v.scalar_tensor_tensor(out=k, in0=t0, scalar=1.0, in1=k, op0=ALU.add, op1=ALU.mult))
            v.wait_ge(S("kk_norm"), B("kk_norm") + 1)
            link(v.tensor_scalar(kss, kss, 1e-12, None, ALU.max))
            link(v.reciprocal(kss, kss))
            link(v.tensor_tensor(heads(kk), heads(kk), per_head(kss), ALU.mult))
            link(v.scalar_tensor_tensor(out=rate, in0=kk, scalar=-1.0, in1=rate, op0=ALU.mult, op1=ALU.mult))
            split(("v", 0, 1))
            mix_lo(2, W3(3, KT), 0)
            mix_lo(2, W3(3, KT), 1)
            split(("v", 1, 0))
            v.wait_ge(S("rkv"), B("rkv") + 8)
            link(v.tensor_tensor(t0, r, k, ALU.mult))
            link(v.tensor_tensor(t0, t0, side[:, :].unsqueeze(1).to_broadcast([P, NT, D]), ALU.mult))
            v.tensor_reduce(bon, heads(t0), AX_X, ALU.add).then_inc(S("bonus"), 1)
            split(("v", 1, 1))
            bk = wide[:, 2048:3 * 2048].rearrange("p (t q x c) -> p t q x c", t=NT, q=RH // 2, x=2)
            v.wait_ge(S("bonus"), B("bonus") + 1)
            for t in range(NT):
                for c in range(2):
                    n = 2 * t + c
                    o = slice(c * 512, (c + 1) * 512)
                    v.wait_ge(S("cum_read"), B("cum_read") + n + 1)
                    v.tensor_tensor(W(3, 1024, 512), ps[:, 4 + n, :], sig[:, t, o], ALU.subtract).then_inc(S("cum_prev"), 1)
                    pin = W(3, 512, 512).rearrange("p (q c) -> p q c", c=2 * HD)
                    v.tensor_tensor(t0[:, t, o], r[:, t, o], W(3, 0, 512), ALU.mult).then_inc(S("scaled"), 1)
                    v.tensor_tensor(bk[:, t, 4 * c:4 * c + 4, 0, :], rate[:, t, o].rearrange("p (q c) -> p q c", c=2 * HD), pin, ALU.mult)\
                     .then_inc(S("scaled"), 1)
                    v.tensor_tensor(bk[:, t, 4 * c:4 * c + 4, 1, :], k[:, t, o].rearrange("p (q c) -> p q c", c=2 * HD), pin, ALU.mult)\
                     .then_inc(S("scaled"), 1)
                    v.wait_ge(S("exps"), B("exps") + n + 1)
                    v.tensor_tensor(kk[:, t, o], kk[:, t, o], W(3, 1536, 512), ALU.mult).then_inc(S("scaled"), 1)

            tmps = WKV_TMP(W, raw)
            ft = W3(8, 2).rearrange("p a (h c) -> p a h c", h=RH)
            gall = WKV_G(W, side)

            def bank(g, i):
                return ps[:, 4 * (g % 2) + i, :]

            def four(ap):
                return ap.rearrange("p (u c) -> p u c", u=4)

            def grams(g, i):
                b = 4 * (g % 2) + i
                return ps[:, b:b + 2, :].rearrange("p b (u x c) -> p (b u) x c", u=2, x=2)

            def bk_out(g):
                v.wait_ge(S("wkv.T"), B("wkv.T") + g + 1)
                v.tensor_copy(tmps[g % 2]["bk"], bank(g, 1)).then_inc(S("wkv.bk"), 1)

            def mask_b(g):
                tmp, gb = tmps[g % 2], grams(g, 0)
                v.wait_ge(S("wkv.gram"), B("wkv.gram") + 2 * g + 1)
                v.tensor_tensor(four(tmp["xt"]), gb[:, :, 0, :], mask4("diag_st"), ALU.mult)
                v.tensor_tensor(four(tmp["mrb"]), gb[:, :, 1, :], mask4("incl_st"), ALU.mult).then_inc(S("wkv.gb"), 1)

            def mask_k(g):
                tmp, gk = tmps[g % 2], grams(g, 2)
                v.wait_ge(S("wkv.gram"), B("wkv.gram") + 2 * g + 2)
                v.tensor_tensor(four(tmp["gk"]), gk[:, :, 0, :], mask4("strict_st"), ALU.mult)
                v.tensor_tensor(four(tmp["mrk"]), gk[:, :, 1, :], mask4("incl_st"), ALU.mult).then_inc(S("wkv.gk"), 1)

            def mask_b_k(g):
                mask_b(g)
                mask_k(g)

            def mask_x(g):
                tmp, b = tmps[g % 2], 4 * (g % 2)
                x = ps[:, b:b + 2, 0:SEQ].rearrange("p b (u c) -> p b u c", u=2)
                v.wait_ge(S("wkv.gram_ts"), B("wkv.gram_ts") + g + 1)
                v.tensor_tensor(tmp["x"].rearrange("p (b u c) -> p b u c", b=2, u=2), x, mask22("diag_ts"), ALU.mult).then_inc(S("wkv.x"), 1)
                v.tensor_tensor(tmp["off"].rearrange("p (b u c) -> p b u c", b=2, u=2), x, mask22("off_ts"), ALU.mult)
                v.wait_ge(S("wkv.gb"), B("wkv.gb") + g + 1)
                v.tensor_tensor(four(tmp["tt"]), four(tmp["xt"]), mask4("ident"), ALU.add).then_inc(S("wkv.t1"), 1)

            def add_to(sem, b, dst, base, done, before=None):
                def step(g):
                    if before:
                        v.wait_ge(S("wkv." + before), B("wkv." + before) + g + 1)
                    v.wait_ge(S("wkv." + sem), B("wkv." + sem) + g + 1)
                    v.tensor_tensor(tmps[g % 2][dst], tmps[g % 2][base], bank(g, b), ALU.add).then_inc(S("wkv." + done), 1)
                return step

            def state_out(g):
                t, h0 = g // 4, HEAD0(g)
                b = bank(g, 3 - t)
                v.wait_ge(S("wkv.fg"), B("wkv.fg") + g + 1)
                v.tensor_tensor(ft[0:64, t, h0:h0 + 4, :], b[0:64, SEQ:2 * SEQ].rearrange("p (u c) -> p u c", u=4),
                                masks[0:64, 0:64].unsqueeze(1).to_broadcast([64, 4, 64]), ALU.add)
                v.tensor_copy(gall[1 + t][0:64, h0:h0 + 4, :], b[0:64, 0:SEQ].rearrange("p (u c) -> p u c", u=4))

            def e_out(g):
                t, h0 = g // 4, HEAD0(g)
                e2 = wide[:, 2048:3 * 2048].rearrange("p (t h x c) -> p t h x c", t=NT, h=RH, x=2)[:, t, h0:h0 + 4, :, :]
                ep = bank(g, 0)[0:64, :].rearrange("p (u x c) -> p u x c", u=4, x=2)
                v.wait_ge(S("wkv.eh"), B("wkv.eh") + g + 1)
                v.memset(e2[0:64, :, 1, :], 0.0)
                v.memset(e2[64:128, :, 0, :], 0.0)
                v.tensor_copy(e2[0:64, :, 0, :], ep[:, :, 0, :])
                v.tensor_copy(e2[64:128, :, 1, :], ep[:, :, 1, :]).then_inc(S("wkv.done"), 1)

            for pair in range(4):
                for step in (bk_out, mask_b_k, mask_x, add_to("t2", 1, "tt", "tt", "t2c", "t1"),
                             add_to("t4", 1, "tt", "tt", "t4c", "t2c"), add_to("t8", 1, "tt", "tt", "t8c", "t4c"),
                             add_to("r2", 1, "r2", "r1", "r2c", "r1c"), add_to("r3", 0, "r2", "r1", "r3c"),
                             add_to("r4", 1, "r2", "r1", "r4c"), state_out, e_out):
                    step(2 * pair)
                    step(2 * pair + 1)

            chain = W(5, 0, D).rearrange("p (h c) -> p h c", h=RH)
            ctmp = W(5, D, D).rearrange("p (h c) -> p h c", h=RH)
            pch = pc.rearrange("p (h c) -> p h c", c=4)

            def decay(c):
                return pch[0:64, :, c:c + 1].to_broadcast([64, RH, HD])

            v.wait_ge(S("pc"), B("pc") + 2)
            v.wait_ge(S("wkv.hc"), B("wkv.hc") + 8)
            v.tensor_tensor(chain[0:64], gall[0][0:64], decay(0), ALU.mult).then_inc(S("state"), 1)
            for c in (1, 2):
                v.wait_ge(S("state_F"), B("state_F") + c)
                for b in range(2):
                    m = v.tensor_tensor(ctmp[0:64, 8 * b:8 * b + 8, :], ps[0:64, b, :].rearrange("p (h c) -> p h c", c=HD),
                                        gall[c][0:64, 8 * b:8 * b + 8, :], ALU.add)
                link(m)
                v.wait_ge(S("state_put"), B("state_put") + c)
                v.tensor_tensor(chain[0:64], ctmp[0:64], decay(c), ALU.mult).then_inc(S("state"), 1)
            split(("o", 0, 0), ("o", 0, 1), ("o", 1, 0))
            y = W3(0, NT)
            for t in range(NT):
                v.wait_ge(S("y_T"), B("y_T") + t + 1)
                for c in range(2):
                    o = slice(c * 512, (c + 1) * 512)
                    v.tensor_tensor(y[:, t, o], y[:, t, o], ps[:, 2 + 2 * t + c, :], ALU.add).then_inc(S("ysum"), 1)
            v.wait_ge(S("ysum"), B("ysum") + 4)
            yh = heads(y)
            t1 = W3(5, NT)
            link(v.tensor_reduce(mean, yh, AX_X, ALU.add))
            link(v.tensor_scalar(mean, mean, 1.0 / HD, None, ALU.mult))
            link(v.tensor_tensor(yh, yh, per_head(mean), ALU.subtract))
            link(v.tensor_tensor(t1, y, y, ALU.mult))
            link(v.tensor_reduce(gvar, heads(t1), AX_X, ALU.add))
            v.tensor_scalar(gvar, gvar, 1.0 / HD, GN_EPS, ALU.mult, ALU.add).then_inc(S("gn_var"), 1)
            v.wait_ge(S("ln_vec"), B("ln_vec") + 32)
            link(v.tensor_tensor(heads(t1), heads(vv), per_head(bon), ALU.mult))
            link(v.tensor_tensor(t1, t1, vec(7, D), ALU.add))
            v.wait_ge(S("gn_std"), B("gn_std") + 1)
            link(v.reciprocal(gvar, gvar))
            link(v.tensor_tensor(yh, yh, per_head(gvar), ALU.mult))
            link(v.tensor_tensor(y, y, vec(7, 0), ALU.mult))
            link(v.tensor_tensor(y, y, t1, ALU.add))
            v.wait_ge(S("gate_T"), B("gate_T") + 1)
            for t in range(NT):
                for c in range(2):
                    o = slice(c * 512, (c + 1) * 512)
                    v.tensor_tensor(y[:, t, o], y[:, t, o], ps[:, 2 + 2 * t + c, :], ALU.mult).then_inc(S("y_gated"), 1)
            copy_lo("rw", (6, 7, 0, 1))
            split(("o", 1, 1))
            add_linear("o", "mix1.add")

            norm("ffn1")
            norm_lo("ffn1", "ffn_norm", KT)
            v.wait_ge(S("c_act"), B("c_act") + 1)
            v.wait_ge(S("acc_bias"), B("acc_bias") + 16)
            ffn_loop("ffn1", plan.at["ffn1"][0], (5, 6, 7))
            v.wait_ge(w_used[2], plan.at["ffn1"][0][2] + NFFN)
            add_residual("ffn1.add")

            norm("fin")
            v.wait_ge(S("fin_vec"), B("fin_vec") + 16)
            v.wait_ge(S("fin.hn"), B("fin.hn") + 2)
            for t in range(NT):
                v.tensor_tensor(h[:, t, :], hn[:, t, :], W(8, 0, D), ALU.mult).then_inc(S("fin.h"), 1)
            v.wait_ge(S("fin.h"), B("fin.h") + 2)
            v.wait_ge(S("mod_T"), B("mod_T") + 1)
            v.tensor_copy(modc, ps[:, 4, 0:32]).then_inc(S("modc"), 1)
            v.wait_ge(S("modc"), B("modc") + 1)
            link(v.scalar_tensor_tensor(out=sc1, in0=modc[:, 8:16], scalar=1.0, in1=cols[:, ROWS["g_pre_mix"]:ROWS["g_pre_mix"] + 8],
                                        op0=ALU.add, op1=ALU.mult))
            link(v.scalar_tensor_tensor(out=sc2, in0=modc[:, 24:32], scalar=1.0, in1=cols[:, ROWS["g_pre_mlp"]:ROWS["g_pre_mlp"] + 8],
                                        op0=ALU.add, op1=ALU.mult))
            norm("pre")
            split(("glu", 0, 0))
            norm_modulated("pre", sc1, modc[:, 0:8])
            v.wait_ge(S("gates_T"), B("gates_T") + 1)
            v.wait_ge(S("post_vec"), B("post_vec") + 32)
            gb1, gb2 = GB1(W), side
            for n, dst in enumerate((gb1, gb2)):
                for c in range(2):
                    o = slice(c * 512, (c + 1) * 512)
                    v.tensor_tensor(dst[:, o], ps[:, 2 * n + c, :], W(6, n * D + c * 512, 512), ALU.mult).then_inc(S("gates"), 1)
            split(("glu", 0, 1), ("glu", 1, 0))
            v.wait_ge(S("pos"), B("pos") + 16)
            link(v.tensor_copy(posf, posi[:, :]))
            freq = masks[:, MFREQ:MFREQ + 32]
            ang = lowr[:, 128:192]
            turns = lowr[:, 192:256]
            for t in range(NT):
                m = v.tensor_scalar(ang[:, t * 32:(t + 1) * 32], freq, posf[:, t:t + 1], None, ALU.mult)
            link(m)
            link(v.tensor_scalar(turns, ang, float(1 / (2 * np.pi)), 12582912.0, ALU.mult, ALU.add))
            link(v.tensor_scalar(turns, turns, 12582912.0, None, ALU.subtract))
            for part in (6.28125, 0.0019340515136718750, float(2 * np.pi - 6.28125 - 0.0019340515136718750)):
                link(v.scalar_tensor_tensor(out=ang, in0=turns, scalar=-part, in1=ang, op0=ALU.mult, op1=ALU.add))
            link(v.tensor_scalar(lowr[:, 0:64], ang, -3.1415925, 3.1415925, ALU.max, ALU.min))
            link(v.scalar_tensor_tensor(out=ang, in0=lowr[:, 0:64], scalar=-1.0, in1=lowr[:, 0:64], op0=ALU.mult, op1=ALU.max))
            v.tensor_scalar(lowr[:, 64:128], ang, -1.0, float(np.pi / 2), ALU.mult, ALU.add).then_inc(S("angle"), 1)
            ub = lowr[:, 512:1024].rearrange("p (t n) -> p t n", t=NT)
            upad = U_PAD(wide)
            nxt = [("glu", 1, 1), ("glu", 2, 0), ("glu", 2, 1), ("glu", 3, 0), ("glu", 3, 1), ("lat", 0, 0), ("lat", 0, 1), ("lat", 1, 0)]
            for c in range(4):
                for t in range(NT):
                    v.wait_ge(S("glu_s"), B("glu_s") + 2 * c + t + 1)
                    v.tensor_tensor(W(U_AT[c][0], U_AT[c][1] + t * 256, 256), ps[:, 2 * (c % 2) + t, 0:256], ub[:, t, :], ALU.mult)\
                     .then_inc(S("glu"), 1)
                split(*nxt[2 * c:2 * c + 2])
            split(("lat", 1, 1), ("gate", 0, 0), ("gate", 0, 1))
            lat = W(3, 0, 2 * 704).rearrange("p (t n) -> p t n", t=NT)
            v.wait_ge(S("lat"), B("lat") + 4)
            for t in range(NT):
                mean_square(lat[:, t, 0:QL], QL, qss[:, t:t + 1], W(2, t * D, QL))
                m = mean_square(lat[:, t, QL:QL + KL], KL, qss[:, 2 + t:3 + t], W(2, t * D + 512, KL))
            m.then_inc(S("lat_ss"), 1)
            v.memset(upad[:, :, 0:CK - 1], 0.0)
            split(("gate", 1, 0))
            v.wait_ge(S("lat_std"), B("lat_std") + 1)
            link(v.reciprocal(qrs, qsd))
            for t in range(NT):
                v.tensor_scalar(lat[:, t, 0:QL], lat[:, t, 0:QL], qrs[:, t:t + 1], None, ALU.mult).then_inc(S("lat_n"), 1)
                v.tensor_scalar(lat[:, t, QL:QL + KL], lat[:, t, QL:QL + KL], qrs[:, 2 + t:3 + t], None, ALU.mult).then_inc(S("lat_n"), 1)
            cv = W3(2, KT)
            n_dve = KT - CONV_PE
            taps = [(kt, k) for tiles in ((0, 1), range(2, n_dve)) for k in range(CK) for kt in tiles]
            step_of = {tap: n + 1 for n, tap in enumerate(taps)}

            def conv(n):
                for _ in range(min(n, len(taps))):
                    kt, k = taps.pop(0)
                    w = cols[:, CONVW + kt * CK + k:CONVW + kt * CK + k + 1]
                    src = upad[:, kt, k:k + SEQ]
                    if k == 0:
                        m = v.tensor_scalar(cv[:, kt, :], src, w, col("conv_b", kt), ALU.mult, ALU.add)
                    else:
                        v.wait_ge(S("conv_step"), B("conv_step") + step_of[kt, k - 1])
                        m = v.scalar_tensor_tensor(out=cv[:, kt, :], in0=src, scalar=w, in1=cv[:, kt, :], op0=ALU.mult, op1=ALU.add)
                    m.then_inc(S("conv_step"), 1)
            v.wait_ge(S("u_put"), B("u_put") + 4)
            for name in [("gate", 1, 1), ("gate", 2, 0), ("gate", 2, 1), ("gate", 3, 0), ("gate", 3, 1), ("uq", 0)]:
                split(name)
                conv(7)
            for b in range(3):
                v.wait_ge(S("lq.xh"), B("lq.xh") + min(2 * b + 2, 5))
                for kt in range(2 * b, min(2 * b + 2, 5)):
                    v.scalar_tensor_tensor(out=xl[:, kt, :], in0=ps[:, 4 + b, (kt % 2) * SEQ:(kt % 2 + 1) * SEQ],
                                           scalar=col("q_norm", kt) if kt < 3 else col("kv_norm", kt - 3), in1=f32(xh[:, kt, :]),
                                           op0=ALU.mult, op1=ALU.subtract).then_inc(S("lq.xl"), 1)
            for name in [("uq", 1), ("uq", 2)]:
                split(name)
                conv(7)
            for name in [("uq", 3), ("ukv", 0), ("ukv", 1)]:
                conv(9)
                split(name)
            qraw = W(8, 0, 2 * 9 * 64).rearrange("p (t n) -> p t n", t=NT)
            ro = W(3, 0, 1280).rearrange("p (t n) -> p t n", t=NT)
            v.wait_ge(S("qraw"), B("qraw") + 2)
            v.wait_ge(S("lq.T"), B("lq.T") + 3)
            for t in range(NT):
                m = v.tensor_copy(qraw[:, t, 512:576], lat[:, t, QL + KL:704])
            link(m)
            v.wait_ge(S("sincos"), B("sincos") + 1)
            ropet = W(10, 0, 2 * 288)
            for t in range(NT):
                src = qraw[:, t, :].rearrange("p (h x c) -> p h x c", x=2, c=32)
                dst = ro[:, t, 0:576].rearrange("p (h x c) -> p h x c", x=2, c=32)
                sn = lowr[:, t * 32:(t + 1) * 32].unsqueeze(1).to_broadcast([P, 9, 32])
                cs = lowr[:, 64 + t * 32:64 + (t + 1) * 32].unsqueeze(1).to_broadcast([P, 9, 32])
                ta = ropet[:, 0:288].rearrange("p (h c) -> p h c", c=32)
                tb = ropet[:, 288:576].rearrange("p (h c) -> p h c", c=32)
                v.tensor_tensor(dst[:, :, 0, :], src[:, :, 0, :], cs, ALU.mult)
                v.tensor_tensor(dst[:, :, 1, :], src[:, :, 1, :], cs, ALU.mult)
                v.tensor_tensor(ta, src[:, :, 1, :], sn, ALU.mult)
                link(v.tensor_tensor(tb, src[:, :, 0, :], sn, ALU.mult))
                v.tensor_tensor(dst[:, :, 0, :], dst[:, :, 0, :], ta, ALU.subtract)
                link(v.tensor_tensor(dst[:, :, 1, :], dst[:, :, 1, :], tb, ALU.add))
                v.tensor_copy(ro[:, t, 576:640], ro[:, t, 512:576]).then_inc(S("roped"), 1)
            pp = [W3(10, NT, 512 * b, 512) for b in range(2)]
            causal = masks[:, MI["causal"]:MI["causal"] + P]

            def finish(i):
                b = i % 2
                v.wait_ge(S("at.e"), B("at.e") + 2 * (i + 1))
                link(v.reciprocal(arec[:, 2 * b:2 * b + 2], asum[:, 2 * b:2 * b + 2]))
                for t in range(NT):
                    nk = P * (t + 1)
                    v.tensor_scalar(pp[b][:, t, 0:nk], pp[b][:, t, 0:nk], arec[:, 2 * b + t:2 * b + t + 1], None, ALU.mult)\
                     .then_inc(S("at.p"), 1)

            def out_lo(i):
                v.wait_ge(S("at.xh"), B("at.xh") + i + 1)
                v.tensor_tensor(xl[:, i, :], ps[:, 4 + i % 2, 0:SEQ], f32(xh[:, i, :]), ALU.subtract).then_inc(S("at.xl"), 1)

            for i in range(NH):
                b = i % 2
                v.wait_ge(S("at.s"), B("at.s") + i + 1)
                if i >= 2:
                    v.wait_ge(S("at.T"), B("at.T") + i - 1)
                v.scalar_tensor_tensor(out=pp[b][:, 0, 0:P], in0=ps[:, b, 0:P], scalar=SCALE, in1=causal, op0=ALU.mult, op1=ALU.add)
                v.tensor_scalar(pp[b][:, 1, 0:P], ps[:, b, SEQ:SEQ + P], SCALE, None, ALU.mult).then_inc(S("at.sc"), 1)
                v.scalar_tensor_tensor(out=pp[b][:, 1, P:SEQ], in0=ps[:, b, SEQ + P:2 * SEQ], scalar=SCALE, in1=causal, op0=ALU.mult,
                                       op1=ALU.add).then_inc(S("at.sc"), 1)
                v.wait_ge(S("at.sc"), B("at.sc") + 2 * (i + 1))
                for t in range(NT):
                    m = v.tensor_reduce(amax[:, 2 * b + t:2 * b + t + 1], pp[b][:, t, 0:P * (t + 1)], AX_X, ALU.max)
                link(m)
                v.tensor_scalar(amax[:, 2 * b:2 * b + 2], amax[:, 2 * b:2 * b + 2], -1.0, None, ALU.mult).then_inc(S("at.max"), 1)
                conv(4)
                finish(i)
                if i < 3:
                    split((("attn_out", 0, 0), ("attn_out", 0, 1), ("attn_out", 1, 0))[i])
                else:
                    conv(5)
                if i:
                    out_lo(i - 1)
            out_lo(NH - 1)
            split(("attn_out", 1, 1), ("conv_out", 0, 0), ("conv_out", 0, 1))
            conv(len(taps))
            v.wait_ge(S("cmean"), B("cmean") + 1)
            cmean = lowr[:, 512:768]
            link(v.tensor_scalar(cmean, ps[:, 4, 0:SEQ], 1.0 / D, None, ALU.mult))
            for k in range(2):
                o = slice(4 * k, 4 * k + 4)
                v.tensor_tensor(cv[:, o, :], cv[:, o, :], cmean.unsqueeze(1).to_broadcast([P, 4, SEQ]), ALU.subtract).then_inc(S("cv_c"), 1)
            v.wait_ge(S("cvar"), B("cvar") + 1)
            v.tensor_scalar(lowr[:, 256:512], ps[:, 5, 0:SEQ], 1.0 / D, EPS, ALU.mult, ALU.add).then_inc(S("cv_ss"), 1)
            v.wait_ge(S("cv_std"), B("cv_std") + 1)
            link(v.reciprocal(lowr[:, 768:1024], lowr[:, 256:512]))
            for k in range(2):
                o = slice(4 * k, 4 * k + 4)
                v.tensor_tensor(cv[:, o, :], cv[:, o, :], lowr[:, 768:1024].unsqueeze(1).to_broadcast([P, 4, SEQ]), ALU.mult).then_inc(S("cv_n"), 1)
            gates = wide[:, 6 * 2048:8 * 2048].rearrange("p (t n) -> p t n", t=NT)
            ym = W3(9, NT)
            for c in range(2):
                used(v, ("attn_out", c, 1))
                for t in range(NT):
                    o = slice(c * 512, (c + 1) * 512)
                    v.tensor_tensor(ym[:, t, o], ps[:, 2 * c + t, :], gates[:, t, D + c * 512:D + (c + 1) * 512], ALU.mult)\
                     .then_inc(S("yb"), 1)
            for k in range(2):
                v.wait_ge(S("cv.xh"), B("cv.xh") + k + 1)
                o = slice(4 * k, 4 * k + 4)
                v.tensor_tensor(xl[:, o, :], cv[:, o, :], f32(xh[:, o, :]), ALU.subtract).then_inc(S("cv.xl"), 4)
            split(("conv_out", 1, 0), ("conv_out", 1, 1), ("out", 0, 0), ("out", 0, 1))
            for c in range(2):
                used(v, ("conv_out", c, 1))
                for t in range(NT):
                    o = slice(c * 512, (c + 1) * 512)
                    g_ = gates[:, t, c * 512:(c + 1) * 512]
                    link(v.tensor_tensor(g_, ps[:, 2 * c + t, :], g_, ALU.mult))
                    v.tensor_tensor(ym[:, t, o], ym[:, t, o], g_, ALU.add).then_inc(S("ymix"), 1)
            copy_lo("ym", (4, 5, 6, 7))
            split(("out", 1, 0), ("out", 1, 1))
            def post(name, src, gb, ready):
                for c in range(2):
                    ready(c)
                v.wait_ge(S(name + ".std"), B(name + ".std") + 1)
                link(v.reciprocal(nrs[name], nsd[name]))
                for t in range(NT):
                    v.scalar_tensor_tensor(out=hn[:, t, :].rearrange("p (b n) -> p b n", b=2), in0=src(t), scalar=nrs[name][:, t:t + 1],
                                           in1=gb.rearrange("p (b n) -> p b n", b=2), op0=ALU.mult, op1=ALU.mult).then_inc(S(name + ".hn"), 1)
                for t in range(NT):
                    v.wait_ge(S(name + ".hn"), B(name + ".hn") + t + 1)
                    v.tensor_tensor(h[:, t, :], h[:, t, :], hn[:, t, :], ALU.add).then_inc(S(name + ".add"), 1)
                v.wait_ge(S(name + ".add"), B(name + ".add") + 2)
            post("post1", POST1(ps), gb1, lambda c: used(v, ("out", c, 1)))
            norm("pre2")
            norm_modulated("pre2", sc2, modc[:, 16:24])
            mlp_loop()
            v.wait_ge(w_used[2], plan.at["mlp"][0][2] + NMLP)
            post("post2", POST2(ps), gb2[:, :], lambda c: None)


U_AT = ((8, 0), (8, 512), (8, 1024), (8, 1536))


def GB1(W):
    return W(10, 1024, D)


def U_PAD(wide):
    n = SEQ + CK - 1
    return wide[:, 0:KT * n].rearrange("p (a n) -> p a n", a=KT)


CONV_PE = 3
PE_TAPS = [(kt, k) for kt in range(KT - CONV_PE, KT) for k in range(CK)]
TAP_BATCH = -(-len(PE_TAPS) // NH)


def CONV_OUT(ps, kt):
    b, o = divmod(kt - KT + 4, 2)
    return ps[:, 6 + b, o * SEQ:(o + 1) * SEQ]


def DIAGS(W, lowr):
    one = [W(3, o, P) for o in range(0, TAP_BATCH * P, P)]
    return one, [W(8, o, P) for o in range(0, 1024, P)] + [lowr[:, 512 + o:512 + o + P] for o in range(0, 512, P)]



def POST1(ps):
    return lambda t: ps[:, t:t + 3:2, :]


def POST2(ps):
    return lambda t: ps[:, 2 * t:2 * t + 2, :]


def HEAD0(g):
    return 4 * (g % 4)


def HN(n):
    return 2 * (n % 2) + n // 2


def HEAD(g, h):
    c = (g // 4) * D + h * HD
    return c, c + HD


def BK(wide, g, h, x, n):
    c = 2048 + (((g // 4) * (RH // 2) + h // 2) * 2 + x) * P + (h % 2) * HD
    return wide[:, c:c + n]


def WKV_TMP(W, raw):
    sets = []
    spots = [W(w, o, 512) for w in (4, 5, 7) for o in range(0, 2048, 512)]
    spots2 = [raw[:, i, o:o + 512] for i in range(3) for o in range(0, 2048, 512)]
    names = ("ar", "bk", "x", "xt", "off", "mrb", "gk", "mrk", "tt", "x2", "x2t", "gkv")
    for s in (spots, spots2):
        t = dict(zip(names, s))
        t["x4"], t["x4t"], t["x8"], t["mt"], t["r1"], t["r2"] = t["x"], t["xt"], t["x2"], t["x2t"], t["ar"], t["bk"]
        sets.append(t)
    return sets


def WKV_G(W, side):
    aps = (W(3, 0, D), W(3, D, D), side[:, :])
    return [a.rearrange("p (h c) -> p h c", h=RH) for a in aps]


INS = ["x", "mix_norm", "ffn_norm", "final_norm", "ab_w_in", "ab_w_out", "sgu_gain", "sgu_w_s", "sgu_bias", "pool_w",
       "pool_scale", "rwkv_mu", "rwkv_w_r", "rwkv_w_k", "rwkv_w_v", "rwkv_w_o", "rwkv_w0", "rwkv_w1", "rwkv_w2", "rwkv_a0",
       "rwkv_a1", "rwkv_a2", "rwkv_g1", "rwkv_g2", "rwkv_k_k", "rwkv_k_a", "rwkv_r_k", "rwkv_ln_w", "rwkv_ln_b",
       "ffn_w_gate", "ffn_w_up", "ffn_w_down", "c_2", "positions_2", "w_ada_2", "b_ada_2", "g_pre_mix_2", "g_post_mix_2",
       "g_pre_mlp_2", "g_post_mlp_2", "w_in_2", "conv_w_2", "conv_b_2", "conv_norm_g_2", "conv_norm_b_2", "w_conv_out_2",
       "q_norm_g_2", "w_uq_2", "kv_norm_g_2", "w_ukv_2", "w_attn_out_2", "w_out_2", "w_mlp_in_2", "w_mlp_out_2"]


def kernel(**inputs):
    import concourse.bacc as bacc
    from concourse.bass_utils import run_bass_kernel_spmd

    nc = bacc.Bacc("TRN2", target_bir_lowering=False, num_devices=1)
    arrays, aps = {}, {}
    for name in INS:
        a = np.ascontiguousarray(inputs[name])
        arrays[f"in_{name}"] = a
        aps[name] = nc.dram_tensor(f"in_{name}", a.shape, mybir.dt.from_np(a.dtype), kind="ExternalInput").ap()
    consts = []
    for name, a in zip(("const_masks", "const_pool"), constants()):
        arrays[name] = a
        consts.append(nc.dram_tensor(name, a.shape, F32, kind="ExternalInput").ap())
    out = nc.dram_tensor("out", (1, SEQ, D), F32, kind="ExternalOutput").ap()
    build(nc, aps, *consts, out)
    r = run_bass_kernel_spmd(nc, [arrays], core_ids=[0])
    return r.results[0]["out"]
```

```python
from contextlib import ExitStack

import numpy as np
import concourse.bass as bass
from concourse import mybir

F32 = mybir.dt.float32
F32R = mybir.dt.float32r
I32 = mybir.dt.int32
ACT = mybir.ActivationFunctionType
ALU = mybir.AluOpType
AX_X = mybir.AxisListType.X

P = 128
D = 1024
SEQ = 256
NT = SEQ // P
KT = D // P
EPS = 1e-6
GN_EPS = 64e-5
FFN = 2816
FC = 256
NFFN = FFN // FC
DFF = 4096
NMLP = DFF // FC
AW = 512
WINDOWS = (2, 4, 8, 16)
RH = 16
HD = 64
CH = 64
RANK = 64
GRANK = 160
NH = 8
NOPE, ROPE, VD = 128, 64, 128
QL, KL = 384, 256
CK = 31
SLOT = 2048
DECAY = float(np.exp(-0.5))
SCALE = float(1.0 / np.sqrt(NOPE + ROPE))

ROWS = {}
VECTORS = (("mix_norm", 16), ("ffn_norm", 16), ("rwkv_mu", 48), ("sgu_bias", 4), ("pool_scale", 4), ("g_pre_mix_2", 8),
           ("g_pre_mlp_2", 8), ("conv_norm_g_2", 8), ("conv_norm_b_2", 8), ("conv_b_2", 8), ("q_norm_g_2", 3), ("kv_norm_g_2", 2))
_at = 0
for _n, _k in VECTORS:
    ROWS[_n] = _at
    _at += _k
CONVW = _at
NCOL = CONVW + KT * CK

MASKS = ("ident", "diag_ts", "off_ts", "diag_st", "strict_st", "incl_st", "causal")
MI = {n: i * P for i, n in enumerate(MASKS)}
MCH = len(MASKS) * P
MFREQ = MCH + 2
MEPS = MFREQ + 32
NMASK = MEPS + 1


def constants():
    a = np.arange(P)
    r, c = a[:, None], a[None, :]
    same = (r // CH) == (c // CH)
    near = (r // 16) == (c // 16)
    m = {
        "ident": r == c,
        "diag_ts": (c < r) & near,
        "off_ts": (c < r) & same & ~near,
        "diag_st": (r < c) & near,
        "strict_st": (r < c) & same,
        "incl_st": (r <= c) & same,
    }
    out = np.zeros((P, NMASK), np.float32)
    for n, v in m.items():
        out[:, MI[n]:MI[n] + P] = v
    out[:, MI["causal"]:MI["causal"] + P] = np.where(c <= r, 0.0, -1e30)
    out[:, MCH:MCH + 2] = (r // CH) == np.arange(2)[None, :]
    freq = 1.0 / (np.float32(10000.0) ** (np.arange(0, ROPE, 2, dtype=np.float32) / np.float32(ROPE)))
    out[:, MFREQ:MFREQ + 32] = freq.astype(np.float32)[None, :]
    out[:, MEPS] = EPS
    pool = np.zeros((P, 3, 4, P), np.float32)
    for g, w in enumerate(WINDOWS):
        inside = (r <= c) & (r > c - w)
        pool[:, 0, g] = np.where(inside, 1.0 / np.minimum(c + 1, w), 0.0) - (r == c)
        pool[:, 1, g] = np.where(inside, 1.0 / w, 0.0) - (r == c)
        pool[:, 2, g] = np.where(r - P > c - w, 1.0 / w, 0.0)
    return out, pool.reshape(P, 12 * P).astype(np.float32)


SHARED = {
    "ff_act": (("ffn0.act", 22), ("ffn1.act", 22), ("mlp.act", 16)),
    "ff_mT": (("ffn0.mT", 11), ("ffn1.mT", 11), ("mlp.mT", 16)),
    "ff_h": (("ffn0.h", 11), ("ffn1.h", 11), ("mlp.h", 16)),
    "ff_gh": (("ffn0.gh", 11), ("ffn1.gh", 11), ("mlp.gh", 16)),
    "ff_gl": (("ffn0.gl", 11), ("ffn1.gl", 11), ("mlp.gl", 16)),
    "pool_1": (("ones", 1), ("fold", 6)),
    "pool_2": (("lowr_one", 1), ("acc_zero", 1)),
    "pe_1": (("cols_T", 1), ("y_T", 2)),
    "pe_2": (("wst_T", 1), ("rw.T", 4)),
    "pe_3": (("mix0.T", 4), ("ffn1.T", 4)),
    "pe_4": (("spatial", 2), ("mod_T", 2)),
    "pe_5": (("pooled_T", 2), ("pre.T", 4)),
    "pe_6": (("yb_T", 2), ("gates_T", 1)),
    "pe_7": (("ya_T", 2), ("u_T", 4)),
    "pe_8": (("ffn0.T", 4), ("lq.T", 3)),
    "pe_9": (("mix1.T", 4), ("ro_T", 3)),
    "pe_10": (("rank_T", 3), ("at.s", 8)),
    "pe_11": (("logit", 8), ("at.T", 8)),
    "pe_12": (("cum", 1), ("conv_mm", 8)),
    "pe_13": (("pc_T", 1), ("at.o", 8)),
    "pe_14": (("wkv.T", 8), ("cmean", 1)),
    "pe_15": (("wkv.gram", 16), ("cvar", 1)),
    "pe_16": (("wkv.gram_ts", 8), ("ym.T", 4)),
    "pe_17": (("wkv.x2", 8), ("pre2.T", 4)),
    "act_1": (("mix0.sq", 1), ("gn_sq", 2), ("pre2.std", 1)),
    "act_2": (("mix0.std", 1), ("gn_std", 2), ("pre2.xh", 2)),
    "act_3": (("mix0.xh", 8), ("rw.xh", 4), ("post2.sq", 2)),
    "act_4": (("u_ready", 2), ("ffn1.sq", 1), ("post2.std", 2)),
    "act_5": (("v_ready", 2), ("ffn1.std", 1)),
    "act_6": (("v_std", 1), ("ffn1.xh", 8)),
    "act_7": (("zb_ready", 2), ("fin.sq", 1)),
    "act_8": (("ab.yh", 4), ("fin.std", 1)),
    "act_9": (("ab.xh", 2), ("pre.sq", 1)),
    "act_10": (("ffn0.sq", 1), ("pre.std", 1)),
    "act_11": (("ffn0.std", 1), ("pre.xh", 2)),
    "act_12": (("ffn0.xh", 8), ("sincos", 1)),
    "act_13": (("c_act", 1), ("glu_s", 8)),
    "act_14": (("mix1.sq", 1), ("lat", 4)),
    "act_15": (("mix1.std", 1), ("u_put", 4)),
    "act_16": (("mix1.hT", 8), ("lat_std", 1)),
    "act_17": (("rank", 3), ("gatev", 8)),
    "act_18": (("sig", 4), ("lq.xh", 5)),
    "act_19": (("rate", 4), ("qn", 4)),
    "act_20": (("rkv.xh", 6), ("vt", 4)),
    "act_21": (("rkv", 12), ("at.pT", 8)),
    "act_22": (("kk_sq", 1), ("qraw", 2)),
    "act_23": (("kk_norm", 1), ("kn", 4)),
    "act_24": (("cum_read", 4), ("ro_put", 3)),
    "act_25": (("exps", 4), ("diag", 62)),
    "act_26": (("pc", 2), ("at.e", 16)),
    "act_27": (("wkv.ar", 8), ("at.xh", 8)),
    "act_28": (("wkv.x2c", 16), ("conv_pe", 2)),
    "act_29": (("wkv.gkvc", 8), ("csq", 2)),
    "act_30": (("wkv.x4c", 16), ("cv_std", 1)),
    "act_31": (("wkv.x8c", 8), ("cv_act", 8)),
    "act_32": (("wkv.r1c", 8), ("cv.xh", 2)),
    "act_33": (("wkv.mtc", 8), ("ym.xh", 4)),
    "act_34": (("wkv.hc", 8), ("post1.sq", 2)),
    "act_35": (("state_put", 3), ("post1.std", 2)),
    "act_36": (("gate_out", 4), ("pre2.sq", 1)),
    "dve_1": (("mix0.ss", 1), ("y_gated", 2), ("post2.add", 2)),
    "dve_2": (("mix0.hn", 2), ("rw.xl", 8)),
    "dve_3": (("cols", 2), ("mix1.add", 4)),
    "dve_4": (("wst", 1), ("ffn1.ss", 1)),
    "dve_5": (("mix0.xl", 8), ("ffn1.hn", 2)),
    "dve_6": (("v_ss", 1), ("ffn1.xl", 8)),
    "dve_7": (("v_normed", 2), ("ffn1.add", 4)),
    "dve_8": (("ya", 8), ("fin.ss", 1)),
    "dve_9": (("pooled", 2), ("fin.h", 2)),
    "dve_10": (("ab.xl", 8), ("pre.ss", 1)),
    "dve_11": (("mix0.add", 4), ("pre.hn", 2)),
    "dve_12": (("ffn0.ss", 1), ("modc", 2)),
    "dve_13": (("ffn0.hn", 2), ("pre.hT", 8)),
    "dve_14": (("ffn0.xl", 8), ("pre.xl", 8)),
    "dve_15": (("ffn0.add", 4), ("angle", 1)),
    "dve_16": (("mix1.ss", 1), ("glu", 8)),
    "dve_17": (("mix1.hn", 2), ("gates", 4)),
    "dve_18": (("mixed", 6), ("lat_ss", 1)),
    "dve_19": (("rkv.xl", 24), ("lq.xl", 5)),
    "dve_20": (("kk", 1), ("lat_n", 4)),
    "dve_21": (("kk_ss", 1), ("conv_step", 186)),
    "dve_22": (("bonus", 1), ("roped", 2)),
    "dve_23": (("cum_prev", 4), ("at.sc", 16)),
    "dve_24": (("scaled", 16), ("at.max", 8)),
    "dve_25": (("wkv.bk", 8), ("at.p", 16)),
    "dve_26": (("wkv.gb", 8), ("at.xl", 8)),
    "dve_27": (("wkv.gk", 8), ("cv_c", 2)),
    "dve_28": (("wkv.x", 8), ("cv_ss", 1)),
    "dve_29": (("wkv.t1", 8), ("cv_n", 2)),
    "dve_30": (("wkv.t2c", 8), ("yb", 4)),
    "dve_31": (("wkv.t4c", 8), ("cv.xl", 8)),
    "dve_32": (("wkv.t8c", 8), ("ymix", 4)),
    "dve_33": (("wkv.r2c", 8), ("ym.xl", 8)),
    "dve_34": (("wkv.r3c", 8), ("post1.hn", 2)),
    "dve_35": (("wkv.r4c", 8), ("post1.add", 2)),
    "dve_36": (("wkv.done", 8), ("pre2.ss", 1)),
    "dve_37": (("state", 3), ("pre2.hn", 2)),
    "dve_38": (("ysum", 4), ("pre2.hT", 8)),
    "dve_39": (("centred", 2), ("pre2.xl", 8)),
    "dve_40": (("gn_var", 2), ("post2.hn", 2)),
}
HOME, BASE = {}, {}
for _home, _names in SHARED.items():
    _at = 0
    for _n, _k in _names:
        HOME[_n], BASE[_n] = _home, _at
        _at += _k


def B(name):
    return BASE.get(name, 0)


class Plan:

    def __init__(self):
        self.uses, self.loads, self.next = [0, 0, 0], [0, 0, 0], 0
        self.order, self.at = [], {}

    def block(self, name, width=SLOT, dmas=1):
        s = self.next
        self.next = (s + 1) % 3
        self.loads[s] += 16 * dmas
        self.at[name] = (s, self.uses[s], self.loads[s], width)
        self.uses[s] += 1
        self.order.append(name)

    def loop(self, name, uses, dmas):
        self.at[name] = (list(self.uses), list(self.loads))
        for s in range(3):
            self.uses[s] += uses[s]
            self.loads[s] += 16 * uses[s] * dmas[s]
        self.uses[0] += 1
        self.loads[0] += 16
        self.next = 1
        self.order.append(name)


def make_plan():
    p = Plan()
    for n in range(3):
        for k in range(2):
            p.block(("ab_in", n, k))
    for n in range(2):
        for k in range(2):
            p.block(("ab_out", n, k))
    p.loop("ffn0", [NFFN, NFFN, NFFN - 1], [2, 2, 1])
    for w in ("k", "r", "v", "o"):
        for n in range(2):
            for k in range(2):
                p.block((w, n, k))
    p.loop("ffn1", [NFFN, NFFN, NFFN - 1], [2, 2, 1])
    for n in range(4):
        for k in range(2):
            p.block(("glu", n, k), dmas=2)
    for n, w in ((0, QL), (1, KL + ROPE)):
        for k in range(2):
            p.block(("lat", n, k), width=4 * w)
    for n in range(4):
        for k in range(2):
            p.block(("gate", n, k))
    for n in range(4):
        p.block(("uq", n), width=3 * 384)
    for n in range(2):
        p.block(("ukv", n))
    for w in ("attn_out", "conv_out", "out"):
        for n in range(2):
            for k in range(2):
                p.block((w, n, k))
    p.loop("mlp", [NMLP // 2, NMLP // 2, NMLP - 1], [1, 1, 1])
    return p


def build(nc, A, masks_d, pool_d, out):
    plan = make_plan()
    ctx = ExitStack()
    with ctx:
        def sb(name, shape, dt=F32):
            return ctx.enter_context(nc.sbuf_tensor(name, shape, dt))

        sems = {}

        def S(name):
            name = HOME.get(name, name)
            if name not in sems:
                sems[name] = ctx.enter_context(nc.semaphore(name.replace(".", "_")))
            return sems[name]

        raw = sb("raw", [P, 3, SLOT])
        wh = sb("wh", [P, 3, SLOT], F32R)
        wl = sb("wl", [P, 3, SLOT], F32R)
        h = sb("h", [P, NT, D])
        xh = sb("xh", [P, KT, SEQ], F32R)
        xl = sb("xl", [P, KT, SEQ], F32R)
        gh = sb("gh", [P, 2, SEQ], F32R)
        gl = sb("gl", [P, 2, SEQ], F32R)
        wide = sb("wide", [P, 11 * 2048])
        side = sb("side", [P, D])
        lowr = sb("lowr", [P, 4 * SEQ])
        masks = sb("masks", [P, NMASK])
        cols = sb("cols", [P, NCOL])
        ones = sb("ones", [P, P])
        small = sb("small", [P, 512])
        posi = sb("posi", [P, NT], I32)
        ps = ctx.enter_context(nc.psum_tensor("ps", [P, 8, 512], F32))

        def W(i, off=0, n=2048):
            return wide[:, i * 2048 + off:i * 2048 + off + n]

        def W3(i, a, off=0, n=2048):
            return W(i, off, n).rearrange("p (a b) -> p a b", a=a)

        ident = masks[:, 0:P]

        eps = masks[:, MEPS:MEPS + 1]

        def mask4(name):
            return masks[:, MI[name]:MI[name] + P].unsqueeze(1).to_broadcast([P, 4, P])

        def mask22(name):
            return masks[:, MI[name]:MI[name] + P].unsqueeze(1).unsqueeze(1).to_broadcast([P, 2, 2, P])

        def col(name, i=0):
            return cols[:, ROWS[name] + i:ROWS[name] + i + 1]

        sm_at = [0]

        def sm(n):
            sm_at[0] += n
            assert sm_at[0] <= 512
            return small[:, sm_at[0] - n:sm_at[0]]

        NORMS = ("mix0", "ffn0", "mix1", "ffn1", "fin", "pre", "post1", "pre2", "post2")
        nss = {n: sm(2) for n in NORMS}
        nsd = {n: sm(2) for n in NORMS}
        nrs = {n: sm(2) for n in NORMS}
        vss, vsd, vrs = sm(2), sm(2), sm(2)
        qss, qsd, qrs = sm(4), sm(4), sm(4)
        kss, bon, mean, gvar = sm(32), sm(32), sm(32), sm(32)
        pc = sm(64)
        ccol, unused = sm(8), sm(1)
        modc = sm(32)
        sc1, sc2 = sm(8), sm(8)
        posf = sm(2)
        amax, asum, arec = sm(4), sm(4), sm(4)

        hn = W3(5, NT)
        silu = W3(10, NT, 0, 512)
        hmid = W3(10, NT, 512, 512)

        raw_loaded = [S(f"raw_loaded{i}") for i in range(3)]
        hi_ready = [S(f"hi_ready{i}") for i in range(3)]
        lo_ready = [S(f"lo_ready{i}") for i in range(3)]
        w_used = [S(f"w_used{i}") for i in range(3)]

        def used(eng, name):
            s, use, _, _ = plan.at[name]
            eng.wait_ge(w_used[s], use + 1)

        def kblock(w, n0, n, k):
            return w[k * 512:(k + 1) * 512, n0:n0 + n].rearrange("(a p) n -> p a n", p=P)

        w_in = A["w_in_2"][0]
        LAT0 = 2 * D
        GATE0 = LAT0 + QL + KL + ROPE
        SRC = {"ab_in": A["ab_w_in"][0], "ab_out": A["ab_w_out"][0], "k": A["rwkv_w_k"][0], "r": A["rwkv_w_r"][0],
               "v": A["rwkv_w_v"][0], "o": A["rwkv_w_o"][0], "attn_out": A["w_attn_out_2"][0],
               "conv_out": A["w_conv_out_2"][0], "out": A["w_out_2"][0]}

        def sources(name):
            s, _, _, width = plan.at[name]
            flat = raw[:, s, 0:width]
            what = name[0]
            if what == "glu":
                v = flat.rearrange("p (a n) -> p a n", a=4)
                n0 = name[1] * 256
                return [(kblock(w_in, n0, 256, name[2]), v[:, :, 0:256]),
                        (kblock(w_in, D + n0, 256, name[2]), v[:, :, 256:512])]
            if what == "lat":
                n0, n = (LAT0, QL) if name[1] == 0 else (LAT0 + QL, KL + ROPE)
                return [(kblock(w_in, n0, n, name[2]), flat.rearrange("p (a n) -> p a n", a=4))]
            if what == "gate":
                return [(kblock(w_in, GATE0 + name[1] * 512, 512, name[2]), flat.rearrange("p (a n) -> p a n", a=4))]
            if what == "uq":
                return [(A["w_uq_2"][0][:, name[1] * 384:(name[1] + 1) * 384].rearrange("(a p) n -> p a n", p=P),
                         flat.rearrange("p (a n) -> p a n", a=3))]
            if what == "ukv":
                return [(A["w_ukv_2"][0][:, name[1] * 1024:(name[1] + 1) * 1024].rearrange("(a p) n -> p a n", p=P),
                         flat.rearrange("p (a n) -> p a n", a=2))]
            return [(kblock(SRC[what], name[1] * 512, 512, name[2]), flat.rearrange("p (a n) -> p a n", a=4))]

        block = ctx.enter_context(nc.Block())

        @block.sync
        def _(sp):
            def load_block(name):
                s, use, _, _ = plan.at[name]
                if name == ("o", 0, 0):
                    sp.wait_ge(S("wkv.done"), B("wkv.done") + 8)
                if use:
                    sp.wait_ge(lo_ready[s], use)
                for src, dst in sources(name):
                    sp.dma_start(dst, src).then_inc(raw_loaded[s], 16)

            def load_ffn(l):
                uses, _ = plan.at[f"ffn{l}"]
                gate, up, down = A["ffn_w_gate"][l], A["ffn_w_up"][l], A["ffn_w_down"][l]

                def load_gu(c):
                    n0 = c * FC if isinstance(c, int) else sp.snap(c * FC)
                    for k in range(2):
                        dst = raw[:, k, :].rearrange("p (a n) -> p a n", a=4)
                        sp.wait_ge(lo_ready[k], uses[k] + c)
                        for j, w in enumerate((gate, up)):
                            sp.dma_start(dst[:, :, j * FC:(j + 1) * FC],
                                         w[k * 512:(k + 1) * 512, bass.ds(n0, FC)].rearrange("(a p) n -> p a n", p=P))\
                              .then_inc(raw_loaded[k], 16)

                def load_down(c, s, use):
                    r0 = c * FC if isinstance(c, int) else sp.snap(c * FC)
                    sp.wait_ge(lo_ready[s], uses[s] + use)
                    sp.dma_start(raw[:, s, :].rearrange("p (a n) -> p a n", a=2),
                                 down[bass.ds(r0, FC), :].rearrange("(a p) n -> p a n", p=P))\
                      .then_inc(raw_loaded[s], 16)

                load_gu(0)
                with sp.Fori(0, NFFN - 1) as i:
                    load_gu(i + 1)
                    load_down(i, 2, i)
                load_down(NFFN - 1, 0, NFFN)

            def load_mlp():
                uses, _ = plan.at["mlp"]
                up, down = A["w_mlp_in_2"][0], A["w_mlp_out_2"][0]

                def load_up(s, c, use):
                    n0 = c * FC if isinstance(c, int) else sp.snap(c * FC)
                    sp.wait_ge(lo_ready[s], uses[s] + use)
                    sp.dma_start(raw[:, s, :].rearrange("p (a n) -> p a n", a=KT),
                                 up[:, bass.ds(n0, FC)].rearrange("(a p) n -> p a n", p=P)).then_inc(raw_loaded[s], 16)

                def load_down(c, s, use):
                    r0 = c * FC if isinstance(c, int) else sp.snap(c * FC)
                    sp.wait_ge(lo_ready[s], uses[s] + use)
                    sp.dma_start(raw[:, s, :].rearrange("p (a n) -> p a n", a=2),
                                 down[bass.ds(r0, FC), :].rearrange("(a p) n -> p a n", p=P)).then_inc(raw_loaded[s], 16)

                load_up(0, 0, 0)
                load_up(1, 1, 0)
                with sp.Fori(0, NMLP // 2 - 1) as i:
                    load_up(0, i * 2 + 2, i + 1)
                    load_down(i * 2, 2, i * 2)
                    load_up(1, i * 2 + 3, i + 1)
                    load_down(i * 2 + 1, 2, i * 2 + 1)
                load_down(NMLP - 2, 2, NMLP - 2)
                load_down(NMLP - 1, 0, NMLP // 2)

            sp.dma_start(h[:, :, :], A["x"][0].rearrange("(t p) n -> p t n", p=P)).then_inc(S("x_loaded"), 16)
            sp.dma_start(W(6, 0, P), A["vectors"][0:P, :]).then_inc(S("rows"), 16)
            for name in plan.order:
                if name in ("ffn0", "ffn1"):
                    load_ffn(int(name[3]))
                elif name == "mlp":
                    load_mlp()
                else:
                    load_block(name)
            sp.wait_ge(S("stored"), B("stored") + 32)

        ada_src = A["w_ada_2"][0].rearrange("(p k) n -> p k n", k=KT)
        NADA = 6 * D // 256
        ada_raw = [W3(w, KT) for w in (3, 4, 7, 9)]
        ada_acc = wide[:, 0:6 * D]

        @block.gpsimd
        def _(pool):
            nc.gpsimd.memset(ones[:, :], 1.0).then_inc(S("ones"), 1)
            pool.wait_ge(S("ones"), B("ones") + 1)
            nc.gpsimd.memset(lowr[64:65, 0:2 * SEQ], 1.0).then_inc(S("lowr_one"), 1)
            pool.wait_ge(S("wst"), B("wst") + 1)
            pool.wait_ge(S("lowr_one"), B("lowr_one") + 1)
            nc.gpsimd.memset(W3(4, 4, 512, 512)[64:128, :, 0:64], 0.0).then_inc(S("wst_masked"), 1)
            pool.wait_ge(S("wkv.done"), B("wkv.done") + 8)
            pool.wait_ge(S("wst_masked"), B("wst_masked") + 1)
            nc.gpsimd.memset(W(4, 0, D)[0:64, :], 0.0).then_inc(S("s0_zero"), 1)
            bterm, gate = W3(6, NT), W3(7, NT)
            by_head = bterm.rearrange("p t (h c) -> p (t h) c", c=HD)
            pool.wait_ge(S("wkv.eh"), B("wkv.eh") + 8)
            pool.wait_ge(S("s0_zero"), B("s0_zero") + 1)
            nc.gpsimd.tensor_tensor(by_head, by_head, bon.unsqueeze(2).to_broadcast([P, NT * RH, HD]), ALU.mult).then_inc(S("fold"), 1)
            pool.wait_ge(S("ln_vec"), B("ln_vec") + 32)
            pool.wait_ge(S("fold"), B("fold") + 1)
            nc.gpsimd.tensor_tensor(bterm, bterm, W(9, D, D).unsqueeze(1).to_broadcast([P, NT, D]), ALU.add).then_inc(S("fold"), 1)
            pool.wait_ge(S("fold"), B("fold") + 2)
            for t in range(NT):
                pool.wait_ge(S("gate_out"), B("gate_out") + 2 * (t + 1))
                nc.gpsimd.tensor_tensor(bterm[:, t, :], bterm[:, t, :], gate[:, t, :], ALU.mult).then_inc(S("fold"), 1)
                pool.wait_ge(S("fold"), B("fold") + 2 * t + 3)
                nc.gpsimd.tensor_tensor(gate[:, t, :], gate[:, t, :], W(9, 0, D), ALU.mult).then_inc(S("fold"), 1)
                pool.wait_ge(S("fold"), B("fold") + 2 * t + 4)
            pool.wait_ge(S("rw.xl"), B("rw.xl") + 8)
            pool.wait_ge(S("mix1.add"), B("mix1.add") + 4)
            nc.gpsimd.memset(ada_acc, 0.0).then_inc(S("acc_zero"), 1)
            pool.wait_ge(S("acc_zero"), B("acc_zero") + 1)
            pool.dma_start(ada_acc[0:1, :], A["b_ada_2"]).then_inc(S("acc_bias"), 16)
            for j in range(NADA // 2):
                if j >= 2:
                    pool.wait_ge(S("ada_step"), B("ada_step") + 16 * (j - 1))
                for b in range(2):
                    pool.dma_start(ada_raw[2 * (j % 2) + b], ada_src[:, :, (2 * j + b) * 256:(2 * j + b + 1) * 256])\
                        .then_inc(S(f"ada{2 * (j % 2) + b}"), 16)

        @block.tensor
        def _(pe):
            def mm3(o, lh, ll, rh, rl, start, stop):
                pe.matmul(o, lh, rh, start=start, stop=False)
                pe.matmul(o, ll, rh, start=False, stop=False)
                return pe.matmul(o, lh, rl, start=False, stop=stop)

            def tok(t):
                return slice(t * P, (t + 1) * P)

            def arrive(name):
                s, use, _, _ = plan.at[name]
                pe.wait_ge(lo_ready[s], use + 1)
                return s

            def half(s, kts, outs, n, start, stop):
                for t in range(NT):
                    for j, kt in enumerate(kts):
                        m = mm3(outs[t], xh[:, kt, tok(t)], xl[:, kt, tok(t)],
                                wh[:, s, j * n:(j + 1) * n], wl[:, s, j * n:(j + 1) * n],
                                start and j == 0, stop and j == len(kts) - 1)
                return m

            def linear(what, xname, n_chunks, xcount=0, n=512, free=None, after=None, by_tile=False):
                for c in range(n_chunks):
                    if free:
                        free(c)
                    o = [ps[:, 2 * t + c if by_tile else 2 * (c % 2) + t, 0:n] for t in range(NT)]
                    for k in range(2):
                        s = arrive((what, c, k))
                        if c == 0:
                            pe.wait_ge(S(xname), B(xname) + xcount + 4 * (k + 1))
                        half(s, range(4 * k, 4 * k + 4), o, n, k == 0, k == 1).then_inc(w_used[s], 1)
                        if after and (c, k) in after:
                            after[c, k]()

            def norm_transposes(name):
                for t in range(NT):
                    pe.wait_ge(S(name + ".hn"), B(name + ".hn") + t + 1)
                    for kt in range(KT):
                        m = pe.transpose(ps[:, 4 + kt // 2, (kt % 2) * SEQ + t * P:(kt % 2) * SEQ + (t + 1) * P],
                                         hn[:, t, kt * P:(kt + 1) * P], ident)
                        if t == NT - 1 and kt % 2:
                            m.then_inc(S(name + ".T"), 1)

            def ffn_loop(l):
                f = f"ffn{l}"
                uses, _ = plan.at[f]

                def gu_half(k, c, b):
                    pe.wait_ge(lo_ready[k], uses[k] + c + 1)
                    pe.wait_ge(lo_ready[k], uses[k] + 1)
                    m = half(k, range(4 * k, 4 * k + 4), [ps[:, b, :], ps[:, b + 1, :]], 512, k == 0, k == 1)
                    m.then_inc(w_used[k], 1)

                def body(i, first, last):
                    if not last:
                        if not first:
                            pe.wait_ge(S(f + ".h"), B(f + ".h") + i + 1)
                        gu_half(0, i + 1, 4)
                    pe.wait_ge(S(f + ".h"), B(f + ".h") + i + 1)
                    pe.wait_ge(S(f + ".h"), B(f + ".h") + 1)
                    for t in range(NT):
                        for j in range(2):
                            m = pe.transpose(ps[:, 6, j * SEQ + t * P:j * SEQ + (t + 1) * P],
                                             hmid[:, t, j * P:(j + 1) * P], ident)
                    m.then_inc(S(f + ".mT"), 1)
                    if not last:
                        gu_half(1, i + 1, 4)
                    pe.wait_ge(S(f + ".gl"), B(f + ".gl") + i + 1)
                    s, use = (0, NFFN) if last else (2, i)
                    pe.wait_ge(lo_ready[s], uses[s] + use + 1)
                    pe.wait_ge(lo_ready[s], uses[s] + 1)
                    for j in range(2):
                        for t in range(NT):
                            for n in range(2):
                                w = slice(j * D + n * 512, j * D + (n + 1) * 512)
                                m = mm3(ps[:, 2 * t + n, :], gh[:, j, tok(t)], gl[:, j, tok(t)], wh[:, s, w], wl[:, s, w],
                                        first and j == 0, last and j == 1)
                    m.then_inc(w_used[s], 1)

                for k in range(2):
                    pe.wait_ge(S(f + ".xl"), B(f + ".xl") + 4 * (k + 1))
                    gu_half(k, 0, 0)
                body(0, True, False)
                with pe.Fori(1, NFFN - 1) as i:
                    body(i, False, False)
                body(NFFN - 1, False, True)

            def mlp_loop():
                uses, _ = plan.at["mlp"]

                def up(s, use, t):
                    if t == 0:
                        pe.wait_ge(lo_ready[s], uses[s] + use + 1)
                        pe.wait_ge(lo_ready[s], uses[s] + 1)
                    for kt in range(KT):
                        m = mm3(ps[:, 4 + s, t * FC:(t + 1) * FC], xh[:, kt, tok(t)], xl[:, kt, tok(t)],
                                wh[:, s, kt * FC:(kt + 1) * FC], wl[:, s, kt * FC:(kt + 1) * FC],
                                kt == 0, kt == KT - 1)
                    if t == NT - 1:
                        m.then_inc(w_used[s], 1)

                def body(c, s_next, use_next, first, last):
                    if not last:
                        if not first:
                            pe.wait_ge(S("mlp.act"), B("mlp.act") + c)
                        up(s_next, use_next, 0)
                    pe.wait_ge(S("mlp.h"), B("mlp.h") + c + 1)
                    pe.wait_ge(S("mlp.h"), B("mlp.h") + 1)
                    for t in range(NT):
                        for j in range(2):
                            m = pe.transpose(ps[:, 6, j * SEQ + t * P:j * SEQ + (t + 1) * P],
                                             hmid[:, t, j * P:(j + 1) * P], ident)
                    m.then_inc(S("mlp.mT"), 1)
                    if not last:
                        up(s_next, use_next, 1)
                    pe.wait_ge(S("mlp.gl"), B("mlp.gl") + c + 1)
                    s, use = (0, NMLP // 2) if last else (2, c)
                    pe.wait_ge(lo_ready[s], uses[s] + use + 1)
                    pe.wait_ge(lo_ready[s], uses[s] + 1)
                    for j in range(2):
                        for t in range(NT):
                            for n in range(2):
                                w = slice(j * D + n * 512, j * D + (n + 1) * 512)
                                m = mm3(ps[:, 2 * t + n, :], gh[:, j, tok(t)], gl[:, j, tok(t)], wh[:, s, w], wl[:, s, w],
                                        first and j == 0, last and j == 1)
                    m.then_inc(w_used[s], 1)

                pe.wait_ge(S("pre2.xl"), B("pre2.xl") + 8)
                up(0, 0, 0)
                up(0, 0, 1)
                body(0, 1, 0, True, False)
                with pe.Fori(0, NMLP // 2 - 1) as i:
                    body(i * 2 + 1, 0, i + 1, False, False)
                    body(i * 2 + 2, 1, i + 1, False, False)
                body(NMLP - 1, 0, 0, False, True)

            def turn(dst, src, nk=P):
                return pe.transpose(dst, src, masks[0:nk, 0:nk])

            pe.wait_ge(S("masks"), B("masks") + 16)
            pe.wait_ge(S("rows"), B("rows") + 16 * 3)
            turn(ps[:, 0, 0:P], W(6, 0, P))
            turn(ps[:, 0, P:P + 5], W(6, P, P)[0:5, :], 5)
            for kt in range(KT):
                m = turn(ps[:, 1, kt * CK:(kt + 1) * CK], W(6, 256 + kt * P, P)[0:CK, :], CK)
            m.then_inc(S("cols_T"), 1)
            pe.wait_ge(S("sgu_w"), B("sgu_w") + 16)
            for i in range(4):
                m = turn(ps[:, 2, i * P:(i + 1) * P], W(4, i * P, P))
            m.then_inc(S("wst_T"), 1)

            norm_transposes("mix0")

            def ab_free(c):
                if c == 0:
                    pe.wait_ge(S("wst"), B("wst") + 1)
                if c == 2:
                    pe.wait_ge(S("u_ready"), B("u_ready") + 2)
            linear("ab_in", "mix0.xl", 3, free=ab_free)
            pe.wait_ge(S("wst_masked"), B("wst_masked") + 1)
            pe.wait_ge(S("v_normed"), B("v_normed") + 2)
            wst = W3(4, 4, 512, 512)
            za = W3(0, NT)
            zb = W3(1, NT, 0, 1024)
            for t in range(NT):
                for i in range(4):
                    m = pe.matmul(ps[:, 4 + t, i * P:(i + 1) * P], wst[:, i, :], za[:, t, AW + i * P:AW + (i + 1) * P],
                                  start=True, stop=True)
                m.then_inc(S("spatial"), 1)
            pe.wait_ge(S("zb_ready"), B("zb_ready") + 2)
            pmat = W(3, 0, 12 * P).rearrange("p (a g n) -> p a g n", a=3, g=4)
            for g in range(4):
                o = ps[:, 6 + g // 2, (g % 2) * SEQ:(g % 2) * SEQ + SEQ]
                zg = [zb[:, t, g * P:(g + 1) * P] for t in range(NT)]
                pe.matmul(o[:, 0:P], zg[0], pmat[:, 0, g, :], start=True, stop=True)
                pe.matmul(o[:, P:SEQ], zg[1], pmat[:, 1, g, :], start=True, stop=False)
                m = pe.matmul(o[:, P:SEQ], zg[0], pmat[:, 2, g, :], start=False, stop=True)
                if g % 2:
                    m.then_inc(S("pooled_T"), 1)
            pe.wait_ge(S("ya"), B("ya") + 8)
            pe.wait_ge(S("pooled"), B("pooled") + 2)
            poolw = W3(4, 4, 1024, 512)
            pooled = W3(2, 4, 0, 1024)
            for g in range(4):
                m = pe.matmul(ps[:, 4 + g // 2, (g % 2) * SEQ:(g % 2) * SEQ + SEQ], poolw[:, g, :], pooled[:, g, :],
                              start=True, stop=True)
                if g % 2:
                    m.then_inc(S("yb_T"), 1)
            ya = W3(2, NT, 1024, 1024)
            for kt in range(4):
                for t in range(NT):
                    m = turn(ps[:, 6 + kt // 2, (kt % 2) * SEQ + t * P:(kt % 2) * SEQ + (t + 1) * P],
                             ya[:, t, kt * P:(kt + 1) * P])
                if kt % 2:
                    m.then_inc(S("ya_T"), 1)
            linear("ab_out", "ab.xl", 2, free=lambda c: pe.wait_ge(S("ab.xl"), B("ab.xl") + 8))
            norm_transposes("ffn0")
            ffn_loop(0)

            norm_transposes("mix1")
            w1 = W3(10, KT, 0, 512)
            a1 = W3(10, KT, 512, 512)
            g1 = W3(6, KT, 0, KT * GRANK)
            mix = {"w": W3(2, KT), "a": W3(3, KT), "g": W3(2, KT)}
            pe.wait_ge(S("rw_w1"), B("rw_w1") + 48)
            pe.wait_ge(S("mix1.hT"), B("mix1.hT") + 8)
            for n, (what, w) in enumerate((("w", w1), ("a", a1))):
                pe.wait_ge(S("mixed"), B("mixed") + n + 1)
                for kt in range(KT):
                    m = pe.matmul(ps[0:RANK, 4 + n, 0:SEQ], w[:, kt, :], mix[what][:, kt, :], start=kt == 0, stop=kt == KT - 1)
                m.then_inc(S("rank_T"), 1)
            pe.wait_ge(S("mixed"), B("mixed") + 3)
            for part, (r0, r1) in enumerate(((0, P), (P, GRANK))):
                for kt in range(KT):
                    m = pe.matmul(ps[0:r1 - r0, 6 + part, 0:SEQ], g1[:, kt, r0:r1], mix["g"][:, kt, :],
                                  start=kt == 0, stop=kt == KT - 1)
            m.then_inc(S("rank_T"), 1)
            pe.wait_ge(S("rw_w2"), B("rw_w2") + 64)
            for n in range(2):
                pe.wait_ge(S("rank"), B("rank") + n + 1)
                pe.wait_ge(S("lowr_one"), B("lowr_one") + 1)
                w2 = W(4, n * D, D)
                for t in range(NT):
                    for c in range(2):
                        if n == 1:
                            pe.wait_ge(S("sig"), B("sig") + 2 * t + c + 1)
                        m = pe.matmul(ps[:, 2 * t + c, :], lowr[0:RANK + 1, n * SEQ + t * P:n * SEQ + (t + 1) * P],
                                      w2[0:RANK + 1, c * 512:(c + 1) * 512], start=True, stop=True)
                        m.then_inc(S("logit"), 1)
            pe.wait_ge(S("rank"), B("rank") + 3)
            sig = W3(7, NT)
            incl = masks[:, MI["incl_st"]:MI["incl_st"] + P]
            for t in range(NT):
                for c in range(2):
                    m = pe.matmul(ps[:, 4 + 2 * t + c, :], incl, sig[:, t, c * 512:(c + 1) * 512], start=True, stop=True)
            m.then_inc(S("cum"), 1)
            def chunk_decay():
                pe.wait_ge(S("exps"), B("exps") + 1)
                for t in range(NT):
                    for hp in range(RH // 2):
                        o = hp * 4 + 2 * t
                        m = pe.matmul(ps[:, 4, o:o + 2], sig[:, t, hp * P:(hp + 1) * P], masks[:, MCH:MCH + 2], start=True, stop=True)
                m.then_inc(S("pc_T"), 1)

            for n, what in enumerate("krv"):
                def rkv_free(c, n=n):
                    if n == 0:
                        if c == 0:
                            pe.wait_ge(S("rate"), B("rate") + 4)
                    else:
                        pe.wait_ge(S("rkv"), B("rkv") + 4 * (n - 1) + 2 * c + 2)
                linear(what, "rkv.xl", 2, xcount=8 * n, free=rkv_free, after={(1, 0): chunk_decay} if n == 2 else None)

            rr, aa, vv = [W(w) for w in (0, 10, 6)]
            tmps = WKV_TMP(W, raw)
            pe.wait_ge(S("scaled"), B("scaled") + 16)
            pe.wait_ge(S("pc"), B("pc") + 2)
            pe.wait_ge(S("rkv"), B("rkv") + 12)

            def bank(g, i):
                return ps[:, 4 * (g % 2) + i, :]

            def T(g, name, n, w=P):
                return tmps[g % 2][name][:, n * w:(n + 1) * w]

            def mul(g, b, l, r, sem):
                for n in range(4):
                    m = pe.matmul(bank(g, b)[:, n * P:(n + 1) * P], T(g, l, n), T(g, r, n), start=True, stop=True)
                m.then_inc(S("wkv." + sem), 1)

            def flip(g):
                if g >= 2:
                    pe.wait_ge(S("wkv.done"), B("wkv.done") + g - 1)
                    pe.wait_ge(S("wkv.hc"), B("wkv.hc") + g - 1)
                for q in range(2):
                    h = HEAD0(g) + 2 * q
                    turn(bank(g, 0)[:, q * SEQ:q * SEQ + P], aa[:, HEAD(g, h)[0]:HEAD(g, h)[0] + P])
                    turn(bank(g, 0)[:, q * SEQ + P:(q + 1) * SEQ], rr[:, HEAD(g, h)[0]:HEAD(g, h)[0] + P])
                    for x in range(2):
                        m = turn(bank(g, 1)[:, x * SEQ + q * P:x * SEQ + (q + 1) * P], BK(wide, g, h, x, P))
                m.then_inc(S("wkv.T"), 1)

            def gram(g):
                pe.wait_ge(S("wkv.ar"), B("wkv.ar") + g + 1)
                pe.wait_ge(S("wkv.bk"), B("wkv.bk") + g + 1)
                for x in range(2):
                    for n in range(4):
                        e, q = n // 2, n % 2
                        rows = slice(64 * e, 64 * e + 64)
                        m = pe.matmul(bank(g, 2 * x + e)[:, q * SEQ:(q + 1) * SEQ],
                                      tmps[g % 2]["bk"][rows, x * SEQ + q * P:x * SEQ + (q + 1) * P],
                                      tmps[g % 2]["ar"][rows, q * SEQ:(q + 1) * SEQ], start=True, stop=True)
                    m.then_inc(S("wkv.gram"), 1)

            def gram_ts(g):
                pe.wait_ge(S("wkv.gb"), B("wkv.gb") + g + 1)
                for n in range(4):
                    e, q = n // 2, n % 2
                    rows = slice(64 * e, 64 * e + 64)
                    m = pe.matmul(bank(g, e)[:, q * P:(q + 1) * P], tmps[g % 2]["ar"][rows, q * SEQ:q * SEQ + P],
                                  tmps[g % 2]["bk"][rows, q * P:(q + 1) * P], start=True, stop=True)
                m.then_inc(S("wkv.gram_ts"), 1)

            def power2(g):
                pe.wait_ge(S("wkv.gk"), B("wkv.gk") + g + 1)
                pe.wait_ge(S("wkv.x"), B("wkv.x") + g + 1)
                mul(g, 2, "xt", "x", "x2")
                mul(g, 3, "x", "xt", "x2t")

            def gram_v(g):
                pe.wait_ge(S("wkv.t1"), B("wkv.t1") + g + 1)
                for n in range(4):
                    v0 = HEAD(g, HEAD0(g) + HN(n))[0]
                    m = pe.matmul(bank(g, 0)[:, n * 64:(n + 1) * 64], T(g, "gk", n), vv[:, v0:v0 + 64], start=True, stop=True)
                m.then_inc(S("wkv.gkv"), 1)

            def power4(g):
                pe.wait_ge(S("wkv.x2c"), B("wkv.x2c") + 2 * (g + 1))
                mul(g, 1, "x2", "tt", "t2")
                mul(g, 2, "x2t", "x2", "x4")
                mul(g, 3, "x2", "x2t", "x4t")

            def power8(g):
                pe.wait_ge(S("wkv.x4c"), B("wkv.x4c") + 2 * (g + 1))
                pe.wait_ge(S("wkv.t2c"), B("wkv.t2c") + g + 1)
                pe.wait_ge(S("wkv.gkvc"), B("wkv.gkvc") + g + 1)
                mul(g, 0, "x4t", "x4", "x8")
                mul(g, 1, "x4", "tt", "t4")

            def inverse(g):
                pe.wait_ge(S("wkv.x8c"), B("wkv.x8c") + g + 1)
                pe.wait_ge(S("wkv.t4c"), B("wkv.t4c") + g + 1)
                mul(g, 1, "x8", "tt", "t8")

            def applied(g):
                pe.wait_ge(S("wkv.t8c"), B("wkv.t8c") + g + 1)
                for n in range(4):
                    a0 = HEAD(g, HEAD0(g) + HN(n))[0]
                    pe.matmul(bank(g, 2)[:, n * P:n * P + 64], T(g, "tt", n), T(g, "gkv", n, 64), start=True, stop=True)
                    m = pe.matmul(bank(g, 2)[:, n * P + 64:(n + 1) * P], T(g, "tt", n), aa[:, a0:a0 + 64], start=True, stop=True)
                m.then_inc(S("wkv.r1"), 1)
                mul(g, 3, "off", "tt", "mt")

            def off_1(g):
                pe.wait_ge(S("wkv.r1c"), B("wkv.r1c") + g + 1)
                pe.wait_ge(S("wkv.mtc"), B("wkv.mtc") + g + 1)
                mul(g, 1, "mt", "r1", "r2")

            def off_2(g):
                pe.wait_ge(S("wkv.r2c"), B("wkv.r2c") + g + 1)
                mul(g, 0, "mt", "r2", "r3")

            def off_3(g):
                pe.wait_ge(S("wkv.r3c"), B("wkv.r3c") + g + 1)
                mul(g, 1, "mt", "r2", "r4")

            def state_parts(g):
                pe.wait_ge(S("wkv.r4c"), B("wkv.r4c") + g + 1)
                for p in range(2):
                    c = 2 * (g // 4) + p
                    rows = slice(64 * p, 64 * p + 64)
                    for n in range(4):
                        h, o = HEAD0(g) + HN(n), HN(n) * 64
                        v0 = HEAD(g, h)[0]
                        u_, w_ = T(g, "r2", n)[rows, 0:64], T(g, "r2", n)[rows, 64:P]
                        b_, k_ = [BK(wide, g, h, x, 64)[rows, :] for x in range(2)]
                        if 0 < c < 3:
                            pe.matmul(bank(g, 2 + p)[0:64, SEQ + o:SEQ + o + 64], w_, b_, start=True, stop=True)
                        if c < 3:
                            pe.matmul(bank(g, 2 + p)[0:64, o:o + 64], b_, u_, start=True, stop=False)
                            m = pe.matmul(bank(g, 2 + p)[0:64, o:o + 64], k_, vv[rows, v0:v0 + 64], start=False, stop=True)
                m.then_inc(S("wkv.fg"), 1)

            def out_parts(g):
                for n in range(4):
                    v0, o = HEAD(g, HEAD0(g) + HN(n))[0], HN(n)
                    pe.matmul(bank(g, 0)[0:64, o * P:(o + 1) * P], T(g, "r2", n)[:, 64:P], T(g, "mrb", n), start=True, stop=False)
                    pe.matmul(bank(g, 0)[0:64, o * P:(o + 1) * P], rr[:, v0:v0 + 64], ident, start=False, stop=True)
                    pe.matmul(bank(g, 1)[:, o * 64:(o + 1) * 64], T(g, "mrb", n), T(g, "r2", n)[:, 0:64], start=True, stop=False)
                    m = pe.matmul(bank(g, 1)[:, o * 64:(o + 1) * 64], T(g, "mrk", n), vv[:, v0:v0 + 64], start=False, stop=True)
                m.then_inc(S("wkv.eh"), 1)

            for pair in range(4):
                for step in (flip, gram, gram_ts, power2, gram_v, power4, power8, inverse, applied, off_1, off_2, off_3,
                             state_parts, out_parts):
                    step(2 * pair)
                    step(2 * pair + 1)

            states = W3(4, NT).rearrange("p t (h c) -> p t h c", h=RH)
            ft = W3(8, 2).rearrange("p a (h c) -> p a h c", h=RH)
            chain = W(5, 0, D).rearrange("p (h c) -> p h c", h=RH)
            g2a, g2b = W(10, 0, D), W(10, D, D)

            def next_state(c):
                pe.wait_ge(S("state"), B("state") + c)
                for i in range(RH):
                    m = pe.matmul(ps[0:64, i // 8, (i % 8) * 64:(i % 8 + 1) * 64], ft[0:64, c - 1, i, :], chain[0:64, i, :],
                                  start=True, stop=True)
                m.then_inc(S("state_F"), 1)

            def gate_product(t, c0=0, c1=2):
                for c in range(c0, c1):
                    o = ps[:, GATE_BANK[t] + c, :]
                    pe.matmul(o, lowr[:, 2 * SEQ + t * P:2 * SEQ + (t + 1) * P], g2a[:, c * 512:(c + 1) * 512], start=True, stop=False)
                    m = pe.matmul(o, lowr[0:GRANK - P, 3 * SEQ + t * P:3 * SEQ + (t + 1) * P], g2b[0:GRANK - P, c * 512:(c + 1) * 512],
                                  start=False, stop=True)
                    m.then_inc(S("gate_T"), 1)

            def from_states(t):
                for i in range(RH):
                    e2 = wide[:, 2048 + (t * RH + i) * P:2048 + (t * RH + i + 1) * P]
                    m = pe.matmul(ps[:, Y_BANK[t] + i // 8, (i % 8) * 64:(i % 8 + 1) * 64], e2, states[:, t, i, :],
                                  start=True, stop=True)
                m.then_inc(S("y_T"), 1)

            pe.wait_ge(S("wkv.done"), B("wkv.done") + 8)
            pe.wait_ge(S("wkv.hc"), B("wkv.hc") + 8)
            pe.wait_ge(S("g2"), B("g2") + 32)
            gate_product(0, 0, 1)
            next_state(1)
            gate_product(0, 1, 2)
            next_state(2)
            pe.wait_ge(S("s0_zero"), B("s0_zero") + 1)
            pe.wait_ge(S("state_put"), B("state_put") + 1)
            from_states(0)
            pe.wait_ge(S("state_put"), B("state_put") + 3)
            from_states(1)
            gate_product(1)
            y = W3(0, NT)
            pe.wait_ge(S("gate_out"), B("gate_out") + 4)
            for t in range(NT):
                pe.wait_ge(S("y_gated"), B("y_gated") + t + 1)
                for kt in range(KT):
                    m = turn(ps[:, RW_BANKS[kt // 2], (kt % 2) * SEQ + t * P:(kt % 2) * SEQ + (t + 1) * P], y[:, t, kt * P:(kt + 1) * P])
                    if t == NT - 1 and kt % 2:
                        m.then_inc(S("rw.T"), 1)

            def o_free(c):
                if c == 1:
                    pe.wait_ge(S("rw.xl"), B("rw.xl") + 8)
            linear("o", "rw.xl", 2, free=o_free)
            norm_transposes("ffn1")
            ffn_loop(1)

            def modulation_columns(b, parts):
                for n, m_ in enumerate(parts):
                    for kt in range(KT):
                        m = pe.matmul(ps[:, b, n * KT + kt:n * KT + kt + 1], ada_acc[:, m_ * D + kt * P:m_ * D + (kt + 1) * P],
                                      ones[:, 0:1], start=True, stop=True)
                m.then_inc(S("mod_T"), 1)

            def gate_rows():
                for n, m_ in enumerate((2, 5)):
                    for c in range(2):
                        m = pe.matmul(ps[:, 4 + 2 * n + c, :], ones[:, :], ada_acc[:, m_ * D + c * 512:m_ * D + (c + 1) * 512],
                                      start=True, stop=True)
                m.then_inc(S("gates_T"), 1)

            pe.wait_ge(S("ones"), B("ones") + 1)
            pe.wait_ge(S("ada_step"), B("ada_step") + 8 * NADA)
            pe.wait_ge(S("ffn1.add"), B("ffn1.add") + 4)
            modulation_columns(0, (0, 1))
            norm_transposes("pre")
            modulation_columns(2, (3, 4))

            def glu_free(c):
                if c < 2:
                    pe.wait_ge(S("modc"), B("modc") + c + 1)
                else:
                    pe.wait_ge(S("glu"), B("glu") + 2 * (c - 1))
            linear("glu", "pre.xl", 4, free=glu_free, after={(0, 1): gate_rows})
            pe.wait_ge(S("gates"), B("gates") + 4)
            for n, nw in ((0, QL), (1, KL + ROPE)):
                pe.wait_ge(S("glu"), B("glu") + 2 * (n + 3))
                o = [ps[:, 2 * (n % 2) + t, 0:nw] for t in range(NT)]
                for k in range(2):
                    s = arrive(("lat", n, k))
                    half(s, range(4 * k, 4 * k + 4), o, nw, k == 0, k == 1).then_inc(w_used[s], 1)
            for c in range(4):
                pe.wait_ge(S("glu"), B("glu") + 2 * (c + 1))
                for j in range(2):
                    for t in range(NT):
                        m = turn(ps[:, 4 + c, j * SEQ + t * P:j * SEQ + (t + 1) * P],
                                 W(U_AT[c][0], U_AT[c][1] + t * 256 + j * P, P))
                m.then_inc(S("u_T"), 1)

            lat = W(3, 0, 2 * 704).rearrange("p (t n) -> p t n", t=NT)

            def turn_latents():
                pe.wait_ge(S("lat_n"), B("lat_n") + 4)
                pe.wait_ge(S("u_put"), B("u_put") + 4)
                for kt in range(5):
                    for t in range(NT):
                        m = turn(ps[:, 4 + kt // 2, (kt % 2) * SEQ + t * P:(kt % 2) * SEQ + (t + 1) * P],
                                 lat[:, t, kt * P:(kt + 1) * P])
                    if kt % 2 or kt == 4:
                        m.then_inc(S("lq.T"), 1)

            def gate_free(c):
                if c == 3:
                    turn_latents()
                if c < 2:
                    pe.wait_ge(S("lat"), B("lat") + 2 * (c + 1))
                else:
                    pe.wait_ge(S("gatev"), B("gatev") + 2 * (c - 1))
            linear("gate", "pre.xl", 4, free=gate_free)
            pe.wait_ge(S("gatev"), B("gatev") + 8)
            pe.wait_ge(S("lq.xl"), B("lq.xl") + 5)
            for j in range(4):
                s = arrive(("uq", j))
                w4 = [x[:, s, 0:3 * 384].rearrange("p (k i c) -> p k i c", k=3, i=2) for x in (wh, wl)]
                if j >= 2:
                    pe.wait_ge(S("qn"), B("qn") + j - 1)
                for i in range(2):
                    for kt in range(3):
                        mm3(ps[:, j % 2, i * SEQ:(i + 1) * SEQ], w4[0][:, kt, i, 0:NOPE], w4[1][:, kt, i, 0:NOPE],
                            xh[:, kt, :], xl[:, kt, :], kt == 0, kt == 2)
                for t in range(NT):
                    for kt in range(3):
                        m = mm3(ps[:, 2 + t, j * P:(j + 1) * P], xh[:, kt, tok(t)], xl[:, kt, tok(t)],
                                w4[0][:, kt, :, NOPE:NOPE + ROPE], w4[1][:, kt, :, NOPE:NOPE + ROPE], kt == 0, kt == 2)
                m.then_inc(w_used[s], 1)
            for j in range(2):
                s = arrive(("ukv", j))
                w4 = [x[:, s, :].rearrange("p (k i c) -> p k i c", k=2, i=4) for x in (wh, wl)]
                bk = UKV_BANK[j]
                if j:
                    pe.wait_ge(S("qn"), B("qn") + 4)
                    pe.wait_ge(S("qraw"), B("qraw") + 2)
                for i in range(4):
                    for kt in range(2):
                        mm3(ps[:, bk + i // 2, (i % 2) * SEQ:(i % 2 + 1) * SEQ], w4[0][:, kt, i, 0:NOPE], w4[1][:, kt, i, 0:NOPE],
                            xh[:, 3 + kt, :], xl[:, 3 + kt, :], kt == 0, kt == 1)
                for t in range(NT):
                    for kt in range(2):
                        m = mm3(ps[:, bk + 2 + t, :], xh[:, 3 + kt, tok(t)], xl[:, 3 + kt, tok(t)],
                                w4[0][:, kt, :, NOPE:NOPE + VD], w4[1][:, kt, :, NOPE:NOPE + VD], kt == 0, kt == 1)
                m.then_inc(w_used[s], 1)
            ro = W(3, 0, 1280).rearrange("p (t n) -> p t n", t=NT)
            pe.wait_ge(S("roped"), B("roped") + 2)
            pe.wait_ge(S("kn"), B("kn") + 2)
            pe.wait_ge(S("vt"), B("vt") + 2)
            for kt in range(5):
                b = 4 + kt // 2
                for t in range(NT):
                    m = turn(ps[:, b, (kt % 2) * SEQ + t * P:(kt % 2) * SEQ + (t + 1) * P], ro[:, t, kt * P:(kt + 1) * P])
                if kt in (1, 3, 4):
                    m.then_inc(S("ro_T"), 1)
            qn = W3(4, NH)
            kn = W3(9, NH)
            qr = W(1, 256, 5 * SEQ).rearrange("p (a n) -> p a n", a=5)
            vt = W3(5, NT)
            pT = [W(8, 1152 + b * 384, 384) for b in range(2)]
            pp = [W3(10, NT, 512 * b, 512) for b in range(2)]
            pe.wait_ge(S("ro_put"), B("ro_put") + 3)
            pe.wait_ge(S("kn"), B("kn") + 4)
            pe.wait_ge(S("vt"), B("vt") + 4)

            def scores(i):
                if i >= 2:
                    pe.wait_ge(S("at.sc"), B("at.sc") + 2 * (i - 1))
                rows = slice(64 * (i % 2), 64 * (i % 2) + 64)
                for t in range(NT):
                    nk = P * (t + 1)
                    o = ps[:, i % 2, t * SEQ:t * SEQ + nk]
                    pe.matmul(o, qn[:, i, tok(t)], kn[:, i, 0:nk], start=True, stop=False)
                    m = pe.matmul(o, qr[rows, i // 2, tok(t)], qr[rows, 4, 0:nk], start=False, stop=True)
                m.then_inc(S("at.s"), 1)

            diags = DIAGS(W, lowr)
            upad = U_PAD(wide)

            def conv_taps(i):
                batch = PE_TAPS[i * TAP_BATCH:(i + 1) * TAP_BATCH]
                pe.wait_ge(S("diag"), B("diag") + i * TAP_BATCH + len(batch))
                for d, (kt, k) in zip(diags[i % 2], batch):
                    m = pe.matmul(CONV_OUT(ps, kt), d, upad[:, kt, k:k + SEQ], start=k == 0, stop=k == CK - 1)
                m.then_inc(S("conv_mm"), 1)

            def weigh(i):
                pe.wait_ge(S("at.p"), B("at.p") + 2 * (i + 1))
                if i >= 2:
                    pe.wait_ge(S("at.pT"), B("at.pT") + i - 1)
                b = i % 2
                turn(ps[:, 2 + b, 0:P], pp[b][:, 0, 0:P])
                turn(ps[:, 2 + b, P:2 * P], pp[b][:, 1, 0:P])
                turn(ps[:, 2 + b, 2 * P:3 * P], pp[b][:, 1, P:SEQ]).then_inc(S("at.T"), 1)
                conv_taps(i)
                pe.wait_ge(S("at.pT"), B("at.pT") + i + 1)
                if i >= 2:
                    pe.wait_ge(S("at.xl"), B("at.xl") + i - 1)
                hc = slice(i * VD, (i + 1) * VD)
                pe.matmul(ps[:, 4 + b, 0:P], vt[:, 0, hc], pT[b][:, 0:P], start=True, stop=True)
                pe.matmul(ps[:, 4 + b, P:SEQ], vt[:, 0, hc], pT[b][:, P:2 * P], start=True, stop=False)
                pe.matmul(ps[:, 4 + b, P:SEQ], vt[:, 1, hc], pT[b][:, 2 * P:3 * P], start=False, stop=True).then_inc(S("at.o"), 1)

            scores(0)
            for i in range(NH):
                if i + 1 < NH:
                    scores(i + 1)
                weigh(i)

            def ao_free(c):
                if c == 0:
                    pe.wait_ge(S("at.pT"), B("at.pT") + NH)
                    pe.wait_ge(S("at.sc"), B("at.sc") + 2 * NH)
            cv, sq = W3(2, KT), W3(5, KT)

            def conv_mean():
                pe.wait_ge(S("at.xl"), B("at.xl") + NH)
                n_dve = KT - CONV_PE
                order = [(0, 2 * CK), (1, 2 * CK)] + [(kt, n_dve * CK) for kt in range(2, n_dve)] + [(kt, 0) for kt in range(n_dve, KT)]
                for n, (kt, steps) in enumerate(order):
                    if steps:
                        pe.wait_ge(S("conv_step"), B("conv_step") + steps)
                    else:
                        pe.wait_ge(S("conv_pe"), B("conv_pe") + kt - n_dve + 1)
                    m = pe.matmul(ps[:, 4, 0:SEQ], ones[:, :], cv[:, kt, :], start=n == 0, stop=n == KT - 1)
                m.then_inc(S("cmean"), 1)

            def conv_var():
                for kt in range(KT):
                    if kt % 4 == 0:
                        pe.wait_ge(S("csq"), B("csq") + kt // 4 + 1)
                    m = pe.matmul(ps[:, 5, 0:SEQ], ones[:, :], sq[:, kt, :], start=kt == 0, stop=kt == KT - 1)
                m.then_inc(S("cvar"), 1)

            linear("attn_out", "at.xl", 2, free=ao_free, after={(0, 0): conv_mean, (0, 1): conv_var})
            linear("conv_out", "cv.xl", 2, free=lambda c: pe.wait_ge(S("yb"), B("yb") + 2 * (c + 1)))
            ym = W3(9, NT)
            for kp in range(4):
                pe.wait_ge(S("ymix"), B("ymix") + 2 * (kp // 2 + 1))
                for j in range(2):
                    for t in range(NT):
                        kt = 2 * kp + j
                        m = turn(ps[:, 4 + kp, j * SEQ + t * P:j * SEQ + (t + 1) * P], ym[:, t, kt * P:(kt + 1) * P])
                m.then_inc(S("ym.T"), 1)
            linear("out", "ym.xl", 2, by_tile=True)
            norm_transposes("pre2")
            mlp_loop()

        @block.scalar
        def _(act):
            n_chain = [0]

            def link(ins):
                ins.then_inc(S("act_chain"), 1)
                n_chain[0] += 1
                act.wait_ge(S("act_chain"), B("act_chain") + n_chain[0])

            def split_hi(s, use, loaded, width=SLOT):
                act.wait_ge(raw_loaded[s], loaded)
                if not isinstance(use, int) or use > 0:
                    act.wait_ge(w_used[s], use)
                if not isinstance(use, int):
                    act.wait_ge(raw_loaded[s], 16)
                act.activation(wh[:, s, 0:width], raw[:, s, 0:width], ACT.Copy).then_inc(hi_ready[s], 1)

            def split(*names):
                for name in names:
                    s, use, loaded, width = plan.at[name]
                    split_hi(s, use, loaded, width)

            def split_all(what, n, k=2):
                split(*[(what, c, j) for c in range(n) for j in range(k)])

            def sqrt_table():
                act.activation(unused, eps, ACT.Sqrt)

            def norm_std(name, ready, count):
                sqrt_table()
                act.wait_ge(S(ready), B(ready) + count)
                act.activation(hn[:, 1, :], h[:, 1, :], ACT.Square, scale=D ** -0.5, accum_out=nss[name][:, 1:2]).then_inc(S(name + ".sq"), 1)
                act.wait_ge(S(name + ".ss"), B(name + ".ss") + 1)
                act.wait_ge(S(name + ".sq"), B(name + ".sq") + 1)
                act.activation(nsd[name], nss[name], ACT.Sqrt, bias=eps).then_inc(S(name + ".std"), 1)

            def post_std(name, src):
                for t in range(NT):
                    act.activation(W3(9, NT)[:, t, :].rearrange("p (b n) -> p b n", b=2), src(t), ACT.Square, scale=D ** -0.5,
                                   accum_out=nss[name][:, t:t + 1]).then_inc(S(name + ".sq"), 1)
                    act.wait_ge(S(name + ".sq"), B(name + ".sq") + t + 1)
                    act.activation(nsd[name][:, t:t + 1], nss[name][:, t:t + 1], ACT.Sqrt, bias=eps).then_inc(S(name + ".std"), 1)

            def norm_hi(name, gain, base, dst=None, sem=".xh"):
                for kp in range(4):
                    act.wait_ge(S(name + ".T"), B(name + ".T") + kp + 1)
                    for j in range(2):
                        kt = 2 * kp + j
                        d = xh if dst is None else dst
                        act.activation(d[:, kt, :], ps[:, 4 + kp, j * SEQ:(j + 1) * SEQ], ACT.Identity,
                                       scale=col(gain, base + kt)).then_inc(S(name + sem), 1)

            def norm_modulated_hi(name):
                hT = W3(7, KT) if name == "pre" else W3(2, KT)
                act.wait_ge(S(name + ".hT"), B(name + ".hT") + KT)
                for k in range(2):
                    o = slice(4 * k, 4 * k + 4)
                    act.activation(xh[:, o, :], hT[:, o, :], ACT.Copy).then_inc(S(name + ".xh"), 1)

            def copy_hi(name, banks):
                for kp, b in enumerate(banks):
                    act.wait_ge(S(name + ".T"), B(name + ".T") + kp + 1)
                    act.activation(xh[:, 2 * kp:2 * kp + 2, :], ps[:, b, :].rearrange("p (a n) -> p a n", a=2), ACT.Copy)\
                       .then_inc(S(name + ".xh"), 1)

            def first_columns(loop, per):
                uses, loads = plan.at[loop]
                for s in range(2):
                    split_hi(s, uses[s], loads[s] + per)

            def ffn_loop(f, uses, loads, per, fn):
                def gu(k, c):
                    split_hi(k, uses[k] + c, loads[k] + per[k] * c + per[k])

                def body(i, last):
                    if last:
                        split_hi(0, uses[0] + NFFN, loads[0] + per[0] * NFFN + per[2])
                    else:
                        gu(0, i + 1)
                    act.wait_ge(w_used[1], uses[1] + i + 1)
                    if not isinstance(i, int):
                        act.wait_ge(S(f + ".h"), B(f + ".h") + i)
                        act.wait_ge(S(f + ".h"), B(f + ".h") + 1)
                    elif i > 0:
                        act.wait_ge(S(f + ".h"), B(f + ".h") + i)
                    for t in range(NT):
                        act.activation(silu[:, t, :], ps[:, FFN_BANK(i) + t, 0:FC], fn).then_inc(S(f + ".act"), 1)
                    if not last:
                        gu(1, i + 1)
                    act.wait_ge(S(f + ".mT"), B(f + ".mT") + i + 1)
                    act.wait_ge(w_used[2], uses[2] + i)
                    act.wait_ge(S(f + ".mT"), B(f + ".mT") + 1)
                    act.activation(gh[:, :, :], ps[:, 6, :].rearrange("p (a n) -> p a n", a=2), ACT.Copy).then_inc(S(f + ".gh"), 1)
                    if not last:
                        split_hi(2, uses[2] + i, loads[2] + per[2] * i + per[2])

                body(0, False)
                with act.Fori(1, NFFN - 1) as i:
                    body(i, False)
                body(NFFN - 1, True)

            def mlp_loop():
                uses, loads = plan.at["mlp"]

                def up(s, use):
                    split_hi(s, uses[s] + use, loads[s] + 16 * use + 16)

                def body(c, s, use, more):
                    if isinstance(c, int) and c == 0:
                        split_hi(2, uses[2], loads[2] + 16)
                    act.wait_ge(w_used[s], uses[s] + use + 1)
                    if not (isinstance(c, int) and c == 0):
                        act.wait_ge(S("mlp.h"), B("mlp.h") + c)
                        act.wait_ge(S("mlp.h"), B("mlp.h") + 1)
                    act.activation(silu[:, :, :], ps[:, 4 + s, :].rearrange("p (t n) -> p t n", t=NT), ACT.Relu)\
                       .then_inc(S("mlp.act"), 1)
                    if more:
                        up(s, use + 1)
                    if isinstance(c, int) and c == NMLP - 1:
                        split_hi(0, uses[0] + NMLP // 2, loads[0] + 16 * (NMLP // 2) + 16)
                    elif not (isinstance(c, int) and c == 0):
                        split_hi(2, uses[2] + c, loads[2] + 16 * c + 16)
                    act.wait_ge(S("mlp.mT"), B("mlp.mT") + c + 1)
                    act.wait_ge(w_used[2], uses[2] + c)
                    act.wait_ge(S("mlp.mT"), B("mlp.mT") + 1)
                    act.activation(gh[:, :, :], ps[:, 6, :].rearrange("p (a n) -> p a n", a=2), ACT.Copy).then_inc(S("mlp.gh"), 1)

                body(0, 0, 0, True)
                with act.Fori(0, NMLP // 2 - 2) as i:
                    body(i * 2 + 1, 1, i, True)
                    body(i * 2 + 2, 0, i + 1, True)
                body(NMLP - 3, 1, NMLP // 2 - 2, True)
                body(NMLP - 2, 0, NMLP // 2 - 1, False)
                body(NMLP - 1, 1, NMLP // 2 - 1, False)

            act.dma_start(masks[:, :], masks_d).then_inc(S("masks"), 16)
            act.dma_start(W(6, P, P)[0:CONVW - P, :], A["vectors"][P:CONVW, :]).then_inc(S("rows"), 16)
            act.dma_start(W(6, 256, D)[0:CK, :], A["conv_w_2"][0]).then_inc(S("rows"), 16)
            act.dma_start(W3(4, 4, 0, 512), A["sgu_w_s"][0].rearrange("h i j -> i h j")).then_inc(S("sgu_w"), 16)
            act.dma_start(ccol, A["c_2"][0].rearrange("(p k) -> p k", k=KT)).then_inc(S("c_loaded"), 16)
            act.dma_start(W3(4, 4, 1024, 512), A["pool_w"][0].rearrange("g c d -> c g d")).then_inc(S("mixw"), 16)
            act.dma_start(W(4, 1536, 512), A["sgu_gain"][0].partition_broadcast(P)).then_inc(S("mixw"), 16)
            act.dma_start(W(3, 0, 12 * P), pool_d).then_inc(S("mixw"), 16)
            act.dma_start(posi[:, :], A["positions_2"][0].rearrange("(t p) -> p t", p=P), allow_slow_non_contiguous=True).then_inc(S("pos"), 16)

            act.wait_ge(S("masks"), B("masks") + 16)
            norm_std("mix0", "x_loaded", 16)
            act.wait_ge(S("cols"), B("cols") + 2)
            split(("ab_in", 0, 0))
            norm_hi("mix0", "mix_norm", 0)
            split(("ab_in", 0, 1), ("ab_in", 1, 0))
            za = W3(0, NT)
            zb = W3(1, NT, 0, 1024)
            used(act, ("ab_in", 0, 1))
            for t in range(NT):
                act.activation(za[:, t, 0:AW], ps[:, t, :], ACT.Gelu).then_inc(S("u_ready"), 1)
            split(("ab_in", 1, 1), ("ab_in", 2, 0), ("ab_in", 2, 1))
            used(act, ("ab_in", 1, 1))
            for t in range(NT):
                act.activation(za[:, t, AW:D], ps[:, 2 + t, :], ACT.Gelu).then_inc(S("v_ready"), 1)
            act.wait_ge(S("v_ss"), B("v_ss") + 1)
            act.activation(vsd, vss, ACT.Sqrt).then_inc(S("v_std"), 1)
            used(act, ("ab_in", 2, 1))
            for t in range(NT):
                act.activation(zb[:, t, :], ps[:, t, :], ACT.Copy).then_inc(S("zb_ready"), 1)
            split(("ab_out", 0, 0), ("ab_out", 0, 1))
            used(act, ("ab_in", 2, 1))
            for b in range(2):
                act.wait_ge(S("yb_T"), B("yb_T") + b + 1)
                for j in range(2):
                    kt = 2 * b + j
                    act.activation(xh[:, 4 + kt, :], ps[:, 4 + b, j * SEQ:(j + 1) * SEQ], ACT.Identity,
                                   scale=col("pool_scale", kt)).then_inc(S("ab.yh"), 1)
            for b in range(2):
                act.wait_ge(S("ya_T"), B("ya_T") + b + 1)
                act.activation(xh[:, 2 * b:2 * b + 2, :], ps[:, 6 + b, :].rearrange("p (a n) -> p a n", a=2), ACT.Copy)\
                   .then_inc(S("ab.xh"), 1)
            split(("ab_out", 1, 0), ("ab_out", 1, 1))

            norm_std("ffn0", "mix0.add", 4)
            first_columns("ffn0", 32)
            norm_hi("ffn0", "ffn_norm", 0)
            u_, l_ = plan.at["ffn0"]
            ffn_loop("ffn0", u_, l_, (32, 32, 16), ACT.Silu)
            act.wait_ge(S("c_loaded"), B("c_loaded") + 16)
            act.activation(ccol, ccol, ACT.Silu).then_inc(S("c_act"), 1)

            act.wait_ge(S("ffn0.h"), B("ffn0.h") + NFFN)
            act.wait_ge(S("ffn0.mT"), B("ffn0.mT") + NFFN)
            act.dma_start(W3(10, KT, 0, 512), A["rwkv_w1"][0].rearrange("(a p) n -> p a n", p=P)).then_inc(S("rw_w1"), 16)
            act.dma_start(W3(10, KT, 512, 512), A["rwkv_a1"][0].rearrange("(a p) n -> p a n", p=P)).then_inc(S("rw_w1"), 16)
            act.dma_start(W3(6, KT, 0, KT * GRANK), A["rwkv_g1"][0].rearrange("(a p) n -> p a n", p=P)).then_inc(S("rw_w1"), 16)
            act.dma_start(W(4, 0, D)[0:RANK, :], A["rwkv_w2"][0]).then_inc(S("rw_w2"), 16)
            act.dma_start(W(4, 0, D)[RANK:RANK + 1, :], A["rwkv_w0"]).then_inc(S("rw_w2"), 16)
            act.dma_start(W(4, D, D)[0:RANK, :], A["rwkv_a2"][0]).then_inc(S("rw_w2"), 16)
            act.dma_start(W(4, D, D)[RANK:RANK + 1, :], A["rwkv_a0"]).then_inc(S("rw_w2"), 16)
            act.dma_start(W(9, 0, D), A["rwkv_k_k"][0].partition_broadcast(P)).then_inc(S("rw_vec"), 16)
            act.dma_start(W(9, D, D), A["rwkv_k_a"][0].partition_broadcast(P)).then_inc(S("rw_vec"), 16)
            act.dma_start(side[:, :], A["rwkv_r_k"][0].rearrange("h c -> (h c)").partition_broadcast(P)).then_inc(S("rw_vec"), 16)
            norm_std("mix1", "ffn0.add", 4)
            norm_hi("mix1", "mix_norm", KT, dst=W3(0, KT), sem=".hT")
            split(("k", 0, 0), ("k", 0, 1), ("k", 1, 0))
            act.wait_ge(S("rank_T"), B("rank_T") + 1)
            act.activation(lowr[0:RANK, 0:SEQ], ps[0:RANK, 4, 0:SEQ], ACT.Tanh).then_inc(S("rank"), 1)
            act.wait_ge(S("rank_T"), B("rank_T") + 2)
            act.activation(lowr[0:RANK, SEQ:2 * SEQ], ps[0:RANK, 5, 0:SEQ], ACT.Copy).then_inc(S("rank"), 1)
            act.wait_ge(S("rank_T"), B("rank_T") + 3)
            act.activation(lowr[:, 2 * SEQ:3 * SEQ], ps[:, 6, 0:SEQ], ACT.Sigmoid)
            act.activation(lowr[0:GRANK - P, 3 * SEQ:4 * SEQ], ps[0:GRANK - P, 7, 0:SEQ], ACT.Sigmoid).then_inc(S("rank"), 1)
            sig = W3(7, NT)
            rate = W3(8, NT)
            for n, (dst, name) in enumerate(((sig, "sig"), (rate, "rate"))):
                for t in range(NT):
                    for c in range(2):
                        act.wait_ge(S("logit"), B("logit") + 4 * n + 2 * t + c + 1)
                        act.activation(dst[:, t, c * 512:(c + 1) * 512], ps[:, 2 * t + c, :], ACT.Sigmoid).then_inc(S(name), 1)
            rkv = {"k": W3(5, NT), "r": W3(4, NT), "v": W3(6, NT)}
            mixes = {"k": W3(3, KT), "r": W3(2, KT), "v": W3(3, KT)}

            def mix_hi(n, what, k):
                act.wait_ge(S("mixed"), B("mixed") + 4 + n)
                if n:
                    used(act, ("krv"[n - 1], 1, k))
                act.activation(xh[:, 4 * k:4 * k + 4, :], mixes[what][:, 4 * k:4 * k + 4, :], ACT.Copy).then_inc(S("rkv.xh"), 1)

            def take(n, what, c):
                used(act, (what, c, 1))
                for t in range(NT):
                    act.activation(rkv[what][:, t, c * 512:(c + 1) * 512], ps[:, 2 * c + t, :], ACT.Copy).then_inc(S("rkv"), 1)

            mix_hi(0, "k", 0)
            mix_hi(0, "k", 1)
            split(("k", 1, 1), ("r", 0, 0))
            take(0, "k", 0)
            mix_hi(1, "r", 0)
            split(("r", 0, 1))
            mix_hi(1, "r", 1)
            split(("r", 1, 0))
            take(0, "k", 1)
            split(("r", 1, 1))
            act.wait_ge(S("kk"), B("kk") + 1)
            act.wait_ge(S("mixed"), B("mixed") + 6)
            act.activation(W3(0, NT), W3(10, NT), ACT.Square).then_inc(S("kk_sq"), 1)
            act.wait_ge(S("kk_ss"), B("kk_ss") + 1)
            act.activation(kss, kss, ACT.Sqrt).then_inc(S("kk_norm"), 1)
            split(("v", 0, 0))
            take(1, "r", 0)
            mix_hi(2, "v", 0)
            split(("v", 0, 1))
            mix_hi(2, "v", 1)
            split(("v", 1, 0))
            take(1, "r", 1)
            split(("v", 1, 1))
            act.wait_ge(S("cum"), B("cum") + 1)
            act.wait_ge(S("rkv.xl"), B("rkv.xl") + 24)

            def decay_exps(n):
                buf = DECAY_BUF[n % 2]
                if n == 1:
                    act.wait_ge(S("bonus"), B("bonus") + 1)
                if n >= 2:
                    act.wait_ge(S("scaled"), B("scaled") + 4 * (n - 1))
                act.activation(W(buf, 0, 512), ps[:, 4 + n, :], ACT.Exp, scale=-DECAY)
                act.activation(W(buf, 512, 512), ps[:, 4 + n, :], ACT.Exp, scale=DECAY).then_inc(S("cum_read"), 1)

            decay_exps(0)
            decay_exps(1)
            for n in range(2 * NT):
                buf = DECAY_BUF[n % 2]
                act.wait_ge(S("cum_prev"), B("cum_prev") + n + 1)
                act.activation(W(buf, 1536, 512), W(buf, 1024, 512), ACT.Exp, scale=-DECAY).then_inc(S("exps"), 1)
                if n + 2 < 2 * NT:
                    decay_exps(n + 2)
                if n == 2:
                    take(2, "v", 0)
            act.wait_ge(S("pc_T"), B("pc_T") + 1)
            pcv = pc.rearrange("p (h x c) -> p h x c", h=RH // 2, x=2)
            for x in range(2):
                act.activation(pcv[0:64, :, x, :], ps[64 * x:64 * x + 64, 4, 0:32].rearrange("p (h c) -> p h c", c=4), ACT.Exp,
                               scale=-DECAY).then_inc(S("pc"), 1)
            take(2, "v", 1)

            tmps = WKV_TMP(W, raw)
            yv = W(0).rearrange("p (t h c) -> p t h c", t=NT, h=RH)
            gall = WKV_G(W, side)

            def bank(g, i):
                return ps[:, 4 * (g % 2) + i, :]

            def out_of(sem, b, dst, done, n=512):
                def step(g):
                    act.wait_ge(S("wkv." + sem), B("wkv." + sem) + g + 1)
                    act.activation(tmps[g % 2][dst][:, 0:n], bank(g, b)[:, 0:n], ACT.Copy).then_inc(S("wkv." + done), 1)
                return step

            def state_out(g):
                if g < 4:
                    act.wait_ge(S("wkv.fg"), B("wkv.fg") + g + 1)
                    act.activation(gall[0][0:64, HEAD0(g):HEAD0(g) + 4, :], bank(g, 2)[0:64, 0:256].rearrange("p (u c) -> p u c", u=4),
                                   ACT.Copy)

            def h_out(g):
                act.wait_ge(S("wkv.eh"), B("wkv.eh") + g + 1)
                act.activation(yv[:, g // 4, HEAD0(g):HEAD0(g) + 4, :], bank(g, 1)[:, 0:256].rearrange("p (u c) -> p u c", u=4), ACT.Copy)\
                   .then_inc(S("wkv.hc"), 1)

            def load_norm(g):
                if g == 7:
                    act.dma_start(W(9, 0, D), A["rwkv_ln_w"][0].partition_broadcast(P)).then_inc(S("ln_vec"), 16)
                    act.dma_start(W(9, D, D), A["rwkv_ln_b"][0].partition_broadcast(P)).then_inc(S("ln_vec"), 16)

            def load_gate(g):
                if g == 7:
                    act.wait_ge(S("wkv.r1"), B("wkv.r1") + 8)
                    act.dma_start(W(10, 0, D), A["rwkv_g2"][0][0:P, :]).then_inc(S("g2"), 16)
                    act.dma_start(W(10, D, D)[0:GRANK - P, :], A["rwkv_g2"][0][P:GRANK, :]).then_inc(S("g2"), 16)

            for pair in range(4):
                for steps in ((out_of("T", 0, "ar", "ar"),),
                              (load_norm,),
                              (out_of("x2", 2, "x2", "x2c"), out_of("x2t", 3, "x2t", "x2c")),
                              (out_of("gkv", 0, "gkv", "gkvc", 256),),
                              (out_of("x4", 2, "x4", "x4c"), out_of("x4t", 3, "x4t", "x4c")),
                              (out_of("x8", 0, "x8", "x8c"),),
                              (out_of("r1", 2, "r1", "r1c"), out_of("mt", 3, "mt", "mtc")),
                              (load_gate,),
                              (state_out,), (h_out,)):
                    for g in (2 * pair, 2 * pair + 1):
                        for step in steps:
                            step(g)

            states, chain = W3(4, NT), W(5, 0, D)
            y, sq, gate = W3(0, NT), W3(5, NT), W3(7, NT)

            def state_put(c):
                p = c % 2
                act.wait_ge(S("state"), B("state") + c)
                act.activation(states[64 * p:64 * p + 64, c // 2, :], chain[0:64, :], ACT.Copy).then_inc(S("state_put"), 1)

            def gate_out(t):
                for c in range(2):
                    act.wait_ge(S("gate_T"), B("gate_T") + 2 * t + c + 1)
                    act.activation(gate[:, t, c * 512:(c + 1) * 512], ps[:, GATE_BANK[t] + c, :], ACT.Copy).then_inc(S("gate_out"), 1)

            def group_std(t):
                act.wait_ge(S("centred"), B("centred") + t + 1)
                act.activation(sq[:, t, :], y[:, t, :], ACT.Square).then_inc(S("gn_sq"), 1)
                o = slice(t * RH, (t + 1) * RH)
                act.wait_ge(S("gn_var"), B("gn_var") + t + 1)
                act.activation(gvar[:, o], gvar[:, o], ACT.Sqrt).then_inc(S("gn_std"), 1)

            act.wait_ge(S("wkv.done"), B("wkv.done") + 8)
            state_put(1)
            gate_out(0)
            state_put(2)
            state_put(3)
            split(("o", 0, 0), ("o", 0, 1))
            group_std(0)
            gate_out(1)
            group_std(1)
            split(("o", 1, 0))
            copy_hi("rw", RW_BANKS)
            split(("o", 1, 1))

            norm_std("ffn1", "mix1.add", 4)
            first_columns("ffn1", 32)
            norm_hi("ffn1", "ffn_norm", KT)
            u_, l_ = plan.at["ffn1"]
            ffn_loop("ffn1", u_, l_, (32, 32, 16), ACT.Silu)

            act.dma_start(W(8, 0, D), A["final_norm"].partition_broadcast(P)).then_inc(S("fin_vec"), 16)
            act.dma_start(W(6, 0, D), A["g_post_mix_2"][0].partition_broadcast(P)).then_inc(S("post_vec"), 16)
            act.dma_start(W(6, D, D), A["g_post_mlp_2"][0].partition_broadcast(P)).then_inc(S("post_vec"), 16)
            norm_std("fin", "ffn1.add", 4)
            norm_std("pre", "fin.h", 2)
            split(("glu", 0, 0), ("glu", 0, 1))
            norm_modulated_hi("pre")
            split(("glu", 1, 0))
            act.wait_ge(S("angle"), B("angle") + 1)
            act.activation(lowr[:, 0:64], lowr[:, 0:64], ACT.Sin)
            act.activation(lowr[:, 64:128], lowr[:, 64:128], ACT.Sin).then_inc(S("sincos"), 1)
            ub = lowr[:, 512:1024].rearrange("p (t n) -> p t n", t=NT)
            nxt = [("glu", 1, 1), ("glu", 2, 0), ("glu", 2, 1), ("glu", 3, 0), ("glu", 3, 1), ("lat", 0, 0), ("lat", 0, 1), ("lat", 1, 0)]
            for c in range(4):
                used(act, ("glu", c, 1))
                if c:
                    act.wait_ge(S("glu"), B("glu") + 2 * c)
                for t in range(NT):
                    act.activation(ub[:, t, :], ps[:, 2 * (c % 2) + t, 256:512], ACT.Sigmoid).then_inc(S("glu_s"), 1)
                split(*nxt[2 * c:2 * c + 2])
            lat = W(3, 0, 2 * 704).rearrange("p (t n) -> p t n", t=NT)
            used(act, ("lat", 0, 1))
            for t in range(NT):
                act.activation(lat[:, t, 0:QL], ps[:, t, 0:QL], ACT.Copy).then_inc(S("lat"), 1)
            split(("lat", 1, 1), ("gate", 0, 0))
            used(act, ("lat", 1, 1))
            for t in range(NT):
                act.activation(lat[:, t, QL:704], ps[:, 2 + t, 0:KL + ROPE], ACT.Copy).then_inc(S("lat"), 1)
            split(("gate", 0, 1))
            up_ = U_PAD(wide)
            for c in range(4):
                act.wait_ge(S("u_T"), B("u_T") + c + 1)
                act.activation(up_[:, 2 * c:2 * c + 2, CK - 1:CK - 1 + SEQ], ps[:, 4 + c, :].rearrange("p (a n) -> p a n", a=2),
                               ACT.Copy).then_inc(S("u_put"), 1)
            split(("gate", 1, 0))
            act.wait_ge(S("lat_ss"), B("lat_ss") + 1)
            act.activation(qsd, qss, ACT.Sqrt).then_inc(S("lat_std"), 1)
            gates = wide[:, 6 * 2048:8 * 2048].rearrange("p (t n) -> p t n", t=NT)
            nxt = [[("gate", 1, 1), ("gate", 2, 0)], [("gate", 2, 1), ("gate", 3, 0)], [("gate", 3, 1), ("uq", 0)], [("uq", 1), ("uq", 2)]]
            for c in range(4):
                used(act, ("gate", c, 1))
                if c == 0:
                    act.wait_ge(S("gates"), B("gates") + 4)
                for t in range(NT):
                    act.activation(gates[:, t, c * 512:(c + 1) * 512], ps[:, 2 * (c % 2) + t, :], ACT.Sigmoid).then_inc(S("gatev"), 1)
                if c < 3:
                    split(*nxt[c])
                else:
                    for kt in range(5):
                        act.wait_ge(S("lq.T"), B("lq.T") + kt // 2 + 1)
                        act.activation(xh[:, kt, :], ps[:, 4 + kt // 2, (kt % 2) * SEQ:(kt % 2 + 1) * SEQ], ACT.Identity,
                                       scale=col("q_norm_g_2", kt) if kt < 3 else col("kv_norm_g_2", kt - 3)).then_inc(S("lq.xh"), 1)
            split(("uq", 1), ("uq", 2))
            qn = W3(4, NH)
            kn = W3(9, NH)
            nxt = [[("uq", 3)], [("ukv", 0)], [("ukv", 1)], []]
            for j in range(4):
                used(act, ("uq", j))
                act.activation(qn[:, 2 * j:2 * j + 2, :], ps[:, j % 2, :].rearrange("p (a n) -> p a n", a=2), ACT.Copy).then_inc(S("qn"), 1)
                split(*nxt[j])
            qraw = W(8, 0, 2 * 9 * 64).rearrange("p (t n) -> p t n", t=NT)
            for t in range(NT):
                act.activation(qraw[:, t, 0:512], ps[:, 2 + t, :], ACT.Copy).then_inc(S("qraw"), 1)
            for j in range(2):
                used(act, ("ukv", j))
                for b in range(2):
                    act.activation(kn[:, 4 * j + 2 * b:4 * j + 2 * b + 2, :], ps[:, UKV_BANK[j] + b, :].rearrange("p (a n) -> p a n", a=2), ACT.Copy)\
                       .then_inc(S("kn"), 1)
                vt = W3(5, NT)
                for t in range(NT):
                    act.activation(vt[:, t, j * 512:(j + 1) * 512], ps[:, UKV_BANK[j] + 2 + t, :], ACT.Copy).then_inc(S("vt"), 1)
                if j == 0:
                    split(("attn_out", 0, 0), ("attn_out", 0, 1))
            qr = W(1, 256, 5 * SEQ).rearrange("p (a n) -> p a n", a=5)
            for b in range(3):
                n = 2 if b < 2 else 1
                act.wait_ge(S("ro_T"), B("ro_T") + b + 1)
                act.activation(qr[:, 2 * b:2 * b + n, :], ps[:, 4 + b, 0:n * SEQ].rearrange("p (a n) -> p a n", a=n), ACT.Copy)\
                   .then_inc(S("ro_put"), 1)
            diags = DIAGS(W, lowr)
            act.wait_ge(S("glu"), B("glu") + 8)
            act.wait_ge(S("roped"), B("roped") + 2)

            def diag_taps(i):
                batch = PE_TAPS[i * TAP_BATCH:(i + 1) * TAP_BATCH]
                if i >= 2:
                    act.wait_ge(S("conv_mm"), B("conv_mm") + i - 1)
                for d, (kt, k) in zip(diags[i % 2], batch):
                    c = CONVW + kt * CK + k
                    act.activation(d, ident, ACT.Copy, scale=cols[:, c:c + 1]).then_inc(S("diag"), 1)
            diag_taps(0)
            pp = [W3(10, NT, 512 * b, 512) for b in range(2)]
            pT = [W(8, 1152 + b * 384, 384) for b in range(2)]

            def weights_T(i):
                act.wait_ge(S("at.T"), B("at.T") + i + 1)
                if i >= 2:
                    act.wait_ge(S("at.o"), B("at.o") + i - 1)
                act.activation(pT[i % 2], ps[:, 2 + i % 2, 0:384], ACT.Copy).then_inc(S("at.pT"), 1)

            def out_hi(i):
                act.wait_ge(S("at.o"), B("at.o") + i + 1)
                act.activation(xh[:, i, :], ps[:, 4 + i % 2, 0:SEQ], ACT.Copy).then_inc(S("at.xh"), 1)
            for i in range(NH):
                b = i % 2
                if i:
                    weights_T(i - 1)
                act.wait_ge(S("at.max"), B("at.max") + i + 1)
                for t in range(NT):
                    nk = P * (t + 1)
                    act.activation(pp[b][:, t, 0:nk], pp[b][:, t, 0:nk], ACT.Exp, bias=amax[:, 2 * b + t:2 * b + t + 1],
                                   accum_out=asum[:, 2 * b + t:2 * b + t + 1]).then_inc(S("at.e"), 1)
                if i + 1 < NH:
                    diag_taps(i + 1)
                if i == 0:
                    split(("attn_out", 1, 0))
                else:
                    out_hi(i - 1)
            weights_T(NH - 1)
            out_hi(NH - 1)
            act.wait_ge(S("conv_mm"), B("conv_mm") + NH)
            for kt in range(KT - CONV_PE, KT):
                act.activation(W3(2, KT)[:, kt, :], CONV_OUT(ps, kt), ACT.Identity, bias=col("conv_b_2", kt)).then_inc(S("conv_pe"), 1)
            split(("attn_out", 1, 1))
            cv = W3(2, KT)
            for k in range(2):
                o = slice(4 * k, 4 * k + 4)
                act.wait_ge(S("cv_c"), B("cv_c") + k + 1)
                if k == 0:
                    act.wait_ge(S("at.o"), B("at.o") + NH)
                act.activation(W3(5, KT)[:, o, :], cv[:, o, :], ACT.Square).then_inc(S("csq"), 1)
            split(("conv_out", 0, 0))
            act.wait_ge(S("cv_ss"), B("cv_ss") + 1)
            act.activation(lowr[:, 256:512], lowr[:, 256:512], ACT.Sqrt).then_inc(S("cv_std"), 1)
            for kt in range(KT):
                act.wait_ge(S("cv_n"), B("cv_n") + kt // 4 + 1)
                act.activation(cv[:, kt, :], cv[:, kt, :], ACT.Silu, bias=col("conv_norm_b_2", kt), scale=col("conv_norm_g_2", kt))\
                   .then_inc(S("cv_act"), 1)
            used(act, ("attn_out", 1, 1))
            for k in range(2):
                o = slice(4 * k, 4 * k + 4)
                act.wait_ge(S("cv_act"), B("cv_act") + 4 * (k + 1))
                act.activation(xh[:, o, :], cv[:, o, :], ACT.Copy).then_inc(S("cv.xh"), 1)
            split(("conv_out", 0, 1), ("conv_out", 1, 0), ("conv_out", 1, 1), ("out", 0, 0), ("out", 0, 1))
            used(act, ("conv_out", 1, 1))
            copy_hi("ym", (4, 5, 6, 7))
            split(("out", 1, 0), ("out", 1, 1))
            sqrt_table()
            used(act, ("out", 0, 1))
            used(act, ("out", 1, 1))
            post_std("post1", POST(ps))
            norm_std("pre2", "post1.add", 2)
            first_columns("mlp", 16)
            norm_modulated_hi("pre2")
            mlp_loop()
            act.wait_ge(w_used[0], plan.at["mlp"][0][0] + NMLP // 2 + 1)
            post_std("post2", POST(ps))
            for t in range(NT):
                act.wait_ge(S("post2.add"), B("post2.add") + t + 1)
                act.dma_start(out[0, t * P:(t + 1) * P, :], h[:, t, :]).then_inc(S("stored"), 16)

        @block.vector
        def _(v):
            n_chain = [0]

            def link(ins):
                ins.then_inc(S("dve_chain"), 1)
                n_chain[0] += 1
                v.wait_ge(S("dve_chain"), B("dve_chain") + n_chain[0])

            def f32(ap):
                return ap.bitcast(F32)

            def split_lo(s, use, width=SLOT):
                v.wait_ge(hi_ready[s], use + 1)
                if not isinstance(use, int):
                    v.wait_ge(hi_ready[s], 1)
                v.tensor_tensor(wl[:, s, 0:width], raw[:, s, 0:width], f32(wh[:, s, 0:width]), ALU.subtract).then_inc(lo_ready[s], 1)

            def split(*names):
                for name in names:
                    s, use, _, width = plan.at[name]
                    split_lo(s, use, width)

            def mean_square(src, n, dst, junk):
                return v.tensor_tensor_reduce(out=junk, in0=src, in1=src, scale=1.0 / n, scalar=EPS, op0=ALU.mult, op1=ALU.add,
                                              accum_out=dst)

            def norm_factors(name):
                v.tensor_tensor_reduce(out=hn[:, 0, :], in0=h[:, 0, :], in1=h[:, 0, :], scale=1.0 / D, scalar=0.0, op0=ALU.mult,
                                       op1=ALU.add, accum_out=nss[name][:, 0:1]).then_inc(S(name + ".ss"), 1)
                v.wait_ge(S(name + ".std"), B(name + ".std") + 1)
                link(v.reciprocal(nrs[name], nsd[name]))

            def norm(name):
                norm_factors(name)
                for t in range(NT):
                    v.tensor_scalar(hn[:, t, :], h[:, t, :], nrs[name][:, t:t + 1], None, ALU.mult).then_inc(S(name + ".hn"), 1)

            def norm_lo(name, gain, base):
                for kp in range(4):
                    v.wait_ge(S(name + ".xh"), B(name + ".xh") + 2 * kp + 2)
                    for j in range(2):
                        kt = 2 * kp + j
                        v.scalar_tensor_tensor(out=xl[:, kt, :], in0=ps[:, 4 + kp, j * SEQ:(j + 1) * SEQ], scalar=col(gain, base + kt),
                                               in1=f32(xh[:, kt, :]), op0=ALU.mult, op1=ALU.subtract).then_inc(S(name + ".xl"), 1)

            def norm_modulated(name, scale, shift):
                hT = W3(7, KT) if name == "pre" else W3(2, KT)
                for kp in range(4):
                    v.wait_ge(S(name + ".T"), B(name + ".T") + kp + 1)
                    for j in range(2):
                        kt = 2 * kp + j
                        v.tensor_scalar(hT[:, kt, :], ps[:, 4 + kp, j * SEQ:(j + 1) * SEQ], scale[:, kt:kt + 1], shift[:, kt:kt + 1],
                                        ALU.mult, ALU.add).then_inc(S(name + ".hT"), 1)
                for k in range(2):
                    v.wait_ge(S(name + ".xh"), B(name + ".xh") + k + 1)
                    o = slice(4 * k, 4 * k + 4)
                    v.wait_ge(S(name + ".hT"), B(name + ".hT") + KT)
                    v.tensor_tensor(xl[:, o, :], hT[:, o, :], f32(xh[:, o, :]), ALU.subtract).then_inc(S(name + ".xl"), 4)

            def copy_lo(name, banks):
                for kp, b in enumerate(banks):
                    v.wait_ge(S(name + ".xh"), B(name + ".xh") + kp + 1)
                    o = slice(2 * kp, 2 * kp + 2)
                    v.tensor_tensor(xl[:, o, :], ps[:, b, :].rearrange("p (a n) -> p a n", a=2), f32(xh[:, o, :]), ALU.subtract)\
                     .then_inc(S(name + ".xl"), 2)

            def add_residual(name):
                for t in range(NT):
                    for c in range(2):
                        o = slice(c * 512, (c + 1) * 512)
                        v.tensor_tensor(h[:, t, o], h[:, t, o], ps[:, 2 * t + c, :], ALU.add).then_inc(S(name), 1)
                v.wait_ge(S(name), B(name) + 4)

            def add_linear(lin, name):
                for c in range(2):
                    used(v, (lin, c, 1))
                    for t in range(NT):
                        o = slice(c * 512, (c + 1) * 512)
                        v.tensor_tensor(h[:, t, o], h[:, t, o], ps[:, 2 * c + t, :], ALU.add).then_inc(S(name), 1)
                v.wait_ge(S(name), B(name) + 4)

            ada_left = [(j, k, b) for j in range(NADA // 2) for k in range(KT) for b in range(2)]

            def ada(count):
                for _ in range(min(count, len(ada_left))):
                    j, k, b = ada_left.pop(0)
                    buf, n = 2 * (j % 2) + b, 16 * j + 2 * k + b
                    if k == 0:
                        v.wait_ge(S(f"ada{buf}"), B(f"ada{buf}") + 16 * (j // 2 + 1))
                    else:
                        v.wait_ge(S("ada_step"), B("ada_step") + n - 1)
                    o = ada_acc[:, (2 * j + b) * 256:(2 * j + b + 1) * 256]
                    v.scalar_tensor_tensor(out=o, in0=ada_raw[buf][:, k, :], scalar=ccol[:, k:k + 1], in1=o,
                                           op0=ALU.mult, op1=ALU.add).then_inc(S("ada_step"), 1)

            def ffn_loop(f, uses, ride=(0, 0, 0)):
                def body(i, last):
                    split_lo(0, uses[0] + i + 1)
                    if not (isinstance(i, int) and i == 0):
                        v.wait_ge(S(f + ".mT"), B(f + ".mT") + i)
                    for t in range(NT):
                        v.wait_ge(S(f + ".act"), B(f + ".act") + i * 2 + t + 1)
                        if not isinstance(i, int):
                            v.wait_ge(S(f + ".act"), B(f + ".act") + 1)
                        m = v.tensor_tensor(hmid[:, t, :], silu[:, t, :], ps[:, FFN_BANK(i) + t, FC:2 * FC], ALU.mult)
                    m.then_inc(S(f + ".h"), 1)
                    ada(ride[0])
                    if not last:
                        split_lo(1, uses[1] + i + 1)
                    ada(ride[1])
                    v.wait_ge(S(f + ".gh"), B(f + ".gh") + i + 1)
                    if not isinstance(i, int):
                        v.wait_ge(S(f + ".gh"), B(f + ".gh") + 1)
                    v.tensor_tensor(gl[:, :, :], ps[:, 6, :].rearrange("p (a n) -> p a n", a=2), f32(gh[:, :, :]), ALU.subtract)\
                     .then_inc(S(f + ".gl"), 1)
                    if not last:
                        split_lo(2, uses[2] + i)
                    ada(ride[2])

                body(0, False)
                if any(ride):
                    for i in range(1, NFFN - 1):
                        body(i, False)
                else:
                    with v.Fori(1, NFFN - 1) as i:
                        body(i, False)
                body(NFFN - 1, True)

            def mlp_loop():
                uses, _ = plan.at["mlp"]

                def body(c, s, use, more):
                    if isinstance(c, int) and c == 0:
                        split_lo(2, uses[2])
                    else:
                        v.wait_ge(S("mlp.mT"), B("mlp.mT") + c)
                    v.wait_ge(S("mlp.act"), B("mlp.act") + c + 1)
                    if not isinstance(c, int):
                        v.wait_ge(S("mlp.act"), B("mlp.act") + 1)
                    v.tensor_tensor(hmid[:, :, :], silu[:, :, :], silu[:, :, :], ALU.mult).then_inc(S("mlp.h"), 1)
                    if more:
                        split_lo(s, uses[s] + use + 1)
                    if isinstance(c, int) and c == NMLP - 1:
                        split_lo(0, uses[0] + NMLP // 2)
                    elif not (isinstance(c, int) and c == 0):
                        split_lo(2, uses[2] + c)
                    v.wait_ge(S("mlp.gh"), B("mlp.gh") + c + 1)
                    if not isinstance(c, int):
                        v.wait_ge(S("mlp.gh"), B("mlp.gh") + 1)
                    v.tensor_tensor(gl[:, :, :], ps[:, 6, :].rearrange("p (a n) -> p a n", a=2), f32(gh[:, :, :]), ALU.subtract)\
                     .then_inc(S("mlp.gl"), 1)

                split_lo(1, uses[1])
                body(0, 0, 0, True)
                with v.Fori(0, NMLP // 2 - 2) as i:
                    body(i * 2 + 1, 1, i, True)
                    body(i * 2 + 2, 0, i + 1, True)
                body(NMLP - 3, 1, NMLP // 2 - 2, True)
                body(NMLP - 2, 0, NMLP // 2 - 1, False)
                body(NMLP - 1, 1, NMLP // 2 - 1, False)

            v.wait_ge(S("x_loaded"), B("x_loaded") + 16)
            norm("mix0")
            v.wait_ge(S("cols_T"), B("cols_T") + 1)
            v.tensor_copy(cols[:, 0:CONVW], ps[:, 0, 0:CONVW]).then_inc(S("cols"), 1)
            v.tensor_copy(cols[:, CONVW:NCOL], ps[:, 1, 0:KT * CK]).then_inc(S("cols"), 1)
            v.wait_ge(S("wst_T"), B("wst_T") + 1)
            v.tensor_copy(W(4, 512, 512), ps[:, 2, :]).then_inc(S("wst"), 1)
            v.wait_ge(S("cols"), B("cols") + 2)
            split(("ab_in", 0, 0))
            norm_lo("mix0", "mix_norm", 0)
            split(*[("ab_in", n, k) for n in range(3) for k in range(2)][1:])
            za = W3(0, NT)
            v.wait_ge(S("v_ready"), B("v_ready") + 2)
            for t in range(NT):
                m = mean_square(za[:, t, AW:D], AW, vss[:, t:t + 1], W(2, t * 512, 512))
            m.then_inc(S("v_ss"), 1)
            v.wait_ge(S("v_std"), B("v_std") + 1)
            link(v.reciprocal(vrs, vsd))
            v.wait_ge(S("mixw"), B("mixw") + 48)
            for t in range(NT):
                v.scalar_tensor_tensor(out=za[:, t, AW:D], in0=za[:, t, AW:D], scalar=vrs[:, t:t + 1], in1=W(4, 1536, 512),
                                       op0=ALU.mult, op1=ALU.mult).then_inc(S("v_normed"), 1)
            ya = W3(2, NT, 1024, 1024)
            v.wait_ge(S("u_ready"), B("u_ready") + 2)
            for t in range(NT):
                v.wait_ge(S("spatial"), B("spatial") + t + 1)
                for i in range(4):
                    o = slice(i * P, (i + 1) * P)
                    v.scalar_tensor_tensor(out=ya[:, t, o], in0=ps[:, 4 + t, o], scalar=col("sgu_bias", i), in1=za[:, t, o],
                                           op0=ALU.add, op1=ALU.mult).then_inc(S("ya"), 1)
            for b in range(2):
                v.wait_ge(S("pooled_T"), B("pooled_T") + b + 1)
                v.tensor_copy(W(2, b * 512, 512), ps[:, 6 + b, :]).then_inc(S("pooled"), 1)
            split(("ab_out", 0, 0), ("ab_out", 0, 1))
            for b in range(2):
                v.wait_ge(S("ab.yh"), B("ab.yh") + 2 * (b + 1))
                for j in range(2):
                    kt = 2 * b + j
                    v.scalar_tensor_tensor(out=xl[:, 4 + kt, :], in0=ps[:, 4 + b, j * SEQ:(j + 1) * SEQ], scalar=col("pool_scale", kt),
                                           in1=f32(xh[:, 4 + kt, :]), op0=ALU.mult, op1=ALU.subtract).then_inc(S("ab.xl"), 1)
            for b in range(2):
                v.wait_ge(S("ab.xh"), B("ab.xh") + b + 1)
                o = slice(2 * b, 2 * b + 2)
                v.tensor_tensor(xl[:, o, :], ps[:, 6 + b, :].rearrange("p (a n) -> p a n", a=2), f32(xh[:, o, :]), ALU.subtract)\
                 .then_inc(S("ab.xl"), 2)
            split(("ab_out", 1, 0), ("ab_out", 1, 1))
            add_linear("ab_out", "mix0.add")

            norm("ffn0")
            split_lo(0, plan.at["ffn0"][0][0])
            norm_lo("ffn0", "ffn_norm", 0)
            split_lo(1, plan.at["ffn0"][0][1])
            ffn_loop("ffn0", plan.at["ffn0"][0])
            v.wait_ge(w_used[0], plan.at["ffn0"][0][0] + NFFN + 1)
            add_residual("ffn0.add")

            norm("mix1")
            hT, xx = W3(0, KT), W3(1, KT)
            v.wait_ge(S("mix1.hT"), B("mix1.hT") + KT)
            v.tensor_tensor(xx[:, :, 1:SEQ], hT[:, :, 0:SEQ - 1], hT[:, :, 1:SEQ], ALU.subtract)
            link(v.tensor_scalar(xx[:, :, 0:1], hT[:, :, 0:1], -1.0, None, ALU.mult))

            def mix(i, dst):
                for kt in range(KT):
                    m = v.scalar_tensor_tensor(out=dst[:, kt, :], in0=xx[:, kt, :], scalar=col("rwkv_mu", i * KT + kt), in1=hT[:, kt, :],
                                               op0=ALU.mult, op1=ALU.add)
                m.then_inc(S("mixed"), 1)

            def mix_lo(n, src, k):
                v.wait_ge(S("rkv.xh"), B("rkv.xh") + 2 * n + k + 1)
                o = slice(4 * k, 4 * k + 4)
                v.tensor_tensor(xl[:, o, :], src[:, o, :], f32(xh[:, o, :]), ALU.subtract).then_inc(S("rkv.xl"), 4)

            mix(1, W3(2, KT))
            mix(4, W3(3, KT))
            v.wait_ge(S("rank_T"), B("rank_T") + 1)
            mix(5, W3(2, KT))
            v.wait_ge(S("rank_T"), B("rank_T") + 2)
            mix(2, W3(3, KT))
            mix_lo(0, W3(3, KT), 0)
            mix_lo(0, W3(3, KT), 1)
            split(("k", 0, 0), ("k", 0, 1), ("k", 1, 0))
            v.wait_ge(S("rank_T"), B("rank_T") + 3)
            mix(0, W3(2, KT))
            v.wait_ge(S("rkv.xl"), B("rkv.xl") + 8)
            mix(3, W3(3, KT))
            split(("k", 1, 1), ("r", 0, 0))
            mix_lo(1, W3(2, KT), 0)
            split(("r", 0, 1))
            mix_lo(1, W3(2, KT), 1)
            split(("r", 1, 0))
            r, k, vv, sig, rate, kk = W3(4, NT), W3(5, NT), W3(6, NT), W3(7, NT), W3(8, NT), W3(10, NT)

            def vec(w, off):
                return W(w, off, D).unsqueeze(1).to_broadcast([P, NT, D])

            def heads(ap):
                return ap.rearrange("p t (h c) -> p (t h) c", c=HD)

            def per_head(ap):
                return ap.unsqueeze(2).to_broadcast([P, NT * RH, HD])

            t0 = W3(0, NT)
            v.wait_ge(S("rw_vec"), B("rw_vec") + 48)
            v.wait_ge(S("rkv"), B("rkv") + 4)
            v.wait_ge(S("mixed"), B("mixed") + 6)
            v.tensor_tensor(kk, k, vec(9, 0), ALU.mult).then_inc(S("kk"), 1)
            split(("r", 1, 1))
            v.wait_ge(S("kk_sq"), B("kk_sq") + 1)
            v.tensor_reduce(kss, heads(t0), AX_X, ALU.add).then_inc(S("kk_ss"), 1)
            split(("v", 0, 0))
            v.wait_ge(S("rate"), B("rate") + 4)
            link(v.scalar_tensor_tensor(out=t0, in0=rate, scalar=-1.0, in1=vec(9, D), op0=ALU.add, op1=ALU.mult))
            link(v.scalar_tensor_tensor(out=k, in0=t0, scalar=1.0, in1=k, op0=ALU.add, op1=ALU.mult))
            mix_lo(2, W3(3, KT), 0)
            split(("v", 0, 1))
            mix_lo(2, W3(3, KT), 1)
            v.wait_ge(S("kk_norm"), B("kk_norm") + 1)
            link(v.tensor_scalar(kss, kss, 1e-12, None, ALU.max))
            link(v.reciprocal(kss, kss))
            link(v.tensor_tensor(heads(kk), heads(kk), per_head(kss), ALU.mult))
            link(v.scalar_tensor_tensor(out=rate, in0=kk, scalar=-1.0, in1=rate, op0=ALU.mult, op1=ALU.mult))
            split(("v", 1, 0))
            v.wait_ge(S("rkv"), B("rkv") + 8)
            link(v.tensor_tensor(t0, r, k, ALU.mult))
            link(v.tensor_tensor(t0, t0, side[:, :].unsqueeze(1).to_broadcast([P, NT, D]), ALU.mult))
            v.tensor_reduce(bon, heads(t0), AX_X, ALU.add).then_inc(S("bonus"), 1)
            split(("v", 1, 1))
            bk = wide[:, 2048:3 * 2048].rearrange("p (t q x c) -> p t q x c", t=NT, q=RH // 2, x=2)
            v.wait_ge(S("bonus"), B("bonus") + 1)
            for t in range(NT):
                for c in range(2):
                    n = 2 * t + c
                    o = slice(c * 512, (c + 1) * 512)
                    buf = DECAY_BUF[n % 2]
                    v.wait_ge(S("cum_read"), B("cum_read") + n + 1)
                    v.tensor_tensor(W(buf, 1024, 512), ps[:, 4 + n, :], sig[:, t, o], ALU.subtract).then_inc(S("cum_prev"), 1)
                    pin = W(buf, 512, 512).rearrange("p (q c) -> p q c", c=2 * HD)
                    v.tensor_tensor(t0[:, t, o], r[:, t, o], W(buf, 0, 512), ALU.mult).then_inc(S("scaled"), 1)
                    v.tensor_tensor(bk[:, t, 4 * c:4 * c + 4, 0, :], rate[:, t, o].rearrange("p (q c) -> p q c", c=2 * HD), pin, ALU.mult)\
                     .then_inc(S("scaled"), 1)
                    v.tensor_tensor(bk[:, t, 4 * c:4 * c + 4, 1, :], k[:, t, o].rearrange("p (q c) -> p q c", c=2 * HD), pin, ALU.mult)\
                     .then_inc(S("scaled"), 1)
                    v.wait_ge(S("exps"), B("exps") + n + 1)
                    v.tensor_tensor(kk[:, t, o], kk[:, t, o], W(buf, 1536, 512), ALU.mult).then_inc(S("scaled"), 1)

            tmps = WKV_TMP(W, raw)
            ft = W3(8, 2).rearrange("p a (h c) -> p a h c", h=RH)
            gall = WKV_G(W, side)

            def bank(g, i):
                return ps[:, 4 * (g % 2) + i, :]

            def four(ap):
                return ap.rearrange("p (u c) -> p u c", u=4)

            def grams(g, i):
                b = 4 * (g % 2) + i
                return ps[:, b:b + 2, :].rearrange("p b (u x c) -> p (b u) x c", u=2, x=2)

            def bk_out(g):
                v.wait_ge(S("wkv.T"), B("wkv.T") + g + 1)
                v.tensor_copy(tmps[g % 2]["bk"], bank(g, 1)).then_inc(S("wkv.bk"), 1)

            def mask_b(g):
                tmp, gb = tmps[g % 2], grams(g, 0)
                v.wait_ge(S("wkv.gram"), B("wkv.gram") + 2 * g + 1)
                v.tensor_tensor(four(tmp["xt"]), gb[:, :, 0, :], mask4("diag_st"), ALU.mult)
                v.tensor_tensor(four(tmp["mrb"]), gb[:, :, 1, :], mask4("incl_st"), ALU.mult).then_inc(S("wkv.gb"), 1)

            def mask_k(g):
                tmp, gk = tmps[g % 2], grams(g, 2)
                v.wait_ge(S("wkv.gram"), B("wkv.gram") + 2 * g + 2)
                v.tensor_tensor(four(tmp["gk"]), gk[:, :, 0, :], mask4("strict_st"), ALU.mult)
                v.tensor_tensor(four(tmp["mrk"]), gk[:, :, 1, :], mask4("incl_st"), ALU.mult).then_inc(S("wkv.gk"), 1)

            def mask_b_k(g):
                mask_b(g)
                mask_k(g)

            def mask_x(g):
                tmp, b = tmps[g % 2], 4 * (g % 2)
                x = ps[:, b:b + 2, 0:SEQ].rearrange("p b (u c) -> p b u c", u=2)
                v.wait_ge(S("wkv.gram_ts"), B("wkv.gram_ts") + g + 1)
                v.tensor_tensor(tmp["x"].rearrange("p (b u c) -> p b u c", b=2, u=2), x, mask22("diag_ts"), ALU.mult).then_inc(S("wkv.x"), 1)
                v.tensor_tensor(tmp["off"].rearrange("p (b u c) -> p b u c", b=2, u=2), x, mask22("off_ts"), ALU.mult)
                v.wait_ge(S("wkv.gb"), B("wkv.gb") + g + 1)
                v.tensor_tensor(four(tmp["tt"]), four(tmp["xt"]), mask4("ident"), ALU.add).then_inc(S("wkv.t1"), 1)

            def add_to(sem, b, dst, base, done, before=None):
                def step(g):
                    if before:
                        v.wait_ge(S("wkv." + before), B("wkv." + before) + g + 1)
                    v.wait_ge(S("wkv." + sem), B("wkv." + sem) + g + 1)
                    v.tensor_tensor(tmps[g % 2][dst], tmps[g % 2][base], bank(g, b), ALU.add).then_inc(S("wkv." + done), 1)
                return step

            def state_out(g):
                t, h0 = g // 4, HEAD0(g)
                b = bank(g, 3 - t)
                v.wait_ge(S("wkv.fg"), B("wkv.fg") + g + 1)
                v.tensor_tensor(ft[0:64, t, h0:h0 + 4, :], b[0:64, SEQ:2 * SEQ].rearrange("p (u c) -> p u c", u=4),
                                masks[0:64, 0:64].unsqueeze(1).to_broadcast([64, 4, 64]), ALU.add)
                v.tensor_copy(gall[1 + t][0:64, h0:h0 + 4, :], b[0:64, 0:SEQ].rearrange("p (u c) -> p u c", u=4))

            def e_out(g):
                t, h0 = g // 4, HEAD0(g)
                e2 = wide[:, 2048:3 * 2048].rearrange("p (t h x c) -> p t h x c", t=NT, h=RH, x=2)[:, t, h0:h0 + 4, :, :]
                ep = bank(g, 0)[0:64, :].rearrange("p (u x c) -> p u x c", u=4, x=2)
                v.wait_ge(S("wkv.eh"), B("wkv.eh") + g + 1)
                v.memset(e2[0:64, :, 1, :], 0.0)
                v.memset(e2[64:128, :, 0, :], 0.0)
                v.tensor_copy(e2[0:64, :, 0, :], ep[:, :, 0, :])
                v.tensor_copy(e2[64:128, :, 1, :], ep[:, :, 1, :]).then_inc(S("wkv.done"), 1)

            for pair in range(4):
                for step in (bk_out, mask_b_k, mask_x, add_to("t2", 1, "tt", "tt", "t2c", "t1"),
                             add_to("t4", 1, "tt", "tt", "t4c", "t2c"), add_to("t8", 1, "tt", "tt", "t8c", "t4c"),
                             add_to("r2", 1, "r2", "r1", "r2c", "r1c"), add_to("r3", 0, "r2", "r1", "r3c"),
                             add_to("r4", 1, "r2", "r1", "r4c"), state_out, e_out):
                    step(2 * pair)
                    step(2 * pair + 1)

            chain = W(5, 0, D).rearrange("p (h c) -> p h c", h=RH)
            ctmp = W(5, D, D).rearrange("p (h c) -> p h c", h=RH)
            pch = pc.rearrange("p (h c) -> p h c", c=4)

            def decay(c):
                return pch[0:64, :, c:c + 1].to_broadcast([64, RH, HD])

            v.wait_ge(S("pc"), B("pc") + 2)
            v.wait_ge(S("wkv.hc"), B("wkv.hc") + 8)
            v.tensor_tensor(chain[0:64], gall[0][0:64], decay(0), ALU.mult).then_inc(S("state"), 1)
            for c in (1, 2):
                v.wait_ge(S("state_F"), B("state_F") + c)
                for b in range(2):
                    m = v.tensor_tensor(ctmp[0:64, 8 * b:8 * b + 8, :], ps[0:64, b, :].rearrange("p (h c) -> p h c", c=HD),
                                        gall[c][0:64, 8 * b:8 * b + 8, :], ALU.add)
                link(m)
                v.wait_ge(S("state_put"), B("state_put") + c)
                v.tensor_tensor(chain[0:64], ctmp[0:64], decay(c), ALU.mult).then_inc(S("state"), 1)
            split(("o", 0, 0))
            y, sq, gate, bterm = W3(0, NT), W3(5, NT), W3(7, NT), W3(6, NT)

            def of_heads(t):
                return y[:, t, :].rearrange("p (h c) -> p h c", c=HD)

            def per_head_of(ap, t):
                return ap[:, t * RH:(t + 1) * RH].unsqueeze(2).to_broadcast([P, RH, HD])

            def centre(t):
                v.wait_ge(S("y_T"), B("y_T") + t + 1)
                for c in range(2):
                    o = slice(c * 512, (c + 1) * 512)
                    v.tensor_tensor(y[:, t, o], y[:, t, o], ps[:, Y_BANK[t] + c, :], ALU.add).then_inc(S("ysum"), 1)
                v.wait_ge(S("ysum"), B("ysum") + 2 * (t + 1))
                link(v.tensor_reduce(mean[:, t * RH:(t + 1) * RH], of_heads(t), AX_X, ALU.add))
                v.scalar_tensor_tensor(out=of_heads(t), in0=per_head_of(mean, t), scalar=-1.0 / HD, in1=of_heads(t),
                                       op0=ALU.mult, op1=ALU.add).then_inc(S("centred"), 1)

            def variance(t):
                hs = slice(t * RH, (t + 1) * RH)
                v.wait_ge(S("gn_sq"), B("gn_sq") + t + 1)
                link(v.tensor_reduce(gvar[:, hs], sq[:, t, :].rearrange("p (h c) -> p h c", c=HD), AX_X, ALU.add))
                v.tensor_scalar(gvar[:, hs], gvar[:, hs], 1.0 / HD, GN_EPS, ALU.mult, ALU.add).then_inc(S("gn_var"), 1)

            def gated(t):
                hs = slice(t * RH, (t + 1) * RH)
                v.wait_ge(S("gn_std"), B("gn_std") + t + 1)
                link(v.reciprocal(gvar[:, hs], gvar[:, hs]))
                v.wait_ge(S("centred"), B("centred") + t + 1)
                link(v.tensor_tensor(of_heads(t), of_heads(t), per_head_of(gvar, t), ALU.mult))
                v.wait_ge(S("fold"), B("fold") + 2 * t + 4)
                link(v.tensor_tensor(y[:, t, :], y[:, t, :], gate[:, t, :], ALU.mult))
                v.tensor_tensor(y[:, t, :], y[:, t, :], bterm[:, t, :], ALU.add).then_inc(S("y_gated"), 1)

            centre(0)
            split(("o", 0, 1))
            variance(0)
            centre(1)
            gated(0)
            variance(1)
            gated(1)
            copy_lo("rw", RW_BANKS)
            split(("o", 1, 0))
            split(("o", 1, 1))
            add_linear("o", "mix1.add")

            norm("ffn1")
            split_lo(0, plan.at["ffn1"][0][0])
            norm_lo("ffn1", "ffn_norm", KT)
            split_lo(1, plan.at["ffn1"][0][1])
            v.wait_ge(S("c_act"), B("c_act") + 1)
            v.wait_ge(S("acc_bias"), B("acc_bias") + 16)
            ffn_loop("ffn1", plan.at["ffn1"][0], (5, 6, 7))
            v.wait_ge(w_used[0], plan.at["ffn1"][0][0] + NFFN + 1)
            add_residual("ffn1.add")

            norm_factors("fin")
            v.wait_ge(S("fin_vec"), B("fin_vec") + 16)
            for t in range(NT):
                v.scalar_tensor_tensor(out=h[:, t, :], in0=h[:, t, :], scalar=nrs["fin"][:, t:t + 1], in1=W(8, 0, D),
                                       op0=ALU.mult, op1=ALU.mult).then_inc(S("fin.h"), 1)
            v.wait_ge(S("fin.h"), B("fin.h") + 2)
            norm("pre")
            split(("glu", 0, 0))
            def modulation(n, scale, gain):
                o = slice(16 * n, 16 * n + 16)
                v.wait_ge(S("mod_T"), B("mod_T") + n + 1)
                v.tensor_copy(modc[:, o], ps[:, 2 * n, 0:16]).then_inc(S("modc"), 1)
                v.wait_ge(S("modc"), B("modc") + n + 1)
                link(v.scalar_tensor_tensor(out=scale, in0=modc[:, 16 * n + 8:16 * n + 16], scalar=1.0,
                                            in1=cols[:, ROWS[gain]:ROWS[gain] + 8], op0=ALU.add, op1=ALU.mult))
            modulation(0, sc1, "g_pre_mix_2")
            norm_modulated("pre", sc1, modc[:, 0:8])
            modulation(1, sc2, "g_pre_mlp_2")
            split(("glu", 0, 1), ("glu", 1, 0))
            v.wait_ge(S("pos"), B("pos") + 16)
            link(v.tensor_copy(posf, posi[:, :]))
            freq = masks[:, MFREQ:MFREQ + 32]
            ang = lowr[:, 128:192]
            turns = lowr[:, 192:256]
            for t in range(NT):
                m = v.tensor_scalar(ang[:, t * 32:(t + 1) * 32], freq, posf[:, t:t + 1], None, ALU.mult)
            link(m)
            link(v.tensor_scalar(turns, ang, float(1 / (2 * np.pi)), 12582912.0, ALU.mult, ALU.add))
            link(v.tensor_scalar(turns, turns, 12582912.0, None, ALU.subtract))
            for part in (6.28125, 0.0019340515136718750, float(2 * np.pi - 6.28125 - 0.0019340515136718750)):
                link(v.scalar_tensor_tensor(out=ang, in0=turns, scalar=-part, in1=ang, op0=ALU.mult, op1=ALU.add))
            link(v.tensor_scalar(lowr[:, 0:64], ang, -3.1415925, 3.1415925, ALU.max, ALU.min))
            link(v.scalar_tensor_tensor(out=ang, in0=lowr[:, 0:64], scalar=-1.0, in1=lowr[:, 0:64], op0=ALU.mult, op1=ALU.max))
            v.tensor_scalar(lowr[:, 64:128], ang, -1.0, float(np.pi / 2), ALU.mult, ALU.add).then_inc(S("angle"), 1)
            ub = lowr[:, 512:1024].rearrange("p (t n) -> p t n", t=NT)
            upad = U_PAD(wide)
            gb1, gb2 = GB1(W), side
            nxt = [("glu", 1, 1), ("glu", 2, 0), ("glu", 2, 1), ("glu", 3, 0), ("glu", 3, 1), ("lat", 0, 0), ("lat", 0, 1), ("lat", 1, 0)]
            for c in range(4):
                for t in range(NT):
                    v.wait_ge(S("glu_s"), B("glu_s") + 2 * c + t + 1)
                    v.tensor_tensor(W(U_AT[c][0], U_AT[c][1] + t * 256, 256), ps[:, 2 * (c % 2) + t, 0:256], ub[:, t, :], ALU.mult)\
                     .then_inc(S("glu"), 1)
                split(*nxt[2 * c:2 * c + 2])
                if c == 0:
                    v.wait_ge(S("gates_T"), B("gates_T") + 1)
                    v.wait_ge(S("post_vec"), B("post_vec") + 32)
                    for n, dst in enumerate((gb1, gb2)):
                        for b in range(2):
                            o = slice(b * 512, (b + 1) * 512)
                            v.tensor_tensor(dst[:, o], ps[:, 4 + 2 * n + b, :], W(6, n * D + b * 512, 512), ALU.mult).then_inc(S("gates"), 1)
            split(("lat", 1, 1), ("gate", 0, 0), ("gate", 0, 1))
            lat = W(3, 0, 2 * 704).rearrange("p (t n) -> p t n", t=NT)
            v.wait_ge(S("lat"), B("lat") + 4)
            for t in range(NT):
                mean_square(lat[:, t, 0:QL], QL, qss[:, t:t + 1], W(2, t * D, QL))
                m = mean_square(lat[:, t, QL:QL + KL], KL, qss[:, 2 + t:3 + t], W(2, t * D + 512, KL))
            m.then_inc(S("lat_ss"), 1)
            v.memset(upad[:, :, 0:CK - 1], 0.0)
            split(("gate", 1, 0))
            v.wait_ge(S("lat_std"), B("lat_std") + 1)
            link(v.reciprocal(qrs, qsd))
            for t in range(NT):
                v.tensor_scalar(lat[:, t, 0:QL], lat[:, t, 0:QL], qrs[:, t:t + 1], None, ALU.mult).then_inc(S("lat_n"), 1)
                v.tensor_scalar(lat[:, t, QL:QL + KL], lat[:, t, QL:QL + KL], qrs[:, 2 + t:3 + t], None, ALU.mult).then_inc(S("lat_n"), 1)
            cv = W3(2, KT)
            n_dve = KT - CONV_PE
            taps = [(kt, k) for tiles in ((0, 1), range(2, n_dve)) for k in range(CK) for kt in tiles]
            step_of = {tap: n + 1 for n, tap in enumerate(taps)}

            def conv(n):
                for _ in range(min(n, len(taps))):
                    kt, k = taps.pop(0)
                    w = cols[:, CONVW + kt * CK + k:CONVW + kt * CK + k + 1]
                    src = upad[:, kt, k:k + SEQ]
                    if k == 0:
                        m = v.tensor_scalar(cv[:, kt, :], src, w, col("conv_b_2", kt), ALU.mult, ALU.add)
                    else:
                        v.wait_ge(S("conv_step"), B("conv_step") + step_of[kt, k - 1])
                        m = v.scalar_tensor_tensor(out=cv[:, kt, :], in0=src, scalar=w, in1=cv[:, kt, :], op0=ALU.mult, op1=ALU.add)
                    m.then_inc(S("conv_step"), 1)
            v.wait_ge(S("u_put"), B("u_put") + 4)
            for name in [("gate", 1, 1), ("gate", 2, 0), ("gate", 2, 1), ("gate", 3, 0), ("gate", 3, 1), ("uq", 0)]:
                split(name)
                conv(7)
            for b in range(3):
                v.wait_ge(S("lq.xh"), B("lq.xh") + min(2 * b + 2, 5))
                for kt in range(2 * b, min(2 * b + 2, 5)):
                    v.scalar_tensor_tensor(out=xl[:, kt, :], in0=ps[:, 4 + b, (kt % 2) * SEQ:(kt % 2 + 1) * SEQ],
                                           scalar=col("q_norm_g_2", kt) if kt < 3 else col("kv_norm_g_2", kt - 3), in1=f32(xh[:, kt, :]),
                                           op0=ALU.mult, op1=ALU.subtract).then_inc(S("lq.xl"), 1)
            for name in [("uq", 1), ("uq", 2)]:
                split(name)
                conv(7)
            for name in [("uq", 3), ("ukv", 0), ("ukv", 1)]:
                conv(9)
                split(name)
            qraw = W(8, 0, 2 * 9 * 64).rearrange("p (t n) -> p t n", t=NT)
            ro = W(3, 0, 1280).rearrange("p (t n) -> p t n", t=NT)
            v.wait_ge(S("qraw"), B("qraw") + 2)
            v.wait_ge(S("lq.T"), B("lq.T") + 3)
            for t in range(NT):
                m = v.tensor_copy(qraw[:, t, 512:576], lat[:, t, QL + KL:704])
            link(m)
            v.wait_ge(S("sincos"), B("sincos") + 1)
            ropet = W(10, 0, 2 * 288)
            for t in range(NT):
                src = qraw[:, t, :].rearrange("p (h x c) -> p h x c", x=2, c=32)
                dst = ro[:, t, 0:576].rearrange("p (h x c) -> p h x c", x=2, c=32)
                sn = lowr[:, t * 32:(t + 1) * 32].unsqueeze(1).to_broadcast([P, 9, 32])
                cs = lowr[:, 64 + t * 32:64 + (t + 1) * 32].unsqueeze(1).to_broadcast([P, 9, 32])
                ta = ropet[:, 0:288].rearrange("p (h c) -> p h c", c=32)
                tb = ropet[:, 288:576].rearrange("p (h c) -> p h c", c=32)
                v.tensor_tensor(dst[:, :, 0, :], src[:, :, 0, :], cs, ALU.mult)
                v.tensor_tensor(dst[:, :, 1, :], src[:, :, 1, :], cs, ALU.mult)
                v.tensor_tensor(ta, src[:, :, 1, :], sn, ALU.mult)
                link(v.tensor_tensor(tb, src[:, :, 0, :], sn, ALU.mult))
                v.tensor_tensor(dst[:, :, 0, :], dst[:, :, 0, :], ta, ALU.subtract)
                link(v.tensor_tensor(dst[:, :, 1, :], dst[:, :, 1, :], tb, ALU.add))
                v.tensor_copy(ro[:, t, 576:640], ro[:, t, 512:576]).then_inc(S("roped"), 1)
            split(("attn_out", 0, 0), ("attn_out", 0, 1))
            conv(10)
            pp = [W3(10, NT, 512 * b, 512) for b in range(2)]
            causal = masks[:, MI["causal"]:MI["causal"] + P]

            def finish(i):
                b = i % 2
                v.wait_ge(S("at.e"), B("at.e") + 2 * (i + 1))
                link(v.reciprocal(arec[:, 2 * b:2 * b + 2], asum[:, 2 * b:2 * b + 2]))
                for t in range(NT):
                    nk = P * (t + 1)
                    v.tensor_scalar(pp[b][:, t, 0:nk], pp[b][:, t, 0:nk], arec[:, 2 * b + t:2 * b + t + 1], None, ALU.mult)\
                     .then_inc(S("at.p"), 1)

            def out_lo(i):
                v.wait_ge(S("at.xh"), B("at.xh") + i + 1)
                v.tensor_tensor(xl[:, i, :], ps[:, 4 + i % 2, 0:SEQ], f32(xh[:, i, :]), ALU.subtract).then_inc(S("at.xl"), 1)

            for i in range(NH):
                b = i % 2
                v.wait_ge(S("at.s"), B("at.s") + i + 1)
                if i >= 2:
                    v.wait_ge(S("at.T"), B("at.T") + i - 1)
                v.scalar_tensor_tensor(out=pp[b][:, 0, 0:P], in0=ps[:, b, 0:P], scalar=SCALE, in1=causal, op0=ALU.mult, op1=ALU.add)
                v.tensor_scalar(pp[b][:, 1, 0:P], ps[:, b, SEQ:SEQ + P], SCALE, None, ALU.mult).then_inc(S("at.sc"), 1)
                v.scalar_tensor_tensor(out=pp[b][:, 1, P:SEQ], in0=ps[:, b, SEQ + P:2 * SEQ], scalar=SCALE, in1=causal, op0=ALU.mult,
                                       op1=ALU.add).then_inc(S("at.sc"), 1)
                v.wait_ge(S("at.sc"), B("at.sc") + 2 * (i + 1))
                for t in range(NT):
                    m = v.tensor_reduce(amax[:, 2 * b + t:2 * b + t + 1], pp[b][:, t, 0:P * (t + 1)], AX_X, ALU.max)
                link(m)
                v.tensor_scalar(amax[:, 2 * b:2 * b + 2], amax[:, 2 * b:2 * b + 2], -1.0, None, ALU.mult).then_inc(S("at.max"), 1)
                conv(3)
                finish(i)
                if i == 1:
                    split(("attn_out", 1, 0))
                conv(4 if i == 1 else 9)
                if i:
                    out_lo(i - 1)
            out_lo(NH - 1)
            conv(len(taps))
            split(("attn_out", 1, 1))
            v.wait_ge(S("cmean"), B("cmean") + 1)
            cmean = lowr[:, 512:768]
            link(v.tensor_scalar(cmean, ps[:, 4, 0:SEQ], 1.0 / D, None, ALU.mult))
            for k in range(2):
                o = slice(4 * k, 4 * k + 4)
                v.tensor_tensor(cv[:, o, :], cv[:, o, :], cmean.unsqueeze(1).to_broadcast([P, 4, SEQ]), ALU.subtract).then_inc(S("cv_c"), 1)
            split(("conv_out", 0, 0))
            v.wait_ge(S("cvar"), B("cvar") + 1)
            v.tensor_scalar(lowr[:, 256:512], ps[:, 5, 0:SEQ], 1.0 / D, EPS, ALU.mult, ALU.add).then_inc(S("cv_ss"), 1)
            v.wait_ge(S("cv_std"), B("cv_std") + 1)
            link(v.reciprocal(lowr[:, 768:1024], lowr[:, 256:512]))
            for k in range(2):
                o = slice(4 * k, 4 * k + 4)
                v.tensor_tensor(cv[:, o, :], cv[:, o, :], lowr[:, 768:1024].unsqueeze(1).to_broadcast([P, 4, SEQ]), ALU.mult).then_inc(S("cv_n"), 1)
            gates = wide[:, 6 * 2048:8 * 2048].rearrange("p (t n) -> p t n", t=NT)
            ym = W3(9, NT)

            def attention_gated(c):
                used(v, ("attn_out", c, 1))
                for t in range(NT):
                    o = slice(c * 512, (c + 1) * 512)
                    v.tensor_tensor(ym[:, t, o], ps[:, 2 * c + t, :], gates[:, t, D + c * 512:D + (c + 1) * 512], ALU.mult)\
                     .then_inc(S("yb"), 1)
            attention_gated(0)
            for k in range(2):
                v.wait_ge(S("cv.xh"), B("cv.xh") + k + 1)
                o = slice(4 * k, 4 * k + 4)
                v.tensor_tensor(xl[:, o, :], cv[:, o, :], f32(xh[:, o, :]), ALU.subtract).then_inc(S("cv.xl"), 4)
            split(("conv_out", 0, 1))
            attention_gated(1)
            split(("conv_out", 1, 0), ("conv_out", 1, 1))
            for c in range(2):
                if c:
                    split(("out", 0, 0), ("out", 0, 1))
                used(v, ("conv_out", c, 1))
                for t in range(NT):
                    o = slice(c * 512, (c + 1) * 512)
                    g_ = gates[:, t, c * 512:(c + 1) * 512]
                    link(v.tensor_tensor(g_, ps[:, 2 * c + t, :], g_, ALU.mult))
                    v.tensor_tensor(ym[:, t, o], ym[:, t, o], g_, ALU.add).then_inc(S("ymix"), 1)
            copy_lo("ym", (4, 5, 6, 7))
            split(("out", 1, 0), ("out", 1, 1))
            def post(name, src, gb, ready):
                for c in range(2):
                    ready(c)
                for t in range(NT):
                    v.wait_ge(S(name + ".std"), B(name + ".std") + t + 1)
                    link(v.reciprocal(nrs[name][:, t:t + 1], nsd[name][:, t:t + 1]))
                    v.scalar_tensor_tensor(out=hn[:, t, :].rearrange("p (b n) -> p b n", b=2), in0=src(t), scalar=nrs[name][:, t:t + 1],
                                           in1=gb.rearrange("p (b n) -> p b n", b=2), op0=ALU.mult, op1=ALU.mult).then_inc(S(name + ".hn"), 1)
                    v.wait_ge(S(name + ".hn"), B(name + ".hn") + t + 1)
                    v.tensor_tensor(h[:, t, :], h[:, t, :], hn[:, t, :], ALU.add).then_inc(S(name + ".add"), 1)
                v.wait_ge(S(name + ".add"), B(name + ".add") + 2)
            post("post1", POST(ps), gb1, lambda c: used(v, ("out", c, 1)))
            norm("pre2")
            split_lo(0, plan.at["mlp"][0][0])
            norm_modulated("pre2", sc2, modc[:, 16:24])
            mlp_loop()
            v.wait_ge(w_used[0], plan.at["mlp"][0][0] + NMLP // 2 + 1)
            post("post2", POST(ps), gb2[:, :], lambda c: None)


U_AT = ((8, 0), (8, 512), (8, 1024), (8, 1536))


def GB1(W):
    return W(10, 1024, D)


GATE_BANK, Y_BANK, RW_BANKS = (6, 2), (4, 0), (6, 7, 2, 3)
DECAY_BUF = (3, 9)
UKV_BANK = (4, 0)


def FFN_BANK(i):
    return 0 if isinstance(i, int) and i == 0 else 4


def U_PAD(wide):
    n = SEQ + CK - 1
    return wide[:, 0:KT * n].rearrange("p (a n) -> p a n", a=KT)


CONV_PE = 2
PE_TAPS = [(kt, k) for kt in range(KT - CONV_PE, KT) for k in range(CK)]
TAP_BATCH = -(-len(PE_TAPS) // NH)


def CONV_OUT(ps, kt):
    b, o = divmod(kt - KT + 4, 2)
    return ps[:, 6 + b, o * SEQ:(o + 1) * SEQ]


def DIAGS(W, lowr):
    one = [W(3, o, P) for o in range(0, TAP_BATCH * P, P)]
    return one, [W(8, o, P) for o in range(0, 1024, P)] + [lowr[:, 512 + o:512 + o + P] for o in range(0, 512, P)]



def POST(ps):
    return lambda t: ps[:, 2 * t:2 * t + 2, :]


def HEAD0(g):
    return 4 * (g % 4)


def HN(n):
    return 2 * (n % 2) + n // 2


def HEAD(g, h):
    c = (g // 4) * D + h * HD
    return c, c + HD


def BK(wide, g, h, x, n):
    c = 2048 + (((g // 4) * (RH // 2) + h // 2) * 2 + x) * P + (h % 2) * HD
    return wide[:, c:c + n]


def WKV_TMP(W, raw):
    sets = []
    spots = [W(w, o, 512) for w in (4, 5, 7) for o in range(0, 2048, 512)]
    spots2 = [raw[:, i, o:o + 512] for i in range(3) for o in range(0, 2048, 512)]
    names = ("ar", "bk", "x", "xt", "off", "mrb", "gk", "mrk", "tt", "x2", "x2t", "gkv")
    for s in (spots, spots2):
        t = dict(zip(names, s))
        t["x4"], t["x4t"], t["x8"], t["mt"], t["r1"], t["r2"] = t["x"], t["xt"], t["x2"], t["x2t"], t["ar"], t["bk"]
        sets.append(t)
    return sets


def WKV_G(W, side):
    aps = (W(3, 0, D), W(3, D, D), side[:, :])
    return [a.rearrange("p (h c) -> p h c", h=RH) for a in aps]


INS = ["x", "final_norm", "ab_w_in", "ab_w_out", "sgu_gain", "sgu_w_s", "pool_w", "rwkv_w_r", "rwkv_w_k", "rwkv_w_v",
       "rwkv_w_o", "rwkv_w0", "rwkv_w1", "rwkv_w2", "rwkv_a0", "rwkv_a1", "rwkv_a2", "rwkv_g1", "rwkv_g2", "rwkv_k_k",
       "rwkv_k_a", "rwkv_r_k", "rwkv_ln_w", "rwkv_ln_b", "ffn_w_gate", "ffn_w_up", "ffn_w_down", "c_2", "positions_2",
       "w_ada_2", "b_ada_2", "g_post_mix_2", "g_post_mlp_2", "w_in_2", "conv_w_2", "w_conv_out_2", "w_uq_2",
       "w_ukv_2", "w_attn_out_2", "w_out_2", "w_mlp_in_2", "w_mlp_out_2"]


def kernel(**inputs):
    import concourse.bacc as bacc
    from concourse.bass_utils import run_bass_kernel_spmd

    nc = bacc.Bacc("TRN2", target_bir_lowering=False, num_devices=1)
    arrays, aps = {}, {}
    for name in INS:
        a = np.ascontiguousarray(inputs[name])
        arrays[f"in_{name}"] = a
        aps[name] = nc.dram_tensor(f"in_{name}", a.shape, mybir.dt.from_np(a.dtype), kind="ExternalInput").ap()
    a = np.concatenate([np.reshape(inputs[name], (-1, P)) for name, _ in VECTORS])
    arrays["vectors"] = a
    aps["vectors"] = nc.dram_tensor("vectors", a.shape, F32, kind="ExternalInput").ap()
    consts = []
    for name, a in zip(("const_masks", "const_pool"), constants()):
        arrays[name] = a
        consts.append(nc.dram_tensor(name, a.shape, F32, kind="ExternalInput").ap())
    out = nc.dram_tensor("out", (1, SEQ, D), F32, kind="ExternalOutput").ap()
    build(nc, aps, *consts, out)
    r = run_bass_kernel_spmd(nc, [arrays], core_ids=[0])
    return r.results[0]["out"]
```
